# Optimizing a Trainium2 kernel written in Bass

```python
import math
import jax
import jax.numpy as jnp
from jax import lax
import numpy as np
import jax, jax.numpy as jnp

D_MODEL = 1024
BATCH = 1
SEQ = 1024
DEPTH = 1

CHUNK = 64
MAX_STREAM_CHUNKS = 64
POOL_WINDOWS = (2, 4, 8, 16)
POOL_GROUPS = len(POOL_WINDOWS)
D_POOL = D_MODEL // 2
POOL_GW = D_POOL // POOL_GROUPS
D_CONV = D_MODEL // 2
CONV_WIDTH = 31
N_HEADS = 8
QK_NOPE = 64
QK_ROPE = 32
V_HEAD = 64
Q_LORA = 384
KV_LORA = 256
ROPE_THETA = 10000.0
Q_BLOCK = 128
N_BRANCH = 3
OFF_CONV = D_POOL
OFF_Q = OFF_CONV + 2 * D_CONV
OFF_KV = OFF_Q + Q_LORA
OFF_KR = OFF_KV + KV_LORA
OFF_GATE = OFF_KR + QK_ROPE
D_IN = OFF_GATE + N_BRANCH * D_MODEL
IN_SPLITS = (OFF_CONV, OFF_Q, OFF_KV, OFF_KR, OFF_GATE)
N_EXPERTS = 16
N_GROUPS = 4
EXPERTS_PER_GROUP = N_EXPERTS // N_GROUPS
TOPK_GROUPS = 1
TOP_K = 2
D_EXPERT = 512
MOE_BLOCK = 128
D_PLE = 256
DEEPNORM_ALPHA = (2 * DEPTH) ** 0.25
DEEPNORM_BETA = (8 * DEPTH) ** -0.25
LN_EPS = 1e-5
RMS_EPS = 1e-6


def layer_norm(x, g, b):
    xf = x.astype(jnp.float32)
    mu = jnp.mean(xf, axis=-1, keepdims=True)
    xc = xf - mu
    var = jnp.mean(xc * xc, axis=-1, keepdims=True)
    return (xc * lax.rsqrt(var + LN_EPS) * g.astype(jnp.float32) + b.astype(jnp.float32)).astype(x.dtype)

def rms_norm(x, g):
    xf = x.astype(jnp.float32)
    ms = jnp.mean(xf * xf, axis=-1, keepdims=True)
    return (xf * lax.rsqrt(ms + RMS_EPS) * g.astype(jnp.float32)).astype(x.dtype)

def rope_tables(positions):
    inv_freq = jnp.power(ROPE_THETA, -jnp.arange(0, QK_ROPE, 2, dtype=jnp.float32) / QK_ROPE)
    ang = positions.astype(jnp.float32)[..., None] * inv_freq
    return jnp.cos(ang), jnp.sin(ang)

def apply_rope(x, cos, sin):
    cos = cos.astype(x.dtype)
    sin = sin.astype(x.dtype)
    x1, x2 = jnp.split(x, 2, axis=-1)
    return jnp.concatenate([x1 * cos - x2 * sin, x2 * cos + x1 * sin], axis=-1)

def pool_mixer(u, w_grp, scale):
    B, S, C = u.shape
    uf = u.astype(jnp.float32)
    cs = jnp.cumsum(uf, axis=1)
    t = jnp.arange(S)
    means = []
    for g, w in enumerate(POOL_WINDOWS):
        csg = cs[..., g * POOL_GW:(g + 1) * POOL_GW]
        lag = jnp.pad(csg[:, :S - w], ((0, 0), (w, 0), (0, 0)))
        cnt = jnp.minimum(t + 1, w).astype(jnp.float32)[None, :, None]
        means.append((csg - lag) / cnt)
    mixed = (jnp.concatenate(means, axis=-1) - uf).astype(u.dtype)
    mixed = jnp.einsum('bsgc,gcd->bsgd', mixed.reshape(B, S, POOL_GROUPS, POOL_GW), w_grp)
    return mixed.reshape(B, S, C) * scale

def conv_module(u2, dw, db, g, b):
    a, gate = jnp.split(u2, 2, axis=-1)
    z = a * jax.nn.sigmoid(gate)
    z = lax.conv_general_dilated(z, dw[:, None, :], window_strides=(1,),
                                 padding=[(CONV_WIDTH - 1, 0)],
                                 dimension_numbers=('NWC', 'WIO', 'NWC'),
                                 feature_group_count=D_CONV) + db
    return jax.nn.silu(layer_norm(z, g, b))

def chunk_causal_attention(q, k, v):
    B, S, H, Dk = q.shape
    nq = S // Q_BLOCK
    scale = Dk ** -0.5
    qb = q.reshape(B, nq, Q_BLOCK, H, Dk).transpose(1, 0, 2, 3, 4)
    key_chunk = jnp.arange(S) // CHUNK

    def block(args):
        qi, i = args
        s = jnp.einsum('bqhd,bkhd->bhqk', qi, k, preferred_element_type=jnp.float32) * scale
        q_chunk = (i * Q_BLOCK + jnp.arange(Q_BLOCK)) // CHUNK
        mask = key_chunk[None, :] <= q_chunk[:, None]
        pr = jax.nn.softmax(jnp.where(mask, s, -jnp.inf), axis=-1).astype(v.dtype)
        return jnp.einsum('bhqk,bkhd->bqhd', pr, v)

    o = lax.map(block, (qb, jnp.arange(nq)))
    return o.transpose(1, 0, 2, 3, 4).reshape(B, S, H, v.shape[-1])

def mla(c_q, c_kv, k_r, cos, sin, q_norm_g, w_uq, kv_norm_g, w_ukv):
    B, S, _ = c_q.shape
    q = jnp.matmul(rms_norm(c_q, q_norm_g), w_uq).reshape(B, S, N_HEADS, QK_NOPE + QK_ROPE)
    q_nope, q_rope = q[..., :QK_NOPE], q[..., QK_NOPE:]
    q_rope = apply_rope(q_rope, cos[:, :, None, :], sin[:, :, None, :])
    kv = jnp.matmul(rms_norm(c_kv, kv_norm_g), w_ukv).reshape(B, S, N_HEADS, QK_NOPE + V_HEAD)
    k_nope, v = kv[..., :QK_NOPE], kv[..., QK_NOPE:]
    k_rope = apply_rope(k_r, cos, sin)
    qf = jnp.concatenate([q_nope, q_rope], axis=-1)
    kf = jnp.concatenate([k_nope, jnp.broadcast_to(k_rope[:, :, None, :], (B, S, N_HEADS, QK_ROPE))], axis=-1)
    o = chunk_causal_attention(qf, kf, v)
    return o.reshape(B, S, N_HEADS * V_HEAD)

def mixer_sublayer(h, cos, sin, w_in, b_gate, pool_w, pool_scale, pool_proj, conv_dw, conv_b,
                   conv_ln_g, conv_ln_b, conv_proj, q_norm_g, w_uq, kv_norm_g, w_ukv, mla_proj, w_out):
    B, S, D = h.shape
    proj = jnp.matmul(h, w_in)
    u_pool, u_conv, c_q, c_kv, k_r, g_logits = jnp.split(proj, IN_SPLITS, axis=-1)
    gates = jax.nn.sigmoid(g_logits.reshape(B, S, N_BRANCH, D) + b_gate)
    y_pool = jnp.matmul(pool_mixer(u_pool, pool_w, pool_scale), pool_proj)
    y_conv = jnp.matmul(conv_module(u_conv, conv_dw, conv_b, conv_ln_g, conv_ln_b), conv_proj)
    y_mla = jnp.matmul(mla(c_q, c_kv, k_r, cos, sin, q_norm_g, w_uq, kv_norm_g, w_ukv), mla_proj)
    merged = gates[:, :, 0] * y_pool + gates[:, :, 1] * y_conv + gates[:, :, 2] * y_mla
    return jnp.matmul(merged, w_out)

def moe_ffn(h, w_router, router_bias, w_up, w_down):
    B, S, D = h.shape
    T = B * S
    A = T * TOP_K
    xt = h.reshape(T, D)
    aff = jax.nn.sigmoid(jnp.matmul(xt, w_router).astype(jnp.float32))
    sel = aff + router_bias.astype(jnp.float32)
    grp_score = jnp.sum(lax.top_k(sel.reshape(T, N_GROUPS, EXPERTS_PER_GROUP), TOP_K)[0], axis=-1)
    _, g_idx = lax.top_k(grp_score, TOPK_GROUPS)
    g_keep = jnp.any(jnp.arange(N_GROUPS)[None, None, :] == g_idx[:, :, None], axis=1)
    e_keep = jnp.repeat(g_keep, EXPERTS_PER_GROUP, axis=-1)
    _, e_idx = lax.top_k(jnp.where(e_keep, sel, -jnp.inf), TOP_K)
    w = jnp.take_along_axis(aff, e_idx, axis=-1)
    w = w / jnp.sum(w, axis=-1, keepdims=True)
    n_slots = ((A + N_EXPERTS * MOE_BLOCK + MOE_BLOCK - 1) // MOE_BLOCK) * MOE_BLOCK
    n_blocks = n_slots // MOE_BLOCK
    flat_e = e_idx.reshape(A)
    order = jnp.argsort(flat_e)
    s_e = flat_e[order]
    s_tok = (order // TOP_K).astype(jnp.int32)
    s_w = w.reshape(A)[order]
    counts = jnp.bincount(flat_e, length=N_EXPERTS)
    start = jnp.cumsum(counts) - counts
    padded = (counts + MOE_BLOCK - 1) // MOE_BLOCK * MOE_BLOCK
    pad_end = jnp.cumsum(padded)
    pad_start = pad_end - padded
    dest = pad_start[s_e] + jnp.arange(A) - start[s_e]
    slot_tok = jnp.full((n_slots,), T, jnp.int32).at[dest].set(s_tok)
    slot_w = jnp.zeros((n_slots,), jnp.float32).at[dest].set(s_w)
    blk_e = jnp.minimum(jnp.searchsorted(pad_end, jnp.arange(n_blocks) * MOE_BLOCK, side='right'),
                        N_EXPERTS - 1)
    xs = jnp.concatenate([xt, jnp.zeros((1, D), xt.dtype)], axis=0)[slot_tok]
    xs = xs.reshape(n_blocks, MOE_BLOCK, D)

    def expert_block(args):
        xb, e = args
        gate, up = jnp.split(jnp.matmul(xb, w_up[e]), 2, axis=-1)
        return jnp.matmul(jax.nn.silu(gate) * up, w_down[e])

    ys = lax.map(expert_block, (xs, blk_e)).reshape(n_slots, D)
    out = jnp.zeros((T + 1, D), h.dtype).at[slot_tok].add(ys * slot_w[:, None].astype(ys.dtype))
    return out[:T].reshape(B, S, D)

def first_inputs(seed: int = 0) -> dict:
    key = jax.random.key(seed)
    ks = iter(jax.random.split(key, 40))
    f32 = jnp.float32
    L, D = DEPTH, D_MODEL

    def dense(shape, fan_in, gain=1.0):
        return jax.random.normal(next(ks), shape, f32) * (gain * fan_in ** -0.5)

    def norm_gain(shape):
        return 1.0 + 0.05 * jax.random.normal(next(ks), shape, f32)

    def small(shape, s=0.02):
        return s * jax.random.normal(next(ks), shape, f32)

    x = jax.random.normal(next(ks), (BATCH, SEQ, D), f32)
    p = jax.random.normal(next(ks), (L, BATCH, SEQ, D_PLE), f32)
    offset = jax.random.randint(next(ks), (BATCH, 1), 0, MAX_STREAM_CHUNKS) * CHUNK
    positions = (offset + jnp.arange(SEQ, dtype=jnp.int32)[None, :]).astype(jnp.int32)
    return {
        'x': x,
        'p': p,
        'positions': positions,
        'ln_in_g': norm_gain((D,)),
        'ln_in_b': small((D,)),
        'w_in': dense((L, D, D_IN), D),
        'b_gate': small((L, N_BRANCH, D), 0.1),
        'pool_w': dense((L, POOL_GROUPS, POOL_GW, POOL_GW), POOL_GW),
        'pool_scale': norm_gain((L, D_POOL)),
        'pool_proj': dense((L, D_POOL, D), D_POOL),
        'conv_dw': dense((L, CONV_WIDTH, D_CONV), CONV_WIDTH),
        'conv_b': small((L, D_CONV)),
        'conv_ln_g': norm_gain((L, D_CONV)),
        'conv_ln_b': small((L, D_CONV)),
        'conv_proj': dense((L, D_CONV, D), D_CONV),
        'q_norm_g': norm_gain((L, Q_LORA)),
        'w_uq': dense((L, Q_LORA, N_HEADS * (QK_NOPE + QK_ROPE)), Q_LORA),
        'kv_norm_g': norm_gain((L, KV_LORA)),
        'w_ukv': dense((L, KV_LORA, N_HEADS * (QK_NOPE + V_HEAD)), KV_LORA),
        'mla_proj': dense((L, N_HEADS * V_HEAD, D), N_HEADS * V_HEAD),
        'w_out': dense((L, D, D), D, DEEPNORM_BETA),
        'ln1_g': norm_gain((L, D)),
        'ln1_b': small((L, D)),
        'w_router': dense((D, N_EXPERTS), D),
        'router_bias': small((N_EXPERTS,), 0.01),
        'exp_w_up': dense((L, N_EXPERTS, D, 2 * D_EXPERT), D),
        'exp_w_down': dense((L, N_EXPERTS, D_EXPERT, D), D_EXPERT, DEEPNORM_BETA),
        'ple_proj': dense((L, D_PLE, D), D_PLE, DEEPNORM_BETA),
        'ple_gate': dense((L, D, D), D),
        'ln2_g': norm_gain((L, D)),
        'ln2_b': small((L, D)),
    }

def first_block(x, p, positions, ln_in_g, ln_in_b, w_in, b_gate, pool_w, pool_scale, pool_proj,
              conv_dw, conv_b, conv_ln_g, conv_ln_b, conv_proj, q_norm_g, w_uq, kv_norm_g, w_ukv,
              mla_proj, w_out, ln1_g, ln1_b, w_router, router_bias, exp_w_up, exp_w_down,
              ple_proj, ple_gate, ln2_g, ln2_b):
    cos, sin = rope_tables(positions)
    h = layer_norm(x, ln_in_g, ln_in_b)
    for i in range(DEPTH):
        y = mixer_sublayer(h, cos, sin, w_in[i], b_gate[i], pool_w[i], pool_scale[i], pool_proj[i],
                           conv_dw[i], conv_b[i], conv_ln_g[i], conv_ln_b[i], conv_proj[i],
                           q_norm_g[i], w_uq[i], kv_norm_g[i], w_ukv[i], mla_proj[i], w_out[i])
        h = layer_norm(DEEPNORM_ALPHA * h + y, ln1_g[i], ln1_b[i])
        e = jnp.matmul(p[i], ple_proj[i]) * jax.nn.sigmoid(jnp.matmul(h, ple_gate[i]))
        m = moe_ffn(h, w_router, router_bias, exp_w_up[i], exp_w_down[i])
        h = layer_norm(DEEPNORM_ALPHA * h + m + e, ln2_g[i], ln2_b[i])
    return h


CTX_LEN = 256
GRID_W = 64
ATTN_HEADS = 4
ATTN_HEAD_DIM = 64
ATTN_V_DIM = 2 * ATTN_HEAD_DIM
ATTN_QK_W = ATTN_HEADS * 2 * ATTN_HEAD_DIM
ATTN_V_W = ATTN_HEADS * ATTN_V_DIM
CONV_W = 512
CONV_K = 3
MIX_W = ATTN_V_W + CONV_W
PROJ_W = 2 * ATTN_QK_W + ATTN_V_W + 3 * CONV_W
ROPE_BASE = 10000.0
ROT_AXIS = ATTN_HEAD_DIM // 2
CAP_FACTOR = 2
D_EXPERT_2 = 1024
EPS = 1e-6


def rmsnorm(x, g):
    xf = x.astype(jnp.float32)
    y = xf * lax.rsqrt(jnp.mean(xf * xf, axis=-1, keepdims=True) + EPS)
    return (y * g.astype(jnp.float32)).astype(x.dtype)

def modulate(x, shift, scale):
    return x * (1 + scale) + shift

def axial_rope_tables(n_tok):
    rows = n_tok // GRID_W
    row = jnp.repeat(jnp.arange(rows, dtype=jnp.float32), GRID_W)
    col = jnp.tile(jnp.arange(GRID_W, dtype=jnp.float32), rows)
    inv = ROPE_BASE ** (-jnp.arange(0, ROT_AXIS, 2, dtype=jnp.float32) / ROT_AXIS)
    ang_r = row[:, None] * inv[None, :]
    ang_c = col[:, None] * inv[None, :]
    ang = jnp.concatenate([ang_r, ang_r, ang_c, ang_c], axis=-1)
    return jnp.cos(ang), jnp.sin(ang)

def apply_rope_2(x, cos, sin):
    q = ROT_AXIS // 2
    a, b, c2, d2 = x[..., :q], x[..., q:2 * q], x[..., 2 * q:3 * q], x[..., 3 * q:]
    rot = jnp.concatenate([-b, a, -d2, c2], axis=-1)
    cs = cos[None, :, None, None, :].astype(x.dtype)
    sn = sin[None, :, None, None, :].astype(x.dtype)
    return x * cs + rot * sn

def diff_attend(q, k, v, lam):
    s = jnp.einsum('bqhmd,bkhmd->bhmqk', q, k, preferred_element_type=jnp.float32)
    a = jax.nn.softmax(s * (1.0 / math.sqrt(ATTN_HEAD_DIM)), axis=-1)
    a = a[:, :, 0] - lam * a[:, :, 1]
    return jnp.einsum('bhqk,bkhe->bqhe', a.astype(v.dtype), v)

def latent_diff_attention(q, k_all, v_all, lam):
    b, t, h, _, d = q.shape
    nblk = t // Q_BLOCK
    qb = q.reshape(b, nblk, Q_BLOCK, h, 2, d).transpose(1, 0, 2, 3, 4, 5)
    o = lax.map(lambda qblk: diff_attend(qblk, k_all, v_all, lam), qb)
    return o.transpose(1, 0, 2, 3, 4).reshape(b, t, h, ATTN_V_DIM)

def split_proj(p):
    b, t, _ = p.shape
    i0 = ATTN_QK_W
    i1 = i0 + ATTN_QK_W
    i2 = i1 + ATTN_V_W
    i3 = i2 + CONV_W
    i4 = i3 + CONV_W
    q = p[..., :i0].reshape(b, t, ATTN_HEADS, 2, ATTN_HEAD_DIM)
    k = p[..., i0:i1].reshape(b, t, ATTN_HEADS, 2, ATTN_HEAD_DIM)
    v = p[..., i1:i2].reshape(b, t, ATTN_HEADS, ATTN_V_DIM)
    return q, k, v, p[..., i2:i3], p[..., i3:i4], p[..., i4:]

def short_conv(gb, gc, xc, conv_w):
    u = gc * xc
    y = lax.conv_general_dilated(u, conv_w[:, None, :].astype(u.dtype), window_strides=(1,),
                                 padding=((CONV_K // 2, CONV_K // 2),),
                                 dimension_numbers=('NWC', 'WIO', 'NWC'),
                                 feature_group_count=CONV_W)
    return gb * y

def head_out(o, subln_g, lam_init):
    b, t = o.shape[:2]
    return (rmsnorm(o, subln_g) * (1.0 - lam_init)).reshape(b, t, ATTN_V_W)

def hybrid_mixer(xn, xn_c, w_in, conv_w, lq1, lk1, lq2, lk2, subln_g, w_out, layer, need_ctx):
    lam_init = 0.8 - 0.6 * math.exp(-0.3 * layer)
    lam = (jnp.exp(jnp.sum(lq1.astype(jnp.float32) * lk1.astype(jnp.float32)))
           - jnp.exp(jnp.sum(lq2.astype(jnp.float32) * lk2.astype(jnp.float32))) + lam_init)
    t = xn.shape[1]
    cos, sin = axial_rope_tables(t)
    q, k, v, gb, gc, xc = split_proj(jnp.einsum('btd,dn->btn', xn, w_in))
    qc, kc, vc, gbc, gcc, xcc = split_proj(jnp.einsum('btd,dn->btn', xn_c, w_in))
    q = apply_rope_2(q, cos, sin)
    k = apply_rope_2(k, cos, sin)
    k_all = jnp.concatenate([kc, k], axis=1)
    v_all = jnp.concatenate([vc, v], axis=1)
    attn = head_out(latent_diff_attention(q, k_all, v_all, lam), subln_g, lam_init)
    conv = short_conv(gb, gc, xc, conv_w)
    out = jnp.einsum('btn,nd->btd', jnp.concatenate([attn, conv], axis=-1), w_out)
    out_c = None
    if need_ctx:
        attn_c = head_out(diff_attend(qc, kc, vc, lam), subln_g, lam_init)
        conv_c = short_conv(gbc, gcc, xcc, conv_w)
        out_c = jnp.einsum('btn,nd->btd', jnp.concatenate([attn_c, conv_c], axis=-1), w_out)
    return out, out_c

def ec_moe(x_tok, w_router, w_gate, w_up, w_down):
    t = x_tok.shape[1]
    cap = CAP_FACTOR * t // N_EXPERTS
    logits = jnp.einsum('btd,de->bte', x_tok, w_router, preferred_element_type=jnp.float32)
    aff = jax.nn.softmax(logits, axis=-1)
    g, idx = lax.top_k(jnp.swapaxes(aff, 1, 2), cap)
    xs = jax.vmap(lambda xt, ix: xt[ix])(x_tok, idx)
    hg = jnp.einsum('becd,edf->becf', xs, w_gate)
    hu = jnp.einsum('becd,edf->becf', xs, w_up)
    y = jnp.einsum('becf,efd->becd', jax.nn.silu(hg) * hu, w_down) * g[..., None].astype(xs.dtype)
    return jax.vmap(lambda ix, val: jnp.zeros((t, D_MODEL), val.dtype)
                    .at[ix.reshape(-1)].add(val.reshape(-1, D_MODEL)))(idx, y)

def second_inputs(seed: int = 0) -> dict:
    key = jax.random.key(seed)
    ks = jax.random.split(key, 24)
    f32 = jnp.float32
    nrm = lambda k, shape, s: jax.random.normal(k, shape, f32) * s
    gain = lambda k: 1.0 + 0.05 * jax.random.normal(k, (DEPTH, D_MODEL), f32)
    return {
        "x": nrm(ks[0], (BATCH, SEQ, D_MODEL), 1.0),
        "c": nrm(ks[1], (BATCH, D_MODEL), 1.0),
        "ctx": nrm(ks[2], (BATCH, CTX_LEN, D_MODEL), 1.0),
        "c_ctx": nrm(ks[3], (D_MODEL,), 1.0),
        "w_ada": nrm(ks[4], (DEPTH, D_MODEL, 6 * D_MODEL), 0.5 * D_MODEL ** -0.5),
        "b_ada": nrm(ks[5], (DEPTH, 6 * D_MODEL), 0.01),
        "norm_pre_mix": gain(ks[6]),
        "norm_post_mix": gain(ks[7]),
        "norm_pre_ffn": gain(ks[8]),
        "norm_post_ffn": gain(ks[9]),
        "w_in": nrm(ks[10], (DEPTH, D_MODEL, PROJ_W), D_MODEL ** -0.5),
        "conv_w": nrm(ks[11], (DEPTH, CONV_K, CONV_W), CONV_K ** -0.5),
        "lambda_q1": nrm(ks[12], (DEPTH, ATTN_HEAD_DIM), 0.1),
        "lambda_k1": nrm(ks[13], (DEPTH, ATTN_HEAD_DIM), 0.1),
        "lambda_q2": nrm(ks[14], (DEPTH, ATTN_HEAD_DIM), 0.1),
        "lambda_k2": nrm(ks[15], (DEPTH, ATTN_HEAD_DIM), 0.1),
        "subln_g": 1.0 + 0.05 * jax.random.normal(ks[16], (DEPTH, ATTN_V_DIM), f32),
        "w_out": nrm(ks[17], (DEPTH, MIX_W, D_MODEL), MIX_W ** -0.5),
        "w_router": nrm(ks[18], (DEPTH, D_MODEL, N_EXPERTS), D_MODEL ** -0.5),
        "w_gate": nrm(ks[19], (DEPTH, N_EXPERTS, D_MODEL, D_EXPERT_2), D_MODEL ** -0.5),
        "w_up": nrm(ks[20], (DEPTH, N_EXPERTS, D_MODEL, D_EXPERT_2), D_MODEL ** -0.5),
        "w_down": nrm(ks[21], (DEPTH, N_EXPERTS, D_EXPERT_2, D_MODEL), D_EXPERT_2 ** -0.5),
    }

def second_block(x, c, ctx, c_ctx, w_ada, b_ada, norm_pre_mix, norm_post_mix, norm_pre_ffn,
              norm_post_ffn, w_in, conv_w, lambda_q1, lambda_k1, lambda_q2, lambda_k2,
              subln_g, w_out, w_router, w_gate, w_up, w_down):
    h = x
    hc = ctx
    for layer in range(DEPTH):
        need_ctx = layer < DEPTH - 1
        mod = jnp.einsum('bd,dn->bn', jax.nn.silu(c), w_ada[layer]) + b_ada[layer]
        mod_c = jnp.einsum('d,dn->n', jax.nn.silu(c_ctx), w_ada[layer]) + b_ada[layer]
        sh1, sc1, g1, sh2, sc2, g2 = [m[:, None, :] for m in jnp.split(mod, 6, axis=-1)]
        csh1, csc1, cg1, csh2, csc2, cg2 = jnp.split(mod_c, 6, axis=-1)
        xn = modulate(rmsnorm(h, norm_pre_mix[layer]), sh1, sc1)
        xn_c = modulate(rmsnorm(hc, norm_pre_mix[layer]), csh1, csc1)
        mix, mix_c = hybrid_mixer(xn, xn_c, w_in[layer], conv_w[layer], lambda_q1[layer],
                                  lambda_k1[layer], lambda_q2[layer], lambda_k2[layer],
                                  subln_g[layer], w_out[layer], layer, need_ctx)
        h = h + g1 * rmsnorm(mix, norm_post_mix[layer])
        if need_ctx:
            hc = hc + cg1 * rmsnorm(mix_c, norm_post_mix[layer])
        xn = modulate(rmsnorm(h, norm_pre_ffn[layer]), sh2, sc2)
        ff = ec_moe(xn, w_router[layer], w_gate[layer], w_up[layer], w_down[layer])
        h = h + g2 * rmsnorm(ff, norm_post_ffn[layer])
        if need_ctx:
            xn_c = modulate(rmsnorm(hc, norm_pre_ffn[layer]), csh2, csc2)
            ff_c = ec_moe(xn_c, w_router[layer], w_gate[layer], w_up[layer], w_down[layer])
            hc = hc + cg2 * rmsnorm(ff_c, norm_post_ffn[layer])
    return h


def setup_inputs(seed=0):
    out = dict(first_inputs(seed))
    for name, value in second_inputs(seed + 1).items():
        if name != "x":
            out[name + "_2"] = value
    return out


def reference(
    x, p, positions, ln_in_g, ln_in_b, w_in, b_gate, pool_w, pool_scale, pool_proj, conv_dw,
    conv_b, conv_ln_g, conv_ln_b, conv_proj, q_norm_g, w_uq, kv_norm_g, w_ukv, mla_proj, w_out,
    ln1_g, ln1_b, w_router, router_bias, exp_w_up, exp_w_down, ple_proj, ple_gate, ln2_g, ln2_b,
    c_2, ctx_2, c_ctx_2, w_ada_2, b_ada_2, norm_pre_mix_2, norm_post_mix_2, norm_pre_ffn_2,
    norm_post_ffn_2, w_in_2, conv_w_2, lambda_q1_2, lambda_k1_2, lambda_q2_2, lambda_k2_2,
    subln_g_2, w_out_2, w_router_2, w_gate_2, w_up_2, w_down_2,
):
    x = first_block(
        x, p, positions, ln_in_g, ln_in_b, w_in, b_gate, pool_w, pool_scale, pool_proj, conv_dw,
        conv_b, conv_ln_g, conv_ln_b, conv_proj, q_norm_g, w_uq, kv_norm_g, w_ukv, mla_proj,
        w_out, ln1_g, ln1_b, w_router, router_bias, exp_w_up, exp_w_down, ple_proj, ple_gate,
        ln2_g, ln2_b,
    )
    return second_block(
        x, c_2, ctx_2, c_ctx_2, w_ada_2, b_ada_2, norm_pre_mix_2, norm_post_mix_2,
        norm_pre_ffn_2, norm_post_ffn_2, w_in_2, conv_w_2, lambda_q1_2, lambda_k1_2,
        lambda_q2_2, lambda_k2_2, subln_g_2, w_out_2, w_router_2, w_gate_2, w_up_2, w_down_2,
    )


_drawn_inputs = setup_inputs


def setup_inputs(seed=0):
    import zlib

    import numpy as np

    out = dict(_drawn_inputs(seed))
    spreads = {}
    factors = {'conv_ln_b': 2.713,
     'q_norm_g': 3.519,
     'kv_norm_g': 3.328,
     'norm_post_ffn_2': 4.045,
     'lambda_q2_2': 5.23,
     'lambda_k2_2': 3.92,
     'subln_g_2': 2.773}
    for name, (base, spread) in spreads.items():
        noise = np.random.default_rng([zlib.crc32(name.encode()), seed]).standard_normal(out[name].shape)
        drawn = base * np.exp(spread * noise) if base else spread * noise
        out[name] = jnp.asarray(drawn.astype(out[name].dtype))
    for name, factor in factors.items():
        out[name] = (out[name] * factor).astype(out[name].dtype)
    return out
```

```python
from contextlib import ExitStack

import numpy as np

import concourse.bass as bass
from concourse import mybir

F32 = mybir.dt.float32
I32 = mybir.dt.int32
ALU = mybir.AluOpType
ACT = mybir.ActivationFunctionType
AX = mybir.AxisListType.X

P = 128
S = 1024
D = 1024
NT = S // P
ND = D // P
HALF = 512
CTX = 256
NTC = CTX // P
SA = S + CTX
NH1, NOPE, ROPE, VH = 8, 64, 32, 64
QD = NOPE + ROPE
TAPS = 31
PADZ = 32
PADU = 16
WINDOWS = (2, 4, 8, 16)
NE, NG, EPG = 16, 4, 4
ALPHA = 2.0 ** 0.25
NBLK = (2 * S + NE * P - 1) // P
LN_EPS, RMS_EPS, RMS2_EPS = 1e-5, 1e-6, 1e-6
FE = 512
NH2, HD2 = 4, 64
NK2 = SA // P
CAP = 2 * S // NE
FE2 = 1024
LAM_INIT = 0.8 - 0.6
BIG = 1e30

COLS = {}


def _columns():
    at = 0
    for name, n in (
        ("ident", 128), ("ones", 128), ("before", 128), ("swap", 128), ("turn", 128),
        ("ln_in_g", 8), ("ln_in_b", 8), ("conv_dw", 4 * TAPS), ("conv_b", 4), ("conv_ln_g", 4),
        ("conv_ln_b", 4), ("pool_scale", 4), ("q_norm", 3), ("kv_norm", 2), ("inv_freq", 1),
        ("sin_sign", 1), ("pool_inv", 64), ("pre_mix", 8), ("subln", 128), ("bias_r", 16),
        ("low16", 16), ("order4", 4), ("block0", NBLK + 1), ("token", NT), ("neg_half", 8),
        ("lams", 4 * HD2), ("c", 8), ("c_ctx", 8), ("zeros", 32),
        ("eps_rms", 1), ("eps_ln", 1), ("conv2", 12),
    ):
        COLS[name] = (at, n)
        at += n
    return at


NCOLS = _columns()
ARENA = 52096
BASE = 2560


class Chain:

    def __init__(self, eng, sem, start=0):
        self.eng, self.sem, self.start, self.n = eng, sem, start, 0

    def did(self, ins):
        ins.then_inc(self.sem, 1)
        self.n += 1

    def wait(self):
        self.eng.wait_ge(self.sem, self.start + self.n)

    def step(self, ins):
        self.did(ins)
        self.wait()


class Core:

    def __init__(self, nc, ctx, ins, out):
        self.nc, self.ins, self.out = nc, ins, out
        self.loaded = nc.alloc_semaphore("constants_loaded")
        self.passed = nc.alloc_semaphore("waits_passed")
        self.used = []
        self.arena = ctx.enter_context(nc.sbuf_tensor("arena", [P, ARENA], F32))
        self.ps = ctx.enter_context(nc.psum_tensor("banks", [P, 8, HALF], F32))

    def place(self, at, *shape, parts=P, dt=None):
        n = int(np.prod(shape))
        assert at + n <= ARENA, (at, shape)
        v = self.arena[0:parts, at:at + n]
        if dt is not None:
            v = v.bitcast(dt)
        if len(shape) == 2:
            v = v.rearrange("p (a b) -> p a b", a=shape[0])
        elif len(shape) == 3:
            v = v.rearrange("p (a b c) -> p a b c", a=shape[0], b=shape[1])
        return v

    def col(self, name, a=0, b=None):
        at, n = COLS[name]
        return self.arena[:, at + a:at + (n if b is None else b)]

    def semaphore(self, name):
        sem = self.nc.alloc_semaphore(name)
        self.used.append(sem)
        return sem

    def waited(self, eng):
        eng.sem_inc(self.passed, 1)

    def free_semaphores(self):
        with self.nc.Block() as block:
            @block.gpsimd
            def _(g):
                self.nc.clear_and_free_semaphores(self.used)
        self.used = []

    def scratch(self, name, shape, dt=F32):
        return self.nc.dram_tensor(name, shape, dt).ap()


def row_on_all(vec, n):
    return vec.rearrange("(a n) -> a n", a=1).broadcast_to([P, n])


def inverse_root(chain, pool, core, out, x, scale, eps):
    n = out.shape[-1]
    core.waited(pool)
    chain.step(pool.tensor_scalar(out, x, float(scale), float(eps), ALU.mult, ALU.add))
    return pool.tensor_tensor(out, out, core.col("neg_half", 0, n), ALU.pow)



def load_constants(core):
    nc = core.nc
    got = core.loaded
    with nc.Block() as block:
        @block.sync
        def _(sp):
            sp.dma_start(core.arena[:, 0:NCOLS], core.ins["packed"]).then_inc(got, 16)
            sp.wait_ge(got, 16)


def input_norm(core, x_at, xhat_dram, hT):
    nc, ps = core.nc, core.ps
    sem = lambda n: core.semaphore("n1_" + n)
    loaded = [sem(f"loaded{i}") for i in range(NT)]
    stats, rstd_done, xhat_done, turned, taken, stored, steps, pool_steps = map(
        sem, ("stats", "rstd", "xhat", "turned", "taken", "stored", "steps", "pool_steps"))
    x = core.place(x_at, NT, D)
    st = core.place(x_at + NT * D, NT, 12)
    mv = core.place(x_at + NT * D + 96, NT, 2)
    rstd = core.place(x_at + NT * D + 112, NT)
    xin = core.ins["x"].rearrange("o (i p) d -> (o i) p d", p=P)
    with nc.Block() as block:
        @block.sync
        def _(sp):
            for i in range(NT):
                sp.dma_start(x[:, i, :], xin[i]).then_inc(loaded[i], 16)
            for i in range(NT):
                sp.wait_ge(xhat_done, i + 1)
                sp.dma_start(xhat_dram[i], x[:, i, :]).then_inc(stored, 16)
            sp.wait_ge(stored, 16 * NT)

        @block.vector
        def _(v):
            c = Chain(v, steps)
            for i in range(NT):
                v.wait_ge(loaded[i], 16)
                for j in range(2):
                    c.did(v.bn_stats(st[:, i, 6 * j:6 * j + 6], x[:, i, HALF * j:HALF * (j + 1)]))
                c.wait()
                v.bn_aggr(mv[:, i, :], st[:, i, :]).then_inc(stats, 1)
            v.wait_ge(stats, NT)
            v.wait_ge(rstd_done, 1)
            for i in range(NT):
                v.tensor_scalar(x[:, i, :], x[:, i, :], mv[:, i, 0:1], rstd[:, i:i + 1],
                                ALU.subtract, ALU.mult).then_inc(xhat_done, 1)

        @block.gpsimd
        def _(g):
            g.wait_ge(stats, NT)
            inverse_root(Chain(g, pool_steps), g, core, rstd, mv[:, :, 1], 1.0,
                         LN_EPS).then_inc(rstd_done, 1)

        @block.tensor
        def _(pe):
            for i in range(NT):
                pe.wait_ge(xhat_done, i + 1)
                for b in range(2):
                    if i >= 2:
                        pe.wait_ge(taken, 2 * (i - 2) + b + 1)
                    for k in range(4):
                        kk = 4 * b + k
                        t = pe.transpose(ps[:, 2 * (i % 2) + b, k * P:(k + 1) * P],
                                         x[:, i, kk * P:(kk + 1) * P], core.col("ident"))
                    t.then_inc(turned, 1)

        @block.scalar
        def _(a):
            for i in range(NT):
                for b in range(2):
                    a.wait_ge(turned, 2 * i + b + 1)
                    for k in range(4):
                        kk = 4 * b + k
                        t = a.activation(hT[:, kk, i * P:(i + 1) * P],
                                         ps[:, 2 * (i % 2) + b, k * P:(k + 1) * P], ACT.Identity,
                                         bias=core.col("ln_in_b", kk, kk + 1),
                                         scale=core.col("ln_in_g", kk, kk + 1))
                    t.then_inc(taken, 1)



def modulation(core, at, mod_dram):
    nc, ps = core.nc, core.ps
    sem = lambda n: core.semaphore("ada_" + n)
    loaded = [sem(f"w{i}") for i in range(2)]
    b_loaded, act_ready, done, taken = map(sem, ("b", "silu", "done", "taken"))
    n_chunks = 6 * D // HALF
    w = [core.place(at + i * ND * HALF, ND, HALF) for i in range(2)]
    row = core.place(at + 2 * ND * HALF, n_chunks * HALF, parts=2)
    bias = core.place(at + 2 * ND * HALF + n_chunks * HALF, n_chunks * HALF, parts=2)
    both = core.place(at + 2 * ND * HALF + 2 * n_chunks * HALF, ND, 2)
    stored = sem("stored")
    with nc.Block() as block:
        @block.sync
        def _(sp):
            sp.dma_start(bias, core.ins["b_ada"].broadcast_to([2, 6 * D])).then_inc(b_loaded, 16)
            with sp.Fori(0, n_chunks // 2) as i:
                for j in range(2):
                    sp.wait_ge(done, i * 2 + j + 1)
                    sp.dma_start(w[j], core.ins["w_ada"][i * 2 + j]).then_inc(loaded[j], 16)
            sp.wait_ge(taken, n_chunks + 2)
            sp.dma_start(mod_dram, row).then_inc(stored, 16)
            sp.wait_ge(stored, 16)

        @block.tensor
        def _(pe):
            pe.sem_inc(done, 2)
            pe.wait_ge(act_ready, 2)
            with pe.Fori(0, n_chunks // 2) as i:
                for j in range(2):
                    pe.wait_ge(loaded[j], i * 16 + 16)
                    pe.wait_ge(taken, i * 2 + j + 1)
                    for k in range(ND):
                        t = pe.matmul(ps[0:2, j, :], both[:, k, :], w[j][:, k, :],
                                      start=(k == 0), stop=(k == ND - 1))
                    t.then_inc(done, 1)

        @block.scalar
        def _(a):
            a.activation(both[:, :, 0], core.col("c"), ACT.Silu).then_inc(act_ready, 1)
            a.activation(both[:, :, 1], core.col("c_ctx"), ACT.Silu).then_inc(act_ready, 1)

        @block.vector
        def _(v):
            v.sem_inc(taken, 2)
            v.wait_ge(b_loaded, 16)
            with v.Fori(0, n_chunks // 2) as i:
                for j in range(2):
                    v.wait_ge(done, i * 2 + j + 3)
                    here = bass.ds(i * (2 * HALF) + j * HALF, HALF)
                    v.tensor_tensor(row[:, here], ps[0:2, j, :], bias[:, here], ALU.add).then_inc(taken, 1)



def loads_of_tiles(sp, w, w_dram, first, pairs, loaded, done, before=0):
    with sp.Fori(0, pairs) as i:
        for j in range(2):
            sp.wait_ge(done, i * 2 + before + j + 1)
            sp.dma_start(w[j], w_dram[i * 2 + (first + j)]).then_inc(loaded[j], 16)


def tile_products(pe, ps, act, w, loaded, done, taken, pairs, widths, before=0):
    nb = len(widths)
    with pe.Fori(0, pairs) as i:
        for j in range(2):
            pe.wait_ge(loaded[j], i * 16 + (8 * before + 16))
            pe.wait_ge(taken[j], i + before // 2 + 1)
            for c, width in enumerate(widths):
                for k in range(ND):
                    m = pe.matmul(ps[:, nb * j + c, 0:width], w[j][:, k, :],
                                  act[:, k, c * HALF:c * HALF + width],
                                  start=(k == 0), stop=(k == ND - 1))
            m.then_inc(done, 1)


def copy_tiles(a, ps, dst, done, taken, pairs, widths, shift=0, before=0):
    nb = len(widths)
    with a.Fori(0, pairs) as i:
        for j in range(2):
            a.wait_ge(done, i * 2 + (before + j + 3))
            a.wait_ge(done, 2)
            for c, width in enumerate(widths):
                m = a.activation(dst[:, bass.ds(i * 2 + j, 1), shift + c * HALF:shift + c * HALF + width],
                                 ps[:, nb * j + c:nb * j + c + 1, 0:width], ACT.Copy)
            m.then_inc(taken[j], 1)


def pool_and_conv_inputs(core, hT, u, z, w_at):
    nc, ps = core.nc, core.ps
    sem = lambda n: core.semaphore("in_" + n)
    loaded = [sem(f"w{i}") for i in range(2)]
    taken = [sem(f"taken{i}") for i in range(2)]
    done, cleared = map(sem, ("done", "cleared"))
    w = [core.place(w_at + i * D, ND, P) for i in range(2)]
    sg = core.place(w_at + 2 * D, S)
    wd = core.ins["w_in_tiles"]
    with nc.Block() as block:
        @block.sync
        def _(sp):
            loads_of_tiles(sp, w, wd, 0, 6, loaded, done)

        @block.gpsimd
        def _(g):
            g.memset(u[:, :, 0:PADU], 0.0).then_inc(cleared, 1)
            g.memset(z[:, :, 0:PADZ], 0.0).then_inc(cleared, 1)
            g.wait_ge(cleared, 2)

        @block.tensor
        def _(pe):
            pe.sem_inc(done, 2)
            tile_products(pe, ps, hT, w, loaded, done, taken, 6, (HALF, HALF))

        @block.scalar
        def _(a):
            a.sem_inc(taken[0], 1)
            a.sem_inc(taken[1], 1)
            copy_tiles(a, ps, u, done, taken, 2, (HALF, HALF), PADU)
            with a.Fori(0, 4) as i:
                a.wait_ge(done, i * 2 + 7)
                a.wait_ge(taken[1], i + 3)
                for c in range(2):
                    m = a.activation(sg[:, c * HALF:(c + 1) * HALF], ps[:, c, :], ACT.Sigmoid)
                m.then_inc(taken[0], 1)

        @block.vector
        def _(v):
            with v.Fori(0, 4) as i:
                v.wait_ge(taken[0], i + 4)
                v.wait_ge(done, i * 2 + 8)
                v.tensor_tensor(z[:, bass.ds(i, 1), PADZ:PADZ + HALF],
                                sg[:, 0:HALF].unsqueeze(1), ps[:, 2:3, :], ALU.mult)
                v.tensor_tensor(z[:, bass.ds(i, 1), PADZ + HALF:PADZ + S],
                                sg[:, HALF:S].unsqueeze(1), ps[:, 3:4, :], ALU.mult).then_inc(taken[1], 1)



def rope_tables(chain, core, pos_i, ang, sin_arg, cos_arg):
    v = chain.eng
    two_pi = 2.0 * np.pi
    c1 = float(np.float32(6.28125))
    c2 = float(np.float32(two_pi - c1))
    c2 = float((np.float32(c2).view(np.uint32) & np.uint32(0xFFFFF000)).view(np.float32))
    c3 = float(np.float32(two_pi - c1 - c2))
    magic = float(1.5 * 2 ** 23)
    limit = float(np.float32(np.pi)) - 1e-6
    chain.step(v.tensor_copy(ang, pos_i))
    chain.step(v.tensor_scalar(ang, ang, core.col("inv_freq"), None, ALU.mult))
    for out, turn in ((sin_arg, 0.0), (cos_arg, 0.25)):
        chain.step(v.tensor_scalar(out, ang, float(1 / two_pi), turn, ALU.mult, ALU.add))
        chain.step(v.tensor_scalar(out, out, magic, magic, ALU.add, ALU.subtract))
    for out, turn, tmp in ((sin_arg, 0.0, pos_i.bitcast(F32)), (cos_arg, 0.25, pos_i.bitcast(F32))):
        chain.step(v.scalar_tensor_tensor(tmp, out, -c1, ang, ALU.mult, ALU.add))
        chain.step(v.scalar_tensor_tensor(tmp, out, -c2, tmp, ALU.mult, ALU.add))
        chain.step(v.scalar_tensor_tensor(tmp, out, -c3, tmp, ALU.mult, ALU.add))
        chain.step(v.tensor_scalar(tmp, tmp, turn * two_pi, limit, ALU.add, ALU.min))
        chain.step(v.tensor_scalar(out, tmp, -limit, None, ALU.max))


def heads_and_branches(core, m):
    nc, ps, hT, u, z, acc, vt = core.nc, core.ps, m["hT"], m["u"], m["z"], m["acc"], m["vt"]
    sem = lambda n: core.semaphore("hb_" + n)
    loaded = [sem(f"w{i}") for i in range(2)]
    taken = [sem(f"taken{i}") for i in range(2)]
    stored = [sem(f"stored{i}") for i in range(2)]
    rows_stored = sem("rows_stored")
    (done, pos_loaded, uq_loaded, ukv_loaded, pw_loaded, steps, taps, trig_args, trig, squared,
     scaled, made, evac, turned, pool_steps, mixed, inverted) = map(sem, (
         "done", "pos_loaded", "uq_loaded", "ukv_loaded", "pw_loaded", "steps", "taps", "trig_args",
         "trig", "squared", "scaled", "made", "evac", "turned", "pool_steps", "mixed", "inverted"))
    at = m["free"]
    t1, t2 = core.place(at, PADU + S), core.place(at + PADU + S, PADU + S)
    wp = core.place(at + 2 * (PADU + S), 4, P)
    at += 2 * (PADU + S) + 4 * P
    lat = core.place(at, 6, S)
    at += 6 * S
    w = [core.place(at + i * D, ND, P) for i in range(2)]
    ksw, qsw1 = core.place(at, S, parts=ROPE), core.place(at + D, S)
    at += 2 * D
    wuq = core.place(at, 3, 6 * P)
    wukv = core.place(at + 18 * P, 2, 2 * HALF)
    at += 18 * P + 4 * HALF
    sin_t, cos_t = core.place(at, S), core.place(at + S, S)
    rs = [core.place(at + 2 * S, S), core.place(at + 3 * S, S)]
    st = [core.place(at + 4 * S, S), core.place(at + 5 * S, S)]
    qraw = [core.place(at + 6 * S, S), core.place(at + 7 * S, S)]
    qsw = [core.place(at + 8 * S, S), qsw1]
    sq = [st[0], st[1], qraw[0], qraw[1], qsw[0]]
    wd = core.ins["w_in_tiles"]
    taps_first = 18
    NTAP = 4
    halves = lambda t: t.rearrange("p (a b) -> p a b", a=2)
    dest = {0: rs[0], 1: rs[1], 6: qraw[0], 7: qraw[1], 8: qsw[0], 9: qsw[1]}
    for n in (2, 3, 4, 5, 11, 12, 13, 14):
        dest[n] = st[n % 2]

    with nc.Block() as block:
        @block.sync
        def _(sp):
            sp.dma_start(rs[1].bitcast(I32), row_on_all(core.ins["positions"], S)).then_inc(pos_loaded, 16)
            loads_of_tiles(sp, w, wd, 12, 3, loaded, done)
            sp.dma_start(wp, core.ins["pool_w_k"]).then_inc(pw_loaded, 16)
            sp.dma_start(wuq, core.ins["w_uq_k"]).then_inc(uq_loaded, 16)
            sp.dma_start(wukv, core.ins["w_ukv_k"]).then_inc(ukv_loaded, 16)
            for n in range(2, 6):
                sp.wait_ge(evac, n + 1)
                sp.dma_start(m["qn"][n - 2], dest[n]).then_inc(stored[n % 2], 16)
            for g in range(2):
                sp.wait_ge(turned, g + 1)
                sp.dma_start(m["qr"][g], qraw[g]).then_inc(rows_stored, 16)
            sp.wait_ge(turned, 3)
            sp.dma_start(m["kr"], lat[0:ROPE, 5, :]).then_inc(rows_stored, 16)
            for n in range(11, 15):
                sp.wait_ge(evac, n + 1)
                sp.dma_start(m["kn"][n - 11], dest[n]).then_inc(stored[n % 2], 16)
            for q in stored:
                sp.wait_ge(q, 16 * 4)
            sp.wait_ge(rows_stored, 16 * 3)

        @block.tensor
        def _(pe):
            pe.sem_inc(done, 2)
            tile_products(pe, ps, hT, w, loaded, done, taken, 3, (HALF, HALF))

            def unit(n, kk, lhs, rhs, rows=P):
                b = 4 + 2 * (n % 2)
                if n >= 2:
                    pe.wait_ge(evac, n - 1)
                for c in range(2):
                    for k in range(kk):
                        t = pe.matmul(ps[0:rows, b + c, :], lhs(k, c), rhs(k, c),
                                      start=(k == 0), stop=(k == kk - 1))
                t.then_inc(made, 1)

            col = lambda t, c: t[:, c * HALF:(c + 1) * HALF]
            pe.wait_ge(squared, 3)
            unit(0, 3, lambda k, c: core.col("ones"), lambda k, c: col(sq[k], c))
            pe.wait_ge(squared, 5)
            unit(1, 2, lambda k, c: core.col("ones"), lambda k, c: col(sq[3 + k], c))
            pe.wait_ge(uq_loaded, 16)
            pe.wait_ge(scaled, 3)
            for t in range(6):
                unit(2 + t, 3, lambda k, c: wuq[:, k, t * P:(t + 1) * P],
                     lambda k, c: col(lat[:, k, :], c))
            for g in range(2):
                pe.wait_ge(evac, 7 + g)
                unit(8 + g, 1, lambda k, c: core.col("swap"), lambda k, c: col(qraw[g], c))
            unit(10, 1, lambda k, c: core.col("swap")[0:ROPE, 0:ROPE],
                 lambda k, c: col(lat[0:ROPE, 5, :], c), ROPE)
            pe.wait_ge(ukv_loaded, 16)
            pe.wait_ge(scaled, 5)
            for t in range(4):
                unit(11 + t, 2, lambda k, c: wukv[:, k, t * P:(t + 1) * P],
                     lambda k, c: col(lat[:, 3 + k, :], c))
            for t in range(4):
                unit(15 + t, 2, lambda k, c: lat[:, 3 + k, (2 * t + c) * P:(2 * t + c + 1) * P],
                     lambda k, c: wukv[:, k, HALF:2 * HALF])
            pe.wait_ge(pw_loaded, 16)
            for g in range(4):
                pe.wait_ge(mixed, g + 1)
                unit(19 + g, 1, lambda k, c: wp[:, g, :], lambda k, c: col(u[:, g, PADU:], c))

        @block.scalar
        def _(a):
            a.sem_inc(taken[0], 1)
            a.sem_inc(taken[1], 1)
            a.wait_ge(trig_args, 2)
            a.activation(sin_t, sin_t, ACT.Sin).then_inc(trig, 1)
            a.activation(cos_t, cos_t, ACT.Sin).then_inc(trig, 1)
            copy_tiles(a, ps, lat, done, taken, 3, (HALF, HALF))
            a.wait_ge(taken[0], 4)
            a.wait_ge(taken[1], 4)
            for k in range(5):
                a.activation(sq[k], lat[:, k, :], ACT.Square).then_inc(squared, 1)
            for n in range(23):
                b = 4 + 2 * (n % 2)
                src = ps[:, b:b + 2, :]
                a.wait_ge(made, n + 1)
                if n in (4, 5):
                    a.wait_ge(stored[n % 2], 16)
                if n >= 11 and n < 15:
                    a.wait_ge(stored[n % 2], 16 * (2 + (n - 11) // 2))
                if n == 6:
                    a.wait_ge(squared, 5)
                if n < 2:
                    a.activation(halves(dest[n]), src, ACT.Sqrt, bias=core.col("eps_rms"),
                                 scale=1.0 / (3 * P if n == 0 else 2 * P)).then_inc(evac, 1)
                elif n == 10:
                    a.activation(halves(ksw), src[0:ROPE], ACT.Copy).then_inc(evac, 1)
                elif n < 15:
                    a.activation(halves(dest[n]), src, ACT.Copy).then_inc(evac, 1)
                elif n < 19:
                    t = n - 15
                    a.activation(vt[:, 2 * t:2 * t + 2, :], src, ACT.Copy).then_inc(evac, 1)
                else:
                    g = n - 19
                    a.activation(halves(u[:, g, PADU:]), src, ACT.Copy,
                                 scale=core.col("pool_scale", g, g + 1)).then_inc(evac, 1)

        @block.vector
        def _(v):
            c = Chain(v, steps)
            v.wait_ge(pos_loaded, 16)
            rope_tables(c, core, rs[1].bitcast(I32), rs[0], sin_t, cos_t)
            c.step(v.tensor_scalar(sin_t, sin_t, core.col("sin_sign"), None, ALU.mult))
            v.tensor_scalar(cos_t, cos_t, 1.0, None, ALU.mult).then_inc(trig_args, 2)

            def tap(k, first=False):
                for ch in range(NTAP):
                    scalar = core.col("conv_dw")[:, bass.ds(k + ch * TAPS, 1)]
                    src = z[:, ch, bass.ds(k + (PADZ - TAPS + 1), S)]
                    if first:
                        v.tensor_scalar(acc[:, ch, :], src, scalar, core.col("conv_b", ch, ch + 1),
                                        ALU.mult, ALU.add).then_inc(taps, 1)
                    else:
                        v.wait_ge(taps, k * NTAP + (ch - NTAP + 1))
                        v.scalar_tensor_tensor(acc[:, ch, :], src, scalar, acc[:, ch, :],
                                               ALU.mult, ALU.add).then_inc(taps, 1)

            tap(0, True)
            with v.Fori(1, taps_first) as k:
                tap(k)
            v.wait_ge(evac, 2)
            for n in range(2):
                v.reciprocal(rs[n], rs[n]).then_inc(inverted, 1)
            for k in range(5):
                n = 0 if k < 3 else 1
                g = core.col("q_norm", k, k + 1) if k < 3 else core.col("kv_norm", k - 3, k - 2)
                v.wait_ge(inverted, n + 1)
                v.scalar_tensor_tensor(lat[:, k, :], lat[:, k, :], g, rs[n],
                                       ALU.mult, ALU.mult).then_inc(scaled, 1)
            with v.Fori(taps_first, TAPS) as k:
                tap(k)
            v.wait_ge(taps, NTAP * TAPS)

        @block.gpsimd
        def _(g):
            c = Chain(g, pool_steps)
            c.did(g.memset(t1[:, 0:PADU], 0.0))
            c.step(g.memset(t2[:, 0:PADU], 0.0))
            for grp in range(4):
                cur = u[:, grp, :]
                for lvl in range(grp + 1):
                    nxt = (t1, t2)[lvl % 2]
                    c.step(g.tensor_tensor(nxt[:, PADU:], cur[:, PADU:],
                                           cur[:, PADU - 2 ** lvl:PADU + S - 2 ** lvl], ALU.add))
                    cur = nxt
                c.did(g.tensor_tensor(cur[:, PADU:2 * PADU], cur[:, PADU:2 * PADU],
                                      core.col("pool_inv", 16 * grp, 16 * grp + 16), ALU.mult))
                c.step(g.tensor_scalar(cur[:, 2 * PADU:], cur[:, 2 * PADU:],
                                       1.0 / WINDOWS[grp], None, ALU.mult))
                g.tensor_tensor(u[:, grp, PADU:], cur[:, PADU:], u[:, grp, PADU:],
                                ALU.subtract).then_inc(mixed, 1)
                g.wait_ge(mixed, grp + 1)
            g.wait_ge(trig, 2)
            for n, (raw, sw, rows) in enumerate(((qraw[0], qsw[0], P), (qraw[1], qsw[1], P),
                                                 (lat[0:ROPE, 5, :], ksw, ROPE))):
                g.wait_ge(evac, 9 + n)
                c.did(g.tensor_tensor(raw, raw, cos_t[0:rows], ALU.mult))
                c.step(g.tensor_tensor(sw, sw, sin_t[0:rows], ALU.mult))
                g.tensor_tensor(raw, raw, sw, ALU.add).then_inc(turned, 1)


def conv_finish(core, m):
    nc, ps, acc = core.nc, core.ps, m["acc"]
    sem = lambda n: core.semaphore("cf_" + n)
    summed, centred, squared, rooted, inverted, normed, shaped = map(sem, (
        "summed", "centred", "squared", "rooted", "inverted", "normed", "shaped"))
    sq = core.place(m["free"], 4, S)
    rstd = core.place(m["free"] + 4 * S, S)
    halves = lambda t: t.rearrange("p (a b) -> p a b", a=2)
    with nc.Block() as block:
        @block.tensor
        def _(pe):
            for b, src, ready in ((0, acc, None), (2, sq, squared)):
                for k in range(4):
                    if ready is not None:
                        pe.wait_ge(ready, k + 1)
                    for c in range(2):
                        t = pe.matmul(ps[:, b + c, :], core.col("ones"),
                                      src[:, k, c * HALF:(c + 1) * HALF], start=(k == 0), stop=(k == 3),
                                      skip_group_check=True)
                t.then_inc(summed, 1)

        @block.vector
        def _(v):
            v.wait_ge(summed, 1)
            for k in range(4):
                v.scalar_tensor_tensor(halves(acc[:, k, :]), ps[:, 0:2, :], -1.0 / (4 * P),
                                       halves(acc[:, k, :]), ALU.mult, ALU.add).then_inc(centred, 1)
            v.wait_ge(rooted, 1)
            v.reciprocal(rstd, rstd).then_inc(inverted, 1)
            v.wait_ge(inverted, 1)
            for k in range(4):
                v.tensor_tensor(acc[:, k, :], acc[:, k, :], rstd, ALU.mult).then_inc(normed, 1)

        @block.scalar
        def _(a):
            for k in range(4):
                a.wait_ge(centred, k + 1)
                a.activation(sq[:, k, :], acc[:, k, :], ACT.Square).then_inc(squared, 1)
            a.wait_ge(summed, 2)
            a.activation(halves(rstd), ps[:, 2:4, :], ACT.Sqrt, bias=core.col("eps_ln"),
                         scale=1.0 / (4 * P)).then_inc(rooted, 1)
            for k in range(4):
                a.wait_ge(normed, k + 1)
                a.activation(acc[:, k, :], acc[:, k, :], ACT.Silu, bias=core.col("conv_ln_b", k, k + 1),
                             scale=core.col("conv_ln_g", k, k + 1)).then_inc(shaped, 1)



def latent_attention(core, m):
    nc, ps, vt, oT = core.nc, core.ps, m["vt"], m["oT"]
    sem = lambda n: core.semaphore("at_" + n)
    q_loaded = [sem(f"q{i}") for i in range(2)]
    scored, biased, exped, turned, moved, summed, normed, steps, o_turned, o_moved = map(sem, (
        "scored", "biased", "exped", "turned", "moved", "summed", "normed", "steps", "o_turned",
        "o_moved"))
    at = m["free"]
    q = [core.place(at + i * 2 * S, S, parts=QD) for i in range(2)]
    k = [core.place(at + i * 2 * S + S, S, parts=QD) for i in range(2)]
    e = [core.place(at + 4 * S + i * S, S) for i in range(2)]
    pt = [core.place(at + 6 * S + i * S, NT, P) for i in range(2)]
    o = core.place(at + 8 * S, NT, NH1 * VH)
    tiny = core.place(at + 12 * S, 32)
    mx, nb, den, rec = (tiny[:, 2 * i:2 * i + 2] for i in range(4))
    scale = float(QD) ** -0.5
    N = 2 * NT
    with nc.Block() as block:
        @block.sync
        def _(sp):
            with sp.Fori(0, NH1 // 2) as it:
                for j in range(2):
                    sp.wait_ge(scored, it * N + (NT * j + NT))
                    h = it * 2 + j
                    for dst, src in ((q[j][0:NOPE], m["qn"].rearrange("t (h r) s -> (t h) r s", h=2)),
                                     (q[j][NOPE:QD], m["qr"].rearrange("t (h r) s -> (t h) r s", h=4)),
                                     (k[j][0:NOPE], m["kn"].rearrange("t (h r) s -> (t h) r s", h=2))):
                        sp.dma_start(dst, src[bass.ds(h, 1)].rearrange("a r s -> (a r) s"))\
                          .then_inc(q_loaded[j], 16)
                    sp.dma_start(k[j][NOPE:QD], m["kr"]).then_inc(q_loaded[j], 16)

        @block.tensor
        def _(pe):
            pe.sem_inc(scored, N)
            pe.sem_inc(turned, 2)
            pe.sem_inc(summed, 2)
            with pe.Fori(0, NH1 // 2) as it:
                def scores(n):
                    i, j = n % NT, n // NT
                    if i == 0:
                        pe.wait_ge(q_loaded[j], it * 64 + 64)
                    pe.wait_ge(exped, it * N + n + 1)
                    keys = (i + 1) * P
                    for c in range(0, keys, HALF):
                        wd = min(HALF, keys - c)
                        t = pe.matmul(ps[:, 2 * (n % 2) + c // HALF, 0:wd], q[j][:, i * P:(i + 1) * P],
                                      k[j][:, c:c + wd], start=True, stop=True)
                    t.then_inc(scored, 1)

                scores(0)
                for n in range(N):
                    i, j = n % NT, n // NT
                    if n + 1 < N:
                        scores(n + 1)
                    pe.wait_ge(exped, it * N + n + 3)
                    pe.wait_ge(moved, it * N + n)
                    for t in range(i + 1):
                        ins = pe.transpose(ps[:, 4 + t // 4, (t % 4) * P:(t % 4 + 1) * P],
                                           e[n % 2][:, t * P:(t + 1) * P], core.col("ident"))
                    ins.then_inc(turned, 1)
                    pe.wait_ge(moved, it * N + n + 1)
                    pe.wait_ge(normed, it * N + n + 1)
                    for t in range(i + 1):
                        ins = pe.matmul(ps[:, 6 + n % 2, 0:VH], pt[n % 2][:, t, :],
                                        vt[:, t, bass.ds(it * (2 * VH) + j * VH, VH)],
                                        start=(t == 0), stop=(t == i))
                    ins.then_inc(summed, 1)
            for i in range(NT):
                pe.wait_ge(normed, NH1 * NT + 2)
                if i >= 2:
                    pe.wait_ge(o_moved, i - 1)
                for t in range(4):
                    ins = pe.transpose(ps[:, i % 2, t * P:(t + 1) * P], o[:, i, t * P:(t + 1) * P],
                                       core.col("ident"))
                ins.then_inc(o_turned, 1)

        @block.vector
        def _(v):
            v.sem_inc(normed, 2)
            per = 3 * N
            with v.Fori(0, NH1 // 2) as it:
                c = Chain(v, steps, it * per)

                def bias(n):
                    i = n % NT
                    v.wait_ge(scored, it * N + n + 1 + N)
                    row = ps[:, 2 * (n % 2):2 * (n % 2) + 2, :].rearrange("p a b -> p (a b)")
                    c.step(v.memset(row[0:64, i * P + 64:(i + 1) * P], -BIG))
                    c.step(v.reduce_max(mx[:, n % 2:n % 2 + 1], row[:, 0:(i + 1) * P], AX))
                    v.tensor_scalar(nb[:, n % 2:n % 2 + 1], mx[:, n % 2:n % 2 + 1], -scale, None,
                                    ALU.mult).then_inc(biased, 1)

                def normalise(n):
                    i, j = n % NT, n // NT
                    v.wait_ge(summed, it * N + n + 3)
                    c.step(v.reciprocal(rec[:, n % 2:n % 2 + 1], den[:, n % 2:n % 2 + 1]))
                    v.tensor_scalar(o[:, i, bass.ds(it * (2 * VH) + j * VH, VH)],
                                    ps[:, 6 + n % 2, 0:VH], rec[:, n % 2:n % 2 + 1], None,
                                    ALU.mult).then_inc(normed, 1)

                bias(0)
                for n in range(N):
                    i = n % NT
                    if n + 1 < N:
                        bias(n + 1)
                    v.wait_ge(turned, it * N + n + 3)
                    v.wait_ge(summed, it * N + n + 1)
                    src = ps[:, 4:6, :].rearrange("p a b -> p (a b)")
                    v.tensor_copy(pt[n % 2].rearrange("p a b -> p (a b)")[:, 0:(i + 1) * P],
                                  src[:, 0:(i + 1) * P]).then_inc(moved, 1)
                    if n:
                        normalise(n - 1)
                normalise(N - 1)
                assert c.n == per
            for i in range(NT):
                v.wait_ge(o_turned, i + 1)
                v.tensor_copy(oT[:, :, i * P:(i + 1) * P],
                              ps[:, i % 2, :].rearrange("p (a b) -> p a b", a=4)).then_inc(o_moved, 1)

        @block.scalar
        def _(a):
            a.sem_inc(exped, 2)
            with a.Fori(0, NH1 // 2) as it:
                for n in range(N):
                    i = n % NT
                    a.wait_ge(biased, it * N + n + 1)
                    a.wait_ge(turned, it * N + n + 1)
                    a.wait_ge(normed, it * N + n + 1)
                    row = ps[:, 2 * (n % 2):2 * (n % 2) + 2, :].rearrange("p a b -> p (a b)")
                    a.activation(e[n % 2][:, 0:(i + 1) * P], row[:, 0:(i + 1) * P], ACT.Exp,
                                 bias=nb[:, n % 2:n % 2 + 1], scale=scale,
                                 accum_out=den[:, n % 2:n % 2 + 1]).then_inc(exped, 1)



MW = 36 * P + 4


def merge(core, m):
    nc, ps, hT, merged = core.nc, core.ps, m["hT"], m["merged"]
    branch = (m["poolT"], m["acc"], m["oT"])
    sem = lambda n: core.semaphore("mg_" + n)
    loaded = [sem(f"w{i}") for i in range(2)]
    made, gated, used, steps = map(sem, ("made", "gated", "used", "steps"))
    w = [core.place(m["free"] + i * MW, MW) for i in range(2)]
    at = m["free"] + 2 * MW
    sg = [core.place(at + i * HALF, HALF) for i in range(2)]
    part = [core.place(at + (2 + i) * HALF, HALF) for i in range(2)]
    NU = 12

    def split(n):
        return n // 6, (n // 3) % 2, n % 3

    with nc.Block() as block:
        @block.sync
        def _(sp):
            with sp.Fori(0, ND // 2) as it:
                for j in range(2):
                    sp.wait_ge(used, it * NU + 6 * j + 6)
                    sp.dma_start(w[j], core.ins["merge_w"][it * 2 + j]).then_inc(loaded[j], 16)

        @block.tensor
        def _(pe):
            with pe.Fori(0, ND // 2) as it:
                for n in range(NU):
                    j, c, b = split(n)
                    if n % 6 == 0:
                        pe.wait_ge(loaded[j], it * 16 + 16)
                    pe.wait_ge(used, it * NU + n + 9)
                    bank = 2 * (n % 4)
                    for k in range(ND):
                        pe.matmul(ps[:, bank, :], w[j][:, (8 * b + k) * P:(8 * b + k + 1) * P],
                                  hT[:, k, c * HALF:(c + 1) * HALF], start=(k == 0), stop=(k == ND - 1))
                    for k in range(4):
                        x = 24 + 4 * b + k
                        t = pe.matmul(ps[:, bank + 1, :], w[j][:, x * P:(x + 1) * P],
                                      branch[b][:, k, c * HALF:(c + 1) * HALF],
                                      start=(k == 0), stop=(k == 3))
                    t.then_inc(made, 1)

        @block.scalar
        def _(a):
            with a.Fori(0, ND // 2) as it:
                for n in range(NU):
                    j, c, b = split(n)
                    a.wait_ge(made, it * NU + n + 1)
                    a.wait_ge(used, it * NU + n + 11)
                    a.activation(sg[n % 2], ps[:, 2 * (n % 4), :], ACT.Sigmoid,
                                 bias=w[j][:, 36 * P + b:36 * P + b + 1]).then_inc(gated, 1)

        @block.vector
        def _(v):
            v.sem_inc(used, NU)
            per = 8
            with v.Fori(0, ND // 2) as it:
                ch = Chain(v, steps, it * per)
                for n in range(NU):
                    j, c, b = split(n)
                    v.wait_ge(gated, it * NU + n + 1)
                    y = ps[:, 2 * (n % 4) + 1, :]
                    dst = merged[:, bass.ds(it * 2 + j, 1), c * HALF:(c + 1) * HALF]
                    ch.wait()
                    if b == 0:
                        v.tensor_tensor(part[0], sg[n % 2], y, ALU.mult).then_inc(used, 1)
                    elif b == 1:
                        v.tensor_tensor(part[1], sg[n % 2], y, ALU.mult).then_inc(used, 1)
                        v.wait_ge(used, it * NU + n + 13)
                        ch.did(v.tensor_tensor(part[0], part[0], part[1], ALU.add))
                    else:
                        v.tensor_tensor(part[1], sg[n % 2], y, ALU.mult).then_inc(used, 1)
                        v.wait_ge(used, it * NU + n + 13)
                        ch.did(v.tensor_tensor(dst, part[0].unsqueeze(1), part[1].unsqueeze(1), ALU.add))
                assert ch.n == per


def stats_of(core, c, v, st, mv, x):
    for j in range(2):
        c.did(v.bn_stats(st[:, 6 * j:6 * j + 6], x[:, HALF * j:HALF * (j + 1)]))
    c.wait()
    core.waited(v)
    return v.bn_aggr(mv, st)


def flat2(ps, b):
    return ps[:, b:b + 2, :].rearrange("p a b -> p (a b)")


def output_and_gate(core, m):
    nc, ps, merged = core.nc, core.ps, m["merged"]
    sem = lambda n: core.semaphore("og_" + n)
    x_loaded = [sem(f"x{i}") for i in range(2)]
    p_loaded = [sem(f"p{i}") for i in range(2)]
    h_stored = [sem(f"h_stored{i}") for i in range(2)]
    r_stored = [sem(f"r_stored{i}") for i in range(2)]
    (wo_loaded, weights, staged, made, taken, var_ready, rstd_ready, h_ready, turned, moved,
     routed, kept, gate_made, ple_made, sig_ready, e_taken, rest_ready, steps, pool_steps, moves) = map(
        sem, ("wo", "weights", "staged", "made", "taken", "var", "rstd", "h_ready", "turned",
              "moved", "routed", "kept", "gate_made", "ple_made", "sig_ready", "e_taken",
              "rest_ready", "steps", "pool_steps", "moves"))
    at = m["low"]
    wo, wg = core.place(at, ND, D), core.place(at + ND * D, ND, D)
    wp = core.place(at + 2 * ND * D, 2, D)
    wr = core.place(at + 2 * ND * D + 2 * D, ND, NE)
    at += 2 * ND * D + 2 * D + ND * NE
    ga, ba, g1, b1 = (core.place(at + i * D, D) for i in range(4))
    work = core.place(at + 4 * D, D)
    at = m["high"]
    names = ("xh0", "xh1", "mt0", "mt1", "h0", "h1", "rest0", "rest1", "hT", "sig")
    b = {n: core.place(at + i * D, D) for i, n in enumerate(names)}
    at += len(names) * D
    pin = [core.place(at + i * 2 * P, 2 * P) for i in range(2)]
    pT = core.place(at + 4 * P, 2, P)
    st, mv = core.place(at + 6 * P, 12), core.place(at + 6 * P + 12, 2)
    rstd = core.place(at + 6 * P + 16, 1)
    tile = lambda x: x.rearrange("p (a b) -> p a b", b=P)
    hT = tile(b["hT"])
    with nc.Block() as block:
        @block.sync
        def _(sp):
            sp.dma_start(wo, core.ins["w_out_k"]).then_inc(wo_loaded, 16)
            for dst, name in ((ga, "ln_in_g"), (ba, "ln_in_b"), (g1, "ln1_g"), (b1, "ln1_b")):
                sp.dma_start(dst, row_on_all(core.ins[name], D)).then_inc(weights, 16)
            sp.dma_start(wr, core.ins["w_router_k"]).then_inc(weights, 16)
            sp.dma_start(wp, core.ins["ple_proj_k"]).then_inc(weights, 16)
            sp.dma_start(wg, core.ins["ple_gate_k"]).then_inc(weights, 16)
            with sp.Fori(0, NT // 2) as it:
                for j in range(2):
                    n = it * 2 + j
                    sp.wait_ge(taken, it * 2 + j + 1)
                    sp.dma_start(b[f"xh{j}"], m["xhat"][n]).then_inc(x_loaded[j], 16)
                    sp.wait_ge(turned, it * 2 + j + 1)
                    sp.dma_start(pin[j], core.ins["p_tiles"][n]).then_inc(p_loaded[j], 16)

        @block.gpsimd
        def _(g):
            def stage(it, j):
                g.wait_ge(made, it * 2 + j + 1)
                g.wait_ge(wo_loaded, 16)
                g.tensor_copy(tile(b[f"mt{j}"]), merged[:, :, bass.ds(it * (2 * P) + j * P, P)])\
                 .then_inc(staged, 1)

            def root(it, j):
                c = Chain(g, pool_steps, it * 2 + j)
                g.wait_ge(var_ready, it * 2 + j + 1)
                inverse_root(c, g, core, rstd, mv[:, 1:2], 1.0, LN_EPS).then_inc(rstd_ready, 1)

            stage(0, 0)
            with g.Fori(0, NT // 2 - 1) as it:
                stage(it, 1)
                root(it, 0)
                stage(it + 1, 0)
                root(it, 1)
            last = NT // 2 - 1
            stage(last, 1)
            root(last, 0)
            root(last, 1)

        @block.tensor
        def _(pe):
            pe.sem_inc(made, 2)
            pe.sem_inc(turned, 2)
            pe.wait_ge(wo_loaded, 16)

            def product(it, j):
                n = it * 2 + j
                pe.wait_ge(staged, n + 1)
                pe.wait_ge(taken, n + 2)
                for c in range(2):
                    for k in range(ND):
                        t = pe.matmul(ps[:, c, :], tile(b[f"mt{j}"])[:, k, :],
                                      wo[:, k, c * HALF:(c + 1) * HALF], start=(k == 0), stop=(k == ND - 1))
                t.then_inc(made, 1)

            def after(it, j):
                n = it * 2 + j
                pe.wait_ge(h_ready, n + 1)
                pe.wait_ge(kept, n)
                for k in range(ND):
                    pe.transpose(ps[:, 2 + k // 4, (k % 4) * P:(k % 4 + 1) * P],
                                 b[f"h{j}"][:, k * P:(k + 1) * P], core.col("ident"))
                pe.wait_ge(p_loaded[j], it * 16 + 16)
                pe.wait_ge(e_taken, n)
                for k in range(2):
                    t = pe.transpose(ps[:, 6, k * P:(k + 1) * P], pin[j][:, k * P:(k + 1) * P],
                                     core.col("ident"))
                t.then_inc(turned, 1)
                pe.wait_ge(moved, n + 1)
                for k in range(ND):
                    t = pe.matmul(ps[:, 2, 0:NE], hT[:, k, :], wr[:, k, :], start=(k == 0), stop=(k == ND - 1))
                t.then_inc(routed, 1)
                pe.wait_ge(sig_ready, n)
                for c in range(2):
                    for k in range(ND):
                        t = pe.matmul(ps[:, 4 + c, :], hT[:, k, :], wg[:, k, c * HALF:(c + 1) * HALF],
                                      start=(k == 0), stop=(k == ND - 1))
                t.then_inc(gate_made, 1)
                for c in range(2):
                    for k in range(2):
                        t = pe.matmul(ps[:, 6 + c, :], pT[:, k, :], wp[:, k, c * HALF:(c + 1) * HALF],
                                      start=(k == 0), stop=(k == 1))
                t.then_inc(ple_made, 1)

            product(0, 0)
            pe.wait_ge(weights, 16 * 7)
            with pe.Fori(0, NT // 2 - 1) as it:
                product(it, 1)
                after(it, 0)
                product(it + 1, 0)
                after(it, 1)
            last = NT // 2 - 1
            product(last, 1)
            after(last, 0)
            after(last, 1)

        @block.scalar
        def _(a):
            with a.Fori(0, NT // 2) as it:
                for j in range(2):
                    n = it * 2 + j
                    a.wait_ge(turned, n + 3)
                    for c in range(2):
                        a.activation(b["hT"][:, c * HALF:(c + 1) * HALF], ps[:, 2 + c, :], ACT.Copy)
                    a.activation(pT.rearrange("p a b -> p (a b)"), ps[:, 6, 0:2 * P], ACT.Copy)\
                     .then_inc(moved, 1)
                    a.wait_ge(gate_made, n + 1)
                    a.wait_ge(e_taken, n)
                    a.activation(b["sig"], flat2(ps, 4), ACT.Sigmoid).then_inc(sig_ready, 1)
                    a.wait_ge(h_ready, n + 1)
                    a.dma_start(m["h1"][n], b[f"h{j}"]).then_inc(h_stored[j], 16)
                    a.wait_ge(rest_ready, n + 1)
                    a.dma_start(m["rest"][n], b[f"rest{j}"]).then_inc(r_stored[j], 16)
            for q in h_stored + r_stored:
                a.wait_ge(q, 16 * (NT // 2))

        @block.vector
        def _(v):
            v.sem_inc(taken, 2)
            c0 = Chain(v, steps)
            v.wait_ge(weights, 16 * 7)
            c0.did(v.tensor_scalar(ga, ga, ALPHA, None, ALU.mult))
            c0.step(v.tensor_scalar(ba, ba, ALPHA, None, ALU.mult))
            per = 6

            def norm(it, j):
                n = it * 2 + j
                c = Chain(v, steps, n * per + c0.n)
                v.wait_ge(x_loaded[j], it * 16 + 16)
                v.wait_ge(h_ready, n)
                c.step(v.tensor_tensor(work, b[f"xh{j}"], ga, ALU.mult))
                c.step(v.tensor_tensor(work, work, ba, ALU.add))
                v.wait_ge(made, n + 3)
                v.tensor_tensor(work, work, flat2(ps, 0), ALU.add).then_inc(taken, 1)
                v.wait_ge(taken, n + 3)
                stats_of(core, c, v, st, mv, work).then_inc(var_ready, 1)
                v.wait_ge(rstd_ready, n + 1)
                c.step(v.tensor_scalar(work, work, mv[:, 0:1], rstd, ALU.subtract, ALU.mult))
                c.step(v.tensor_tensor(work, work, g1, ALU.mult))
                v.wait_ge(h_stored[j], it * 16)
                v.tensor_tensor(b[f"h{j}"], work, b1, ALU.add).then_inc(h_ready, 1)
                assert c.n == per

            def residual(it, j):
                n = it * 2 + j
                v.wait_ge(routed, n + 1)
                v.tensor_copy(m["logits"][:, bass.ds(it * (2 * NE) + j * NE, NE)], ps[:, 2, 0:NE])\
                 .then_inc(kept, 1)
                v.wait_ge(sig_ready, n + 1)
                v.wait_ge(ple_made, n + 1)
                v.wait_ge(r_stored[j], it * 16)
                v.tensor_tensor(b[f"rest{j}"], b["sig"], flat2(ps, 6), ALU.mult).then_inc(e_taken, 1)
                v.wait_ge(e_taken, n + 1)
                v.scalar_tensor_tensor(b[f"rest{j}"], b[f"h{j}"], ALPHA, b[f"rest{j}"],
                                       ALU.mult, ALU.add).then_inc(rest_ready, 1)

            norm(0, 0)
            with v.Fori(0, NT // 2 - 1) as it:
                norm(it, 1)
                residual(it, 0)
                norm(it + 1, 0)
                residual(it, 1)
            last = NT // 2 - 1
            norm(last, 1)
            residual(last, 0)
            residual(last, 1)



def first_best(c, v, out, x, rank, peak, tmp, n):
    shape = list(x.shape)
    spread = lambda t: t.unsqueeze(2).to_broadcast(shape)
    c.step(v.tensor_reduce(peak, x, AX, ALU.max))
    c.step(v.tensor_tensor(tmp, x, spread(peak), ALU.is_equal))
    c.step(v.tensor_tensor(tmp, tmp, rank.unsqueeze(1).to_broadcast(shape), ALU.mult))
    c.step(v.tensor_reduce(peak, tmp, AX, ALU.max))
    c.step(v.tensor_tensor(out, tmp, spread(peak), ALU.is_equal))


def route(core, m):
    nc, ps = core.nc, core.ps
    sem = lambda n: core.semaphore("rt_" + n)
    (sig, steps, picked, counted, cleared, ready, listed, tok_loaded, tok_f, tok_turned,
     zeroed) = map(
        sem, ("sig", "steps", "picked", "counted", "cleared", "ready", "listed", "tok_loaded",
              "tok_f", "tok_turned", "zeroed"))
    at = m["free"]

    def take(*shape):
        nonlocal at
        n = int(np.prod(shape))
        at += n
        return core.place(at - n, *shape)

    aff, sel, tmp, selm, oh1, oh2, pick, rank = (take(NT, NE) for _ in range(8))
    pair, gs = take(NT * NG), take(NT * NG)
    keep, gtmp = take(NT, NG), take(NT, NG)
    peak, wk, off = take(NT), take(NT, 2), take(NT + 1, NE)
    nb, pend, pstart = take(NE), take(NE), take(NE)
    cmp = take(NBLK, NE)
    blk, need, slot = take(NBLK), take(NBLK), take(NBLK)
    dest = take(2, NT)
    rowsf = take(P)
    spread_t = lambda t: t.unsqueeze(1).to_broadcast([P, NT, NE])
    fl = lambda t: t.rearrange("p a b -> p (a b)")
    quads = lambda t: fl(t).rearrange("p (q e) -> p q e", e=EPG)
    toks = m["slot_token_rows"]
    with nc.Block() as block:
        @block.vector
        def _(v):
            c = Chain(v, steps)
            v.wait_ge(sig, 1)
            c.step(v.tensor_tensor(sel, aff, spread_t(core.col("bias_r")), ALU.add))
            q = quads(sel)
            first = True
            for x in range(EPG):
                for y in range(x + 1, EPG):
                    dst = gs if first else pair
                    c.step(v.tensor_tensor(dst, q[:, :, x], q[:, :, y], ALU.add))
                    if not first:
                        c.step(v.tensor_tensor(gs, gs, pair, ALU.max))
                    first = False
            first_best(c, v, keep, gs.rearrange("p (t g) -> p t g", g=NG), core.col("order4"), peak, gtmp, NG)
            kb = fl(keep)
            c.step(v.tensor_scalar(pair, kb, BIG, -BIG, ALU.mult, ALU.add))
            wide = lambda t: t.unsqueeze(2).to_broadcast([P, NT * NG, EPG])
            c.step(v.tensor_tensor(quads(selm), quads(sel), wide(kb), ALU.mult))
            c.step(v.tensor_tensor(quads(selm), quads(selm), wide(pair), ALU.add))
            first_best(c, v, oh1, selm, core.col("low16"), peak, tmp, NE)
            c.step(v.tensor_scalar(tmp, oh1, -BIG, None, ALU.mult))
            c.step(v.tensor_tensor(selm, selm, tmp, ALU.add))
            first_best(c, v, oh2, selm, core.col("low16"), peak, tmp, NE)
            v.tensor_tensor(pick, oh1, oh2, ALU.add).then_inc(picked, 1)
            for i, oh in enumerate((oh1, oh2)):
                c.step(v.tensor_tensor(tmp, aff, oh, ALU.mult))
                c.step(v.tensor_reduce(wk[:, :, i], tmp, AX, ALU.add))
            c.step(v.tensor_tensor(peak, wk[:, :, 0], wk[:, :, 1], ALU.add))
            c.step(v.reciprocal(peak, peak))
            c.step(v.tensor_tensor(m["weights"].rearrange("p (a b) -> p a b", b=2), wk,
                                   peak.unsqueeze(2).to_broadcast([P, NT, 2]), ALU.mult))
            v.wait_ge(counted, 1)
            tot = ps[:, 1, 0:P].rearrange("p (a b) -> p a b", b=NE)
            c.step(v.memset(off[:, 0, :], 0.0))
            for i in range(NT):
                c.step(v.tensor_tensor(off[:, i + 1, :], off[:, i, :], tot[:, i, :], ALU.add))
            c.did(v.tensor_tensor(fl(rank), fl(off[:, 0:NT, :]), ps[:, 0, 0:P], ALU.add))
            c.step(v.tensor_scalar(nb, off[:, NT, :], 0.0, None, ALU.is_gt))
            for i in range(1, NT):
                c.step(v.scalar_tensor_tensor(nb, off[:, NT, :], float(P * i), nb, ALU.is_gt, ALU.add))
            c.step(v.tensor_tensor_scan(pend, core.col("ones", 0, NE), nb, 0.0, ALU.mult, ALU.add))
            c.step(v.tensor_tensor(pstart, pend, nb, ALU.subtract))
            c.step(v.tensor_scalar(pstart, pstart, float(P), None, ALU.mult))
            c.step(v.tensor_tensor(rank, rank, spread_t(pstart), ALU.add))
            for i, oh in enumerate((oh1, oh2)):
                c.step(v.tensor_tensor(tmp, rank, oh, ALU.mult))
                c.step(v.tensor_reduce(dest[:, i, :], tmp, AX, ALU.add))
            c.step(v.tensor_copy(m["dest"], fl(dest)))
            v.tensor_copy(m["token"], core.col("token")).then_inc(ready, 1)
            c.step(v.tensor_tensor(cmp, pend.unsqueeze(1).to_broadcast([P, NBLK, NE]),
                                   core.col("block0", 0, NBLK).unsqueeze(2).to_broadcast([P, NBLK, NE]),
                                   ALU.is_le))
            c.step(v.tensor_reduce(blk, cmp, AX, ALU.add))
            c.step(v.tensor_scalar(blk, blk, float(NE - 1), None, ALU.min))
            c.step(v.memset(need[:, 0:1], 1.0))
            c.step(v.tensor_tensor(need[:, 1:], blk[:, 1:], blk[:, 0:NBLK - 1], ALU.not_equal))
            c.step(v.tensor_tensor_scan(slot, need, core.col("zeros", 0, NBLK), 0.0,
                                        ALU.not_equal, ALU.add))
            for i, x in enumerate((blk, need, slot)):
                c.did(v.tensor_copy(m["plan"][:, i * NBLK:(i + 1) * NBLK], x))
            v.wait_ge(tok_loaded, 16)
            v.tensor_copy(rowsf[0:NBLK], toks).then_inc(tok_f, 1)
            v.wait_ge(tok_turned, 1)
            c.did(v.tensor_copy(m["slot_token"], ps[:, 2, 0:NBLK]))

        @block.tensor
        def _(pe):
            pe.wait_ge(picked, 1)
            pe.matmul(ps[:, 0, 0:P], core.col("before"), fl(pick), start=True, stop=True)
            pe.matmul(ps[:, 1, 0:P], core.col("ones"), fl(pick), start=True, stop=True).then_inc(counted, 1)
            pe.wait_ge(tok_f, 1)
            pe.transpose(ps[:, 2, 0:NBLK], rowsf[0:NBLK], core.col("ident")[0:NBLK, 0:NBLK])\
              .then_inc(tok_turned, 1)

        @block.scalar
        def _(a):
            a.activation(fl(aff), m["logits"], ACT.Sigmoid).then_inc(sig, 1)

        @block.sync
        def _(sp):
            sp.wait_ge(zeroed, 1)
            sp.dma_start(m["slot_dram"].rearrange("(a b) c -> a (b c)", b=P), m["zero_i"][0:NBLK])\
              .then_inc(cleared, 16)
            sp.wait_ge(listed, 16 * 2 * NT)
            sp.dma_start(toks, m["slot_dram"].rearrange("(a b) c -> a (b c)", b=P)).then_inc(tok_loaded, 16)
            sp.wait_ge(tok_loaded, 16)

        @block.gpsimd
        def _(g):
            g.memset(m["zero_i"], 0).then_inc(zeroed, 1)
            g.wait_ge(cleared, 16)
            g.wait_ge(ready, 1)
            for i in range(NT):
                for j in range(2):
                    x = j * NT + i
                    g.indirect_dma_start(m["slot_dram"], bass.IndirectOffsetOnAxis(
                        ap=m["dest"][:, x:x + 1], axis=0), m["token"][:, i:i + 1], None).then_inc(listed, 16)
            g.wait_ge(listed, 16 * 2 * NT)


def grouped_experts(core, m):
    nc, ps = core.nc, core.ps
    sem = lambda n: core.semaphore("e1_" + n)
    (up_loaded, down_loaded, gathered, picked, x_turned, x_moved, up_done, silu_done, h_ready,
     h_turned, h_moved, down_done, y_taken, y_stored) = map(sem, (
         "up_loaded", "down_loaded", "gathered", "picked", "x_turned", "x_moved", "up_done",
         "silu_done", "h_ready", "h_turned", "h_moved", "down_done", "y_taken", "y_stored"))
    at = m["low"]
    WUP, WDN = ND * 2 * FE, 4 * D
    slots = core.place(at, 2 * (WUP + WDN))
    at += 2 * (WUP + WDN)
    x, xT, yo = core.place(at, D), core.place(at + D, ND, P), core.place(at + 2 * D, D)
    sg, h = core.place(at + 3 * D, FE), core.place(at + 3 * D + FE, FE)
    hT = core.place(at + 4 * D, 4, P)
    idx = core.place(at + 5 * D, 1, dt=I32)
    plan = m["plan"]
    W = WUP + WDN

    with nc.Block() as block:
        @block.sync
        def _(sp):
            def load(j, ups, left=None):
                e = sp.value_load(plan[0:1, bass.ds(j, 1)], min_val=0, max_val=NE - 1)
                need = sp.value_load(plan[0:1, bass.ds(j + NBLK, 1)], min_val=0, max_val=1)
                s = sp.value_load(plan[0:1, bass.ds(j + 2 * NBLK, 1)], min_val=0, max_val=1)
                if left is not None:
                    sp.wait_ge(left, j - 1)
                    core.waited(sp)
                if ups:
                    sp.wait_ge(up_loaded, j * 16)
                    sp.dma_start(slots[:, bass.ds(s * W, WUP)],
                                 core.ins["exp_up_k"][bass.ds(e, 1)].rearrange("a p n -> (a p) n"),
                                 cond=need, bounds_check="skip_entire_dma").then_inc(up_loaded, 16)
                else:
                    sp.wait_ge(down_loaded, j * 16)
                    sp.dma_start(slots[:, bass.ds(s * W + WUP, WDN)],
                                 core.ins["exp_down_k"][bass.ds(e, 1)].rearrange("a p n -> (a p) n"),
                                 cond=need, bounds_check="skip_entire_dma").then_inc(down_loaded, 16)

            load(0, True)
            load(0, False)
            load(1, True)
            load(1, False)
            with sp.Fori(2, NBLK) as j:
                load(j, True, up_done)
                load(j, False, down_done)

        @block.gpsimd
        def _(g):
            with g.Fori(0, NBLK) as j:
                g.wait_ge(x_turned, j)
                g.wait_ge(gathered, j * 16)
                g.tensor_copy(idx, m["slot_token"][:, bass.ds(j, 1)]).then_inc(picked, 1)
                g.wait_ge(picked, j + 1)
                core.waited(g)
                g.indirect_dma_start(x, None, m["h1_rows"], bass.IndirectOffsetOnAxis(ap=idx, axis=0))\
                 .then_inc(gathered, 16)

        @block.tensor
        def _(pe):
            def turn_x(j):
                pe.wait_ge(gathered, j * 16 + 16)
                pe.wait_ge(x_moved, j)
                for k in range(ND):
                    t = pe.transpose(ps[:, 2 + k // 4, (k % 4) * P:(k % 4 + 1) * P],
                                     x[:, k * P:(k + 1) * P], core.col("ident"))
                t.then_inc(x_turned, 1)

            def place_of(j):
                return pe.value_load(plan[0:1, bass.ds(j + 2 * NBLK, 1)], min_val=0, max_val=1)

            def up(j, s):
                pe.wait_ge(x_moved, j + 1)
                pe.wait_ge(up_loaded, j * 16 + 16)
                pe.wait_ge(h_ready, j)
                for c in range(2):
                    for k in range(ND):
                        t = pe.matmul(ps[:, c, :], xT[:, k, :],
                                      slots[:, bass.ds(s * W + (k * 2 * FE + c * FE), FE)],
                                      start=(k == 0), stop=(k == ND - 1))
                t.then_inc(up_done, 1)

            def turn_h(j):
                pe.wait_ge(h_ready, j + 1)
                pe.wait_ge(h_moved, j)
                for k in range(4):
                    t = pe.transpose(ps[:, 4, k * P:(k + 1) * P], h[:, k * P:(k + 1) * P], core.col("ident"))
                t.then_inc(h_turned, 1)

            def down(j, s):
                pe.wait_ge(h_moved, j + 1)
                pe.wait_ge(down_loaded, j * 16 + 16)
                pe.wait_ge(y_taken, j)
                for c in range(2):
                    for k in range(4):
                        t = pe.matmul(ps[:, 5 + c, :], hT[:, k, :],
                                      slots[:, bass.ds(s * W + (WUP + k * D + c * HALF), HALF)],
                                      start=(k == 0), stop=(k == 3))
                t.then_inc(down_done, 1)

            turn_x(0)
            up(0, place_of(0))
            turn_x(1)
            turn_h(0)
            with pe.Fori(1, NBLK - 1) as j:
                up(j, place_of(j))
                down(j - 1, place_of(j - 1))
                turn_x(j + 1)
                turn_h(j)
            last = NBLK - 1
            up(last, place_of(last))
            down(last - 1, place_of(last - 1))
            turn_h(last)
            down(last, place_of(last))

        @block.scalar
        def _(a):
            def move_x(j):
                a.wait_ge(x_turned, j + 1)
                a.wait_ge(up_done, j)
                a.activation(xT.rearrange("p a b -> p (a b)"), flat2(ps, 2), ACT.Copy).then_inc(x_moved, 1)

            def silu(j):
                a.wait_ge(up_done, j + 1)
                a.wait_ge(h_ready, j)
                a.activation(sg, ps[:, 0, :], ACT.Silu).then_inc(silu_done, 1)

            def store(j):
                a.wait_ge(y_taken, j + 1)
                a.dma_start(m["y1"][j], yo).then_inc(y_stored, 16)

            move_x(0)
            silu(0)
            move_x(1)
            with a.Fori(1, NBLK - 1) as j:
                silu(j)
                move_x(j + 1)
                store(j - 1)
            silu(NBLK - 1)
            store(NBLK - 2)
            store(NBLK - 1)
            a.wait_ge(y_stored, 16 * NBLK)

        @block.vector
        def _(v):
            def gate(j):
                v.wait_ge(silu_done, j + 1)
                v.wait_ge(h_turned, j)
                v.tensor_tensor(h, sg, ps[:, 1, :], ALU.mult).then_inc(h_ready, 1)

            def move_h(j):
                v.wait_ge(h_turned, j + 1)
                v.wait_ge(down_done, j)
                v.tensor_copy(hT.rearrange("p a b -> p (a b)"), ps[:, 4, :]).then_inc(h_moved, 1)

            def take_y(j):
                v.wait_ge(down_done, j + 1)
                v.wait_ge(y_stored, j * 16)
                v.tensor_copy(yo, flat2(ps, 5)).then_inc(y_taken, 1)

            gate(0)
            move_h(0)
            with v.Fori(1, NBLK - 1) as j:
                gate(j)
                take_y(j - 1)
                move_h(j)
            gate(NBLK - 1)
            take_y(NBLK - 2)
            move_h(NBLK - 1)
            take_y(NBLK - 1)



def prepare_columns(core, m):
    nc = core.nc
    sem = lambda n: core.semaphore("pc_" + n)
    loaded, steps, exped, lam = map(sem, ("loaded", "steps", "exped", "lam"))
    mod = m["mod"]
    cols = m["mod_cols"]
    tiny = m["tiny"]
    tmp = core.place(m["free"], HD2)
    with nc.Block() as block:
        @block.sync
        def _(sp):
            with nc.allow_non_contiguous_dma(reason="four vectors of 1024 as columns, once"):
                for i, (row, part) in enumerate(((0, 0), (0, 1), (1, 0), (1, 1))):
                    sp.dma_start(cols[:, i * ND:(i + 1) * ND],
                                 mod[row, part * D:(part + 1) * D].rearrange("(k p) -> p k", p=P))\
                      .then_inc(loaded, 16)
            sp.wait_ge(loaded, 16 * 4)

        @block.vector
        def _(v):
            c = Chain(v, steps)
            lams = core.col("lams")
            for i in range(2):
                c.step(v.tensor_tensor(tmp, lams[:, 2 * i * HD2:(2 * i + 1) * HD2],
                                       lams[:, (2 * i + 1) * HD2:(2 * i + 2) * HD2], ALU.mult))
                c.step(v.tensor_reduce(tiny[:, i:i + 1], tmp, AX, ALU.add))
            v.tensor_copy(tiny[:, 2:4], tiny[:, 0:2]).then_inc(lam, 1)
            v.wait_ge(exped, 1)
            c.step(v.tensor_tensor(m["neg_lam"], tiny[:, 3:4], tiny[:, 2:3], ALU.subtract))
            c.step(v.tensor_scalar(m["neg_lam"], m["neg_lam"], -LAM_INIT, None, ALU.add))
            v.wait_ge(loaded, 16 * 4)
            for i in range(2):
                sc = cols[:, (2 * i + 1) * ND:(2 * i + 2) * ND]
                c.step(v.scalar_tensor_tensor(sc, sc, 1.0, core.col("pre_mix"), ALU.add, ALU.mult))

        @block.scalar
        def _(a):
            a.wait_ge(lam, 1)
            a.activation(tiny[:, 2:4], tiny[:, 2:4], ACT.Exp).then_inc(exped, 1)


def prepare_rows(core, m):
    nc = core.nc
    sem = lambda n: core.semaphore("pr_" + n)
    loaded, steps = map(sem, ("loaded", "steps"))
    with nc.Block() as block:
        @block.sync
        def _(sp):
            for i, part in enumerate((2, 3, 4, 5)):
                sp.dma_start(m["rows"][i], row_on_all(m["mod"][0, part * D:(part + 1) * D], D))\
                  .then_inc(loaded, 16)
            for i, name in enumerate(("norm_post_mix", "norm_pre_ffn", "norm_post_ffn")):
                sp.dma_start(m["rows"][4 + i], row_on_all(core.ins[name], D)).then_inc(loaded, 16)

        @block.vector
        def _(v):
            c = Chain(v, steps)
            v.wait_ge(loaded, 16 * 7)
            g1, _, sc2, g2, pm, pf, pff = m["rows"][0:7]
            c.did(v.tensor_tensor(g1, g1, pm, ALU.mult))
            c.did(v.scalar_tensor_tensor(sc2, sc2, 1.0, pf, ALU.add, ALU.mult))
            c.step(v.tensor_tensor(g2, g2, pff, ALU.mult))


def context_input(core, m):
    nc, ps, xnT = core.nc, core.ps, m["xnT"]
    sem = lambda n: core.semaphore("cx_" + n)
    loaded, squared, rooted, scaled, turned, moved, pool_steps = map(sem, (
        "loaded", "squared", "rooted", "scaled", "turned", "moved", "pool_steps"))
    at = m["free"]
    x = core.place(at, NTC, D)
    sq = core.place(at + NTC * D, D)
    ss, rs = core.place(at + (NTC + 1) * D, NTC), core.place(at + (NTC + 1) * D + 4, NTC)
    cols = m["mod_cols"]
    with nc.Block() as block:
        @block.sync
        def _(sp):
            sp.dma_start(x, core.ins["ctx"].rearrange("o (i p) d -> p (o i) d", p=P)).then_inc(loaded, 16)

        @block.scalar
        def _(a):
            a.wait_ge(loaded, 16)
            for i in range(NTC):
                a.activation(sq, x[:, i, :], ACT.Square, accum_out=ss[:, i:i + 1]).then_inc(squared, 1)
                a.wait_ge(squared, i + 1)
            for i in range(NTC):
                for k in range(ND):
                    if k % 4 == 0:
                        a.wait_ge(turned, 2 * i + k // 4 + 1)
                    a.activation(xnT[:, k, S + i * P:S + (i + 1) * P],
                                 ps[:, 2 * i + k // 4, (k % 4) * P:(k % 4 + 1) * P], ACT.Identity,
                                 scale=cols[:, 3 * ND + k:3 * ND + k + 1],
                                 bias=cols[:, 2 * ND + k:2 * ND + k + 1]).then_inc(moved, 1)

        @block.gpsimd
        def _(g):
            g.wait_ge(squared, NTC)
            inverse_root(Chain(g, pool_steps), g, core, rs, ss, 1.0 / D, RMS2_EPS).then_inc(rooted, 1)

        @block.vector
        def _(v):
            v.wait_ge(rooted, 1)
            for i in range(NTC):
                v.tensor_scalar(x[:, i, :], x[:, i, :], rs[:, i:i + 1], None, ALU.mult).then_inc(scaled, 1)

        @block.tensor
        def _(pe):
            for i in range(NTC):
                pe.wait_ge(scaled, i + 1)
                for k in range(ND):
                    t = pe.transpose(ps[:, 2 * i + k // 4, (k % 4) * P:(k % 4 + 1) * P],
                                     x[:, i, k * P:(k + 1) * P], core.col("ident"))
                    if k % 4 == 3:
                        t.then_inc(turned, 1)


def combine_experts(core, m):
    nc, ps, xnT = core.nc, core.ps, m["xnT"]
    sem = lambda n: core.semaphore("ce_" + n)
    r_loaded = [sem(f"r{i}") for i in range(2)]
    h_stored = [sem(f"h_stored{i}") for i in range(2)]
    gathered = [sem(f"y{i}") for i in range(2)]
    (weights, picked, summed, var_ready, rstd_ready, h_ready, squared, rs_ready, scaled, turned,
     moved, steps, pool_steps) = map(sem, (
         "weights", "picked", "summed", "var", "rstd", "h_ready", "squared", "rs_ready", "scaled",
         "turned", "moved", "steps", "pool_steps"))
    at = m["free"]

    def take(*shape, dt=None):
        nonlocal at
        n = int(np.prod(shape))
        at += n
        return core.place(at - n, *shape, dt=dt)

    g2, b2, work, sq = (take(D) for _ in range(4))
    rest, h = [take(D), take(D)], [take(D), take(D)]
    y = [[take(D), take(D)], [take(D), take(D)]]
    xr = take(D)
    st, mv, rstd, ss, rs = take(12), take(2), take(1), take(1), take(1)
    idx = [take(1, dt=I32), take(1, dt=I32)]
    cols = m["mod_cols"]
    with nc.Block() as block:
        @block.sync
        def _(sp):
            sp.dma_start(g2, row_on_all(core.ins["ln2_g"], D)).then_inc(weights, 16)
            sp.dma_start(b2, row_on_all(core.ins["ln2_b"], D)).then_inc(weights, 16)
            with sp.Fori(0, NT // 2) as it:
                for j in range(2):
                    sp.wait_ge(summed, it * 2 + j + 1)
                    sp.dma_start(rest[j], m["rest"][it * 2 + j]).then_inc(r_loaded[j], 16)

        @block.gpsimd
        def _(g):
            with g.Fori(0, NT // 2) as it:
                for j in range(2):
                    n = it * 2 + j
                    g.wait_ge(summed, n + 1)
                    for i in range(2):
                        if i == 1 or j == 1:
                            q, left = (gathered[j], it * 32 + 16) if i == 1 else (gathered[0], it * 32 + 32)
                        else:
                            q, left = gathered[1], it * 32
                        g.wait_ge(q, left)
                        core.waited(g)
                        g.tensor_copy(idx[i], m["dest"][:, bass.ds(it * 2 + (j + i * NT), 1)])\
                         .then_inc(picked, 1)
                        g.wait_ge(picked, n * 2 + i + 1)
                        core.waited(g)
                        g.indirect_dma_start(y[j][i], None, m["y1_rows"], bass.IndirectOffsetOnAxis(
                            ap=idx[i], axis=0)).then_inc(gathered[j], 16)
                    c = Chain(g, pool_steps, n * 2)
                    g.wait_ge(var_ready, n + 1)
                    inverse_root(c, g, core, rstd, mv[:, 1:2], 1.0, LN_EPS).then_inc(rstd_ready, 1)
                    g.wait_ge(squared, n + 1)
                    inverse_root(c, g, core, rs, ss, 1.0 / D, RMS2_EPS).then_inc(rs_ready, 1)

        @block.vector
        def _(v):
            v.sem_inc(summed, 2)
            v.wait_ge(weights, 32)
            per = 5
            with v.Fori(0, NT // 2) as it:
                for j in range(2):
                    n = it * 2 + j
                    c = Chain(v, steps, n * per)
                    w = m["weights"]
                    v.wait_ge(r_loaded[j], it * 16 + 16)
                    v.wait_ge(gathered[j], it * 32 + 32)
                    v.wait_ge(h_ready, n)
                    c.step(v.scalar_tensor_tensor(work, y[j][0], w[:, bass.ds(it * 4 + 2 * j, 1)], rest[j],
                                                  ALU.mult, ALU.add))
                    v.scalar_tensor_tensor(work, y[j][1], w[:, bass.ds(it * 4 + (2 * j + 1), 1)], work,
                                           ALU.mult, ALU.add).then_inc(summed, 1)
                    v.wait_ge(summed, n + 3)
                    stats_of(core, c, v, st, mv, work).then_inc(var_ready, 1)
                    v.wait_ge(rstd_ready, n + 1)
                    c.step(v.tensor_scalar(work, work, mv[:, 0:1], rstd, ALU.subtract, ALU.mult))
                    c.step(v.tensor_tensor(work, work, g2, ALU.mult))
                    v.wait_ge(h_stored[j], it * 16)
                    v.tensor_tensor(h[j], work, b2, ALU.add).then_inc(h_ready, 1)
                    v.wait_ge(rs_ready, n + 1)
                    v.wait_ge(turned, n)
                    v.tensor_scalar(xr, h[j], rs, None, ALU.mult).then_inc(scaled, 1)
                    assert c.n == per

        @block.tensor
        def _(pe):
            with pe.Fori(0, NT) as n:
                pe.wait_ge(scaled, n + 1)
                pe.wait_ge(moved, n)
                for k in range(ND):
                    t = pe.transpose(ps[:, k // 4, (k % 4) * P:(k % 4 + 1) * P],
                                     xr[:, k * P:(k + 1) * P], core.col("ident"))
                t.then_inc(turned, 1)

        @block.scalar
        def _(a):
            with a.Fori(0, NT // 2) as it:
                for j in range(2):
                    n = it * 2 + j
                    a.wait_ge(h_ready, n + 1)
                    a.activation(sq, h[j], ACT.Square, accum_out=ss).then_inc(squared, 1)
                    a.dma_start(m["h2"][n], h[j]).then_inc(h_stored[j], 16)
                    a.wait_ge(turned, n + 1)
                    a.wait_ge(turned, 1)
                    for k in range(ND):
                        t = a.activation(xnT[:, k, bass.ds(it * (2 * P) + j * P, P)],
                                         ps[:, k // 4, (k % 4) * P:(k % 4 + 1) * P], ACT.Identity,
                                         scale=cols[:, ND + k:ND + k + 1], bias=cols[:, k:k + 1])
                    t.then_inc(moved, 1)
            for q in h_stored:
                a.wait_ge(q, 16 * (NT // 2))



def second_projections(core, m):
    nc, ps, xnT = core.nc, core.ps, m["xnT"]
    sem = lambda n: core.semaphore("p2_" + n)
    loaded = [sem(f"w{i}") for i in range(2)]
    taken = [sem(f"taken{i}") for i in range(2)]
    done = sem("done")
    w = [core.place(m["free"] + i * D, ND, P) for i in range(2)]
    wd = core.ins["w_in2_tiles"]
    with nc.Block() as block:
        @block.sync
        def _(sp):
            loads_of_tiles(sp, w, wd, 0, 12, loaded, done)

        @block.tensor
        def _(pe):
            pe.sem_inc(done, 2)
            tile_products(pe, ps, xnT, w, loaded, done, taken, 8, (HALF, HALF))
            pe.wait_ge(taken[1], 9)
            tile_products(pe, ps, xnT, w, loaded, done, taken, 4, (HALF, HALF, CTX), before=16)

        @block.scalar
        def _(a):
            a.sem_inc(taken[0], 1)
            a.sem_inc(taken[1], 1)
            copy_tiles(a, ps, m["qconv"], done, taken, 8, (HALF, HALF))
            copy_tiles(a, ps, m["kv"], done, taken, 4, (HALF, HALF, CTX), before=16)


def rotate_and_convolve(core, m):
    nc, ps = core.nc, core.ps
    sem = lambda n: core.semaphore("rc_" + n)
    (tables, swapped, sined, cosined, added, v_turned, v_moved, product, copied, steps) = map(sem, (
        "tables", "swapped", "sined", "cosined", "added", "v_turned", "v_moved", "product",
        "copied", "steps"))
    qc, kv, q2, k2, vt = m["qconv"], m["kv"], m["q2"], m["k2"], m["v2"]
    cos_t, sin_t = core.place(m["tables"], S), core.place(m["tables"] + S, S)
    tmp = [core.place(m["tmp"] + i * S, S) for i in range(2)]
    raw = [qc[:, h, :] for h in range(4)] + [kv[:, h, 0:S] for h in range(4)]
    dst = [q2[:, h] for h in range(4)] + [k2[:, h] for h in range(4)]
    gb, gc, xc = (qc[:, 4 * i:4 * i + 4, :] for i in (1, 2, 3))
    acc = m["conv2"]
    NU = 8
    with nc.Block() as block:
        @block.sync
        def _(sp):
            sp.dma_start(cos_t, core.ins["cos2"]).then_inc(tables, 16)
            sp.dma_start(sin_t, core.ins["sin2"]).then_inc(tables, 16)

        @block.tensor
        def _(pe):
            for n in range(NU):
                if n >= 2:
                    pe.wait_ge(sined, n - 1)
                for c in range(2):
                    t = pe.matmul(ps[:, 2 * (n % 2) + c, :], core.col("turn"),
                                  raw[n][:, c * HALF:(c + 1) * HALF], start=True, stop=True)
                t.then_inc(swapped, 1)
            for i in range(NK2):
                if i >= 2:
                    pe.wait_ge(v_moved, i - 1)
                for h in range(4):
                    t = pe.transpose(ps[:, 4 + i % 2, h * P:(h + 1) * P],
                                     kv[:, 4 + h, i * P:(i + 1) * P], core.col("ident"))
                t.then_inc(v_turned, 1)

        @block.gpsimd
        def _(g):
            g.wait_ge(tables, 32)
            for n in range(NU):
                g.wait_ge(swapped, n + 1)
                g.tensor_tensor(raw[n], raw[n], cos_t, ALU.mult).then_inc(cosined, 1)

        @block.vector
        def _(v):
            c = Chain(v, steps)
            for h in range(4):
                v.tensor_tensor(gc[:, h, :], gc[:, h, :], xc[:, h, :], ALU.mult).then_inc(product, 1)
            v.wait_ge(tables, 32)
            for n in range(NU):
                v.wait_ge(swapped, n + 1)
                v.tensor_tensor(tmp[n % 2], flat2(ps, 2 * (n % 2)), sin_t, ALU.mult).then_inc(sined, 1)
                v.wait_ge(sined, n + 1)
                v.wait_ge(cosined, n + 1)
                for i in range(2):
                    rows = slice(64 * i, 64 * i + 64)
                    v.tensor_tensor(dst[n][:, i, 0:S], tmp[n % 2][rows], raw[n][rows], ALU.add)\
                     .then_inc(added, 1)
            v.wait_ge(product, 4)
            wc = lambda h, t: core.col("conv2", 3 * h + t, 3 * h + t + 1)
            for h in range(4):
                src = gc[:, h, :]
                c.did(v.tensor_scalar(acc[:, h, :], src, wc(h, 1), None, ALU.mult))
            c.wait()
            for h in range(4):
                src = gc[:, h, :]
                c.did(v.scalar_tensor_tensor(acc[:, h, 1:S], src[:, 0:S - 1], wc(h, 0), acc[:, h, 1:S],
                                             ALU.mult, ALU.add))
            c.wait()
            for h in range(4):
                src = gc[:, h, :]
                c.did(v.scalar_tensor_tensor(acc[:, h, 0:S - 1], src[:, 1:S], wc(h, 2), acc[:, h, 0:S - 1],
                                             ALU.mult, ALU.add))
            c.wait()
            for h in range(4):
                c.did(v.tensor_tensor(acc[:, h, :], acc[:, h, :], gb[:, h, :], ALU.mult))

        @block.scalar
        def _(a):
            for h in range(4):
                for i in range(2):
                    a.activation(k2[:, h, i, S:SA], kv[64 * i:64 * i + 64, h, S:SA], ACT.Copy)\
                     .then_inc(copied, 1)
            a.wait_ge(added, 2 * NU)
            for i in range(NK2):
                a.wait_ge(v_turned, i + 1)
                a.activation(vt[:, i, :], ps[:, 4 + i % 2, :], ACT.Copy).then_inc(v_moved, 1)


def differential_attention(core, m):
    nc, ps, q2, k2, vt = core.nc, core.ps, m["q2"], m["k2"], m["v2"]
    sem = lambda n: core.semaphore("da_" + n)
    (staged, scored, biased, exped, combined, turned, moved, summed, kept, steps) = map(sem, (
        "staged", "scored", "biased", "exped", "combined", "turned", "moved", "summed", "kept", "steps"))
    at = m["free"]

    def take(*shape, parts=P):
        nonlocal at
        n = int(np.prod(shape))
        at += n
        return core.place(at - n, *shape, parts=parts)

    q = [take(2, P, parts=64) for _ in range(2)]
    e = [take(2, SA) for _ in range(2)]
    at_ = [take(NK2, P) for _ in range(2)]
    mx, nb, den, co = take(4), take(4), take(4), take(4)
    o = m["o2"]
    kf = k2.rearrange("p a b c -> p (a b c)")
    scale = float(HD2) ** -0.5
    G = NH2 * NT
    GROUPS = ((0, 4), (4, 8), (8, NK2))
    last = G // 2 - 1
    full = ps[:].rearrange("p a b -> p (a b)")

    def where(it, j):
        return it // (NT // 2), (it % (NT // 2)) * 2 + j

    with nc.Block() as block:
        @block.gpsimd
        def _(g):
            with g.Fori(0, G // 2) as it:
                for j in range(2):
                    h, i = where(it, j)
                    g.wait_ge(scored, (it * 2 + j) * 2 + 2)
                    g.wait_ge(scored, 4)
                    g.tensor_copy(q[j], q2.rearrange("p a b c -> p (a b) c")[
                        :, bass.ds(h * 2, 2), bass.ds(i * P, P)]).then_inc(staged, 1)

        @block.tensor
        def _(pe):
            pe.sem_inc(scored, 4)
            pe.sem_inc(turned, 6)
            pe.sem_inc(summed, 2)

            def scores(it, j):
                g = it * 2 + j
                h, _ = where(it, j)
                pe.wait_ge(staged, g + 1)
                for i in range(2):
                    pe.wait_ge(exped, g * 2 + i + 1)
                    for c, wd in enumerate((HALF, HALF, CTX)):
                        t = pe.matmul(ps[:, 3 * i + c, 0:wd], q[j][:, i, :],
                                      kf[:, bass.ds(h * (2 * SA) + (i * SA + c * HALF), wd)],
                                      start=True, stop=True, skip_group_check=True)
                    t.then_inc(scored, 1)

            def sums(it, j):
                g = it * 2 + j
                h, _ = where(it, j)
                pe.wait_ge(combined, g + 1)
                for r, (a, b) in enumerate(GROUPS):
                    bank = 6 + (j * 3 + r) % 2
                    pe.wait_ge(moved, g * 3 + r + 1)
                    if r == 1:
                        pe.wait_ge(kept, g + 2)
                    for t in range(a, b):
                        ins = pe.transpose(ps[:, bank, (t - a) * P:(t - a + 1) * P],
                                           e[j][:, 1, t * P:(t + 1) * P], core.col("ident"))
                    ins.then_inc(turned, 1)
                pe.wait_ge(moved, g * 3 + 5)
                for t in range(NK2):
                    ins = pe.matmul(ps[:, 6 + j, CTX:CTX + P], at_[j][:, t, :],
                                    vt[:, t, bass.ds(h * P, P)], start=(t == 0), stop=(t == NK2 - 1),
                                    skip_group_check=True)
                ins.then_inc(summed, 1)

            scores(0, 0)
            with pe.Fori(0, last) as it:
                scores(it, 1)
                sums(it, 0)
                scores(it + 1, 0)
                sums(it, 1)
            scores(last, 1)
            sums(last, 0)
            sums(last, 1)

        @block.vector
        def _(v):
            v.sem_inc(kept, 2)
            per = 4

            def bias(c, it, j):
                g = it * 2 + j
                for i in range(2):
                    x = 2 * j + i
                    v.wait_ge(scored, g * 2 + i + 5)
                    c.step(v.reduce_max(mx[:, x:x + 1], full[:, 3 * i * HALF:3 * i * HALF + SA], AX))
                    v.tensor_scalar(nb[:, x:x + 1], mx[:, x:x + 1], -scale, None, ALU.mult).then_inc(biased, 1)

            def combine(c, it, j):
                g = it * 2 + j
                x = 2 * j
                v.wait_ge(exped, g * 2 + 4)
                c.step(v.reciprocal(co[:, x:x + 2], den[:, x:x + 2]))
                c.step(v.tensor_scalar(e[j][:, 1, :], e[j][:, 1, :], co[:, x + 1:x + 2], m["neg_lam"],
                                       ALU.mult, ALU.mult))
                v.scalar_tensor_tensor(e[j][:, 1, :], e[j][:, 0, :], co[:, x:x + 1], e[j][:, 1, :],
                                       ALU.mult, ALU.add).then_inc(combined, 1)

            def keep(it, j):
                g = it * 2 + j
                h, i = where(it, j)
                v.wait_ge(summed, g + 3)
                v.tensor_copy(o.rearrange("p a b -> p (a b)")[:, bass.ds(i * (NH2 * P) + h * P, P)],
                              ps[:, 6 + j, CTX:CTX + P]).then_inc(kept, 1)

            c = Chain(v, steps)
            bias(c, 0, 0)
            with v.Fori(0, last) as it:
                c = Chain(v, steps, it * (2 * per) + 2)
                combine(c, it, 0)
                bias(c, it, 1)
                keep(it, 0)
                combine(c, it, 1)
                bias(c, it + 1, 0)
                keep(it, 1)
                assert c.n == 2 * per
            c = Chain(v, steps, last * 2 * per + 2)
            combine(c, last, 0)
            bias(c, last, 1)
            keep(last, 0)
            combine(c, last, 1)
            keep(last, 1)

        @block.scalar
        def _(a):
            a.sem_inc(exped, 2)
            a.sem_inc(moved, 2)

            def exp(it, j, i):
                g = it * 2 + j
                x = 2 * j + i
                a.wait_ge(biased, g * 2 + i + 1)
                a.wait_ge(turned, g * 3 + 3)
                a.activation(e[j][:, i, :], full[:, 3 * i * HALF:3 * i * HALF + SA], ACT.Exp,
                             bias=nb[:, x:x + 1], scale=scale, accum_out=den[:, x:x + 1]).then_inc(exped, 1)

            def move(it, j, r):
                g = it * 2 + j
                lo, hi = GROUPS[r]
                a.wait_ge(turned, g * 3 + r + 7)
                a.wait_ge(summed, g + 1)
                a.activation(at_[j].rearrange("p a b -> p (a b)")[:, lo * P:hi * P],
                             ps[:, 6 + (j * 3 + r) % 2, 0:(hi - lo) * P], ACT.Copy).then_inc(moved, 1)

            def step(it, j, nxt):
                move(it, j, 0)
                move(it, j, 1)
                if nxt:
                    exp(*nxt, 0)
                move(it, j, 2)
                if nxt:
                    exp(*nxt, 1)

            exp(0, 0, 0)
            exp(0, 0, 1)
            with a.Fori(0, last) as it:
                step(it, 0, (it, 1))
                step(it, 1, (it + 1, 0))
            step(last, 0, (last, 1))
            step(last, 1, None)


def attention_output(core, m):
    nc, ps, o, oT = core.nc, core.ps, m["o2"], m["o2T"]
    sem = lambda n: core.semaphore("ao_" + n)
    squared, reduced, rooted, normed, turned, moved, pool_steps = map(sem, (
        "squared", "reduced", "rooted", "normed", "turned", "moved", "pool_steps"))
    sq = core.place(m["free"], NT * NH2, P)
    ss = core.place(m["free"] + NT * NH2 * P, NT * NH2)
    rs = core.place(m["free"] + NT * NH2 * P + 64, NT * NH2)
    rows = o.rearrange("p a (h e) -> p (a h) e", e=P)
    with nc.Block() as block:
        @block.scalar
        def _(a):
            a.activation(sq, rows, ACT.Square).then_inc(squared, 1)
            for i in range(NT):
                a.wait_ge(turned, i + 1)
                a.activation(oT[:, :, i * P:(i + 1) * P],
                             ps[:, i % 2, :].rearrange("p (a b) -> p a b", b=P), ACT.Copy).then_inc(moved, 1)

        @block.vector
        def _(v):
            v.wait_ge(squared, 1)
            v.tensor_reduce(ss, sq, AX, ALU.add).then_inc(reduced, 1)
            v.wait_ge(rooted, 1)
            for i in range(NT):
                r = rows[:, NH2 * i:NH2 * (i + 1), :]
                s_ = rs[:, NH2 * i:NH2 * (i + 1)].unsqueeze(2).to_broadcast([P, NH2, P])
                v.tensor_tensor(r, r, s_, ALU.mult).then_inc(normed, 1)
                v.wait_ge(normed, 2 * i + 1)
                v.scalar_tensor_tensor(r, r, 1.0 - LAM_INIT,
                                       core.col("subln").unsqueeze(1).to_broadcast([P, NH2, P]),
                                       ALU.mult, ALU.mult).then_inc(normed, 1)

        @block.gpsimd
        def _(g):
            g.wait_ge(reduced, 1)
            c = Chain(g, pool_steps)
            for i in range(4):
                t = inverse_root(c, g, core, rs[:, 8 * i:8 * i + 8], ss[:, 8 * i:8 * i + 8], 1.0 / P, RMS2_EPS)
                if i < 3:
                    c.did(t)
                else:
                    t.then_inc(rooted, 1)

        @block.tensor
        def _(pe):
            for i in range(NT):
                pe.wait_ge(normed, 2 * i + 2)
                if i >= 2:
                    pe.wait_ge(moved, i - 1)
                for h in range(NH2):
                    t = pe.transpose(ps[:, i % 2, h * P:(h + 1) * P], o[:, i, h * P:(h + 1) * P],
                                     core.col("ident"))
                t.then_inc(turned, 1)


def mix_output(core, m):
    nc, ps = core.nc, core.ps
    sem = lambda n: core.semaphore("mo_" + n)
    h_loaded = [sem(f"h{i}") for i in range(2)]
    h_stored = [sem(f"h_stored{i}") for i in range(2)]
    x_stored = [sem(f"x_stored{i}") for i in range(2)]
    (weights, zeroed, staged, made, squared, rooted, taken, h_ready, h_squared, h_rooted, x_ready,
     turned, moved, routed, kept, steps, pool_steps, ff_cleared) = map(sem, (
         "weights", "zeroed", "staged", "made", "squared", "rooted", "taken", "h_ready",
         "h_squared", "h_rooted", "x_ready", "turned", "moved", "routed", "kept", "steps",
         "pool_steps", "ff_cleared"))
    at = m["free"]

    def take(*shape):
        nonlocal at
        n = int(np.prod(shape))
        at += n
        return core.place(at - n, *shape)

    wo, wr = take(ND, D), take(ND, NE)
    mt = [take(ND, P) for _ in range(2)]
    hin, h, xn = ([take(D) for _ in range(2)] for _ in range(3))
    xT, sq, t, zero = take(ND, P), take(D), take(D), take(D)
    ss, rs, hs, hr = (take(1) for _ in range(4))
    g1, sh2, sc2 = m["rows"][0:3]
    with nc.Block() as block:
        @block.sync
        def _(sp):
            sp.dma_start(wr, core.ins["w_router2_k"]).then_inc(weights, 16)
            sp.dma_start(wo, core.ins["w_out2_k"]).then_inc(weights, 16)
            with sp.Fori(0, NT // 2) as it:
                for j in range(2):
                    sp.wait_ge(h_ready, it * 2 + j + 1)
                    sp.dma_start(hin[j], m["h2"][it * 2 + j]).then_inc(h_loaded[j], 16)
            sp.wait_ge(zeroed, 1)
            for i in range(NT):
                sp.dma_start(m["ff"][i], zero).then_inc(ff_cleared, 16)
            sp.wait_ge(ff_cleared, 16 * NT)

        @block.gpsimd
        def _(g):
            g.memset(zero, 0.0).then_inc(zeroed, 1)

            def stage(it, j):
                g.wait_ge(made, it * 2 + j + 1)
                core.waited(g)
                for i, src in ((0, m["o2T"]), (4, m["conv2"])):
                    g.tensor_copy(mt[j][:, i:i + 4, :], src[:, :, bass.ds(it * (2 * P) + j * P, P)])\
                     .then_inc(staged, 1)

            def roots(it, j):
                n = it * 2 + j
                c = Chain(g, pool_steps, n * 2)
                g.wait_ge(squared, n + 1)
                inverse_root(c, g, core, rs, ss, 1.0 / D, RMS2_EPS).then_inc(rooted, 1)
                g.wait_ge(h_squared, n + 1)
                inverse_root(c, g, core, hr, hs, 1.0 / D, RMS2_EPS).then_inc(h_rooted, 1)

            stage(0, 0)
            with g.Fori(0, NT // 2 - 1) as it:
                stage(it, 1)
                roots(it, 0)
                stage(it + 1, 0)
                roots(it, 1)
            last = NT // 2 - 1
            stage(last, 1)
            roots(last, 0)
            roots(last, 1)

        @block.tensor
        def _(pe):
            pe.sem_inc(made, 2)
            pe.wait_ge(weights, 32)

            def product(it, j):
                n = it * 2 + j
                pe.wait_ge(staged, n * 2 + 2)
                pe.wait_ge(taken, n + 1)
                for c in range(2):
                    for k in range(ND):
                        x = pe.matmul(ps[:, 2 * j + c, :], mt[j][:, k, :],
                                      wo[:, k, c * HALF:(c + 1) * HALF], start=(k == 0), stop=(k == ND - 1))
                x.then_inc(made, 1)

            def after(it, j):
                n = it * 2 + j
                pe.wait_ge(x_ready, n + 1)
                for k in range(ND):
                    x = pe.transpose(ps[:, 4 + k // 4, (k % 4) * P:(k % 4 + 1) * P],
                                     xn[j][:, k * P:(k + 1) * P], core.col("ident"))
                x.then_inc(turned, 1)
                pe.wait_ge(moved, n + 1)
                pe.wait_ge(kept, n)
                for k in range(ND):
                    x = pe.matmul(ps[:, 6, 0:NE], xT[:, k, :], wr[:, k, :], start=(k == 0), stop=(k == ND - 1))
                x.then_inc(routed, 1)

            product(0, 0)
            with pe.Fori(0, NT // 2 - 1) as it:
                product(it, 1)
                after(it, 0)
                product(it + 1, 0)
                after(it, 1)
            last = NT // 2 - 1
            product(last, 1)
            after(last, 0)
            after(last, 1)

        @block.scalar
        def _(a):
            with a.Fori(0, NT // 2) as it:
                for j in range(2):
                    n = it * 2 + j
                    a.wait_ge(made, n + 3)
                    a.wait_ge(h_squared, n)
                    a.activation(sq, flat2(ps, 2 * j), ACT.Square, accum_out=ss).then_inc(squared, 1)
                    a.wait_ge(h_ready, n + 3)
                    a.wait_ge(squared, n + 1)
                    a.activation(sq, h[j], ACT.Square, accum_out=hs).then_inc(h_squared, 1)
                    a.dma_start(m["h3"][n], h[j]).then_inc(h_stored[j], 16)
                    a.wait_ge(x_ready, n + 1)
                    a.dma_start(m["xn"][n], xn[j]).then_inc(x_stored[j], 16)
                    a.wait_ge(turned, n + 1)
                    a.wait_ge(routed, n)
                    a.activation(xT.rearrange("p a b -> p (a b)"), flat2(ps, 4), ACT.Copy).then_inc(moved, 1)
            for q in h_stored + x_stored:
                a.wait_ge(q, 16 * (NT // 2))

        @block.vector
        def _(v):
            v.sem_inc(taken, 2)
            v.sem_inc(h_ready, 2)
            per = 1

            def step(it, j):
                n = it * 2 + j
                c = Chain(v, steps, n * per)
                v.wait_ge(x_ready, n)
                v.wait_ge(rooted, n + 1)
                v.scalar_tensor_tensor(t, flat2(ps, 2 * j), rs, g1, ALU.mult, ALU.mult).then_inc(taken, 1)
                v.wait_ge(taken, n + 3)
                v.wait_ge(h_loaded[j], it * 16 + 16)
                v.wait_ge(h_stored[j], it * 16)
                v.tensor_tensor(h[j], t, hin[j], ALU.add).then_inc(h_ready, 1)
                v.wait_ge(h_rooted, n + 1)
                v.wait_ge(h_ready, n + 3)
                c.step(v.scalar_tensor_tensor(t, h[j], hr, sc2, ALU.mult, ALU.mult))
                v.wait_ge(x_stored[j], it * 16)
                v.tensor_tensor(xn[j], t, sh2, ALU.add).then_inc(x_ready, 1)
                assert c.n == per
                v.wait_ge(routed, n + 1)
                v.tensor_copy(m["logits2"][:, bass.ds(it * (2 * NE) + j * NE, NE)], ps[:, 6, 0:NE])\
                 .then_inc(kept, 1)

            with v.Fori(0, NT // 2) as it:
                step(it, 0)
                step(it, 1)



def expert_choice(core, m):
    nc, ps = core.nc, core.ps
    sem = lambda n: core.semaphore("ec_" + n)
    centred, exped, ready, turned, steps, chosen, back = map(sem, (
        "centred", "exped", "ready", "turned", "steps", "chosen", "back"))
    at = m["free"]
    aff = core.place(at, NT, NE)
    peak = core.place(at + P, NT)
    affT = core.place(at + 2 * P, S, parts=NE)
    val = core.place(at + 2 * P + S, CAP, parts=NE)
    idx = core.place(at + 3 * P + S, CAP, parts=NE, dt=mybir.dt.uint32)
    idf = core.place(at + 4 * P + S, CAP, parts=NE)
    fl = aff.rearrange("p a b -> p (a b)")
    spread = peak.unsqueeze(2).to_broadcast([P, NT, NE])
    with nc.Block() as block:
        @block.vector
        def _(v):
            c = Chain(v, steps)
            lg = m["logits2"].rearrange("p (a b) -> p a b", b=NE)
            c.step(v.tensor_reduce(peak, lg, AX, ALU.max))
            v.tensor_tensor(aff, lg, spread, ALU.subtract).then_inc(centred, 1)
            v.wait_ge(exped, 1)
            c.step(v.tensor_reduce(peak, aff, AX, ALU.add))
            c.step(v.reciprocal(peak, peak))
            v.tensor_tensor(aff, aff, spread, ALU.mult).then_inc(ready, 1)
            v.wait_ge(turned, 1)
            c.step(v.tensor_copy(affT, flat2(ps, 0)[0:NE]))
            for r in range(CAP // 8):
                best, where = val[:, 8 * r:8 * r + 8], idx[:, 8 * r:8 * r + 8]
                c.step(v.max(best, affT))
                c.step(v.max_index(where, best, affT))
                c.step(v.match_replace(affT, best, affT, -1.0))
            v.tensor_copy(idf, idx).then_inc(chosen, 1)
            v.wait_ge(back, 1)
            c.did(v.tensor_copy(m["ec_weight"], ps[:, 2, 0:NE]))
            c.did(v.tensor_copy(m["ec_token"], ps[:, 3, 0:NE]))

        @block.scalar
        def _(a):
            a.wait_ge(centred, 1)
            a.activation(fl, fl, ACT.Exp).then_inc(exped, 1)

        @block.tensor
        def _(pe):
            pe.wait_ge(ready, 1)
            for i in range(NT):
                t = pe.transpose(ps[0:NE, i // 4, (i % 4) * P:(i % 4 + 1) * P], aff[:, i, :], core.col("ident"))
            t.then_inc(turned, 1)
            pe.wait_ge(chosen, 1)
            pe.transpose(ps[:, 2, 0:NE], val, core.col("ident")[0:NE, 0:NE])
            pe.transpose(ps[:, 3, 0:NE], idf, core.col("ident")[0:NE, 0:NE]).then_inc(back, 1)


def chosen_experts(core, m):
    nc, ps = core.nc, core.ps
    sem = lambda n: core.semaphore("e2_" + n)
    NDN = 4
    gu_loaded = [sem(f"gu{k}") for k in range(ND)]
    dn_loaded = [sem(f"dn{k}") for k in range(NDN)]
    (gu_used, dn_used, x_staged, gathered, x_turned, x_moved, silu_done, h_ready, h_turned, h_moved,
     y_ready, y_staged, added) = map(sem, (
         "gu_used", "dn_used", "x_staged", "gathered", "x_turned", "x_moved", "silu_done",
         "h_ready", "h_turned", "h_moved", "y_ready", "y_staged", "added"))
    at = m["free"]

    def take(*shape, dt=None):
        nonlocal at
        n = int(np.prod(shape))
        at += n
        return core.place(at - n, *shape, dt=dt)

    gu = [take(2 * FE2) for _ in range(ND)]
    dn = [take(2, D) for _ in range(NDN)]
    x, xT, sg, h, hT, yo = take(D), take(ND, P), take(FE2), take(FE2), take(FE2 // P, P), take(D)
    xi, yi = take(1, dt=I32), take(1, dt=I32)
    token = m["ec_token"]
    with nc.Block() as block:
        @block.sync
        def _(sp):
            def load_gu(e):
                for k in range(ND):
                    sp.wait_ge(gu_used, e * ND + k + 1)
                    sp.dma_start(gu[k], core.ins["gate_up2"][e * ND + k]).then_inc(gu_loaded[k], 16)

            def load_dn(e):
                for k in range(NDN):
                    sp.wait_ge(dn_used, e * NDN + k + 1)
                    sp.dma_start(dn[k], core.ins["down2"][e * NDN + k]).then_inc(dn_loaded[k], 16)

            load_gu(0)
            with sp.Fori(0, NE - 1) as e:
                load_gu(e + 1)
                load_dn(e)
            load_dn(NE - 1)

        @block.gpsimd
        def _(g):
            def gather(e):
                g.wait_ge(x_turned, e)
                g.wait_ge(gathered, e * 16)
                g.tensor_copy(xi, token[:, bass.ds(e, 1)]).then_inc(x_staged, 1)
                g.wait_ge(x_staged, e + 1)
                core.waited(g)
                g.indirect_dma_start(x, None, m["xn_rows"], bass.IndirectOffsetOnAxis(ap=xi, axis=0))\
                 .then_inc(gathered, 16)

            def add(e):
                g.wait_ge(added, e * 16)
                g.tensor_copy(yi, token[:, bass.ds(e, 1)]).then_inc(y_staged, 1)
                g.wait_ge(y_staged, e + 1)
                g.wait_ge(y_ready, e + 1)
                core.waited(g)
                g.indirect_dma_start(m["ff_rows"], bass.IndirectOffsetOnAxis(ap=yi, axis=0), yo, None,
                                     compute_op=ALU.add).then_inc(added, 16)

            gather(0)
            gather(1)
            with g.Fori(2, NE) as e:
                gather(e)
                add(e - 2)
            add(NE - 2)
            add(NE - 1)
            g.wait_ge(added, 16 * NE)

        @block.tensor
        def _(pe):
            pe.sem_inc(gu_used, ND)
            pe.sem_inc(dn_used, NDN)

            def turn_x(e):
                pe.wait_ge(gathered, e * 16 + 16)
                if not isinstance(e, int):
                    pe.wait_ge(h_moved, e - 1)
                for k in range(ND):
                    t = pe.transpose(ps[:, 4 + k // 4, (k % 4) * P:(k % 4 + 1) * P],
                                     x[:, k * P:(k + 1) * P], core.col("ident"))
                t.then_inc(x_turned, 1)

            def up(e):
                pe.wait_ge(x_moved, e + 1)
                pe.wait_ge(h_ready, e)
                for k in range(ND):
                    pe.wait_ge(gu_loaded[k], e * 16 + 16)
                    for c in range(4):
                        t = pe.matmul(ps[:, c, :], xT[:, k, :], gu[k][:, c * HALF:(c + 1) * HALF],
                                      start=(k == 0), stop=(k == ND - 1), skip_group_check=True)
                    t.then_inc(gu_used, 1)

            def turn_h(e):
                pe.wait_ge(h_ready, e + 1)
                pe.wait_ge(x_moved, NE if isinstance(e, int) and e == NE - 1 else e + 2)
                for k in range(FE2 // P):
                    t = pe.transpose(ps[:, 4 + k // 4, (k % 4) * P:(k % 4 + 1) * P],
                                     h[:, k * P:(k + 1) * P], core.col("ident"))
                t.then_inc(h_turned, 1)

            def down(e):
                pe.wait_ge(h_moved, e + 1)
                pe.wait_ge(y_ready, e)
                for k in range(FE2 // P):
                    pe.wait_ge(dn_loaded[k // 2], e * 16 + 16)
                    for c in range(2):
                        t = pe.matmul(ps[:, 6 + c, :], hT[:, k, :], dn[k // 2][:, k % 2, c * HALF:(c + 1) * HALF],
                                      start=(k == 0), stop=(k == FE2 // P - 1), skip_group_check=True)
                    if k % 2:
                        t.then_inc(dn_used, 1)

            turn_x(0)
            up(0)
            turn_x(1)
            turn_h(0)
            with pe.Fori(1, NE - 1) as e:
                up(e)
                turn_x(e + 1)
                down(e - 1)
                turn_h(e)
            up(NE - 1)
            down(NE - 2)
            turn_h(NE - 1)
            down(NE - 1)

        @block.scalar
        def _(a):
            def move_x(e):
                a.wait_ge(x_turned, e + 1)
                a.wait_ge(gu_used, e * ND + ND)
                a.activation(xT.rearrange("p a b -> p (a b)"), flat2(ps, 4), ACT.Copy).then_inc(x_moved, 1)

            def silu(e):
                a.wait_ge(gu_used, e * ND + 2 * ND)
                a.wait_ge(h_ready, e)
                a.activation(sg, flat2(ps, 0), ACT.Silu).then_inc(silu_done, 1)

            move_x(0)
            silu(0)
            with a.Fori(1, NE) as e:
                move_x(e)
                silu(e)

        @block.vector
        def _(v):
            def gate(e):
                v.wait_ge(silu_done, e + 1)
                v.wait_ge(h_turned, e)
                v.tensor_tensor(h, sg, flat2(ps, 2), ALU.mult).then_inc(h_ready, 1)

            def move_h(e):
                v.wait_ge(h_turned, e + 1)
                v.wait_ge(dn_used, e * NDN + NDN)
                v.tensor_copy(hT.rearrange("p a b -> p (a b)"), flat2(ps, 4)).then_inc(h_moved, 1)

            def weigh(e):
                v.wait_ge(dn_used, e * NDN + 2 * NDN)
                v.wait_ge(added, e * 16)
                v.tensor_scalar(yo, flat2(ps, 6), m["ec_weight"][:, bass.ds(e, 1)], None,
                                ALU.mult).then_inc(y_ready, 1)

            gate(0)
            move_h(0)
            with v.Fori(1, NE) as e:
                gate(e)
                weigh(e - 1)
                move_h(e)
            weigh(NE - 1)


def last_residual(core, m):
    nc = core.nc
    sem = lambda n: core.semaphore("lr_" + n)
    NB = 4
    loaded = [sem(f"loaded{i}") for i in range(NB)]
    squared, rooted, ready, stored, pool_steps, scaled = map(sem, (
        "squared", "rooted", "ready", "stored", "pool_steps", "scaled"))
    at = m["free"]
    ff = [core.place(at + 2 * i * D, D) for i in range(NT)]
    h = [core.place(at + (2 * i + 1) * D, D) for i in range(NT)]
    sq = core.place(at + 2 * NT * D, D)
    ss, rs = core.place(at + (2 * NT + 1) * D, NT), core.place(at + (2 * NT + 1) * D + NT, NT)
    g2 = m["rows"][3]
    out = core.out.rearrange("o (i p) d -> (o i) p d", p=P)
    with nc.Block() as block:
        @block.sync
        def _(sp):
            for i in range(NT):
                sp.dma_start(ff[i], m["ff"][i]).then_inc(loaded[i % NB], 16)
                sp.dma_start(h[i], m["h3"][i]).then_inc(loaded[i % NB], 16)
                if i % NB == NB - 1 and i < NT - 1:
                    for q in loaded:
                        sp.wait_ge(q, 32 * (i // NB + 1))
            for i in range(NT):
                sp.wait_ge(ready, i + 1)
                sp.dma_start(out[i], h[i]).then_inc(stored, 16)
            sp.wait_ge(stored, 16 * NT)

        @block.scalar
        def _(a):
            for i in range(NT):
                a.wait_ge(loaded[i % NB], 32 * (i // NB + 1))
                if i:
                    a.wait_ge(squared, i)
                a.activation(sq, ff[i], ACT.Square, accum_out=ss[:, i:i + 1]).then_inc(squared, 1)

        @block.gpsimd
        def _(g):
            c = Chain(g, pool_steps)
            for i in range(NT):
                g.wait_ge(squared, i + 1)
                inverse_root(c, g, core, rs[:, i:i + 1], ss[:, i:i + 1], 1.0 / D, RMS2_EPS).then_inc(rooted, 1)

        @block.vector
        def _(v):
            for i in range(NT):
                v.wait_ge(rooted, i + 1)
                v.wait_ge(loaded[i % NB], 32 * (i // NB + 1))
                v.scalar_tensor_tensor(ff[i], ff[i], rs[:, i:i + 1], g2, ALU.mult, ALU.mult).then_inc(scaled, 1)
                v.wait_ge(scaled, i + 1)
                v.tensor_tensor(h[i], h[i], ff[i], ALU.add).then_inc(ready, 1)



def build(nc, ins, out):
    with ExitStack() as ctx:
        core = Core(nc, ctx, ins, out)
        small = NCOLS

        def keep(*shape, **kw):
            nonlocal small
            n = int(np.prod(shape))
            small += n
            assert small <= BASE, small
            return core.place(small - n, *shape, **kw)

        def at(x):
            return BASE + x

        def run(stage, *args):
            stage(core, *args)

        dram = core.scratch
        m = {
            "xhat": dram("xhat", [NT, P, D]), "h1": dram("h1", [NT, P, D]),
            "rest": dram("rest", [NT, P, D]), "qn": dram("q_nope", [4, P, S]),
            "qr": dram("q_rope", [2, P, S]), "kn": dram("k_nope", [4, P, S]),
            "kr": dram("k_rope", [ROPE, S]), "mod": dram("modulation", [2, 6 * D]),
            "slot_dram": dram("slot_token", [NBLK * P, 1], I32), "y1": dram("y1", [NBLK, P, D]),
            "h2": dram("h2", [NT, P, D]), "h3": dram("h3", [NT, P, D]), "xn": dram("xn", [NT, P, D]),
            "ff": dram("ff", [NT, P, D]),
            "logits": keep(P), "weights": keep(2 * NT), "dest": keep(2 * NT, dt=I32),
            "token": keep(NT, dt=I32), "plan": keep(3 * NBLK, dt=I32),
            "slot_token": keep(NBLK, dt=I32), "slot_token_rows": keep(P, parts=NBLK, dt=I32),
            "zero_i": keep(P, dt=I32), "mod_cols": keep(4 * ND), "tiny": keep(4), "neg_lam": keep(1),
            "logits2": keep(P), "ec_weight": keep(NE), "ec_token": keep(NE, dt=I32),
        }
        for name in ("h1", "y1", "xn", "ff"):
            m[name + "_rows"] = m[name].rearrange("a p d -> (a p) d")

        m["hT"] = core.place(at(0), ND, S)
        m["u"] = core.place(at(8192), 4, PADU + S)
        m["z"] = core.place(at(12352), 4, PADZ + S)
        m["acc"] = core.place(at(16576), 4, S)
        m["vt"] = core.place(at(20672), NT, HALF)
        m["poolT"] = m["u"][:, :, PADU:]
        m["oT"] = core.place(at(24768), 4, S)
        m["merged"] = core.place(at(28864), ND, S)
        run(load_constants)
        run(modulation, at(0), m["mod"])
        run(input_norm, at(8192), m["xhat"], m["hT"])
        run(pool_and_conv_inputs, m["hT"], m["u"], m["z"], at(16576))
        m["free"] = at(24768)
        run(heads_and_branches, m)
        run(conv_finish, m)
        m["free"] = at(28864)
        run(latent_attention, m)
        m["free"] = at(37056)
        run(merge, m)
        m["low"], m["high"] = at(0), at(37056)
        run(output_and_gate, m)
        m["free"] = at(0)
        core.free_semaphores()
        run(route, m)
        run(grouped_experts, m)

        m["free"] = at(0)
        run(prepare_columns, m)
        m["xnT"] = core.place(at(0), ND, SA)
        m["free"] = at(10240)
        run(context_input, m)
        run(combine_experts, m)
        m["qconv"] = core.place(at(10240), 16, S)
        m["kv"] = core.place(at(26624), 8, SA)
        m["free"] = at(36864)
        run(second_projections, m)
        m["q2"] = core.place(at(0), 4, 2, S, parts=64)
        m["k2"] = core.place(at(36864), 4, 2, SA, parts=64)
        m["tables"], m["tmp"] = at(47104), at(8192)
        m["v2"] = core.place(at(8192), NK2, HALF)
        m["conv2"] = core.place(at(22528), 4, S)
        core.free_semaphores()
        run(rotate_and_convolve, m)
        m["free"] = at(13312)
        m["o2"] = core.place(at(26624), NT, HALF)
        run(differential_attention, m)
        m["o2T"] = core.place(at(30720), 4, S)
        m["free"] = at(0)
        run(attention_output, m)
        m["rows"] = [core.place(at(34816 + i * D), D) for i in range(7)]
        run(prepare_rows, m)
        run(mix_output, m)
        run(expert_choice, m)
        run(chosen_experts, m)
        run(last_residual, m)


def columns(a, n):
    return np.asarray(a).reshape(n, P).T


def constants(f):
    part = np.arange(P)
    c = {name: np.zeros((P, n), np.float32) for name, (_, n) in COLS.items()}
    c["ident"][:] = np.eye(P)
    c["ones"][:] = 1
    c["before"][:] = part[:, None] < part[None, :]
    other = (part // 32) * 32 + (part % 32 + 16) % 32
    c["swap"][other, part] = 1
    c["turn"][other, part] = np.where(part % 32 < 16, -1, 1)
    c["sin_sign"][:, 0] = np.where(part % 32 < 16, -1, 1)
    freq = (10000.0 ** (-np.arange(0, ROPE, 2) / ROPE)).astype(np.float32)
    c["inv_freq"][:, 0] = freq[part % 16]
    for g, w in enumerate(WINDOWS):
        c["pool_inv"][:, 16 * g:16 * g + 16] = 1.0 / np.minimum(np.arange(16) + 1, w)
    c["low16"][:] = NE - np.arange(NE)
    c["order4"][:] = NG - np.arange(NG)
    c["block0"][:] = np.arange(NBLK + 1)
    c["token"][:] = np.arange(NT)[None, :] * P + part[:, None]
    c["neg_half"][:] = -0.5
    c["eps_rms"][:] = RMS_EPS
    c["eps_ln"][:] = LN_EPS
    for name, key in (("ln_in_g", "ln_in_g"), ("ln_in_b", "ln_in_b"), ("conv_b", "conv_b"),
                      ("conv_ln_g", "conv_ln_g"), ("conv_ln_b", "conv_ln_b"),
                      ("pool_scale", "pool_scale"), ("q_norm", "q_norm_g"), ("kv_norm", "kv_norm_g"),
                      ("pre_mix", "norm_pre_mix_2"), ("c", "c_2"), ("c_ctx", "c_ctx_2")):
        c[name][:] = columns(f[key], COLS[name][1])
    c["conv_dw"][:] = f["conv_dw"].reshape(TAPS, 4, P).transpose(2, 1, 0).reshape(P, 4 * TAPS)
    c["conv2"][:] = f["conv_w_2"].reshape(3, 4, P).transpose(2, 1, 0).reshape(P, 12)
    c["subln"][:] = f["subln_g_2"].reshape(1, P)
    c["bias_r"][:] = f["router_bias"].reshape(1, NE)
    c["lams"][:] = np.concatenate([f[k].reshape(-1) for k in (
        "lambda_q1_2", "lambda_k1_2", "lambda_q2_2", "lambda_k2_2")])[None, :]
    return np.ascontiguousarray(np.concatenate([c[name] for name in COLS], axis=1))


def by_k(w):
    return w.reshape(-1, P, w.shape[-1]).transpose(1, 0, 2)


def tiles_of(w):
    return w.reshape(ND, P, -1, P).transpose(2, 1, 0, 3)


def kernel(**inputs):
    import concourse.bacc as bacc
    from concourse.bass_utils import run_bass_kernel_spmd

    f = {k: np.asarray(v) for k, v in inputs.items()}
    w_in = f["w_in"][0]
    at = {"pool": 0, "a": 512, "gate": 1024, "cq": 1536, "ckv": 1920, "kr": 2176, "gates": 2208}
    first = [w_in[:, 0:512]]
    for t in range(4):
        first += [w_in[:, at["gate"] + t * P:at["gate"] + (t + 1) * P],
                  w_in[:, at["a"] + t * P:at["a"] + (t + 1) * P]]
    first += [w_in[:, at["cq"]:at["kr"] + ROPE], np.zeros((D, P - ROPE), np.float32)]
    uq = f["w_uq"][0].reshape(3 * P, NH1, QD)
    ukv = f["w_ukv"][0].reshape(2 * P, NH1, NOPE + VH)
    w2 = f["w_in_2"][0]
    part = lambda i: w2[:, i * HALF:(i + 1) * HALF]
    gates = w_in[:, at["gates"]:].reshape(ND, P, 3, ND, P).transpose(3, 1, 2, 0, 4).reshape(ND, P, 24 * P)
    projs = np.stack([f[k][0] for k in ("pool_proj", "conv_proj", "mla_proj")])
    projs = projs.reshape(3, 4, P, ND, P).transpose(3, 2, 0, 1, 4).reshape(ND, P, 12 * P)
    biases = f["b_gate"][0].reshape(3, ND, P).transpose(1, 2, 0)
    pad = np.zeros((ND, P, 1), np.float32)
    axis = np.arange(S)
    inv = (np.float32(10000.0) ** (-np.arange(0, 32, 2, dtype=np.float32) / np.float32(32))).astype(np.float32)
    row = (axis // 64).astype(np.float32)[:, None] * inv
    colm = (axis % 64).astype(np.float32)[:, None] * inv
    ang = np.concatenate([row, row, colm, colm], axis=1).T
    ang = np.concatenate([ang, ang], axis=0)
    slab = lambda w: w.reshape(NE, ND, P, FE2)
    arrays = {
        "packed": constants(f), "x": f["x"], "ctx": f["ctx_2"], "b_ada": f["b_ada_2"],
        "w_ada": f["w_ada_2"][0].reshape(ND, P, 12, HALF).transpose(2, 1, 0, 3),
        "w_in_tiles": tiles_of(np.concatenate(first, axis=1)),
        "positions": f["positions"].reshape(S),
        "w_uq_k": by_k(np.concatenate([uq[:, :, :NOPE].reshape(3 * P, -1), uq[:, :, NOPE:].reshape(3 * P, -1)],
                                      axis=1)),
        "w_ukv_k": by_k(np.concatenate([ukv[:, :, :NOPE].reshape(2 * P, -1),
                                        ukv[:, :, NOPE:].reshape(2 * P, -1)], axis=1)),
        "pool_w_k": f["pool_w"][0].transpose(1, 0, 2),
        "merge_w": np.concatenate([gates, projs, biases, pad], axis=2),
        "w_out_k": by_k(f["w_out"][0]), "w_router_k": by_k(f["w_router"]),
        "ln_in_g": f["ln_in_g"], "ln_in_b": f["ln_in_b"], "ln1_g": f["ln1_g"][0], "ln1_b": f["ln1_b"][0],
        "ln2_g": f["ln2_g"][0], "ln2_b": f["ln2_b"][0], "norm_post_mix": f["norm_post_mix_2"][0],
        "norm_pre_ffn": f["norm_pre_ffn_2"][0], "norm_post_ffn": f["norm_post_ffn_2"][0],
        "ple_proj_k": by_k(f["ple_proj"][0]), "ple_gate_k": by_k(f["ple_gate"][0]),
        "p_tiles": f["p"].reshape(NT, P, 2 * P),
        "exp_up_k": f["exp_w_up"][0].reshape(NE, ND, P, 2 * FE).transpose(0, 2, 1, 3).reshape(NE, P, -1),
        "exp_down_k": f["exp_w_down"][0].reshape(NE, 4, P, D).transpose(0, 2, 1, 3).reshape(NE, P, -1),
        "w_in2_tiles": tiles_of(np.concatenate([part(0), part(3), part(4), part(5), part(1), part(2)], axis=1)),
        "cos2": np.cos(ang), "sin2": np.sin(ang),
        "w_out2_k": by_k(f["w_out_2"][0]), "w_router2_k": by_k(f["w_router_2"][0]),
        "gate_up2": np.concatenate([slab(f["w_gate_2"][0]), slab(f["w_up_2"][0])], axis=3)
                      .reshape(NE * ND, P, 2 * FE2),
        "down2": f["w_down_2"][0].reshape(NE * 4, 2, P, D).transpose(0, 2, 1, 3),
    }
    arrays = {k: np.ascontiguousarray(v) for k, v in arrays.items()}
    for k, v in arrays.items():
        assert v.dtype == (np.int32 if k == "positions" else np.float32), (k, v.dtype)
    nc = bacc.Bacc("TRN2", target_bir_lowering=False, num_devices=1)
    ins = {k: nc.dram_tensor("in_" + k, v.shape, I32 if v.dtype == np.int32 else F32,
                             kind="ExternalInput").ap() for k, v in arrays.items()}
    out = nc.dram_tensor("out", (1, S, D), F32, kind="ExternalOutput").ap()
    build(nc, ins, out)
    r = run_bass_kernel_spmd(nc, [{"in_" + k: v for k, v in arrays.items()}], core_ids=[0])
    return r.results[0]["out"]
```

```python
from contextlib import ExitStack

import numpy as np

import concourse.bass as bass
from concourse import mybir

F32 = mybir.dt.float32
I32 = mybir.dt.int32
F32R = mybir.dt.float32r
ALU = mybir.AluOpType
ACT = mybir.ActivationFunctionType
AX = mybir.AxisListType.X

P = 128
S = 1024
D = 1024
NT = S // P
ND = D // P
HALF = 512
CTX = 256
NTC = CTX // P
SA = S + CTX
NH1, NOPE, ROPE, VH = 8, 64, 32, 64
QD = NOPE + ROPE
TAPS = 31
PADZ = 32
PADU = 16
WINDOWS = (2, 4, 8, 16)
NE, NG, EPG = 16, 4, 4
ALPHA = 2.0 ** 0.25
NBLK = (2 * S + NE * P - 1) // P
LN_EPS, RMS_EPS, RMS2_EPS = 1e-5, 1e-6, 1e-6
FE = 512
NH2, HD2 = 4, 64
NK2 = SA // P
CAP = 2 * S // NE
FE2 = 1024
LAM_INIT = 0.8 - 0.6
BIG = 1e30

COLS = {}


def _columns():
    at = 0
    for name, n in (
        ("ident", 128), ("ones", 128), ("before", 128), ("swap", 128), ("turn", 128),
        ("ln_in_g", 8), ("ln_in_b", 8), ("conv_dw", 4 * TAPS), ("conv_b", 4), ("conv_ln_g", 4),
        ("conv_ln_b", 4), ("pool_scale", 4), ("q_norm", 3), ("kv_norm", 2), ("inv_freq", 1),
        ("sin_sign", 1), ("pool_inv", 64), ("pre_mix", 8), ("subln", 128), ("bias_r", 16),
        ("low16", 16), ("order4", 4), ("block0", NBLK + 1), ("token", NT), ("neg_half", 8),
        ("lams", 4 * HD2), ("c", 8), ("c_ctx", 8), ("zeros", 32),
        ("eps_rms", 1), ("eps_ln", 1), ("conv2", 12),
    ):
        COLS[name] = (at, n)
        at += n
    return at


NCOLS = _columns()
ARENA = 52096
BASE = 2560
UPPER = BASE + 20672


class Chain:

    def __init__(self, eng, sem, start=0):
        self.eng, self.sem, self.start, self.n = eng, sem, start, 0

    def did(self, ins):
        ins.then_inc(self.sem, 1)
        self.n += 1

    def wait(self):
        self.eng.wait_ge(self.sem, self.start + self.n)

    def step(self, ins):
        self.did(ins)
        self.wait()


class Core:

    def __init__(self, nc, ctx, ins, out):
        self.nc, self.ins, self.out = nc, ins, out
        self.upper = None
        self.loaded = nc.alloc_semaphore("constants_loaded")
        self.passed = nc.alloc_semaphore("waits_passed")
        self.used = []
        self.arena = ctx.enter_context(nc.sbuf_tensor("arena", [P, UPPER], F32))
        self.ps = ctx.enter_context(nc.psum_tensor("banks", [P, 8, HALF], F32))

    def open_upper(self, ctx, name, dt=F32):
        self.upper = ctx.enter_context(self.nc.sbuf_tensor(name, [P, ARENA - UPPER], dt))

    def place(self, at, *shape, parts=P, dt=None):
        n = int(np.prod(shape))
        assert at + n <= (UPPER if at < UPPER else ARENA), (at, shape)
        if at < UPPER:
            v = self.arena[0:parts, at:at + n]
        else:
            v = self.upper[0:parts, at - UPPER:at - UPPER + n]
        if dt is not None:
            v = v.bitcast(dt)
        if len(shape) == 2:
            v = v.rearrange("p (a b) -> p a b", a=shape[0])
        elif len(shape) == 3:
            v = v.rearrange("p (a b c) -> p a b c", a=shape[0], b=shape[1])
        return v

    def col(self, name, a=0, b=None):
        at, n = COLS[name]
        return self.arena[:, at + a:at + (n if b is None else b)]

    def semaphore(self, name):
        sem = self.nc.alloc_semaphore(name)
        self.used.append(sem)
        return sem

    def waited(self, eng):
        eng.sem_inc(self.passed, 1)

    def free_semaphores(self):
        with self.nc.Block() as block:
            @block.gpsimd
            def _(g):
                self.nc.clear_and_free_semaphores(self.used)
        self.used = []

    def scratch(self, name, shape, dt=F32):
        return self.nc.dram_tensor(name, shape, dt).ap()


def rounded(ap):
    return ap.bitcast(F32R)


def plain(ap):
    return ap.bitcast(F32)


def three_passes(pe, out, lhs, rhs, first, last):
    (lh, ll), (rh, rl) = lhs, rhs
    pe.matmul(out, rounded(lh), rounded(rh), start=first, stop=False, skip_group_check=True)
    pe.matmul(out, rounded(lh), rounded(rl), start=False, stop=False, skip_group_check=True)
    return pe.matmul(out, rounded(ll), rounded(rh), start=False, stop=last, skip_group_check=True)


def row_on_all(vec, n):
    return vec.rearrange("(a n) -> a n", a=1).broadcast_to([P, n])


def inverse_root(chain, pool, core, out, x, scale, eps):
    n = out.shape[-1]
    core.waited(pool)
    chain.step(pool.tensor_scalar(out, x, float(scale), float(eps), ALU.mult, ALU.add))
    return pool.tensor_tensor(out, out, core.col("neg_half", 0, n), ALU.pow)



def load_constants(core):
    nc = core.nc
    got = core.loaded
    with nc.Block() as block:
        @block.sync
        def _(sp):
            sp.dma_start(core.arena[:, 0:NCOLS], core.ins["packed"]).then_inc(got, 16)
            sp.wait_ge(got, 16)


def input_norm(core, x_at, xhat_dram, hT):
    nc, ps = core.nc, core.ps
    sem = lambda n: core.semaphore("n1_" + n)
    loaded = [sem(f"loaded{i}") for i in range(NT)]
    stats, rstd_done, xhat_done, turned, taken, stored, steps, pool_steps = map(
        sem, ("stats", "rstd", "xhat", "turned", "taken", "stored", "steps", "pool_steps"))
    x = core.place(x_at, NT, D)
    st = core.place(x_at + NT * D, NT, 12)
    mv = core.place(x_at + NT * D + 96, NT, 2)
    rstd = core.place(x_at + NT * D + 112, NT)
    xin = core.ins["x"].rearrange("o (i p) d -> (o i) p d", p=P)
    with nc.Block() as block:
        @block.sync
        def _(sp):
            for i in range(NT):
                sp.dma_start(x[:, i, :], xin[i]).then_inc(loaded[i], 16)
            for i in range(NT):
                sp.wait_ge(xhat_done, i + 1)
                sp.dma_start(xhat_dram[i], x[:, i, :]).then_inc(stored, 16)
            sp.wait_ge(stored, 16 * NT)

        @block.vector
        def _(v):
            c = Chain(v, steps)
            for i in range(NT):
                v.wait_ge(loaded[i], 16)
                for j in range(2):
                    c.did(v.bn_stats(st[:, i, 6 * j:6 * j + 6], x[:, i, HALF * j:HALF * (j + 1)]))
                c.wait()
                v.bn_aggr(mv[:, i, :], st[:, i, :]).then_inc(stats, 1)
            v.wait_ge(stats, NT)
            v.wait_ge(rstd_done, 1)
            for i in range(NT):
                v.tensor_scalar(x[:, i, :], x[:, i, :], mv[:, i, 0:1], rstd[:, i:i + 1],
                                ALU.subtract, ALU.mult).then_inc(xhat_done, 1)

        @block.gpsimd
        def _(g):
            g.wait_ge(stats, NT)
            inverse_root(Chain(g, pool_steps), g, core, rstd, mv[:, :, 1], 1.0,
                         LN_EPS).then_inc(rstd_done, 1)

        @block.tensor
        def _(pe):
            for i in range(NT):
                pe.wait_ge(xhat_done, i + 1)
                for b in range(2):
                    if i >= 2:
                        pe.wait_ge(taken, 2 * (i - 2) + b + 1)
                    for k in range(4):
                        kk = 4 * b + k
                        t = pe.transpose(ps[:, 2 * (i % 2) + b, k * P:(k + 1) * P],
                                         x[:, i, kk * P:(kk + 1) * P], core.col("ident"))
                    t.then_inc(turned, 1)

        @block.scalar
        def _(a):
            for i in range(NT):
                for b in range(2):
                    a.wait_ge(turned, 2 * i + b + 1)
                    for k in range(4):
                        kk = 4 * b + k
                        t = a.activation(hT[:, kk, i * P:(i + 1) * P],
                                         ps[:, 2 * (i % 2) + b, k * P:(k + 1) * P], ACT.Identity,
                                         bias=core.col("ln_in_b", kk, kk + 1),
                                         scale=core.col("ln_in_g", kk, kk + 1))
                    t.then_inc(taken, 1)



def modulation(core, at, mod_dram):
    nc, ps = core.nc, core.ps
    sem = lambda n: core.semaphore("ada_" + n)
    loaded = [sem(f"w{i}") for i in range(2)]
    b_loaded, act_ready, done, taken = map(sem, ("b", "silu", "done", "taken"))
    n_chunks = 6 * D // HALF
    w = [core.place(at + i * ND * HALF, ND, HALF) for i in range(2)]
    row = core.place(at + 2 * ND * HALF, n_chunks * HALF, parts=2)
    bias = core.place(at + 2 * ND * HALF + n_chunks * HALF, n_chunks * HALF, parts=2)
    both = core.place(at + 2 * ND * HALF + 2 * n_chunks * HALF, ND, 2)
    stored = sem("stored")
    with nc.Block() as block:
        @block.sync
        def _(sp):
            sp.dma_start(bias, core.ins["b_ada"].broadcast_to([2, 6 * D])).then_inc(b_loaded, 16)
            with sp.Fori(0, n_chunks // 2) as i:
                for j in range(2):
                    sp.wait_ge(done, i * 2 + j + 1)
                    sp.dma_start(w[j], core.ins["w_ada"][i * 2 + j]).then_inc(loaded[j], 16)
            sp.wait_ge(taken, n_chunks + 2)
            sp.dma_start(mod_dram, row).then_inc(stored, 16)
            sp.wait_ge(stored, 16)

        @block.tensor
        def _(pe):
            pe.sem_inc(done, 2)
            pe.wait_ge(act_ready, 2)
            with pe.Fori(0, n_chunks // 2) as i:
                for j in range(2):
                    pe.wait_ge(loaded[j], i * 16 + 16)
                    pe.wait_ge(taken, i * 2 + j + 1)
                    for k in range(ND):
                        t = pe.matmul(ps[0:2, j, :], both[:, k, :], w[j][:, k, :],
                                      start=(k == 0), stop=(k == ND - 1))
                    t.then_inc(done, 1)

        @block.scalar
        def _(a):
            a.activation(both[:, :, 0], core.col("c"), ACT.Silu).then_inc(act_ready, 1)
            a.activation(both[:, :, 1], core.col("c_ctx"), ACT.Silu).then_inc(act_ready, 1)

        @block.vector
        def _(v):
            v.sem_inc(taken, 2)
            v.wait_ge(b_loaded, 16)
            with v.Fori(0, n_chunks // 2) as i:
                for j in range(2):
                    v.wait_ge(done, i * 2 + j + 3)
                    here = bass.ds(i * (2 * HALF) + j * HALF, HALF)
                    v.tensor_tensor(row[:, here], ps[0:2, j, :], bias[:, here], ALU.add).then_inc(taken, 1)



def loads_of_tiles(sp, w, w_dram, first, pairs, loaded, done, before=0):
    with sp.Fori(0, pairs) as i:
        for j in range(2):
            sp.wait_ge(done, i * 2 + before + j + 1)
            sp.dma_start(w[j], w_dram[i * 2 + (first + j)]).then_inc(loaded[j], 16)


def tile_products(pe, ps, act, w, loaded, done, taken, pairs, widths, before=0):
    nb = len(widths)
    with pe.Fori(0, pairs) as i:
        for j in range(2):
            pe.wait_ge(loaded[j], i * 16 + (8 * before + 16))
            pe.wait_ge(taken[j], i + before // 2 + 1)
            for c, width in enumerate(widths):
                for k in range(ND):
                    m = pe.matmul(ps[:, nb * j + c, 0:width], w[j][:, k, :],
                                  act[:, k, c * HALF:c * HALF + width],
                                  start=(k == 0), stop=(k == ND - 1))
            m.then_inc(done, 1)


def copy_tiles(a, ps, dst, done, taken, pairs, widths, shift=0, before=0):
    nb = len(widths)
    with a.Fori(0, pairs) as i:
        for j in range(2):
            a.wait_ge(done, i * 2 + (before + j + 3))
            a.wait_ge(done, 2)
            for c, width in enumerate(widths):
                m = a.activation(dst[:, bass.ds(i * 2 + j, 1), shift + c * HALF:shift + c * HALF + width],
                                 ps[:, nb * j + c:nb * j + c + 1, 0:width], ACT.Copy)
            m.then_inc(taken[j], 1)


def pool_and_conv_inputs(core, hT, u, z, w_at):
    nc, ps = core.nc, core.ps
    sem = lambda n: core.semaphore("in_" + n)
    loaded = [sem(f"w{i}") for i in range(2)]
    taken = [sem(f"taken{i}") for i in range(2)]
    done, cleared = map(sem, ("done", "cleared"))
    w = [core.place(w_at + i * D, ND, P) for i in range(2)]
    sg = core.place(w_at + 2 * D, S)
    wd = core.ins["w_in_tiles"]
    with nc.Block() as block:
        @block.sync
        def _(sp):
            loads_of_tiles(sp, w, wd, 0, 6, loaded, done)

        @block.gpsimd
        def _(g):
            g.memset(u[:, :, 0:PADU], 0.0).then_inc(cleared, 1)
            g.memset(z[:, :, 0:PADZ], 0.0).then_inc(cleared, 1)
            g.wait_ge(cleared, 2)

        @block.tensor
        def _(pe):
            pe.sem_inc(done, 2)
            tile_products(pe, ps, hT, w, loaded, done, taken, 6, (HALF, HALF))

        @block.scalar
        def _(a):
            a.sem_inc(taken[0], 1)
            a.sem_inc(taken[1], 1)
            copy_tiles(a, ps, u, done, taken, 2, (HALF, HALF), PADU)
            with a.Fori(0, 4) as i:
                a.wait_ge(done, i * 2 + 7)
                a.wait_ge(taken[1], i + 3)
                for c in range(2):
                    m = a.activation(sg[:, c * HALF:(c + 1) * HALF], ps[:, c, :], ACT.Sigmoid)
                m.then_inc(taken[0], 1)

        @block.vector
        def _(v):
            with v.Fori(0, 4) as i:
                v.wait_ge(taken[0], i + 4)
                v.wait_ge(done, i * 2 + 8)
                v.tensor_tensor(z[:, bass.ds(i, 1), PADZ:PADZ + HALF],
                                sg[:, 0:HALF].unsqueeze(1), ps[:, 2:3, :], ALU.mult)
                v.tensor_tensor(z[:, bass.ds(i, 1), PADZ + HALF:PADZ + S],
                                sg[:, HALF:S].unsqueeze(1), ps[:, 3:4, :], ALU.mult).then_inc(taken[1], 1)



def rope_tables(chain, core, pos_i, ang, sin_arg, cos_arg):
    v = chain.eng
    two_pi = 2.0 * np.pi
    c1 = float(np.float32(6.28125))
    c2 = float(np.float32(two_pi - c1))
    c2 = float((np.float32(c2).view(np.uint32) & np.uint32(0xFFFFF000)).view(np.float32))
    c3 = float(np.float32(two_pi - c1 - c2))
    magic = float(1.5 * 2 ** 23)
    limit = float(np.float32(np.pi)) - 1e-6
    chain.step(v.tensor_copy(ang, pos_i))
    chain.step(v.tensor_scalar(ang, ang, core.col("inv_freq"), None, ALU.mult))
    for out, turn in ((sin_arg, 0.0), (cos_arg, 0.25)):
        chain.step(v.tensor_scalar(out, ang, float(1 / two_pi), turn, ALU.mult, ALU.add))
        chain.step(v.tensor_scalar(out, out, magic, magic, ALU.add, ALU.subtract))
    for out, turn, tmp in ((sin_arg, 0.0, pos_i.bitcast(F32)), (cos_arg, 0.25, pos_i.bitcast(F32))):
        chain.step(v.scalar_tensor_tensor(tmp, out, -c1, ang, ALU.mult, ALU.add))
        chain.step(v.scalar_tensor_tensor(tmp, out, -c2, tmp, ALU.mult, ALU.add))
        chain.step(v.scalar_tensor_tensor(tmp, out, -c3, tmp, ALU.mult, ALU.add))
        chain.step(v.tensor_scalar(tmp, tmp, turn * two_pi, limit, ALU.add, ALU.min))
        chain.step(v.tensor_scalar(out, tmp, -limit, None, ALU.max))


def heads_and_branches(core, m):
    nc, ps, hT, u, z, acc, vt = core.nc, core.ps, m["hT"], m["u"], m["z"], m["acc"], m["vt"]
    sem = lambda n: core.semaphore("hb_" + n)
    loaded = [sem(f"w{i}") for i in range(2)]
    taken = [sem(f"taken{i}") for i in range(2)]
    stored = [sem(f"stored{i}") for i in range(2)]
    rows_stored = sem("rows_stored")
    (done, pos_loaded, uq_loaded, ukv_loaded, pw_loaded, steps, taps, trig_args, trig, squared,
     scaled, made, evac, turned, pool_steps, mixed, inverted) = map(sem, (
         "done", "pos_loaded", "uq_loaded", "ukv_loaded", "pw_loaded", "steps", "taps", "trig_args",
         "trig", "squared", "scaled", "made", "evac", "turned", "pool_steps", "mixed", "inverted"))
    at = m["free"]
    t1, t2 = core.place(at, PADU + S), core.place(at + PADU + S, PADU + S)
    wp = core.place(at + 2 * (PADU + S), 4, P)
    at += 2 * (PADU + S) + 4 * P
    lat = core.place(at, 6, S)
    at += 6 * S
    w = [core.place(at + i * D, ND, P) for i in range(2)]
    ksw, qsw1 = core.place(at, S, parts=ROPE), core.place(at + D, S)
    at += 2 * D
    wuq = core.place(at, 3, 6 * P)
    wukv = core.place(at + 18 * P, 2, 2 * HALF)
    at += 18 * P + 4 * HALF
    sin_t, cos_t = core.place(at, S), core.place(at + S, S)
    rs = [core.place(at + 2 * S, S), core.place(at + 3 * S, S)]
    st = [core.place(at + 4 * S, S), core.place(at + 5 * S, S)]
    qraw = [core.place(at + 6 * S, S), core.place(at + 7 * S, S)]
    qsw = [core.place(at + 8 * S, S), qsw1]
    sq = [st[0], st[1], qraw[0], qraw[1], qsw[0]]
    wd = core.ins["w_in_tiles"]
    taps_first = 18
    NTAP = 4
    halves = lambda t: t.rearrange("p (a b) -> p a b", a=2)
    dest = {0: rs[0], 1: rs[1], 6: qraw[0], 7: qraw[1], 8: qsw[0], 9: qsw[1]}
    for n in (2, 3, 4, 5, 11, 12, 13, 14):
        dest[n] = st[n % 2]

    with nc.Block() as block:
        @block.sync
        def _(sp):
            sp.dma_start(rs[1].bitcast(I32), row_on_all(core.ins["positions"], S)).then_inc(pos_loaded, 16)
            loads_of_tiles(sp, w, wd, 12, 3, loaded, done)
            sp.dma_start(wp, core.ins["pool_w_k"]).then_inc(pw_loaded, 16)
            sp.dma_start(wuq, core.ins["w_uq_k"]).then_inc(uq_loaded, 16)
            sp.dma_start(wukv, core.ins["w_ukv_k"]).then_inc(ukv_loaded, 16)
            for n in range(2, 6):
                sp.wait_ge(evac, n + 1)
                sp.dma_start(m["qn"][n - 2], dest[n]).then_inc(stored[n % 2], 16)
            for g in range(2):
                sp.wait_ge(turned, g + 1)
                sp.dma_start(m["qr"][g], qraw[g]).then_inc(rows_stored, 16)
            sp.wait_ge(turned, 3)
            sp.dma_start(m["kr"], lat[0:ROPE, 5, :]).then_inc(rows_stored, 16)
            for n in range(11, 15):
                sp.wait_ge(evac, n + 1)
                sp.dma_start(m["kn"][n - 11], dest[n]).then_inc(stored[n % 2], 16)
            for q in stored:
                sp.wait_ge(q, 16 * 4)
            sp.wait_ge(rows_stored, 16 * 3)

        @block.tensor
        def _(pe):
            pe.sem_inc(done, 2)
            tile_products(pe, ps, hT, w, loaded, done, taken, 3, (HALF, HALF))

            def unit(n, kk, lhs, rhs, rows=P):
                b = 4 + 2 * (n % 2)
                if n >= 2:
                    pe.wait_ge(evac, n - 1)
                for c in range(2):
                    for k in range(kk):
                        t = pe.matmul(ps[0:rows, b + c, :], lhs(k, c), rhs(k, c),
                                      start=(k == 0), stop=(k == kk - 1))
                t.then_inc(made, 1)

            col = lambda t, c: t[:, c * HALF:(c + 1) * HALF]
            pe.wait_ge(squared, 3)
            unit(0, 3, lambda k, c: core.col("ones"), lambda k, c: col(sq[k], c))
            pe.wait_ge(squared, 5)
            unit(1, 2, lambda k, c: core.col("ones"), lambda k, c: col(sq[3 + k], c))
            pe.wait_ge(uq_loaded, 16)
            pe.wait_ge(scaled, 3)
            for t in range(6):
                unit(2 + t, 3, lambda k, c: wuq[:, k, t * P:(t + 1) * P],
                     lambda k, c: col(lat[:, k, :], c))
            for g in range(2):
                pe.wait_ge(evac, 7 + g)
                unit(8 + g, 1, lambda k, c: core.col("swap"), lambda k, c: col(qraw[g], c))
            unit(10, 1, lambda k, c: core.col("swap")[0:ROPE, 0:ROPE],
                 lambda k, c: col(lat[0:ROPE, 5, :], c), ROPE)
            pe.wait_ge(ukv_loaded, 16)
            pe.wait_ge(scaled, 5)
            for t in range(4):
                unit(11 + t, 2, lambda k, c: wukv[:, k, t * P:(t + 1) * P],
                     lambda k, c: col(lat[:, 3 + k, :], c))
            for t in range(4):
                unit(15 + t, 2, lambda k, c: lat[:, 3 + k, (2 * t + c) * P:(2 * t + c + 1) * P],
                     lambda k, c: wukv[:, k, HALF:2 * HALF])
            pe.wait_ge(pw_loaded, 16)
            for g in range(4):
                pe.wait_ge(mixed, g + 1)
                unit(19 + g, 1, lambda k, c: wp[:, g, :], lambda k, c: col(u[:, g, PADU:], c))

        @block.scalar
        def _(a):
            a.sem_inc(taken[0], 1)
            a.sem_inc(taken[1], 1)
            a.wait_ge(trig_args, 2)
            a.activation(sin_t, sin_t, ACT.Sin).then_inc(trig, 1)
            a.activation(cos_t, cos_t, ACT.Sin).then_inc(trig, 1)
            copy_tiles(a, ps, lat, done, taken, 3, (HALF, HALF))
            a.wait_ge(taken[0], 4)
            a.wait_ge(taken[1], 4)
            for k in range(5):
                a.activation(sq[k], lat[:, k, :], ACT.Square).then_inc(squared, 1)
            for n in range(23):
                b = 4 + 2 * (n % 2)
                src = ps[:, b:b + 2, :]
                a.wait_ge(made, n + 1)
                if n in (4, 5):
                    a.wait_ge(stored[n % 2], 16)
                if n >= 11 and n < 15:
                    a.wait_ge(stored[n % 2], 16 * (2 + (n - 11) // 2))
                if n == 6:
                    a.wait_ge(squared, 5)
                if n < 2:
                    a.activation(halves(dest[n]), src, ACT.Sqrt, bias=core.col("eps_rms"),
                                 scale=1.0 / (3 * P if n == 0 else 2 * P)).then_inc(evac, 1)
                elif n == 10:
                    a.activation(halves(ksw), src[0:ROPE], ACT.Copy).then_inc(evac, 1)
                elif n < 15:
                    a.activation(halves(dest[n]), src, ACT.Copy).then_inc(evac, 1)
                elif n < 19:
                    t = n - 15
                    a.activation(vt[:, 2 * t:2 * t + 2, :], src, ACT.Copy).then_inc(evac, 1)
                else:
                    g = n - 19
                    a.activation(halves(u[:, g, PADU:]), src, ACT.Copy,
                                 scale=core.col("pool_scale", g, g + 1)).then_inc(evac, 1)

        @block.vector
        def _(v):
            c = Chain(v, steps)
            v.wait_ge(pos_loaded, 16)
            rope_tables(c, core, rs[1].bitcast(I32), rs[0], sin_t, cos_t)
            c.step(v.tensor_scalar(sin_t, sin_t, core.col("sin_sign"), None, ALU.mult))
            v.tensor_scalar(cos_t, cos_t, 1.0, None, ALU.mult).then_inc(trig_args, 2)

            def tap(k, first=False):
                for ch in range(NTAP):
                    scalar = core.col("conv_dw")[:, bass.ds(k + ch * TAPS, 1)]
                    src = z[:, ch, bass.ds(k + (PADZ - TAPS + 1), S)]
                    if first:
                        v.tensor_scalar(acc[:, ch, :], src, scalar, core.col("conv_b", ch, ch + 1),
                                        ALU.mult, ALU.add).then_inc(taps, 1)
                    else:
                        v.wait_ge(taps, k * NTAP + (ch - NTAP + 1))
                        v.scalar_tensor_tensor(acc[:, ch, :], src, scalar, acc[:, ch, :],
                                               ALU.mult, ALU.add).then_inc(taps, 1)

            tap(0, True)
            with v.Fori(1, taps_first) as k:
                tap(k)
            v.wait_ge(evac, 2)
            for n in range(2):
                v.reciprocal(rs[n], rs[n]).then_inc(inverted, 1)
            for k in range(5):
                n = 0 if k < 3 else 1
                g = core.col("q_norm", k, k + 1) if k < 3 else core.col("kv_norm", k - 3, k - 2)
                v.wait_ge(inverted, n + 1)
                v.scalar_tensor_tensor(lat[:, k, :], lat[:, k, :], g, rs[n],
                                       ALU.mult, ALU.mult).then_inc(scaled, 1)
            with v.Fori(taps_first, TAPS) as k:
                tap(k)
            v.wait_ge(taps, NTAP * TAPS)

        @block.gpsimd
        def _(g):
            c = Chain(g, pool_steps)
            c.did(g.memset(t1[:, 0:PADU], 0.0))
            c.step(g.memset(t2[:, 0:PADU], 0.0))
            for grp in range(4):
                cur = u[:, grp, :]
                for lvl in range(grp + 1):
                    nxt = (t1, t2)[lvl % 2]
                    c.step(g.tensor_tensor(nxt[:, PADU:], cur[:, PADU:],
                                           cur[:, PADU - 2 ** lvl:PADU + S - 2 ** lvl], ALU.add))
                    cur = nxt
                c.did(g.tensor_tensor(cur[:, PADU:2 * PADU], cur[:, PADU:2 * PADU],
                                      core.col("pool_inv", 16 * grp, 16 * grp + 16), ALU.mult))
                c.step(g.tensor_scalar(cur[:, 2 * PADU:], cur[:, 2 * PADU:],
                                       1.0 / WINDOWS[grp], None, ALU.mult))
                g.tensor_tensor(u[:, grp, PADU:], cur[:, PADU:], u[:, grp, PADU:],
                                ALU.subtract).then_inc(mixed, 1)
                g.wait_ge(mixed, grp + 1)
            g.wait_ge(trig, 2)
            for n, (raw, sw, rows) in enumerate(((qraw[0], qsw[0], P), (qraw[1], qsw[1], P),
                                                 (lat[0:ROPE, 5, :], ksw, ROPE))):
                g.wait_ge(evac, 9 + n)
                c.did(g.tensor_tensor(raw, raw, cos_t[0:rows], ALU.mult))
                c.step(g.tensor_tensor(sw, sw, sin_t[0:rows], ALU.mult))
                g.tensor_tensor(raw, raw, sw, ALU.add).then_inc(turned, 1)


def conv_finish(core, m):
    nc, ps, acc = core.nc, core.ps, m["acc"]
    sem = lambda n: core.semaphore("cf_" + n)
    summed, centred, squared, rooted, inverted, normed, shaped = map(sem, (
        "summed", "centred", "squared", "rooted", "inverted", "normed", "shaped"))
    sq = core.place(m["free"], 4, S)
    rstd = core.place(m["free"] + 4 * S, S)
    halves = lambda t: t.rearrange("p (a b) -> p a b", a=2)
    with nc.Block() as block:
        @block.tensor
        def _(pe):
            for b, src, ready in ((0, acc, None), (2, sq, squared)):
                for k in range(4):
                    if ready is not None:
                        pe.wait_ge(ready, k + 1)
                    for c in range(2):
                        t = pe.matmul(ps[:, b + c, :], core.col("ones"),
                                      src[:, k, c * HALF:(c + 1) * HALF], start=(k == 0), stop=(k == 3),
                                      skip_group_check=True)
                t.then_inc(summed, 1)

        @block.vector
        def _(v):
            v.wait_ge(summed, 1)
            for k in range(4):
                v.scalar_tensor_tensor(halves(acc[:, k, :]), ps[:, 0:2, :], -1.0 / (4 * P),
                                       halves(acc[:, k, :]), ALU.mult, ALU.add).then_inc(centred, 1)
            v.wait_ge(rooted, 1)
            v.reciprocal(rstd, rstd).then_inc(inverted, 1)
            v.wait_ge(inverted, 1)
            for k in range(4):
                v.tensor_tensor(acc[:, k, :], acc[:, k, :], rstd, ALU.mult).then_inc(normed, 1)

        @block.scalar
        def _(a):
            for k in range(4):
                a.wait_ge(centred, k + 1)
                a.activation(sq[:, k, :], acc[:, k, :], ACT.Square).then_inc(squared, 1)
            a.wait_ge(summed, 2)
            a.activation(halves(rstd), ps[:, 2:4, :], ACT.Sqrt, bias=core.col("eps_ln"),
                         scale=1.0 / (4 * P)).then_inc(rooted, 1)
            for k in range(4):
                a.wait_ge(normed, k + 1)
                a.activation(acc[:, k, :], acc[:, k, :], ACT.Silu, bias=core.col("conv_ln_b", k, k + 1),
                             scale=core.col("conv_ln_g", k, k + 1)).then_inc(shaped, 1)



def latent_attention(core, m):
    nc, ps, vt, oT = core.nc, core.ps, m["vt"], m["oT"]
    sem = lambda n: core.semaphore("at_" + n)
    q_loaded = [sem(f"q{i}") for i in range(2)]
    scored, biased, exped, turned, moved, summed, normed, steps, o_turned, o_moved = map(sem, (
        "scored", "biased", "exped", "turned", "moved", "summed", "normed", "steps", "o_turned",
        "o_moved"))
    at = m["free"]
    q = [core.place(at + i * 2 * S, S, parts=QD) for i in range(2)]
    k = [core.place(at + i * 2 * S + S, S, parts=QD) for i in range(2)]
    e = [core.place(at + 4 * S + i * S, S) for i in range(2)]
    pt = [core.place(at + 6 * S + i * S, NT, P) for i in range(2)]
    o = core.place(at + 8 * S, NT, NH1 * VH)
    tiny = core.place(at + 12 * S, 16)
    mx, nb, den, rec = (tiny[:, 4 * i:4 * i + 4] for i in range(4))
    scale = float(QD) ** -0.5
    N = 2 * NT
    with nc.Block() as block:
        @block.sync
        def _(sp):
            with sp.Fori(0, NH1 // 2) as it:
                for j in range(2):
                    sp.wait_ge(scored, it * N + (NT * j + NT))
                    h = it * 2 + j
                    for dst, src in ((q[j][0:NOPE], m["qn"].rearrange("t (h r) s -> (t h) r s", h=2)),
                                     (q[j][NOPE:QD], m["qr"].rearrange("t (h r) s -> (t h) r s", h=4)),
                                     (k[j][0:NOPE], m["kn"].rearrange("t (h r) s -> (t h) r s", h=2))):
                        sp.dma_start(dst, src[bass.ds(h, 1)].rearrange("a r s -> (a r) s"))\
                          .then_inc(q_loaded[j], 16)
                    sp.dma_start(k[j][NOPE:QD], m["kr"]).then_inc(q_loaded[j], 16)

        @block.tensor
        def _(pe):
            pe.sem_inc(scored, N)
            pe.sem_inc(turned, 2)
            pe.sem_inc(summed, 2)
            with pe.Fori(0, NH1 // 2) as it:
                def scores(n):
                    i, j = n % NT, n // NT
                    if i == 0:
                        pe.wait_ge(q_loaded[j], it * 64 + 64)
                    pe.wait_ge(exped, it * N + n + 1)
                    keys = (i + 1) * P
                    for c in range(0, keys, HALF):
                        wd = min(HALF, keys - c)
                        t = pe.matmul(ps[:, 2 * (n % 2) + c // HALF, 0:wd], q[j][:, i * P:(i + 1) * P],
                                      k[j][:, c:c + wd], start=True, stop=True)
                    t.then_inc(scored, 1)

                def turn(n):
                    i = n % NT
                    pe.wait_ge(exped, it * N + n + 3)
                    pe.wait_ge(moved, it * N + n)
                    for t in range(i + 1):
                        ins = pe.transpose(ps[:, 4 + t // 4, (t % 4) * P:(t % 4 + 1) * P],
                                           e[n % 2][:, t * P:(t + 1) * P], core.col("ident"))
                    ins.then_inc(turned, 1)

                def sums(n):
                    i, j = n % NT, n // NT
                    pe.wait_ge(moved, it * N + n + 1)
                    pe.wait_ge(normed, it * N + n + 3)
                    for t in range(i + 1):
                        ins = pe.matmul(ps[:, 6 + n % 2, 0:VH], pt[n % 2][:, t, :],
                                        vt[:, t, bass.ds(it * (2 * VH) + j * VH, VH)],
                                        start=(t == 0), stop=(t == i))
                    ins.then_inc(summed, 1)

                scores(0)
                scores(1)
                for n in range(N):
                    turn(n)
                    if n + 2 < N:
                        scores(n + 2)
                    if n:
                        sums(n - 1)
                sums(N - 1)
            for i in range(NT):
                pe.wait_ge(normed, NH1 * NT + 4)
                if i >= 2:
                    pe.wait_ge(o_moved, i - 1)
                for t in range(4):
                    ins = pe.transpose(ps[:, i % 2, t * P:(t + 1) * P], o[:, i, t * P:(t + 1) * P],
                                       core.col("ident"))
                ins.then_inc(o_turned, 1)

        @block.vector
        def _(v):
            v.sem_inc(normed, 4)
            per = 3 * N
            with v.Fori(0, NH1 // 2) as it:
                c = Chain(v, steps, it * per)

                def bias(n):
                    i = n % NT
                    v.wait_ge(scored, it * N + n + 1 + N)
                    row = ps[:, 2 * (n % 2):2 * (n % 2) + 2, :].rearrange("p a b -> p (a b)")
                    c.step(v.memset(row[0:64, i * P + 64:(i + 1) * P], -BIG))
                    c.step(v.reduce_max(mx[:, n % 2:n % 2 + 1], row[:, 0:(i + 1) * P], AX))
                    v.tensor_scalar(nb[:, n % 2:n % 2 + 1], mx[:, n % 2:n % 2 + 1], -scale, None,
                                    ALU.mult).then_inc(biased, 1)

                def normalise(n):
                    i, j, x = n % NT, n // NT, n % 4
                    v.wait_ge(summed, it * N + n + 3)
                    c.step(v.reciprocal(rec[:, x:x + 1], den[:, x:x + 1]))
                    v.tensor_scalar(o[:, i, bass.ds(it * (2 * VH) + j * VH, VH)],
                                    ps[:, 6 + n % 2, 0:VH], rec[:, x:x + 1], None,
                                    ALU.mult).then_inc(normed, 1)

                bias(0)
                bias(1)
                for n in range(N):
                    if n + 2 < N:
                        bias(n + 2)
                    if n:
                        normalise(n - 1)
                normalise(N - 1)
                assert c.n == per
            for i in range(NT):
                v.wait_ge(o_turned, i + 1)
                v.tensor_copy(oT[:, :, i * P:(i + 1) * P],
                              ps[:, i % 2, :].rearrange("p (a b) -> p a b", a=4)).then_inc(o_moved, 1)

        @block.scalar
        def _(a):
            a.sem_inc(exped, 2)
            with a.Fori(0, NH1 // 2) as it:
                def exp(n):
                    i = n % NT
                    a.wait_ge(biased, it * N + n + 1)
                    a.wait_ge(turned, it * N + n + 1)
                    a.wait_ge(normed, it * N + n + 1)
                    row = ps[:, 2 * (n % 2):2 * (n % 2) + 2, :].rearrange("p a b -> p (a b)")
                    a.activation(e[n % 2][:, 0:(i + 1) * P], row[:, 0:(i + 1) * P], ACT.Exp,
                                 bias=nb[:, n % 2:n % 2 + 1], scale=scale,
                                 accum_out=den[:, n % 4:n % 4 + 1]).then_inc(exped, 1)

                exp(0)
                for n in range(N):
                    i = n % NT
                    if n + 1 < N:
                        exp(n + 1)
                    a.wait_ge(turned, it * N + n + 3)
                    a.wait_ge(summed, it * N + n + 1)
                    src = ps[:, 4:6, :].rearrange("p a b -> p (a b)")
                    a.activation(pt[n % 2].rearrange("p a b -> p (a b)")[:, 0:(i + 1) * P],
                                 src[:, 0:(i + 1) * P], ACT.Copy).then_inc(moved, 1)



MW = 36 * P + 4


def merge(core, m):
    nc, ps, hT, merged = core.nc, core.ps, m["hT"], m["merged"]
    branch = (m["poolT"], m["acc"], m["oT"])
    sem = lambda n: core.semaphore("mg_" + n)
    loaded = [sem(f"w{i}") for i in range(2)]
    made, gated, used, steps = map(sem, ("made", "gated", "used", "steps"))
    w = [core.place(m["free"] + i * MW, MW) for i in range(2)]
    at = m["free"] + 2 * MW
    sg = [core.place(at + i * HALF, HALF) for i in range(2)]
    part = [core.place(at + (2 + i) * HALF, HALF) for i in range(2)]
    NU = 12

    def split(n):
        return n // 6, (n // 3) % 2, n % 3

    with nc.Block() as block:
        @block.sync
        def _(sp):
            with sp.Fori(0, ND // 2) as it:
                for j in range(2):
                    sp.wait_ge(used, it * NU + 6 * j + 6)
                    sp.dma_start(w[j], core.ins["merge_w"][it * 2 + j]).then_inc(loaded[j], 16)

        @block.tensor
        def _(pe):
            with pe.Fori(0, ND // 2) as it:
                for n in range(NU):
                    j, c, b = split(n)
                    if n % 6 == 0:
                        pe.wait_ge(loaded[j], it * 16 + 16)
                    pe.wait_ge(used, it * NU + n + 9)
                    bank = 2 * (n % 4)
                    for k in range(ND):
                        pe.matmul(ps[:, bank, :], w[j][:, (8 * b + k) * P:(8 * b + k + 1) * P],
                                  hT[:, k, c * HALF:(c + 1) * HALF], start=(k == 0), stop=(k == ND - 1))
                    for k in range(4):
                        x = 24 + 4 * b + k
                        t = pe.matmul(ps[:, bank + 1, :], w[j][:, x * P:(x + 1) * P],
                                      branch[b][:, k, c * HALF:(c + 1) * HALF],
                                      start=(k == 0), stop=(k == 3))
                    t.then_inc(made, 1)

        @block.scalar
        def _(a):
            with a.Fori(0, ND // 2) as it:
                for n in range(NU):
                    j, c, b = split(n)
                    a.wait_ge(made, it * NU + n + 1)
                    a.wait_ge(used, it * NU + n + 11)
                    a.activation(sg[n % 2], ps[:, 2 * (n % 4), :], ACT.Sigmoid,
                                 bias=w[j][:, 36 * P + b:36 * P + b + 1]).then_inc(gated, 1)

        @block.vector
        def _(v):
            v.sem_inc(used, NU)
            per = 8
            with v.Fori(0, ND // 2) as it:
                ch = Chain(v, steps, it * per)
                for n in range(NU):
                    j, c, b = split(n)
                    v.wait_ge(gated, it * NU + n + 1)
                    y = ps[:, 2 * (n % 4) + 1, :]
                    dst = merged[:, bass.ds(it * 2 + j, 1), c * HALF:(c + 1) * HALF]
                    ch.wait()
                    if b == 0:
                        v.tensor_tensor(part[0], sg[n % 2], y, ALU.mult).then_inc(used, 1)
                    elif b == 1:
                        v.tensor_tensor(part[1], sg[n % 2], y, ALU.mult).then_inc(used, 1)
                        v.wait_ge(used, it * NU + n + 13)
                        ch.did(v.tensor_tensor(part[0], part[0], part[1], ALU.add))
                    else:
                        v.tensor_tensor(part[1], sg[n % 2], y, ALU.mult).then_inc(used, 1)
                        v.wait_ge(used, it * NU + n + 13)
                        ch.did(v.tensor_tensor(dst, part[0].unsqueeze(1), part[1].unsqueeze(1), ALU.add))
                assert ch.n == per


def stats_of(core, c, v, st, mv, x):
    for j in range(2):
        c.did(v.bn_stats(st[:, 6 * j:6 * j + 6], x[:, HALF * j:HALF * (j + 1)]))
    c.wait()
    core.waited(v)
    return v.bn_aggr(mv, st)


def flat2(ps, b):
    return ps[:, b:b + 2, :].rearrange("p a b -> p (a b)")


def output_and_gate(core, m):
    nc, ps, merged = core.nc, core.ps, m["merged"]
    sem = lambda n: core.semaphore("og_" + n)
    x_loaded = [sem(f"x{i}") for i in range(2)]
    p_loaded = [sem(f"p{i}") for i in range(2)]
    h_stored = [sem(f"h_stored{i}") for i in range(2)]
    r_stored = [sem(f"r_stored{i}") for i in range(2)]
    (wo_loaded, weights, staged, made, taken, var_ready, rstd_ready, h_ready, turned, moved,
     routed, kept, gate_made, ple_made, sig_ready, e_taken, rest_ready, steps, pool_steps, moves) = map(
        sem, ("wo", "weights", "staged", "made", "taken", "var", "rstd", "h_ready", "turned",
              "moved", "routed", "kept", "gate_made", "ple_made", "sig_ready", "e_taken",
              "rest_ready", "steps", "pool_steps", "moves"))
    at = m["low"]
    wo, wg = core.place(at, ND, D), core.place(at + ND * D, ND, D)
    wp = core.place(at + 2 * ND * D, 2, D)
    wr = core.place(at + 2 * ND * D + 2 * D, ND, NE)
    at = UPPER
    ga, ba, g1, b1 = (core.place(at + i * D, D) for i in range(4))
    work = core.place(at + 4 * D, D)
    at = m["high"]
    names = ("xh0", "xh1", "mt0", "mt1", "h0", "h1", "rest0", "rest1", "hT", "sig")
    b = {n: core.place(at + i * D, D) for i, n in enumerate(names)}
    at += len(names) * D
    pin = [core.place(at + i * 2 * P, 2 * P) for i in range(2)]
    pT = core.place(at + 4 * P, 2, P)
    st, mv = core.place(at + 6 * P, 12), core.place(at + 6 * P + 12, 2)
    rstd = core.place(at + 6 * P + 16, 1)
    tile = lambda x: x.rearrange("p (a b) -> p a b", b=P)
    hT = tile(b["hT"])
    with nc.Block() as block:
        @block.sync
        def _(sp):
            sp.dma_start(wo, core.ins["w_out_k"]).then_inc(wo_loaded, 16)
            for dst, name in ((ga, "ln_in_g"), (ba, "ln_in_b"), (g1, "ln1_g"), (b1, "ln1_b")):
                sp.dma_start(dst, row_on_all(core.ins[name], D)).then_inc(weights, 16)
            sp.dma_start(wr, core.ins["w_router_k"]).then_inc(weights, 16)
            sp.dma_start(wp, core.ins["ple_proj_k"]).then_inc(weights, 16)
            sp.dma_start(wg, core.ins["ple_gate_k"]).then_inc(weights, 16)
            with sp.Fori(0, NT // 2) as it:
                for j in range(2):
                    n = it * 2 + j
                    sp.wait_ge(taken, it * 2 + j + 1)
                    sp.dma_start(b[f"xh{j}"], m["xhat"][n]).then_inc(x_loaded[j], 16)
                    sp.wait_ge(turned, it * 2 + j + 1)
                    sp.dma_start(pin[j], core.ins["p_tiles"][n]).then_inc(p_loaded[j], 16)

        @block.gpsimd
        def _(g):
            def stage(it, j):
                g.wait_ge(made, it * 2 + j + 1)
                g.wait_ge(wo_loaded, 16)
                g.tensor_copy(tile(b[f"mt{j}"]), merged[:, :, bass.ds(it * (2 * P) + j * P, P)])\
                 .then_inc(staged, 1)

            def root(it, j):
                c = Chain(g, pool_steps, it * 2 + j)
                g.wait_ge(var_ready, it * 2 + j + 1)
                inverse_root(c, g, core, rstd, mv[:, 1:2], 1.0, LN_EPS).then_inc(rstd_ready, 1)

            stage(0, 0)
            with g.Fori(0, NT // 2 - 1) as it:
                stage(it, 1)
                root(it, 0)
                stage(it + 1, 0)
                root(it, 1)
            last = NT // 2 - 1
            stage(last, 1)
            root(last, 0)
            root(last, 1)

        @block.tensor
        def _(pe):
            pe.sem_inc(made, 2)
            pe.sem_inc(turned, 2)
            pe.wait_ge(wo_loaded, 16)

            def product(it, j):
                n = it * 2 + j
                pe.wait_ge(staged, n + 1)
                pe.wait_ge(taken, n + 2)
                for c in range(2):
                    for k in range(ND):
                        t = pe.matmul(ps[:, c, :], tile(b[f"mt{j}"])[:, k, :],
                                      wo[:, k, c * HALF:(c + 1) * HALF], start=(k == 0), stop=(k == ND - 1))
                t.then_inc(made, 1)

            def after(it, j):
                n = it * 2 + j
                pe.wait_ge(h_ready, n + 1)
                pe.wait_ge(kept, n)
                for k in range(ND):
                    pe.transpose(ps[:, 2 + k // 4, (k % 4) * P:(k % 4 + 1) * P],
                                 b[f"h{j}"][:, k * P:(k + 1) * P], core.col("ident"))
                pe.wait_ge(p_loaded[j], it * 16 + 16)
                pe.wait_ge(e_taken, n)
                for k in range(2):
                    t = pe.transpose(ps[:, 6, k * P:(k + 1) * P], pin[j][:, k * P:(k + 1) * P],
                                     core.col("ident"))
                t.then_inc(turned, 1)
                pe.wait_ge(moved, n + 1)
                for k in range(ND):
                    t = pe.matmul(ps[:, 2, 0:NE], hT[:, k, :], wr[:, k, :], start=(k == 0), stop=(k == ND - 1))
                t.then_inc(routed, 1)
                pe.wait_ge(sig_ready, n)
                for c in range(2):
                    for k in range(ND):
                        t = pe.matmul(ps[:, 4 + c, :], hT[:, k, :], wg[:, k, c * HALF:(c + 1) * HALF],
                                      start=(k == 0), stop=(k == ND - 1))
                t.then_inc(gate_made, 1)
                for c in range(2):
                    for k in range(2):
                        t = pe.matmul(ps[:, 6 + c, :], pT[:, k, :], wp[:, k, c * HALF:(c + 1) * HALF],
                                      start=(k == 0), stop=(k == 1))
                t.then_inc(ple_made, 1)

            product(0, 0)
            pe.wait_ge(weights, 16 * 7)
            with pe.Fori(0, NT // 2 - 1) as it:
                product(it, 1)
                after(it, 0)
                product(it + 1, 0)
                after(it, 1)
            last = NT // 2 - 1
            product(last, 1)
            after(last, 0)
            after(last, 1)

        @block.scalar
        def _(a):
            with a.Fori(0, NT // 2) as it:
                for j in range(2):
                    n = it * 2 + j
                    a.wait_ge(turned, n + 3)
                    for c in range(2):
                        a.activation(b["hT"][:, c * HALF:(c + 1) * HALF], ps[:, 2 + c, :], ACT.Copy)
                    a.activation(pT.rearrange("p a b -> p (a b)"), ps[:, 6, 0:2 * P], ACT.Copy)\
                     .then_inc(moved, 1)
                    a.wait_ge(gate_made, n + 1)
                    a.wait_ge(e_taken, n)
                    a.activation(b["sig"], flat2(ps, 4), ACT.Sigmoid).then_inc(sig_ready, 1)
                    a.wait_ge(h_ready, n + 1)
                    a.dma_start(m["h1"][n], b[f"h{j}"]).then_inc(h_stored[j], 16)
                    a.wait_ge(rest_ready, n + 1)
                    a.dma_start(m["rest"][n], b[f"rest{j}"]).then_inc(r_stored[j], 16)
            for q in h_stored + r_stored:
                a.wait_ge(q, 16 * (NT // 2))

        @block.vector
        def _(v):
            v.sem_inc(taken, 2)
            c0 = Chain(v, steps)
            v.wait_ge(weights, 16 * 7)
            c0.did(v.tensor_scalar(ga, ga, ALPHA, None, ALU.mult))
            c0.step(v.tensor_scalar(ba, ba, ALPHA, None, ALU.mult))
            per = 6

            def norm(it, j):
                n = it * 2 + j
                c = Chain(v, steps, n * per + c0.n)
                v.wait_ge(x_loaded[j], it * 16 + 16)
                v.wait_ge(h_ready, n)
                c.step(v.tensor_tensor(work, b[f"xh{j}"], ga, ALU.mult))
                c.step(v.tensor_tensor(work, work, ba, ALU.add))
                v.wait_ge(made, n + 3)
                v.tensor_tensor(work, work, flat2(ps, 0), ALU.add).then_inc(taken, 1)
                v.wait_ge(taken, n + 3)
                stats_of(core, c, v, st, mv, work).then_inc(var_ready, 1)
                v.wait_ge(rstd_ready, n + 1)
                c.step(v.tensor_scalar(work, work, mv[:, 0:1], rstd, ALU.subtract, ALU.mult))
                c.step(v.tensor_tensor(work, work, g1, ALU.mult))
                v.wait_ge(h_stored[j], it * 16)
                v.tensor_tensor(b[f"h{j}"], work, b1, ALU.add).then_inc(h_ready, 1)
                assert c.n == per

            def residual(it, j):
                n = it * 2 + j
                v.wait_ge(routed, n + 1)
                v.tensor_copy(m["logits"][:, bass.ds(it * (2 * NE) + j * NE, NE)], ps[:, 2, 0:NE])\
                 .then_inc(kept, 1)
                v.wait_ge(sig_ready, n + 1)
                v.wait_ge(ple_made, n + 1)
                v.wait_ge(r_stored[j], it * 16)
                v.tensor_tensor(b[f"rest{j}"], b["sig"], flat2(ps, 6), ALU.mult).then_inc(e_taken, 1)
                v.wait_ge(e_taken, n + 1)
                v.scalar_tensor_tensor(b[f"rest{j}"], b[f"h{j}"], ALPHA, b[f"rest{j}"],
                                       ALU.mult, ALU.add).then_inc(rest_ready, 1)

            norm(0, 0)
            with v.Fori(0, NT // 2 - 1) as it:
                norm(it, 1)
                residual(it, 0)
                norm(it + 1, 0)
                residual(it, 1)
            last = NT // 2 - 1
            norm(last, 1)
            residual(last, 0)
            residual(last, 1)



def first_best(c, v, out, x, rank, peak, tmp, n):
    shape = list(x.shape)
    spread = lambda t: t.unsqueeze(2).to_broadcast(shape)
    c.step(v.tensor_reduce(peak, x, AX, ALU.max))
    c.step(v.tensor_tensor(tmp, x, spread(peak), ALU.is_equal))
    c.step(v.tensor_tensor(tmp, tmp, rank.unsqueeze(1).to_broadcast(shape), ALU.mult))
    c.step(v.tensor_reduce(peak, tmp, AX, ALU.max))
    c.step(v.tensor_tensor(out, tmp, spread(peak), ALU.is_equal))


def route(core, m):
    nc, ps = core.nc, core.ps
    sem = lambda n: core.semaphore("rt_" + n)
    (sig, steps, picked, counted, cleared, ready, listed, tok_loaded, tok_f, tok_turned,
     zeroed) = map(
        sem, ("sig", "steps", "picked", "counted", "cleared", "ready", "listed", "tok_loaded",
              "tok_f", "tok_turned", "zeroed"))
    at = m["free"]

    def take(*shape):
        nonlocal at
        n = int(np.prod(shape))
        at += n
        return core.place(at - n, *shape)

    aff, sel, tmp, selm, oh1, oh2, pick, rank = (take(NT, NE) for _ in range(8))
    pair, gs = take(NT * NG), take(NT * NG)
    keep, gtmp = take(NT, NG), take(NT, NG)
    peak, wk, off = take(NT), take(NT, 2), take(NT + 1, NE)
    nb, pend, pstart = take(NE), take(NE), take(NE)
    cmp = take(NBLK, NE)
    blk, need, slot = take(NBLK), take(NBLK), take(NBLK)
    dest = take(2, NT)
    rowsf = take(P)
    spread_t = lambda t: t.unsqueeze(1).to_broadcast([P, NT, NE])
    fl = lambda t: t.rearrange("p a b -> p (a b)")
    quads = lambda t: fl(t).rearrange("p (q e) -> p q e", e=EPG)
    toks = m["slot_token_rows"]
    with nc.Block() as block:
        @block.vector
        def _(v):
            c = Chain(v, steps)
            v.wait_ge(sig, 1)
            c.step(v.tensor_tensor(sel, aff, spread_t(core.col("bias_r")), ALU.add))
            q = quads(sel)
            first = True
            for x in range(EPG):
                for y in range(x + 1, EPG):
                    dst = gs if first else pair
                    c.step(v.tensor_tensor(dst, q[:, :, x], q[:, :, y], ALU.add))
                    if not first:
                        c.step(v.tensor_tensor(gs, gs, pair, ALU.max))
                    first = False
            first_best(c, v, keep, gs.rearrange("p (t g) -> p t g", g=NG), core.col("order4"), peak, gtmp, NG)
            kb = fl(keep)
            c.step(v.tensor_scalar(pair, kb, BIG, -BIG, ALU.mult, ALU.add))
            wide = lambda t: t.unsqueeze(2).to_broadcast([P, NT * NG, EPG])
            c.step(v.tensor_tensor(quads(selm), quads(sel), wide(kb), ALU.mult))
            c.step(v.tensor_tensor(quads(selm), quads(selm), wide(pair), ALU.add))
            first_best(c, v, oh1, selm, core.col("low16"), peak, tmp, NE)
            c.step(v.tensor_scalar(tmp, oh1, -BIG, None, ALU.mult))
            c.step(v.tensor_tensor(selm, selm, tmp, ALU.add))
            first_best(c, v, oh2, selm, core.col("low16"), peak, tmp, NE)
            v.tensor_tensor(pick, oh1, oh2, ALU.add).then_inc(picked, 1)
            for i, oh in enumerate((oh1, oh2)):
                c.step(v.tensor_tensor(tmp, aff, oh, ALU.mult))
                c.step(v.tensor_reduce(wk[:, :, i], tmp, AX, ALU.add))
            c.step(v.tensor_tensor(peak, wk[:, :, 0], wk[:, :, 1], ALU.add))
            c.step(v.reciprocal(peak, peak))
            c.step(v.tensor_tensor(m["weights"].rearrange("p (a b) -> p a b", b=2), wk,
                                   peak.unsqueeze(2).to_broadcast([P, NT, 2]), ALU.mult))
            v.wait_ge(counted, 1)
            tot = ps[:, 1, 0:P].rearrange("p (a b) -> p a b", b=NE)
            c.step(v.memset(off[:, 0, :], 0.0))
            for i in range(NT):
                c.step(v.tensor_tensor(off[:, i + 1, :], off[:, i, :], tot[:, i, :], ALU.add))
            c.did(v.tensor_tensor(fl(rank), fl(off[:, 0:NT, :]), ps[:, 0, 0:P], ALU.add))
            c.step(v.tensor_scalar(nb, off[:, NT, :], 0.0, None, ALU.is_gt))
            for i in range(1, NT):
                c.step(v.scalar_tensor_tensor(nb, off[:, NT, :], float(P * i), nb, ALU.is_gt, ALU.add))
            c.step(v.tensor_tensor_scan(pend, core.col("ones", 0, NE), nb, 0.0, ALU.mult, ALU.add))
            c.step(v.tensor_tensor(pstart, pend, nb, ALU.subtract))
            c.step(v.tensor_scalar(pstart, pstart, float(P), None, ALU.mult))
            c.step(v.tensor_tensor(rank, rank, spread_t(pstart), ALU.add))
            for i, oh in enumerate((oh1, oh2)):
                c.step(v.tensor_tensor(tmp, rank, oh, ALU.mult))
                c.step(v.tensor_reduce(dest[:, i, :], tmp, AX, ALU.add))
            c.step(v.tensor_copy(m["dest"], fl(dest)))
            v.tensor_copy(m["token"], core.col("token")).then_inc(ready, 1)
            c.step(v.tensor_tensor(cmp, pend.unsqueeze(1).to_broadcast([P, NBLK, NE]),
                                   core.col("block0", 0, NBLK).unsqueeze(2).to_broadcast([P, NBLK, NE]),
                                   ALU.is_le))
            c.step(v.tensor_reduce(blk, cmp, AX, ALU.add))
            c.step(v.tensor_scalar(blk, blk, float(NE - 1), None, ALU.min))
            c.step(v.memset(need[:, 0:1], 1.0))
            c.step(v.tensor_tensor(need[:, 1:], blk[:, 1:], blk[:, 0:NBLK - 1], ALU.not_equal))
            c.step(v.tensor_tensor_scan(slot, need, core.col("zeros", 0, NBLK), 0.0,
                                        ALU.not_equal, ALU.add))
            for i, x in enumerate((blk, need, slot)):
                c.did(v.tensor_copy(m["plan"][:, i * NBLK:(i + 1) * NBLK], x))
            v.wait_ge(tok_loaded, 16)
            v.tensor_copy(rowsf[0:NBLK], toks).then_inc(tok_f, 1)
            v.wait_ge(tok_turned, 1)
            c.did(v.tensor_copy(m["slot_token"], ps[:, 2, 0:NBLK]))

        @block.tensor
        def _(pe):
            pe.wait_ge(picked, 1)
            pe.matmul(ps[:, 0, 0:P], core.col("before"), fl(pick), start=True, stop=True)
            pe.matmul(ps[:, 1, 0:P], core.col("ones"), fl(pick), start=True, stop=True).then_inc(counted, 1)
            pe.wait_ge(tok_f, 1)
            pe.transpose(ps[:, 2, 0:NBLK], rowsf[0:NBLK], core.col("ident")[0:NBLK, 0:NBLK])\
              .then_inc(tok_turned, 1)

        @block.scalar
        def _(a):
            a.activation(fl(aff), m["logits"], ACT.Sigmoid).then_inc(sig, 1)

        @block.sync
        def _(sp):
            sp.wait_ge(zeroed, 1)
            sp.dma_start(m["slot_dram"].rearrange("(a b) c -> a (b c)", b=P), m["zero_i"][0:NBLK])\
              .then_inc(cleared, 16)
            sp.wait_ge(listed, 16 * 2 * NT)
            sp.dma_start(toks, m["slot_dram"].rearrange("(a b) c -> a (b c)", b=P)).then_inc(tok_loaded, 16)
            sp.wait_ge(tok_loaded, 16)

        @block.gpsimd
        def _(g):
            g.memset(m["zero_i"], 0).then_inc(zeroed, 1)
            g.wait_ge(cleared, 16)
            g.wait_ge(ready, 1)
            for i in range(NT):
                for j in range(2):
                    x = j * NT + i
                    g.indirect_dma_start(m["slot_dram"], bass.IndirectOffsetOnAxis(
                        ap=m["dest"][:, x:x + 1], axis=0), m["token"][:, i:i + 1], None).then_inc(listed, 16)
            g.wait_ge(listed, 16 * 2 * NT)


def grouped_experts(core, m):
    nc, ps = core.nc, core.ps
    sem = lambda n: core.semaphore("e1_" + n)
    NU, NS, W = 4, 6, 2 * D
    loaded = [sem(f"slab{s}") for s in range(NS)]
    high_made = {True: sem("high_up"), False: sem("high_down")}
    low_made = {True: sem("low_up"), False: sem("low_down")}
    used = {True: sem("up_used"), False: sem("down_used")}
    (gathered, picked, x_turned, x_high, x_low, silu_done, h_ready, h_turned, h_high, h_low,
     y_taken, y_stored) = map(sem, (
         "gathered", "picked", "x_turned", "x_high", "x_low", "silu_done", "h_ready", "h_turned",
         "h_high", "h_low", "y_taken", "y_stored"))
    at = m["low"]

    def take(*shape, dt=None):
        nonlocal at
        n = int(np.prod(shape))
        at += n
        return core.place(at - n, *shape, dt=dt)

    raw = [take(W) for _ in range(NS)]
    x, yo = take(D), take(D)
    sg, h = take(FE), take(FE)
    idx = take(1, dt=I32)
    at = UPPER
    high, low = ([take(W) for _ in range(NS)] for _ in range(2))
    xT = take(ND, P), take(ND, P)
    hT = take(4, P), take(4, P)
    plan = m["plan"]
    fl = lambda t: t.rearrange("p a b -> p (a b)")
    slabs = {True: range(0, NU), False: range(NU, NS)}

    def count(up, j, s):
        return j * NU + s + 1 if up else j * (NS - NU) + (s - NU) + 1

    with nc.Block() as block:
        @block.sync
        def _(sp):
            def load(j, up):
                e = sp.value_load(plan[0:1, bass.ds(j, 1)], min_val=0, max_val=NE - 1)
                need = sp.value_load(plan[0:1, bass.ds(j + NBLK, 1)], min_val=0, max_val=1)
                src = core.ins["exp_up_k"] if up else core.ins["exp_down_k"]
                for s in slabs[up]:
                    c = (s - slabs[up][0]) * W
                    sp.wait_ge(low_made[up], count(up, j, s))
                    core.waited(sp)
                    sp.dma_start(raw[s], src[bass.ds(e, 1), :, c:c + W].rearrange("a p n -> (a p) n"),
                                 cond=need, bounds_check="skip_entire_dma").then_inc(loaded[s], 16)

            load(0, True)
            with sp.Fori(0, NBLK - 1) as j:
                load(j + 1, True)
                load(j, False)
            load(NBLK - 1, False)
            for q in loaded:
                sp.wait_ge(q, 16 * NBLK)

        @block.gpsimd
        def _(g):
            def gather(j):
                g.wait_ge(x_turned, j)
                g.wait_ge(gathered, j * 16)
                core.waited(g)
                g.tensor_copy(idx, m["slot_token"][:, bass.ds(j, 1)]).then_inc(picked, 1)
                g.wait_ge(picked, j + 1)
                core.waited(g)
                g.indirect_dma_start(x, None, m["h1_rows"], bass.IndirectOffsetOnAxis(ap=idx, axis=0))\
                 .then_inc(gathered, 16)

            def store_y(j):
                g.wait_ge(y_taken, j + 1)
                core.waited(g)
                g.dma_start(m["y1"][j], yo).then_inc(y_stored, 16)

            gather(0)
            gather(1)
            gather(2)
            with g.Fori(1, NBLK - 2) as j:
                gather(j + 2)
                store_y(j - 1)
            for j in range(NBLK - 3, NBLK):
                store_y(j)
            g.wait_ge(y_stored, 16 * NBLK)

        @block.tensor
        def _(pe):
            def turn_x(j):
                pe.wait_ge(gathered, j * 16 + 16)
                pe.wait_ge(x_low, j)
                for k in range(ND):
                    t = pe.transpose(ps[:, 2 + k // 4, (k % 4) * P:(k % 4 + 1) * P],
                                     x[:, k * P:(k + 1) * P], core.col("ident"))
                t.then_inc(x_turned, 1)

            def products(j, up, act, bank):
                ks = 2 * len(slabs[up])
                for s in slabs[up]:
                    pe.wait_ge(low_made[up], count(up, j, s) + len(slabs[up]))
                    for k in range(2):
                        kk = 2 * (s - slabs[up][0]) + k
                        for c in range(2):
                            here = slice(k * D + c * HALF, k * D + (c + 1) * HALF)
                            t = three_passes(pe, ps[:, bank + c, :], (act[0][:, kk, :], act[1][:, kk, :]),
                                             (high[s][:, here], low[s][:, here]), kk == 0, kk == ks - 1)
                    t.then_inc(used[up], 1)

            def up(j):
                pe.wait_ge(x_low, j + 1)
                pe.wait_ge(h_ready, j)
                products(j, True, xT, 0)

            def turn_h(j):
                pe.wait_ge(h_ready, j + 1)
                pe.wait_ge(h_low, j)
                for k in range(4):
                    t = pe.transpose(ps[:, 4, k * P:(k + 1) * P], h[:, k * P:(k + 1) * P], core.col("ident"))
                t.then_inc(h_turned, 1)

            def down(j):
                pe.wait_ge(h_low, j + 1)
                pe.wait_ge(y_taken, j)
                products(j, False, hT, 5)

            turn_x(0)
            up(0)
            turn_x(1)
            turn_h(0)
            with pe.Fori(1, NBLK - 1) as j:
                up(j)
                turn_x(j + 1)
                down(j - 1)
                turn_h(j)
            last = NBLK - 1
            up(last)
            down(last - 1)
            turn_h(last)
            down(last)

        @block.scalar
        def _(a):
            def split(j, s):
                up = s < NU
                a.wait_ge(loaded[s], j * 16 + 16)
                a.wait_ge(used[up], count(up, j - 1, s) if not isinstance(j, int) or j else 0)
                a.activation(rounded(high[s]), raw[s], ACT.Copy).then_inc(high_made[up], 1)

            def move_x(j):
                a.wait_ge(x_turned, j + 1)
                a.wait_ge(used[True], j * NU)
                a.activation(rounded(fl(xT[0])), flat2(ps, 2), ACT.Copy).then_inc(x_high, 1)

            def silu(j):
                a.wait_ge(used[True], count(True, j, NU - 1))
                a.wait_ge(h_ready, j)
                a.activation(sg, ps[:, 0, :], ACT.Silu).then_inc(silu_done, 1)

            move_x(0)
            for s in range(NU):
                split(0, s)

            def take_y(j):
                a.wait_ge(used[False], count(False, j, NS - 1))
                a.wait_ge(y_stored, j * 16)
                a.activation(yo, flat2(ps, 5), ACT.Copy).then_inc(y_taken, 1)

            def step(j, more):
                if more:
                    for s in range(NU - 1):
                        split(j + 1, s)
                silu(j)
                if more:
                    split(j + 1, NU - 1)
                    move_x(j + 1)
                if not isinstance(j, int) or j:
                    take_y(j - 1)
                for s in range(NU, NS):
                    split(j, s)

            step(0, True)
            with a.Fori(1, NBLK - 1) as j:
                step(j, True)
            step(NBLK - 1, False)
            take_y(NBLK - 1)

        @block.vector
        def _(v):
            v.sem_inc(low_made[True], NU)
            v.sem_inc(low_made[False], NS - NU)

            def split(j, s):
                up = s < NU
                v.wait_ge(high_made[up], count(up, j, s))
                v.tensor_tensor(rounded(low[s]), raw[s], plain(high[s]), ALU.subtract).then_inc(low_made[up], 1)

            def move_x(j):
                v.wait_ge(x_high, j + 1)
                v.tensor_tensor(rounded(fl(xT[1])), flat2(ps, 2), plain(fl(xT[0])), ALU.subtract).then_inc(x_low, 1)

            def gate(j):
                v.wait_ge(silu_done, j + 1)
                v.wait_ge(h_turned, j)
                v.tensor_tensor(h, sg, ps[:, 1, :], ALU.mult).then_inc(h_ready, 1)

            def move_h(j):
                v.wait_ge(h_turned, j + 1)
                v.wait_ge(used[False], j * (NS - NU))
                v.tensor_copy(rounded(fl(hT[0])), ps[:, 4, :]).then_inc(h_high, 1)
                v.wait_ge(h_high, j + 1)
                v.tensor_tensor(rounded(fl(hT[1])), ps[:, 4, :], plain(fl(hT[0])), ALU.subtract).then_inc(h_low, 1)

            move_x(0)
            for s in range(NU):
                split(0, s)

            def step(j, more):
                if more:
                    for s in range(NU - 1):
                        split(j + 1, s)
                gate(j)
                if more:
                    split(j + 1, NU - 1)
                    move_x(j + 1)
                for s in range(NU, NS):
                    split(j, s)
                move_h(j)

            step(0, True)
            with v.Fori(1, NBLK - 1) as j:
                step(j, True)
            step(NBLK - 1, False)



def prepare_columns(core, m):
    nc = core.nc
    sem = lambda n: core.semaphore("pc_" + n)
    loaded, steps, exped, lam = map(sem, ("loaded", "steps", "exped", "lam"))
    mod = m["mod"]
    cols = m["mod_cols"]
    tiny = m["tiny"]
    tmp = core.place(m["free"], HD2)
    with nc.Block() as block:
        @block.sync
        def _(sp):
            with nc.allow_non_contiguous_dma(reason="four vectors of 1024 as columns, once"):
                for i, (row, part) in enumerate(((0, 0), (0, 1), (1, 0), (1, 1))):
                    sp.dma_start(cols[:, i * ND:(i + 1) * ND],
                                 mod[row, part * D:(part + 1) * D].rearrange("(k p) -> p k", p=P))\
                      .then_inc(loaded, 16)
            sp.wait_ge(loaded, 16 * 4)

        @block.vector
        def _(v):
            c = Chain(v, steps)
            lams = core.col("lams")
            for i in range(2):
                c.step(v.tensor_tensor(tmp, lams[:, 2 * i * HD2:(2 * i + 1) * HD2],
                                       lams[:, (2 * i + 1) * HD2:(2 * i + 2) * HD2], ALU.mult))
                c.step(v.tensor_reduce(tiny[:, i:i + 1], tmp, AX, ALU.add))
            v.tensor_copy(tiny[:, 2:4], tiny[:, 0:2]).then_inc(lam, 1)
            v.wait_ge(exped, 1)
            c.step(v.tensor_tensor(m["neg_lam"], tiny[:, 3:4], tiny[:, 2:3], ALU.subtract))
            c.step(v.tensor_scalar(m["neg_lam"], m["neg_lam"], -LAM_INIT, None, ALU.add))
            v.wait_ge(loaded, 16 * 4)
            for i in range(2):
                sc = cols[:, (2 * i + 1) * ND:(2 * i + 2) * ND]
                c.step(v.scalar_tensor_tensor(sc, sc, 1.0, core.col("pre_mix"), ALU.add, ALU.mult))

        @block.scalar
        def _(a):
            a.wait_ge(lam, 1)
            a.activation(tiny[:, 2:4], tiny[:, 2:4], ACT.Exp).then_inc(exped, 1)


def prepare_rows(core, m):
    nc = core.nc
    sem = lambda n: core.semaphore("pr_" + n)
    loaded, steps = map(sem, ("loaded", "steps"))
    with nc.Block() as block:
        @block.sync
        def _(sp):
            for i, part in enumerate((2, 3, 4, 5)):
                sp.dma_start(m["rows"][i], row_on_all(m["mod"][0, part * D:(part + 1) * D], D))\
                  .then_inc(loaded, 16)
            for i, name in enumerate(("norm_post_mix", "norm_pre_ffn", "norm_post_ffn")):
                sp.dma_start(m["rows"][4 + i], row_on_all(core.ins[name], D)).then_inc(loaded, 16)

        @block.vector
        def _(v):
            c = Chain(v, steps)
            v.wait_ge(loaded, 16 * 7)
            g1, _, sc2, g2, pm, pf, pff = m["rows"][0:7]
            c.did(v.tensor_tensor(g1, g1, pm, ALU.mult))
            c.did(v.scalar_tensor_tensor(sc2, sc2, 1.0, pf, ALU.add, ALU.mult))
            c.step(v.tensor_tensor(g2, g2, pff, ALU.mult))


def context_input(core, m):
    nc, ps, xnT = core.nc, core.ps, m["xnT"]
    sem = lambda n: core.semaphore("cx_" + n)
    loaded, squared, rooted, scaled, turned, moved, pool_steps = map(sem, (
        "loaded", "squared", "rooted", "scaled", "turned", "moved", "pool_steps"))
    at = m["free"]
    x = core.place(at, NTC, D)
    sq = core.place(at + NTC * D, D)
    ss, rs = core.place(at + (NTC + 1) * D, NTC), core.place(at + (NTC + 1) * D + 4, NTC)
    cols = m["mod_cols"]
    with nc.Block() as block:
        @block.sync
        def _(sp):
            sp.dma_start(x, core.ins["ctx"].rearrange("o (i p) d -> p (o i) d", p=P)).then_inc(loaded, 16)

        @block.scalar
        def _(a):
            a.wait_ge(loaded, 16)
            for i in range(NTC):
                a.activation(sq, x[:, i, :], ACT.Square, accum_out=ss[:, i:i + 1]).then_inc(squared, 1)
                a.wait_ge(squared, i + 1)
            for i in range(NTC):
                for k in range(ND):
                    if k % 4 == 0:
                        a.wait_ge(turned, 2 * i + k // 4 + 1)
                    a.activation(xnT[:, k, S + i * P:S + (i + 1) * P],
                                 ps[:, 2 * i + k // 4, (k % 4) * P:(k % 4 + 1) * P], ACT.Identity,
                                 scale=cols[:, 3 * ND + k:3 * ND + k + 1],
                                 bias=cols[:, 2 * ND + k:2 * ND + k + 1]).then_inc(moved, 1)

        @block.gpsimd
        def _(g):
            g.wait_ge(squared, NTC)
            inverse_root(Chain(g, pool_steps), g, core, rs, ss, 1.0 / D, RMS2_EPS).then_inc(rooted, 1)

        @block.vector
        def _(v):
            v.wait_ge(rooted, 1)
            for i in range(NTC):
                v.tensor_scalar(x[:, i, :], x[:, i, :], rs[:, i:i + 1], None, ALU.mult).then_inc(scaled, 1)

        @block.tensor
        def _(pe):
            for i in range(NTC):
                pe.wait_ge(scaled, i + 1)
                for k in range(ND):
                    t = pe.transpose(ps[:, 2 * i + k // 4, (k % 4) * P:(k % 4 + 1) * P],
                                     x[:, i, k * P:(k + 1) * P], core.col("ident"))
                    if k % 4 == 3:
                        t.then_inc(turned, 1)


def combine_experts(core, m):
    nc, ps, xnT = core.nc, core.ps, m["xnT"]
    sem = lambda n: core.semaphore("ce_" + n)
    r_loaded = [sem(f"r{i}") for i in range(2)]
    h_stored = [sem(f"h_stored{i}") for i in range(2)]
    gathered = [sem(f"y{i}") for i in range(2)]
    (weights, picked, summed, var_ready, rstd_ready, h_ready, squared, rs_ready, scaled, turned,
     moved, steps, pool_steps) = map(sem, (
         "weights", "picked", "summed", "var", "rstd", "h_ready", "squared", "rs_ready", "scaled",
         "turned", "moved", "steps", "pool_steps"))
    at = m["free"]

    def take(*shape, dt=None):
        nonlocal at
        n = int(np.prod(shape))
        at += n
        return core.place(at - n, *shape, dt=dt)

    g2, b2, sq, xr = (take(D) for _ in range(4))
    work, rest, h = ([take(D), take(D)] for _ in range(3))
    y = [[take(D), take(D)], [take(D), take(D)]]
    st, mv, rstd, ss, rs = ([take(n) for _ in range(2)] for n in (12, 2, 1, 1, 1))
    idx = [[take(1, dt=I32), take(1, dt=I32)] for _ in range(2)]
    cols = m["mod_cols"]
    last = NT // 2 - 1
    with nc.Block() as block:
        @block.sync
        def _(sp):
            sp.dma_start(g2, row_on_all(core.ins["ln2_g"], D)).then_inc(weights, 16)
            sp.dma_start(b2, row_on_all(core.ins["ln2_b"], D)).then_inc(weights, 16)
            with sp.Fori(0, NT // 2) as it:
                for j in range(2):
                    sp.wait_ge(summed, it * 2 + j + 1)
                    sp.dma_start(rest[j], m["rest"][it * 2 + j]).then_inc(r_loaded[j], 16)

        @block.gpsimd
        def _(g):
            def gather(it, j):
                n = it * 2 + j
                g.wait_ge(summed, n + 1)
                for i in range(2):
                    core.waited(g)
                    g.tensor_copy(idx[j][i], m["dest"][:, bass.ds(it * 2 + (j + i * NT), 1)])\
                     .then_inc(picked, 1)
                    g.wait_ge(picked, n * 2 + i + 1)
                    core.waited(g)
                    g.indirect_dma_start(y[j][i], None, m["y1_rows"], bass.IndirectOffsetOnAxis(
                        ap=idx[j][i], axis=0)).then_inc(gathered[j], 16)

            def norm_root(c, it, j):
                g.wait_ge(var_ready, it * 2 + j + 1)
                inverse_root(c, g, core, rstd[j], mv[j][:, 1:2], 1.0, LN_EPS).then_inc(rstd_ready, 1)

            def rms_root(c, it, j):
                g.wait_ge(squared, it * 2 + j + 1)
                inverse_root(c, g, core, rs[j], ss[j], 1.0 / D, RMS2_EPS).then_inc(rs_ready, 1)

            gather(0, 0)
            gather(0, 1)
            norm_root(Chain(g, pool_steps), 0, 0)
            with g.Fori(0, last) as it:
                c = Chain(g, pool_steps, it * 4 + 1)
                norm_root(c, it, 1)
                gather(it + 1, 0)
                rms_root(c, it, 0)
                norm_root(c, it + 1, 0)
                gather(it + 1, 1)
                rms_root(c, it, 1)
            c = Chain(g, pool_steps, last * 4 + 1)
            norm_root(c, last, 1)
            rms_root(c, last, 0)
            rms_root(c, last, 1)

        @block.vector
        def _(v):
            v.sem_inc(summed, 2)
            v.sem_inc(h_ready, 2)
            v.wait_ge(weights, 32)
            w = m["weights"]

            def combine(c, it, j):
                n = it * 2 + j
                v.wait_ge(r_loaded[j], it * 16 + 16)
                v.wait_ge(gathered[j], it * 32 + 32)
                v.wait_ge(h_ready, n + 1)
                c.step(v.scalar_tensor_tensor(work[j], y[j][0], w[:, bass.ds(it * 4 + 2 * j, 1)], rest[j],
                                              ALU.mult, ALU.add))
                v.scalar_tensor_tensor(work[j], y[j][1], w[:, bass.ds(it * 4 + (2 * j + 1), 1)], work[j],
                                       ALU.mult, ALU.add).then_inc(summed, 1)
                v.wait_ge(summed, n + 3)
                stats_of(core, c, v, st[j], mv[j], work[j]).then_inc(var_ready, 1)

            def norm(c, it, j):
                n = it * 2 + j
                v.wait_ge(rstd_ready, n + 1)
                c.step(v.tensor_scalar(work[j], work[j], mv[j][:, 0:1], rstd[j], ALU.subtract, ALU.mult))
                c.step(v.tensor_tensor(work[j], work[j], g2, ALU.mult))
                v.wait_ge(h_stored[j], it * 16)
                v.wait_ge(scaled, n + 1)
                v.tensor_tensor(h[j], work[j], b2, ALU.add).then_inc(h_ready, 1)

            combine(Chain(v, steps), 0, 0)
            with v.Fori(0, last) as it:
                c = Chain(v, steps, it * 10 + 3)
                combine(c, it, 1)
                norm(c, it, 0)
                combine(c, it + 1, 0)
                norm(c, it, 1)
                assert c.n == 10
            c = Chain(v, steps, last * 10 + 3)
            combine(c, last, 1)
            norm(c, last, 0)
            norm(c, last, 1)

        @block.tensor
        def _(pe):
            with pe.Fori(0, NT) as n:
                pe.wait_ge(scaled, n + 3)
                pe.wait_ge(moved, n)
                for k in range(ND):
                    t = pe.transpose(ps[:, k // 4, (k % 4) * P:(k % 4 + 1) * P],
                                     xr[:, k * P:(k + 1) * P], core.col("ident"))
                t.then_inc(turned, 1)

        @block.scalar
        def _(a):
            a.sem_inc(scaled, 2)

            def square(it, j):
                n = it * 2 + j
                a.wait_ge(h_ready, n + 3)
                a.wait_ge(squared, n)
                a.activation(sq, h[j], ACT.Square, accum_out=ss[j]).then_inc(squared, 1)
                a.dma_start(m["h2"][n], h[j]).then_inc(h_stored[j], 16)

            def scale(it, j):
                n = it * 2 + j
                a.wait_ge(rs_ready, n + 1)
                a.wait_ge(turned, n)
                a.activation(xr, h[j], ACT.Copy, scale=rs[j]).then_inc(scaled, 1)

            def move(it, j):
                a.wait_ge(turned, it * 2 + j + 1)
                core.waited(a)
                for k in range(ND):
                    t = a.activation(xnT[:, k, bass.ds(it * (2 * P) + j * P, P)],
                                     ps[:, k // 4, (k % 4) * P:(k % 4 + 1) * P], ACT.Identity,
                                     scale=cols[:, ND + k:ND + k + 1], bias=cols[:, k:k + 1])
                t.then_inc(moved, 1)

            square(0, 0)
            with a.Fori(0, last) as it:
                scale(it, 0)
                square(it, 1)
                move(it, 0)
                scale(it, 1)
                square(it + 1, 0)
                move(it, 1)
            scale(last, 0)
            square(last, 1)
            move(last, 0)
            scale(last, 1)
            move(last, 1)
            for q in h_stored:
                a.wait_ge(q, 16 * (NT // 2))



def second_projections(core, m):
    nc, ps, xnT = core.nc, core.ps, m["xnT"]
    sem = lambda n: core.semaphore("p2_" + n)
    loaded = [sem(f"w{i}") for i in range(2)]
    taken = [sem(f"taken{i}") for i in range(2)]
    done = sem("done")
    w = [core.place(m["free"] + i * D, ND, P) for i in range(2)]
    wd = core.ins["w_in2_tiles"]
    with nc.Block() as block:
        @block.sync
        def _(sp):
            loads_of_tiles(sp, w, wd, 0, 12, loaded, done)

        @block.tensor
        def _(pe):
            pe.sem_inc(done, 2)
            tile_products(pe, ps, xnT, w, loaded, done, taken, 8, (HALF, HALF))
            pe.wait_ge(taken[1], 9)
            tile_products(pe, ps, xnT, w, loaded, done, taken, 4, (HALF, HALF, CTX), before=16)

        @block.scalar
        def _(a):
            a.sem_inc(taken[0], 1)
            a.sem_inc(taken[1], 1)
            copy_tiles(a, ps, m["qconv"], done, taken, 8, (HALF, HALF))
            copy_tiles(a, ps, m["kv"], done, taken, 4, (HALF, HALF, CTX), before=16)


def rotate_and_convolve(core, m):
    nc, ps = core.nc, core.ps
    sem = lambda n: core.semaphore("rc_" + n)
    (tables, swapped, sined, cosined, added, v_turned, v_moved, product, copied, steps) = map(sem, (
        "tables", "swapped", "sined", "cosined", "added", "v_turned", "v_moved", "product",
        "copied", "steps"))
    qc, kv, q2, k2, vt = m["qconv"], m["kv"], m["q2"], m["k2"], m["v2"]
    cos_t, sin_t = core.place(m["tables"], S), core.place(m["tables"] + S, S)
    tmp = [core.place(m["tmp"] + i * S, S) for i in range(2)]
    raw = [qc[:, h, :] for h in range(4)] + [kv[:, h, 0:S] for h in range(4)]
    dst = [q2[:, h] for h in range(4)] + [k2[:, h] for h in range(4)]
    gb, gc, xc = (qc[:, 4 * i:4 * i + 4, :] for i in (1, 2, 3))
    acc = m["conv2"]
    NU = 8
    with nc.Block() as block:
        @block.sync
        def _(sp):
            sp.dma_start(cos_t, core.ins["cos2"]).then_inc(tables, 16)
            sp.dma_start(sin_t, core.ins["sin2"]).then_inc(tables, 16)

        @block.tensor
        def _(pe):
            for n in range(NU):
                if n >= 2:
                    pe.wait_ge(sined, n - 1)
                for c in range(2):
                    t = pe.matmul(ps[:, 2 * (n % 2) + c, :], core.col("turn"),
                                  raw[n][:, c * HALF:(c + 1) * HALF], start=True, stop=True)
                t.then_inc(swapped, 1)
            for i in range(NK2):
                if i >= 2:
                    pe.wait_ge(v_moved, i - 1)
                for h in range(4):
                    t = pe.transpose(ps[:, 4 + i % 2, h * P:(h + 1) * P],
                                     kv[:, 4 + h, i * P:(i + 1) * P], core.col("ident"))
                t.then_inc(v_turned, 1)

        @block.gpsimd
        def _(g):
            g.wait_ge(tables, 32)
            for n in range(NU):
                g.wait_ge(swapped, n + 1)
                g.tensor_tensor(raw[n], raw[n], cos_t, ALU.mult).then_inc(cosined, 1)

        @block.vector
        def _(v):
            c = Chain(v, steps)
            for h in range(4):
                v.tensor_tensor(gc[:, h, :], gc[:, h, :], xc[:, h, :], ALU.mult).then_inc(product, 1)
            v.wait_ge(tables, 32)
            for n in range(NU):
                v.wait_ge(swapped, n + 1)
                v.tensor_tensor(tmp[n % 2], flat2(ps, 2 * (n % 2)), sin_t, ALU.mult).then_inc(sined, 1)
                v.wait_ge(sined, n + 1)
                v.wait_ge(cosined, n + 1)
                for i in range(2):
                    rows = slice(64 * i, 64 * i + 64)
                    v.tensor_tensor(dst[n][:, i, 0:S], tmp[n % 2][rows], raw[n][rows], ALU.add)\
                     .then_inc(added, 1)
            v.wait_ge(product, 4)
            wc = lambda h, t: core.col("conv2", 3 * h + t, 3 * h + t + 1)
            for h in range(4):
                src = gc[:, h, :]
                c.did(v.tensor_scalar(acc[:, h, :], src, wc(h, 1), None, ALU.mult))
            c.wait()
            for h in range(4):
                src = gc[:, h, :]
                c.did(v.scalar_tensor_tensor(acc[:, h, 1:S], src[:, 0:S - 1], wc(h, 0), acc[:, h, 1:S],
                                             ALU.mult, ALU.add))
            c.wait()
            for h in range(4):
                src = gc[:, h, :]
                c.did(v.scalar_tensor_tensor(acc[:, h, 0:S - 1], src[:, 1:S], wc(h, 2), acc[:, h, 0:S - 1],
                                             ALU.mult, ALU.add))
            c.wait()
            for h in range(4):
                c.did(v.tensor_tensor(acc[:, h, :], acc[:, h, :], gb[:, h, :], ALU.mult))

        @block.scalar
        def _(a):
            for h in range(4):
                for i in range(2):
                    a.activation(k2[:, h, i, S:SA], kv[64 * i:64 * i + 64, h, S:SA], ACT.Copy)\
                     .then_inc(copied, 1)
            a.wait_ge(added, 2 * NU)
            for i in range(NK2):
                a.wait_ge(v_turned, i + 1)
                a.activation(vt[:, i, :], ps[:, 4 + i % 2, :], ACT.Copy).then_inc(v_moved, 1)


def differential_attention(core, m):
    nc, ps, q2, k2, vt = core.nc, core.ps, m["q2"], m["k2"], m["v2"]
    sem = lambda n: core.semaphore("da_" + n)
    (staged, scored, biased, exped, combined, turned, moved, summed, kept, steps) = map(sem, (
        "staged", "scored", "biased", "exped", "combined", "turned", "moved", "summed", "kept", "steps"))
    at = m["free"]

    def take(*shape, parts=P):
        nonlocal at
        n = int(np.prod(shape))
        at += n
        return core.place(at - n, *shape, parts=parts)

    q = [take(2, P, parts=64) for _ in range(2)]
    e = [take(2, SA) for _ in range(2)]
    at_ = [take(NK2, P) for _ in range(2)]
    mx, nb, den, co = take(4), take(4), take(4), take(4)
    o = m["o2"]
    kf = k2.rearrange("p a b c -> p (a b c)")
    scale = float(HD2) ** -0.5
    G = NH2 * NT
    GROUPS = ((0, 4), (4, 8), (8, NK2))
    last = G // 2 - 1
    full = ps[:].rearrange("p a b -> p (a b)")

    def where(it, j):
        return it // (NT // 2), (it % (NT // 2)) * 2 + j

    with nc.Block() as block:
        @block.gpsimd
        def _(g):
            def stage(it, j):
                h, i = where(it, j)
                g.wait_ge(scored, (it * 2 + j) * 2 + 2)
                core.waited(g)
                g.tensor_copy(q[j], q2.rearrange("p a b c -> p (a b) c")[
                    :, bass.ds(h * 2, 2), bass.ds(i * P, P)]).then_inc(staged, 1)

            stage(0, 0)
            stage(0, 1)
            with g.Fori(0, last) as it:
                for j in range(2):
                    stage(it + 1, j)

        @block.tensor
        def _(pe):
            pe.sem_inc(scored, 4)
            pe.sem_inc(turned, 6)
            pe.sem_inc(summed, 2)

            def scores(it, j, i):
                g = it * 2 + j
                h, _ = where(it, j)
                pe.wait_ge(staged, g + 1)
                pe.wait_ge(exped, g * 2 + i + 1)
                for c, wd in enumerate((HALF, HALF, CTX)):
                    t = pe.matmul(ps[:, 3 * i + c, 0:wd], q[j][:, i, :],
                                  kf[:, bass.ds(h * (2 * SA) + (i * SA + c * HALF), wd)],
                                  start=True, stop=True, skip_group_check=True)
                    if c == 0:
                        yield
                t.then_inc(scored, 1)

            def turn(it, j, r):
                g = it * 2 + j
                lo, hi = GROUPS[r]
                if r == 0:
                    pe.wait_ge(combined, g + 1)
                pe.wait_ge(moved, g * 3 + r + 1)
                if r == 1:
                    pe.wait_ge(kept, g + 2)
                for t in range(lo, hi):
                    ins = pe.transpose(ps[:, 6 + (j * 3 + r) % 2, (t - lo) * P:(t - lo + 1) * P],
                                       e[j][:, 1, t * P:(t + 1) * P], core.col("ident"))
                ins.then_inc(turned, 1)

            def sums(it, j):
                g = it * 2 + j
                h, _ = where(it, j)
                pe.wait_ge(moved, g * 3 + 5)
                for t in range(NK2):
                    ins = pe.matmul(ps[:, 6 + j, CTX:CTX + P], at_[j][:, t, :],
                                    vt[:, t, bass.ds(h * P, P)], start=(t == 0), stop=(t == NK2 - 1),
                                    skip_group_check=True)
                ins.then_inc(summed, 1)

            def step(it, j, nxt):
                if nxt:
                    for _ in scores(*nxt, 0):
                        pass
                turn(it, j, 0)
                turn(it, j, 1)
                if nxt:
                    for _ in scores(*nxt, 1):
                        turn(it, j, 2)
                else:
                    turn(it, j, 2)
                sums(it, j)

            for i in range(2):
                for _ in scores(0, 0, i):
                    pass
            with pe.Fori(0, last) as it:
                step(it, 0, (it, 1))
                step(it, 1, (it + 1, 0))
            step(last, 0, (last, 1))
            step(last, 1, None)

        @block.vector
        def _(v):
            v.sem_inc(kept, 2)
            per = 6

            def bias(c, it, j):
                g = it * 2 + j
                for i in range(2):
                    x = 2 * j + i
                    v.wait_ge(scored, g * 2 + i + 5)
                    c.step(v.reduce_max(mx[:, x:x + 1], full[:, 3 * i * HALF:3 * i * HALF + SA], AX))
                    v.tensor_scalar(nb[:, x:x + 1], mx[:, x:x + 1], -scale, None, ALU.mult).then_inc(biased, 1)

            def first(c, it, j):
                x = 2 * j
                v.wait_ge(exped, (it * 2 + j) * 2 + 3)
                c.step(v.reciprocal(co[:, x:x + 1], den[:, x:x + 1]))
                c.step(v.tensor_scalar(e[j][:, 0, :], e[j][:, 0, :], co[:, x:x + 1], None, ALU.mult))

            def combine(c, it, j):
                x = 2 * j + 1
                v.wait_ge(exped, (it * 2 + j) * 2 + 4)
                c.step(v.reciprocal(co[:, x:x + 1], den[:, x:x + 1]))
                c.step(v.tensor_tensor(co[:, x:x + 1], co[:, x:x + 1], m["neg_lam"], ALU.mult))
                v.scalar_tensor_tensor(e[j][:, 1, :], e[j][:, 1, :], co[:, x:x + 1], e[j][:, 0, :],
                                       ALU.mult, ALU.add).then_inc(combined, 1)

            def keep(it, j):
                g = it * 2 + j
                h, i = where(it, j)
                v.wait_ge(summed, g + 3)
                v.tensor_copy(o.rearrange("p a b -> p (a b)")[:, bass.ds(i * (NH2 * P) + h * P, P)],
                              ps[:, 6 + j, CTX:CTX + P]).then_inc(kept, 1)

            c = Chain(v, steps)
            bias(c, 0, 0)
            first(c, 0, 0)
            combine(c, 0, 0)
            bias(c, 0, 1)
            first(c, 0, 1)
            before = c.n
            with v.Fori(0, last) as it:
                c = Chain(v, steps, it * (2 * per) + before)
                combine(c, it, 1)
                keep(it, 0)
                bias(c, it + 1, 0)
                first(c, it + 1, 0)
                combine(c, it + 1, 0)
                keep(it, 1)
                bias(c, it + 1, 1)
                first(c, it + 1, 1)
                assert c.n == 2 * per
            c = Chain(v, steps, last * 2 * per + before)
            combine(c, last, 1)
            keep(last, 0)
            keep(last, 1)

        @block.scalar
        def _(a):
            a.sem_inc(exped, 2)
            a.sem_inc(moved, 2)

            def exp(it, j, i):
                g = it * 2 + j
                x = 2 * j + i
                a.wait_ge(biased, g * 2 + i + 1)
                a.wait_ge(turned, g * 3 + 3)
                a.activation(e[j][:, i, :], full[:, 3 * i * HALF:3 * i * HALF + SA], ACT.Exp,
                             bias=nb[:, x:x + 1], scale=scale, accum_out=den[:, x:x + 1]).then_inc(exped, 1)

            def move(it, j, r):
                g = it * 2 + j
                lo, hi = GROUPS[r]
                a.wait_ge(turned, g * 3 + r + 7)
                a.wait_ge(summed, g + 1)
                a.activation(at_[j].rearrange("p a b -> p (a b)")[:, lo * P:hi * P],
                             ps[:, 6 + (j * 3 + r) % 2, 0:(hi - lo) * P], ACT.Copy).then_inc(moved, 1)

            def step(it, j, nxt):
                move(it, j, 0)
                move(it, j, 1)
                if nxt:
                    exp(*nxt, 0)
                move(it, j, 2)
                if nxt:
                    exp(*nxt, 1)

            exp(0, 0, 0)
            exp(0, 0, 1)
            with a.Fori(0, last) as it:
                step(it, 0, (it, 1))
                step(it, 1, (it + 1, 0))
            step(last, 0, (last, 1))
            step(last, 1, None)


def attention_output(core, m):
    nc, ps, o, oT = core.nc, core.ps, m["o2"], m["o2T"]
    sem = lambda n: core.semaphore("ao_" + n)
    squared, reduced, rooted, normed, turned, moved, pool_steps = map(sem, (
        "squared", "reduced", "rooted", "normed", "turned", "moved", "pool_steps"))
    sq = core.place(m["free"], NT * NH2, P)
    ss = core.place(m["free"] + NT * NH2 * P, NT * NH2)
    rs = core.place(m["free"] + NT * NH2 * P + 64, NT * NH2)
    rows = o.rearrange("p a (h e) -> p (a h) e", e=P)
    with nc.Block() as block:
        @block.scalar
        def _(a):
            a.activation(sq, rows, ACT.Square).then_inc(squared, 1)
            for i in range(NT):
                a.wait_ge(turned, i + 1)
                a.activation(oT[:, :, i * P:(i + 1) * P],
                             ps[:, i % 2, :].rearrange("p (a b) -> p a b", b=P), ACT.Copy).then_inc(moved, 1)

        @block.vector
        def _(v):
            v.wait_ge(squared, 1)
            v.tensor_reduce(ss, sq, AX, ALU.add).then_inc(reduced, 1)
            v.wait_ge(rooted, 1)
            for i in range(NT):
                r = rows[:, NH2 * i:NH2 * (i + 1), :]
                s_ = rs[:, NH2 * i:NH2 * (i + 1)].unsqueeze(2).to_broadcast([P, NH2, P])
                v.tensor_tensor(r, r, s_, ALU.mult).then_inc(normed, 1)
                v.wait_ge(normed, 2 * i + 1)
                v.scalar_tensor_tensor(r, r, 1.0 - LAM_INIT,
                                       core.col("subln").unsqueeze(1).to_broadcast([P, NH2, P]),
                                       ALU.mult, ALU.mult).then_inc(normed, 1)

        @block.gpsimd
        def _(g):
            g.wait_ge(reduced, 1)
            c = Chain(g, pool_steps)
            for i in range(4):
                t = inverse_root(c, g, core, rs[:, 8 * i:8 * i + 8], ss[:, 8 * i:8 * i + 8], 1.0 / P, RMS2_EPS)
                if i < 3:
                    c.did(t)
                else:
                    t.then_inc(rooted, 1)

        @block.tensor
        def _(pe):
            for i in range(NT):
                pe.wait_ge(normed, 2 * i + 2)
                if i >= 2:
                    pe.wait_ge(moved, i - 1)
                for h in range(NH2):
                    t = pe.transpose(ps[:, i % 2, h * P:(h + 1) * P], o[:, i, h * P:(h + 1) * P],
                                     core.col("ident"))
                t.then_inc(turned, 1)


def mix_output(core, m):
    nc, ps = core.nc, core.ps
    sem = lambda n: core.semaphore("mo_" + n)
    h_loaded = [sem(f"h{i}") for i in range(2)]
    h_stored = [sem(f"h_stored{i}") for i in range(2)]
    x_stored = [sem(f"x_stored{i}") for i in range(2)]
    (weights, zeroed, staged, made, squared, rooted, taken, h_ready, h_squared, h_rooted, x_ready,
     turned, moved, routed, kept, steps, pool_steps, ff_cleared) = map(sem, (
         "weights", "zeroed", "staged", "made", "squared", "rooted", "taken", "h_ready",
         "h_squared", "h_rooted", "x_ready", "turned", "moved", "routed", "kept", "steps",
         "pool_steps", "ff_cleared"))
    at = m["free"]

    def take(*shape):
        nonlocal at
        n = int(np.prod(shape))
        at += n
        return core.place(at - n, *shape)

    wo, wr = take(ND, D), take(ND, NE)
    mt = [take(ND, P) for _ in range(2)]
    hin, h, xn = ([take(D) for _ in range(2)] for _ in range(3))
    xT, sq, t, zero = take(ND, P), take(D), take(D), take(D)
    ss, rs, hs, hr = (take(1) for _ in range(4))
    g1, sh2, sc2 = m["rows"][0:3]
    with nc.Block() as block:
        @block.sync
        def _(sp):
            sp.dma_start(wr, core.ins["w_router2_k"]).then_inc(weights, 16)
            sp.dma_start(wo, core.ins["w_out2_k"]).then_inc(weights, 16)
            with sp.Fori(0, NT // 2) as it:
                for j in range(2):
                    sp.wait_ge(h_ready, it * 2 + j + 1)
                    sp.dma_start(hin[j], m["h2"][it * 2 + j]).then_inc(h_loaded[j], 16)
            sp.wait_ge(zeroed, 1)
            for i in range(NT):
                sp.dma_start(m["ff"][i], zero).then_inc(ff_cleared, 16)
            sp.wait_ge(ff_cleared, 16 * NT)

        @block.gpsimd
        def _(g):
            g.memset(zero, 0.0).then_inc(zeroed, 1)

            def stage(it, j):
                g.wait_ge(made, it * 2 + j + 1)
                core.waited(g)
                for i, src in ((0, m["o2T"]), (4, m["conv2"])):
                    g.tensor_copy(mt[j][:, i:i + 4, :], src[:, :, bass.ds(it * (2 * P) + j * P, P)])\
                     .then_inc(staged, 1)

            def roots(it, j):
                n = it * 2 + j
                c = Chain(g, pool_steps, n * 2)
                g.wait_ge(squared, n + 1)
                inverse_root(c, g, core, rs, ss, 1.0 / D, RMS2_EPS).then_inc(rooted, 1)
                g.wait_ge(h_squared, n + 1)
                inverse_root(c, g, core, hr, hs, 1.0 / D, RMS2_EPS).then_inc(h_rooted, 1)

            stage(0, 0)
            with g.Fori(0, NT // 2 - 1) as it:
                stage(it, 1)
                roots(it, 0)
                stage(it + 1, 0)
                roots(it, 1)
            last = NT // 2 - 1
            stage(last, 1)
            roots(last, 0)
            roots(last, 1)

        @block.tensor
        def _(pe):
            pe.sem_inc(made, 2)
            pe.wait_ge(weights, 32)

            def product(it, j):
                n = it * 2 + j
                pe.wait_ge(staged, n * 2 + 2)
                pe.wait_ge(taken, n + 1)
                for c in range(2):
                    for k in range(ND):
                        x = pe.matmul(ps[:, 2 * j + c, :], mt[j][:, k, :],
                                      wo[:, k, c * HALF:(c + 1) * HALF], start=(k == 0), stop=(k == ND - 1))
                x.then_inc(made, 1)

            def after(it, j):
                n = it * 2 + j
                pe.wait_ge(x_ready, n + 1)
                for k in range(ND):
                    x = pe.transpose(ps[:, 4 + k // 4, (k % 4) * P:(k % 4 + 1) * P],
                                     xn[j][:, k * P:(k + 1) * P], core.col("ident"))
                x.then_inc(turned, 1)
                pe.wait_ge(moved, n + 1)
                pe.wait_ge(kept, n)
                for k in range(ND):
                    x = pe.matmul(ps[:, 6, 0:NE], xT[:, k, :], wr[:, k, :], start=(k == 0), stop=(k == ND - 1))
                x.then_inc(routed, 1)

            product(0, 0)
            with pe.Fori(0, NT // 2 - 1) as it:
                product(it, 1)
                after(it, 0)
                product(it + 1, 0)
                after(it, 1)
            last = NT // 2 - 1
            product(last, 1)
            after(last, 0)
            after(last, 1)

        @block.scalar
        def _(a):
            with a.Fori(0, NT // 2) as it:
                for j in range(2):
                    n = it * 2 + j
                    a.wait_ge(made, n + 3)
                    a.wait_ge(h_squared, n)
                    a.activation(sq, flat2(ps, 2 * j), ACT.Square, accum_out=ss).then_inc(squared, 1)
                    a.wait_ge(h_ready, n + 3)
                    a.wait_ge(squared, n + 1)
                    a.activation(sq, h[j], ACT.Square, accum_out=hs).then_inc(h_squared, 1)
                    a.dma_start(m["h3"][n], h[j]).then_inc(h_stored[j], 16)
                    a.wait_ge(x_ready, n + 1)
                    a.dma_start(m["xn"][n], xn[j]).then_inc(x_stored[j], 16)
                    a.wait_ge(turned, n + 1)
                    a.wait_ge(routed, n)
                    a.activation(xT.rearrange("p a b -> p (a b)"), flat2(ps, 4), ACT.Copy).then_inc(moved, 1)
            for q in h_stored + x_stored:
                a.wait_ge(q, 16 * (NT // 2))

        @block.vector
        def _(v):
            v.sem_inc(taken, 2)
            v.sem_inc(h_ready, 2)
            per = 1

            def step(it, j):
                n = it * 2 + j
                c = Chain(v, steps, n * per)
                v.wait_ge(x_ready, n)
                v.wait_ge(rooted, n + 1)
                v.scalar_tensor_tensor(t, flat2(ps, 2 * j), rs, g1, ALU.mult, ALU.mult).then_inc(taken, 1)
                v.wait_ge(taken, n + 3)
                v.wait_ge(h_loaded[j], it * 16 + 16)
                v.wait_ge(h_stored[j], it * 16)
                v.tensor_tensor(h[j], t, hin[j], ALU.add).then_inc(h_ready, 1)
                v.wait_ge(h_rooted, n + 1)
                v.wait_ge(h_ready, n + 3)
                c.step(v.scalar_tensor_tensor(t, h[j], hr, sc2, ALU.mult, ALU.mult))
                v.wait_ge(x_stored[j], it * 16)
                v.tensor_tensor(xn[j], t, sh2, ALU.add).then_inc(x_ready, 1)
                assert c.n == per
                v.wait_ge(routed, n + 1)
                v.tensor_copy(m["logits2"][:, bass.ds(it * (2 * NE) + j * NE, NE)], ps[:, 6, 0:NE])\
                 .then_inc(kept, 1)

            with v.Fori(0, NT // 2) as it:
                step(it, 0)
                step(it, 1)



def expert_choice(core, m):
    nc, ps = core.nc, core.ps
    sem = lambda n: core.semaphore("ec_" + n)
    centred, exped, ready, turned, steps, chosen, back = map(sem, (
        "centred", "exped", "ready", "turned", "steps", "chosen", "back"))
    at = m["free"]
    aff = core.place(at, NT, NE)
    peak = core.place(at + P, NT)
    affT = core.place(at + 2 * P, S, parts=NE)
    val = core.place(at + 2 * P + S, CAP, parts=NE)
    idx = core.place(at + 3 * P + S, CAP, parts=NE, dt=mybir.dt.uint32)
    idf = core.place(at + 4 * P + S, CAP, parts=NE)
    fl = aff.rearrange("p a b -> p (a b)")
    spread = peak.unsqueeze(2).to_broadcast([P, NT, NE])
    with nc.Block() as block:
        @block.vector
        def _(v):
            c = Chain(v, steps)
            lg = m["logits2"].rearrange("p (a b) -> p a b", b=NE)
            c.step(v.tensor_reduce(peak, lg, AX, ALU.max))
            v.tensor_tensor(aff, lg, spread, ALU.subtract).then_inc(centred, 1)
            v.wait_ge(exped, 1)
            c.step(v.tensor_reduce(peak, aff, AX, ALU.add))
            c.step(v.reciprocal(peak, peak))
            v.tensor_tensor(aff, aff, spread, ALU.mult).then_inc(ready, 1)
            v.wait_ge(turned, 1)
            c.step(v.tensor_copy(affT, flat2(ps, 0)[0:NE]))
            for r in range(CAP // 8):
                best, where = val[:, 8 * r:8 * r + 8], idx[:, 8 * r:8 * r + 8]
                c.step(v.max(best, affT))
                c.step(v.max_index(where, best, affT))
                c.step(v.match_replace(affT, best, affT, -1.0))
            v.tensor_copy(idf, idx).then_inc(chosen, 1)
            v.wait_ge(back, 1)
            c.did(v.tensor_copy(m["ec_weight"], ps[:, 2, 0:NE]))
            c.did(v.tensor_copy(m["ec_token"], ps[:, 3, 0:NE]))

        @block.scalar
        def _(a):
            a.wait_ge(centred, 1)
            a.activation(fl, fl, ACT.Exp).then_inc(exped, 1)

        @block.tensor
        def _(pe):
            pe.wait_ge(ready, 1)
            for i in range(NT):
                t = pe.transpose(ps[0:NE, i // 4, (i % 4) * P:(i % 4 + 1) * P], aff[:, i, :], core.col("ident"))
            t.then_inc(turned, 1)
            pe.wait_ge(chosen, 1)
            pe.transpose(ps[:, 2, 0:NE], val, core.col("ident")[0:NE, 0:NE])
            pe.transpose(ps[:, 3, 0:NE], idf, core.col("ident")[0:NE, 0:NE]).then_inc(back, 1)


def chosen_experts(core, m):
    nc, ps = core.nc, core.ps
    sem = lambda n: core.semaphore("e2_" + n)
    NDN = 4
    gu_loaded = [sem(f"gu{k}") for k in range(ND)]
    dn_loaded = [sem(f"dn{k}") for k in range(NDN)]
    (gu_used, dn_used, x_staged, gathered, x_turned, x_moved, silu_done, h_ready, h_turned, h_moved,
     y_ready, y_staged, added) = map(sem, (
         "gu_used", "dn_used", "x_staged", "gathered", "x_turned", "x_moved", "silu_done",
         "h_ready", "h_turned", "h_moved", "y_ready", "y_staged", "added"))
    at = m["free"]

    def take(*shape, dt=None):
        nonlocal at
        n = int(np.prod(shape))
        at += n
        return core.place(at - n, *shape, dt=dt)

    gu = [take(2 * FE2) for _ in range(ND)]
    at = m["free_upper"]
    dn = [take(2, D) for _ in range(NDN)]
    x, xT, sg, h, hT, yo = take(D), take(ND, P), take(FE2), take(FE2), take(FE2 // P, P), take(D)
    xi, yi = take(1, dt=I32), take(1, dt=I32)
    token = m["ec_token"]
    with nc.Block() as block:
        @block.sync
        def _(sp):
            def load_gu(e):
                for k in range(ND):
                    sp.wait_ge(gu_used, e * ND + k + 1)
                    sp.dma_start(gu[k], core.ins["gate_up2"][e * ND + k]).then_inc(gu_loaded[k], 16)

            def load_dn(e):
                for k in range(NDN):
                    sp.wait_ge(dn_used, e * NDN + k + 1)
                    sp.dma_start(dn[k], core.ins["down2"][e * NDN + k]).then_inc(dn_loaded[k], 16)

            load_gu(0)
            with sp.Fori(0, NE - 1) as e:
                load_gu(e + 1)
                load_dn(e)
            load_dn(NE - 1)

        @block.gpsimd
        def _(g):
            def gather(e):
                g.wait_ge(x_turned, e)
                g.wait_ge(gathered, e * 16)
                g.tensor_copy(xi, token[:, bass.ds(e, 1)]).then_inc(x_staged, 1)
                g.wait_ge(x_staged, e + 1)
                core.waited(g)
                g.indirect_dma_start(x, None, m["xn_rows"], bass.IndirectOffsetOnAxis(ap=xi, axis=0))\
                 .then_inc(gathered, 16)

            def add(e):
                g.wait_ge(added, e * 16)
                g.tensor_copy(yi, token[:, bass.ds(e, 1)]).then_inc(y_staged, 1)
                g.wait_ge(y_staged, e + 1)
                g.wait_ge(y_ready, e + 1)
                core.waited(g)
                g.indirect_dma_start(m["ff_rows"], bass.IndirectOffsetOnAxis(ap=yi, axis=0), yo, None,
                                     compute_op=ALU.add).then_inc(added, 16)

            gather(0)
            gather(1)
            with g.Fori(2, NE) as e:
                gather(e)
                add(e - 2)
            add(NE - 2)
            add(NE - 1)
            g.wait_ge(added, 16 * NE)

        @block.tensor
        def _(pe):
            pe.sem_inc(gu_used, ND)
            pe.sem_inc(dn_used, NDN)

            def turn_x(e):
                pe.wait_ge(gathered, e * 16 + 16)
                if not isinstance(e, int):
                    pe.wait_ge(h_moved, e - 1)
                for k in range(ND):
                    t = pe.transpose(ps[:, 4 + k // 4, (k % 4) * P:(k % 4 + 1) * P],
                                     x[:, k * P:(k + 1) * P], core.col("ident"))
                t.then_inc(x_turned, 1)

            def up(e):
                pe.wait_ge(x_moved, e + 1)
                pe.wait_ge(h_ready, e)
                for k in range(ND):
                    pe.wait_ge(gu_loaded[k], e * 16 + 16)
                    for c in range(4):
                        t = pe.matmul(ps[:, c, :], xT[:, k, :], gu[k][:, c * HALF:(c + 1) * HALF],
                                      start=(k == 0), stop=(k == ND - 1), skip_group_check=True)
                    t.then_inc(gu_used, 1)

            def turn_h(e):
                pe.wait_ge(h_ready, e + 1)
                pe.wait_ge(x_moved, NE if isinstance(e, int) and e == NE - 1 else e + 2)
                for k in range(FE2 // P):
                    t = pe.transpose(ps[:, 4 + k // 4, (k % 4) * P:(k % 4 + 1) * P],
                                     h[:, k * P:(k + 1) * P], core.col("ident"))
                t.then_inc(h_turned, 1)

            def down(e):
                pe.wait_ge(h_moved, e + 1)
                pe.wait_ge(y_ready, e)
                for k in range(FE2 // P):
                    pe.wait_ge(dn_loaded[k // 2], e * 16 + 16)
                    for c in range(2):
                        t = pe.matmul(ps[:, 6 + c, :], hT[:, k, :], dn[k // 2][:, k % 2, c * HALF:(c + 1) * HALF],
                                      start=(k == 0), stop=(k == FE2 // P - 1), skip_group_check=True)
                    if k % 2:
                        t.then_inc(dn_used, 1)

            turn_x(0)
            up(0)
            turn_x(1)
            turn_h(0)
            with pe.Fori(1, NE - 1) as e:
                up(e)
                turn_x(e + 1)
                down(e - 1)
                turn_h(e)
            up(NE - 1)
            down(NE - 2)
            turn_h(NE - 1)
            down(NE - 1)

        @block.scalar
        def _(a):
            def move_x(e):
                a.wait_ge(x_turned, e + 1)
                a.wait_ge(gu_used, e * ND + ND)
                a.activation(xT.rearrange("p a b -> p (a b)"), flat2(ps, 4), ACT.Copy).then_inc(x_moved, 1)

            def silu(e):
                a.wait_ge(gu_used, e * ND + 2 * ND)
                a.wait_ge(h_ready, e)
                a.activation(sg, flat2(ps, 0), ACT.Silu).then_inc(silu_done, 1)

            move_x(0)
            silu(0)
            with a.Fori(1, NE) as e:
                move_x(e)
                silu(e)

        @block.vector
        def _(v):
            def gate(e):
                v.wait_ge(silu_done, e + 1)
                v.wait_ge(h_turned, e)
                v.tensor_tensor(h, sg, flat2(ps, 2), ALU.mult).then_inc(h_ready, 1)

            def move_h(e):
                v.wait_ge(h_turned, e + 1)
                v.wait_ge(dn_used, e * NDN + NDN)
                v.tensor_copy(hT.rearrange("p a b -> p (a b)"), flat2(ps, 4)).then_inc(h_moved, 1)

            def weigh(e):
                v.wait_ge(dn_used, e * NDN + 2 * NDN)
                v.wait_ge(added, e * 16)
                v.tensor_scalar(yo, flat2(ps, 6), m["ec_weight"][:, bass.ds(e, 1)], None,
                                ALU.mult).then_inc(y_ready, 1)

            gate(0)
            move_h(0)
            with v.Fori(1, NE) as e:
                gate(e)
                weigh(e - 1)
                move_h(e)
            weigh(NE - 1)


def last_residual(core, m):
    nc = core.nc
    sem = lambda n: core.semaphore("lr_" + n)
    NB = 4
    loaded = [sem(f"loaded{i}") for i in range(NB)]
    squared, rooted, ready, stored, pool_steps, scaled = map(sem, (
        "squared", "rooted", "ready", "stored", "pool_steps", "scaled"))
    at = m["free"]
    ff = [core.place(at + 2 * i * D, D) for i in range(NT)]
    h = [core.place(at + (2 * i + 1) * D, D) for i in range(NT)]
    sq = core.place(at + 2 * NT * D, D)
    ss, rs = core.place(at + (2 * NT + 1) * D, NT), core.place(at + (2 * NT + 1) * D + NT, NT)
    g2 = m["rows"][3]
    out = core.out.rearrange("o (i p) d -> (o i) p d", p=P)
    with nc.Block() as block:
        @block.sync
        def _(sp):
            for i in range(NT):
                sp.dma_start(ff[i], m["ff"][i]).then_inc(loaded[i % NB], 16)
                sp.dma_start(h[i], m["h3"][i]).then_inc(loaded[i % NB], 16)
                if i % NB == NB - 1 and i < NT - 1:
                    for q in loaded:
                        sp.wait_ge(q, 32 * (i // NB + 1))
            for i in range(NT):
                sp.wait_ge(ready, i + 1)
                sp.dma_start(out[i], h[i]).then_inc(stored, 16)
            sp.wait_ge(stored, 16 * NT)

        @block.scalar
        def _(a):
            for i in range(NT):
                a.wait_ge(loaded[i % NB], 32 * (i // NB + 1))
                if i:
                    a.wait_ge(squared, i)
                a.activation(sq, ff[i], ACT.Square, accum_out=ss[:, i:i + 1]).then_inc(squared, 1)

        @block.gpsimd
        def _(g):
            c = Chain(g, pool_steps)
            for i in range(NT):
                g.wait_ge(squared, i + 1)
                inverse_root(c, g, core, rs[:, i:i + 1], ss[:, i:i + 1], 1.0 / D, RMS2_EPS).then_inc(rooted, 1)

        @block.vector
        def _(v):
            for i in range(NT):
                v.wait_ge(rooted, i + 1)
                v.wait_ge(loaded[i % NB], 32 * (i // NB + 1))
                v.scalar_tensor_tensor(ff[i], ff[i], rs[:, i:i + 1], g2, ALU.mult, ALU.mult).then_inc(scaled, 1)
                v.wait_ge(scaled, i + 1)
                v.tensor_tensor(h[i], h[i], ff[i], ALU.add).then_inc(ready, 1)



def build(nc, ins, out):
    with ExitStack() as ctx:
        core = Core(nc, ctx, ins, out)
        small = NCOLS

        def keep(*shape, **kw):
            nonlocal small
            n = int(np.prod(shape))
            small += n
            assert small <= BASE, small
            return core.place(small - n, *shape, **kw)

        def at(x):
            return BASE + x

        def run(stage, *args):
            stage(core, *args)

        dram = core.scratch
        m = {
            "xhat": dram("xhat", [NT, P, D]), "h1": dram("h1", [NT, P, D]),
            "rest": dram("rest", [NT, P, D]), "qn": dram("q_nope", [4, P, S]),
            "qr": dram("q_rope", [2, P, S]), "kn": dram("k_nope", [4, P, S]),
            "kr": dram("k_rope", [ROPE, S]), "mod": dram("modulation", [2, 6 * D]),
            "slot_dram": dram("slot_token", [NBLK * P, 1], I32), "y1": dram("y1", [NBLK, P, D]),
            "h2": dram("h2", [NT, P, D]), "h3": dram("h3", [NT, P, D]), "xn": dram("xn", [NT, P, D]),
            "ff": dram("ff", [NT, P, D]),
            "logits": keep(P), "weights": keep(2 * NT), "dest": keep(2 * NT, dt=I32),
            "token": keep(NT, dt=I32), "plan": keep(3 * NBLK, dt=I32),
            "slot_token": keep(NBLK, dt=I32), "slot_token_rows": keep(P, parts=NBLK, dt=I32),
            "zero_i": keep(P, dt=I32), "mod_cols": keep(4 * ND), "tiny": keep(4), "neg_lam": keep(1),
            "logits2": keep(P), "ec_weight": keep(NE), "ec_token": keep(NE, dt=I32),
        }
        for name in ("h1", "y1", "xn", "ff"):
            m[name + "_rows"] = m[name].rearrange("a p d -> (a p) d")

        kind = ExitStack()
        core.open_upper(kind, "upper_first")
        m["hT"] = core.place(at(0), ND, S)
        m["u"] = core.place(at(8192), 4, PADU + S)
        m["z"] = core.place(at(12352), 4, PADZ + S)
        m["acc"] = core.place(at(16576), 4, S)
        m["vt"] = core.place(at(20672), NT, HALF)
        m["poolT"] = m["u"][:, :, PADU:]
        m["oT"] = core.place(at(24768), 4, S)
        m["merged"] = core.place(at(28864), ND, S)
        run(load_constants)
        run(modulation, at(0), m["mod"])
        run(input_norm, at(8192), m["xhat"], m["hT"])
        run(pool_and_conv_inputs, m["hT"], m["u"], m["z"], at(16576))
        m["free"] = at(24768)
        run(heads_and_branches, m)
        run(conv_finish, m)
        m["free"] = at(28864)
        run(latent_attention, m)
        m["free"] = at(37056)
        run(merge, m)
        m["low"], m["high"] = at(0), at(37056)
        run(output_and_gate, m)
        m["free"] = at(0)
        core.free_semaphores()
        run(route, m)
        kind.close()
        with ExitStack() as kind:
            core.open_upper(kind, "upper_split", F32R)
            run(grouped_experts, m)

        core.open_upper(ctx, "upper_second")
        m["free"] = at(0)
        run(prepare_columns, m)
        m["xnT"] = core.place(at(0), ND, SA)
        m["free"] = UPPER
        run(context_input, m)
        run(combine_experts, m)
        m["qconv"] = core.place(UPPER, 16, S)
        m["kv"] = core.place(at(37056), 8, SA)
        m["free"] = at(10240)
        run(second_projections, m)
        m["q2"] = core.place(at(0), 4, 2, S, parts=64)
        m["k2"] = core.place(at(10240), 4, 2, SA, parts=64)
        m["tables"], m["tmp"] = at(47296), at(8192)
        m["v2"] = core.place(at(37056), NK2, HALF)
        m["conv2"] = core.place(at(32960), 4, S)
        core.free_semaphores()
        run(rotate_and_convolve, m)
        m["free"] = UPPER
        m["o2"] = core.place(at(42176), NT, HALF)
        run(differential_attention, m)
        m["o2T"] = core.place(at(28864), 4, S)
        m["free"] = at(0)
        run(attention_output, m)
        m["rows"] = [core.place(UPPER + i * D, D) for i in range(7)]
        run(prepare_rows, m)
        run(mix_output, m)
        run(expert_choice, m)
        m["free_upper"] = at(28864)
        run(chosen_experts, m)
        m["free"] = at(28864)
        run(last_residual, m)


def columns(a, n):
    return np.asarray(a).reshape(n, P).T


def constants(f):
    part = np.arange(P)
    c = {name: np.zeros((P, n), np.float32) for name, (_, n) in COLS.items()}
    c["ident"][:] = np.eye(P)
    c["ones"][:] = 1
    c["before"][:] = part[:, None] < part[None, :]
    other = (part // 32) * 32 + (part % 32 + 16) % 32
    c["swap"][other, part] = 1
    c["turn"][other, part] = np.where(part % 32 < 16, -1, 1)
    c["sin_sign"][:, 0] = np.where(part % 32 < 16, -1, 1)
    freq = (10000.0 ** (-np.arange(0, ROPE, 2) / ROPE)).astype(np.float32)
    c["inv_freq"][:, 0] = freq[part % 16]
    for g, w in enumerate(WINDOWS):
        c["pool_inv"][:, 16 * g:16 * g + 16] = 1.0 / np.minimum(np.arange(16) + 1, w)
    c["low16"][:] = NE - np.arange(NE)
    c["order4"][:] = NG - np.arange(NG)
    c["block0"][:] = np.arange(NBLK + 1)
    c["token"][:] = np.arange(NT)[None, :] * P + part[:, None]
    c["neg_half"][:] = -0.5
    c["eps_rms"][:] = RMS_EPS
    c["eps_ln"][:] = LN_EPS
    for name, key in (("ln_in_g", "ln_in_g"), ("ln_in_b", "ln_in_b"), ("conv_b", "conv_b"),
                      ("conv_ln_g", "conv_ln_g"), ("conv_ln_b", "conv_ln_b"),
                      ("pool_scale", "pool_scale"), ("q_norm", "q_norm_g"), ("kv_norm", "kv_norm_g"),
                      ("pre_mix", "norm_pre_mix_2"), ("c", "c_2"), ("c_ctx", "c_ctx_2")):
        c[name][:] = columns(f[key], COLS[name][1])
    c["conv_dw"][:] = f["conv_dw"].reshape(TAPS, 4, P).transpose(2, 1, 0).reshape(P, 4 * TAPS)
    c["conv2"][:] = f["conv_w_2"].reshape(3, 4, P).transpose(2, 1, 0).reshape(P, 12)
    c["subln"][:] = f["subln_g_2"].reshape(1, P)
    c["bias_r"][:] = f["router_bias"].reshape(1, NE)
    c["lams"][:] = np.concatenate([f[k].reshape(-1) for k in (
        "lambda_q1_2", "lambda_k1_2", "lambda_q2_2", "lambda_k2_2")])[None, :]
    return np.ascontiguousarray(np.concatenate([c[name] for name in COLS], axis=1))


def by_k(w):
    return w.reshape(-1, P, w.shape[-1]).transpose(1, 0, 2)


def tiles_of(w):
    return w.reshape(ND, P, -1, P).transpose(2, 1, 0, 3)


def kernel(**inputs):
    import concourse.bacc as bacc
    from concourse.bass_utils import run_bass_kernel_spmd

    f = {k: np.asarray(v) for k, v in inputs.items()}
    w_in = f["w_in"][0]
    at = {"pool": 0, "a": 512, "gate": 1024, "cq": 1536, "ckv": 1920, "kr": 2176, "gates": 2208}
    first = [w_in[:, 0:512]]
    for t in range(4):
        first += [w_in[:, at["gate"] + t * P:at["gate"] + (t + 1) * P],
                  w_in[:, at["a"] + t * P:at["a"] + (t + 1) * P]]
    first += [w_in[:, at["cq"]:at["kr"] + ROPE], np.zeros((D, P - ROPE), np.float32)]
    uq = f["w_uq"][0].reshape(3 * P, NH1, QD)
    ukv = f["w_ukv"][0].reshape(2 * P, NH1, NOPE + VH)
    w2 = f["w_in_2"][0]
    part = lambda i: w2[:, i * HALF:(i + 1) * HALF]
    gates = w_in[:, at["gates"]:].reshape(ND, P, 3, ND, P).transpose(3, 1, 2, 0, 4).reshape(ND, P, 24 * P)
    projs = np.stack([f[k][0] for k in ("pool_proj", "conv_proj", "mla_proj")])
    projs = projs.reshape(3, 4, P, ND, P).transpose(3, 2, 0, 1, 4).reshape(ND, P, 12 * P)
    biases = f["b_gate"][0].reshape(3, ND, P).transpose(1, 2, 0)
    pad = np.zeros((ND, P, 1), np.float32)
    axis = np.arange(S)
    inv = (np.float32(10000.0) ** (-np.arange(0, 32, 2, dtype=np.float32) / np.float32(32))).astype(np.float32)
    row = (axis // 64).astype(np.float32)[:, None] * inv
    colm = (axis % 64).astype(np.float32)[:, None] * inv
    ang = np.concatenate([row, row, colm, colm], axis=1).T
    ang = np.concatenate([ang, ang], axis=0)
    slab = lambda w: w.reshape(NE, ND, P, FE2)
    arrays = {
        "packed": constants(f), "x": f["x"], "ctx": f["ctx_2"], "b_ada": f["b_ada_2"],
        "w_ada": f["w_ada_2"][0].reshape(ND, P, 12, HALF).transpose(2, 1, 0, 3),
        "w_in_tiles": tiles_of(np.concatenate(first, axis=1)),
        "positions": f["positions"].reshape(S),
        "w_uq_k": by_k(np.concatenate([uq[:, :, :NOPE].reshape(3 * P, -1), uq[:, :, NOPE:].reshape(3 * P, -1)],
                                      axis=1)),
        "w_ukv_k": by_k(np.concatenate([ukv[:, :, :NOPE].reshape(2 * P, -1),
                                        ukv[:, :, NOPE:].reshape(2 * P, -1)], axis=1)),
        "pool_w_k": f["pool_w"][0].transpose(1, 0, 2),
        "merge_w": np.concatenate([gates, projs, biases, pad], axis=2),
        "w_out_k": by_k(f["w_out"][0]), "w_router_k": by_k(f["w_router"]),
        "ln_in_g": f["ln_in_g"], "ln_in_b": f["ln_in_b"], "ln1_g": f["ln1_g"][0], "ln1_b": f["ln1_b"][0],
        "ln2_g": f["ln2_g"][0], "ln2_b": f["ln2_b"][0], "norm_post_mix": f["norm_post_mix_2"][0],
        "norm_pre_ffn": f["norm_pre_ffn_2"][0], "norm_post_ffn": f["norm_post_ffn_2"][0],
        "ple_proj_k": by_k(f["ple_proj"][0]), "ple_gate_k": by_k(f["ple_gate"][0]),
        "p_tiles": f["p"].reshape(NT, P, 2 * P),
        "exp_up_k": f["exp_w_up"][0].reshape(NE, ND, P, 2 * FE).transpose(0, 2, 1, 3).reshape(NE, P, -1),
        "exp_down_k": f["exp_w_down"][0].reshape(NE, 4, P, D).transpose(0, 2, 1, 3).reshape(NE, P, -1),
        "w_in2_tiles": tiles_of(np.concatenate([part(0), part(3), part(4), part(5), part(1), part(2)], axis=1)),
        "cos2": np.cos(ang), "sin2": np.sin(ang),
        "w_out2_k": by_k(f["w_out_2"][0]), "w_router2_k": by_k(f["w_router_2"][0]),
        "gate_up2": np.concatenate([slab(f["w_gate_2"][0]), slab(f["w_up_2"][0])], axis=3)
                      .reshape(NE * ND, P, 2 * FE2),
        "down2": f["w_down_2"][0].reshape(NE * 4, 2, P, D).transpose(0, 2, 1, 3),
    }
    arrays = {k: np.ascontiguousarray(v) for k, v in arrays.items()}
    for k, v in arrays.items():
        assert v.dtype == (np.int32 if k == "positions" else np.float32), (k, v.dtype)
    nc = bacc.Bacc("TRN2", target_bir_lowering=False, num_devices=1)
    ins = {k: nc.dram_tensor("in_" + k, v.shape, I32 if v.dtype == np.int32 else F32,
                             kind="ExternalInput").ap() for k, v in arrays.items()}
    out = nc.dram_tensor("out", (1, S, D), F32, kind="ExternalOutput").ap()
    build(nc, ins, out)
    r = run_bass_kernel_spmd(nc, [{"in_" + k: v for k, v in arrays.items()}], core_ids=[0])
    return r.results[0]["out"]
```

```python
from contextlib import ExitStack

import numpy as np

import concourse.bass as bass
from concourse import mybir

F32 = mybir.dt.float32
I32 = mybir.dt.int32
F32R = mybir.dt.float32r
ALU = mybir.AluOpType
ACT = mybir.ActivationFunctionType
AX = mybir.AxisListType.X

P = 128
S = 1024
D = 1024
NT = S // P
ND = D // P
HALF = 512
CTX = 256
NTC = CTX // P
SA = S + CTX
NH1, NOPE, ROPE, VH = 8, 64, 32, 64
QD = NOPE + ROPE
TAPS = 31
PADZ = 32
PADU = 16
WINDOWS = (2, 4, 8, 16)
NE, NG, EPG = 16, 4, 4
ALPHA = 2.0 ** 0.25
NBLK = (2 * S + NE * P - 1) // P
LN_EPS, RMS_EPS, RMS2_EPS = 1e-5, 1e-6, 1e-6
FE = 512
NH2, HD2 = 4, 64
NK2 = SA // P
CAP = 2 * S // NE
FE2 = 1024
NDN = 4
LAM_INIT = 0.8 - 0.6
BIG = 1e30

COLS = {}


def _columns():
    at = 0
    for name, n in (
        ("ident", 128), ("ones", 128), ("before", 128), ("swap", 128), ("turn", 128),
        ("ln_in_g", 8), ("ln_in_b", 8), ("conv_dw", 4 * TAPS), ("conv_b", 4), ("conv_ln_g", 4),
        ("conv_ln_b", 4), ("pool_scale", 4), ("q_norm", 3), ("kv_norm", 2), ("inv_freq", 1),
        ("sin_sign", 1), ("pool_inv", 64), ("pre_mix", 8), ("subln", 128), ("bias_r", 16),
        ("low16", 16), ("order4", 4), ("block0", NBLK + 1), ("token", NT), ("neg_half", 8),
        ("lams", 4 * HD2), ("c", 8), ("c_ctx", 8), ("zeros", 32),
        ("eps_rms", 1), ("eps_ln", 1), ("conv2", 12),
    ):
        COLS[name] = (at, n)
        at += n
    return at


NCOLS = _columns()
ARENA = 52096
BASE = 2560
UPPER = BASE + 20672


class Chain:

    def __init__(self, eng, sem, start=0):
        self.eng, self.sem, self.start, self.n = eng, sem, start, 0

    def did(self, ins):
        ins.then_inc(self.sem, 1)
        self.n += 1

    def wait(self):
        self.eng.wait_ge(self.sem, self.start + self.n)

    def step(self, ins):
        self.did(ins)
        self.wait()


class Core:

    def __init__(self, nc, ctx, ins, out):
        self.nc, self.ins, self.out = nc, ins, out
        self.regions = {}
        self.loaded = nc.alloc_semaphore("constants_loaded")
        self.passed = nc.alloc_semaphore("waits_passed")
        self.used = []
        self.arena = ctx.enter_context(nc.sbuf_tensor("arena", [P, UPPER], F32))
        self.ps = ctx.enter_context(nc.psum_tensor("banks", [P, 8, HALF], F32))

    def open_upper(self, ctx, name, dt=F32, first=UPPER, end=ARENA):
        self.regions[first] = end, ctx.enter_context(self.nc.sbuf_tensor(name, [P, end - first], dt))

    def place(self, at, *shape, parts=P, dt=None):
        n = int(np.prod(shape))
        first, end, tensor = 0, UPPER, self.arena
        for x in self.regions:
            if first < x <= at:
                first, (end, tensor) = x, self.regions[x]
        assert at + n <= end, (at, shape)
        v = tensor[0:parts, at - first:at - first + n]
        if dt is not None:
            v = v.bitcast(dt)
        if len(shape) == 2:
            v = v.rearrange("p (a b) -> p a b", a=shape[0])
        elif len(shape) == 3:
            v = v.rearrange("p (a b c) -> p a b c", a=shape[0], b=shape[1])
        return v

    def col(self, name, a=0, b=None):
        at, n = COLS[name]
        return self.arena[:, at + a:at + (n if b is None else b)]

    def semaphore(self, name):
        sem = self.nc.alloc_semaphore(name)
        self.used.append(sem)
        return sem

    def waited(self, eng):
        eng.sem_inc(self.passed, 1)

    def free_semaphores(self):
        with self.nc.Block() as block:
            @block.gpsimd
            def _(g):
                self.nc.clear_and_free_semaphores(self.used)
        self.used = []

    def scratch(self, name, shape, dt=F32):
        return self.nc.dram_tensor(name, shape, dt).ap()


def rounded(ap):
    return ap.bitcast(F32R)


def plain(ap):
    return ap.bitcast(F32)


def three_passes(pe, out, lhs, rhs, first, last):
    (lh, ll), (rh, rl) = lhs, rhs
    pe.matmul(out, rounded(lh), rounded(rh), start=first, stop=False, skip_group_check=True)
    pe.matmul(out, rounded(lh), rounded(rl), start=False, stop=False, skip_group_check=True)
    return pe.matmul(out, rounded(ll), rounded(rh), start=False, stop=last, skip_group_check=True)


def row_on_all(vec, n):
    return vec.rearrange("(a n) -> a n", a=1).broadcast_to([P, n])


def inverse_root(chain, pool, core, out, x, scale, eps):
    n = out.shape[-1]
    core.waited(pool)
    chain.step(pool.tensor_scalar(out, x, float(scale), float(eps), ALU.mult, ALU.add))
    return pool.tensor_tensor(out, out, core.col("neg_half", 0, n), ALU.pow)



def load_constants(core):
    nc = core.nc
    got = core.loaded
    with nc.Block() as block:
        @block.sync
        def _(sp):
            sp.dma_start(core.arena[:, 0:NCOLS], core.ins["packed"]).then_inc(got, 16)
            sp.wait_ge(got, 16)


def norm_and_modulation(core, x_at, xhat_dram, hT, at, mod_dram):
    nc, ps = core.nc, core.ps
    sem = lambda n: core.semaphore("n1_" + n)
    loaded = [sem(f"loaded{i}") for i in range(NT)]
    w_loaded = [sem(f"w{i}") for i in range(2)]
    (stats, rstd_done, xhat_done, turned, taken, stored, steps, pool_steps, b_loaded, act_ready,
     done, mod_taken, mod_stored) = map(
        sem, ("stats", "rstd", "xhat", "turned", "taken", "stored", "steps", "pool_steps",
              "b_loaded", "silu", "done", "mod_taken", "mod_stored"))
    x = core.place(x_at, NT, D)
    st = core.place(x_at + NT * D, NT, 12)
    mv = core.place(x_at + NT * D + 96, NT, 2)
    rstd = core.place(x_at + NT * D + 112, NT)
    xin = core.ins["x"].rearrange("o (i p) d -> (o i) p d", p=P)
    NC, NB = 6 * D // HALF, 4
    w = [core.place(at + i * ND * HALF, ND, HALF) for i in range(2)]
    at += 2 * ND * HALF
    row = core.place(at, NC * HALF, parts=2)
    bias = core.place(at + NC * HALF, NC * HALF, parts=2)
    both = core.place(at + 2 * NC * HALF, ND, 2)
    with nc.Block() as block:
        @block.sync
        def _(sp):
            for j in range(2):
                sp.dma_start(w[j], core.ins["w_ada"][j]).then_inc(w_loaded[j], 16)
            for i in range(NT):
                sp.dma_start(x[:, i, :], xin[i]).then_inc(loaded[i], 16)
            sp.dma_start(bias, core.ins["b_ada"].broadcast_to([2, 6 * D])).then_inc(b_loaded, 16)
            with sp.Fori(1, NC // 2) as i:
                for j in range(2):
                    sp.wait_ge(done, i * 2 + j + 1)
                    sp.dma_start(w[j], core.ins["w_ada"][i * 2 + j]).then_inc(w_loaded[j], 16)
            sp.wait_ge(mod_taken, NC + NB)
            sp.dma_start(mod_dram, row).then_inc(mod_stored, 16)
            sp.wait_ge(mod_stored, 16)

        @block.vector
        def _(v):
            v.sem_inc(mod_taken, NB)
            c = Chain(v, steps)
            for i in range(NT):
                v.wait_ge(loaded[i], 16)
                for j in range(2):
                    c.did(v.bn_stats(st[:, i, 6 * j:6 * j + 6], x[:, i, HALF * j:HALF * (j + 1)]))
                c.wait()
                v.bn_aggr(mv[:, i, :], st[:, i, :]).then_inc(stats, 1)
            v.wait_ge(stats, NT)
            v.wait_ge(rstd_done, 1)
            for i in range(NT):
                v.tensor_scalar(x[:, i, :], x[:, i, :], mv[:, i, 0:1], rstd[:, i:i + 1],
                                ALU.subtract, ALU.mult).then_inc(xhat_done, 1)
            v.wait_ge(b_loaded, 16)
            with v.Fori(0, NC // NB) as i:
                for j in range(NB):
                    v.wait_ge(done, i * NB + j + 3)
                    here = bass.ds(i * (NB * HALF) + j * HALF, HALF)
                    v.tensor_tensor(row[:, here], ps[0:2, 4 + j, :], bias[:, here],
                                    ALU.add).then_inc(mod_taken, 1)

        @block.gpsimd
        def _(g):
            g.wait_ge(stats, NT)
            inverse_root(Chain(g, pool_steps), g, core, rstd, mv[:, :, 1], 1.0,
                         LN_EPS).then_inc(rstd_done, 1)

        @block.tensor
        def _(pe):
            pe.sem_inc(done, 2)
            pe.wait_ge(act_ready, 2)

            def chunks(i):
                for j in range(NB):
                    pe.wait_ge(w_loaded[j % 2], i * (8 * NB) + 16 * (j // 2 + 1))
                    pe.wait_ge(mod_taken, i * NB + j + 1)
                    for k in range(ND):
                        t = pe.matmul(ps[0:2, 4 + j, :], both[:, k, :], w[j % 2][:, k, :],
                                      start=(k == 0), stop=(k == ND - 1))
                    t.then_inc(done, 1)

            with pe.Fori(0, NC // NB - 1) as i:
                chunks(i)
            for i in range(NT):
                pe.wait_ge(xhat_done, i + 1)
                for b in range(2):
                    if i >= 2:
                        pe.wait_ge(taken, 2 * (i - 2) + b + 1)
                    for k in range(4):
                        kk = 4 * b + k
                        t = pe.transpose(ps[:, 2 * (i % 2) + b, k * P:(k + 1) * P],
                                         x[:, i, kk * P:(kk + 1) * P], core.col("ident"))
                    t.then_inc(turned, 1)
            chunks(NC // NB - 1)

        @block.scalar
        def _(a):
            a.activation(both[:, :, 0], core.col("c"), ACT.Silu).then_inc(act_ready, 1)
            a.activation(both[:, :, 1], core.col("c_ctx"), ACT.Silu).then_inc(act_ready, 1)
            for i in range(NT):
                a.wait_ge(xhat_done, i + 1)
                a.dma_start(xhat_dram[i], x[:, i, :]).then_inc(stored, 16)
            for i in range(NT):
                for b in range(2):
                    a.wait_ge(turned, 2 * i + b + 1)
                    for k in range(4):
                        kk = 4 * b + k
                        t = a.activation(hT[:, kk, i * P:(i + 1) * P],
                                         ps[:, 2 * (i % 2) + b, k * P:(k + 1) * P], ACT.Identity,
                                         bias=core.col("ln_in_b", kk, kk + 1),
                                         scale=core.col("ln_in_g", kk, kk + 1))
                    t.then_inc(taken, 1)
            a.wait_ge(stored, 16 * NT)



def conv_tap(v, core, z, acc, taps, k, before):
    for ch in range(4):
        scalar = core.col("conv_dw")[:, bass.ds(k + ch * TAPS, 1)]
        src = z[:, ch, bass.ds(k + (PADZ - TAPS + 1), S)]
        v.wait_ge(taps, before + ch - 3)
        v.scalar_tensor_tensor(acc[:, ch, :], src, scalar, acc[:, ch, :], ALU.mult, ALU.add).then_inc(taps, 1)


STEP_TAPS = 2
FIRST_TAPS = 1 + 10 * STEP_TAPS


def first_projections(core, m):
    nc, ps, hT, u, z, acc, lat = core.nc, core.ps, m["hT"], m["u"], m["z"], m["acc"], m["lat"]
    sem = lambda n: core.semaphore("in_" + n)
    loaded, high_made, low_made, taken = ([sem(f"{n}{i}") for i in range(2)] for n in (
        "w", "high", "low", "taken"))
    done, cleared, h_high, h_low, gated, taps = map(sem, (
        "done", "cleared", "h_high", "h_low", "gated", "taps"))
    w = [core.place(m["w_at"] + i * D, ND, P) for i in range(2)]
    sg = core.place(m["acc_at"], S)
    at = m["split"]
    hh, hl = core.place(at, ND, S), core.place(at + ND * S, ND, S)
    at += 2 * ND * S
    wh, wl = ([core.place(at + (2 * p + i) * D, ND, P) for i in range(2)] for p in range(2))
    fl = lambda t: t.rearrange("p a b -> p (a b)")
    NPAIR = 9

    with nc.Block() as block:
        @block.sync
        def _(sp):
            for j in range(2):
                sp.dma_start(w[j], core.ins["w_in_tiles"][j]).then_inc(loaded[j], 16)
            with sp.Fori(1, NPAIR) as i:
                for j in range(2):
                    sp.wait_ge(low_made[j], i)
                    sp.dma_start(w[j], core.ins["w_in_tiles"][i * 2 + j]).then_inc(loaded[j], 16)

        @block.gpsimd
        def _(g):
            g.memset(u[:, :, 0:PADU], 0.0).then_inc(cleared, 1)
            g.memset(z[:, :, 0:PADZ], 0.0).then_inc(cleared, 1)

        @block.tensor
        def _(pe):
            pe.wait_ge(h_low, ND)
            with pe.Fori(0, NPAIR) as i:
                for j in range(2):
                    pe.wait_ge(low_made[j], i + 1)
                    pe.wait_ge(taken[j], i + 1)
                    for c in range(2):
                        for k in range(ND):
                            here = slice(c * HALF, (c + 1) * HALF)
                            t = three_passes(pe, ps[:, 2 * j + c, :], (wh[j][:, k, :], wl[j][:, k, :]),
                                             (hh[:, k, here], hl[:, k, here]), k == 0, k == ND - 1)
                    t.then_inc(done, 1)

        @block.scalar
        def _(a):
            a.sem_inc(taken[0], 1)
            a.sem_inc(taken[1], 1)
            for k in range(ND):
                a.activation(rounded(hh[:, k, :]), hT[:, k, :], ACT.Copy).then_inc(h_high, 1)

            def split(i, j):
                a.wait_ge(loaded[j], i * 16 + 16)
                if not isinstance(i, int) or i:
                    a.wait_ge(done, i * 2 + (j - 1))
                a.activation(rounded(fl(wh[j])), fl(w[j]), ACT.Copy).then_inc(high_made[j], 1)

            split(0, 0)
            split(0, 1)
            with a.Fori(0, 4) as i:
                a.wait_ge(done, i * 2 + 1)
                a.wait_ge(taken[1], i + 1)
                for c in range(2):
                    t = a.activation(sg[:, c * HALF:(c + 1) * HALF], ps[:, c, :], ACT.Sigmoid)
                t.then_inc(taken[0], 1)
                split(i + 1, 0)
                split(i + 1, 1)

            def keep(i, dst, first, shift, more):
                for j in range(2):
                    a.wait_ge(done, i * 2 + j + 1)
                    core.waited(a)
                    for c in range(2):
                        at = shift + c * HALF
                        t = a.activation(dst[:, bass.ds(i * 2 + (j - 2 * first), 1), at:at + HALF],
                                         ps[:, 2 * j + c:2 * j + c + 1, :], ACT.Copy)
                    t.then_inc(taken[j], 1)
                    if more:
                        split(i + 1, j)

            with a.Fori(4, 6) as i:
                keep(i, u, 4, PADU, True)
            with a.Fori(6, NPAIR - 1) as i:
                keep(i, lat, 6, 0, True)
            keep(NPAIR - 1, lat, 6, 0, False)

        @block.vector
        def _(v):
            for k in range(ND):
                v.wait_ge(h_high, k + 1)
                v.tensor_tensor(rounded(hl[:, k, :]), hT[:, k, :], plain(hh[:, k, :]),
                                ALU.subtract).then_inc(h_low, 1)

            def split(i, j):
                v.wait_ge(high_made[j], i + 1)
                v.tensor_tensor(rounded(fl(wl[j])), fl(w[j]), plain(fl(wh[j])),
                                ALU.subtract).then_inc(low_made[j], 1)

            split(0, 0)
            split(0, 1)
            with v.Fori(0, 4) as i:
                split(i + 1, 0)
                v.wait_ge(taken[0], i + 2)
                v.wait_ge(done, i * 2 + 2)
                for c in range(2):
                    at = PADZ + c * HALF
                    t = v.tensor_tensor(z[:, bass.ds(i, 1), at:at + HALF],
                                        sg[:, c * HALF:(c + 1) * HALF].unsqueeze(1),
                                        ps[:, 2 + c:3 + c, :], ALU.mult)
                t.then_inc(taken[1], 1)
                split(i + 1, 1)
            v.wait_ge(taken[1], 5)
            v.wait_ge(cleared, 2)
            for ch in range(4):
                v.tensor_scalar(acc[:, ch, :], z[:, ch, PADZ - TAPS + 1:PADZ - TAPS + 1 + S],
                                core.col("conv_dw", ch * TAPS, ch * TAPS + 1),
                                core.col("conv_b", ch, ch + 1), ALU.mult, ALU.add).then_inc(taps, 1)

            def step(i, more):
                for j in range(2):
                    if more:
                        split(i + 1, j)
                    for x in range(STEP_TAPS):
                        k = i * (2 * STEP_TAPS) + (j * STEP_TAPS + x + 1 - 8 * STEP_TAPS)
                        conv_tap(v, core, z, acc, taps, k, k * 4)

            with v.Fori(4, NPAIR - 1) as i:
                step(i, True)
            step(NPAIR - 1, False)
            v.wait_ge(taps, 4 * FIRST_TAPS)



def rope_tables(chain, core, pos_i, ang, sin_arg, cos_arg):
    v = chain.eng
    two_pi = 2.0 * np.pi
    c1 = float(np.float32(6.28125))
    c2 = float(np.float32(two_pi - c1))
    c2 = float((np.float32(c2).view(np.uint32) & np.uint32(0xFFFFF000)).view(np.float32))
    c3 = float(np.float32(two_pi - c1 - c2))
    magic = float(1.5 * 2 ** 23)
    limit = float(np.float32(np.pi)) - 1e-6
    chain.step(v.tensor_copy(ang, pos_i))
    chain.step(v.tensor_scalar(ang, ang, core.col("inv_freq"), None, ALU.mult))
    for out, turn in ((sin_arg, 0.0), (cos_arg, 0.25)):
        chain.step(v.tensor_scalar(out, ang, float(1 / two_pi), turn, ALU.mult, ALU.add))
        chain.step(v.tensor_scalar(out, out, magic, magic, ALU.add, ALU.subtract))
    for out, turn, tmp in ((sin_arg, 0.0, pos_i.bitcast(F32)), (cos_arg, 0.25, pos_i.bitcast(F32))):
        chain.step(v.scalar_tensor_tensor(tmp, out, -c1, ang, ALU.mult, ALU.add))
        chain.step(v.scalar_tensor_tensor(tmp, out, -c2, tmp, ALU.mult, ALU.add))
        chain.step(v.scalar_tensor_tensor(tmp, out, -c3, tmp, ALU.mult, ALU.add))
        chain.step(v.tensor_scalar(tmp, tmp, turn * two_pi, limit, ALU.add, ALU.min))
        chain.step(v.tensor_scalar(out, tmp, -limit, None, ALU.max))


def heads_and_branches(core, m):
    nc, ps, lat, u, z, acc, vt = core.nc, core.ps, m["lat"], m["u"], m["z"], m["acc"], m["vt"]
    sem = lambda n: core.semaphore("hb_" + n)
    stored = [sem(f"stored{i}") for i in range(2)]
    rows_stored = sem("rows_stored")
    (pos_loaded, uq_loaded, ukv_loaded, pw_loaded, steps, taps, trig_args, trig, squared,
     scaled, made, evac, turned, pool_steps, mixed, inverted) = map(sem, (
         "pos_loaded", "uq_loaded", "ukv_loaded", "pw_loaded", "steps", "taps", "trig_args",
         "trig", "squared", "scaled", "made", "evac", "turned", "pool_steps", "mixed", "inverted"))
    at = m["w_at"]
    t1, t2 = core.place(at, PADU + S), core.place(at + PADU + S, PADU + S)
    at = m["free"]
    wp = core.place(at, 4, P)
    ksw, qsw1 = core.place(at + 4 * P, S, parts=ROPE), core.place(at + 4 * P + S, S)
    at += 4 * P + 2 * S
    wuq = core.place(at, 3, 6 * P)
    wukv = core.place(at + 18 * P, 2, 2 * HALF)
    at += 18 * P + 4 * HALF
    sin_t, cos_t = core.place(at, S), core.place(at + S, S)
    rs = [core.place(at + 2 * S, S), core.place(at + 3 * S, S)]
    st = [core.place(at + 4 * S, S), core.place(at + 5 * S, S)]
    qraw = [core.place(at + 6 * S, S), core.place(at + 7 * S, S)]
    qsw = [core.place(at + 8 * S, S), qsw1]
    sq = [st[0], st[1], qraw[0], qraw[1], qsw[0]]
    positions, angles = qsw1.bitcast(I32), vt.rearrange("p a b -> p (a b)")[:, 0:S]
    halves = lambda t: t.rearrange("p (a b) -> p a b", a=2)
    dest = {0: rs[0], 1: rs[1], 6: qraw[0], 7: qraw[1], 8: qsw[0], 9: qsw[1]}
    for n in (2, 3, 4, 5, 11, 12, 13, 14):
        dest[n] = st[n % 2]

    with nc.Block() as block:
        @block.sync
        def _(sp):
            sp.dma_start(positions, row_on_all(core.ins["positions"], S)).then_inc(pos_loaded, 16)
            sp.dma_start(wp, core.ins["pool_w_k"]).then_inc(pw_loaded, 16)
            sp.dma_start(wuq, core.ins["w_uq_k"]).then_inc(uq_loaded, 16)
            sp.dma_start(wukv, core.ins["w_ukv_k"]).then_inc(ukv_loaded, 16)
            for n in range(2, 6):
                sp.wait_ge(evac, n + 1)
                sp.dma_start(m["qn"][n - 2], dest[n]).then_inc(stored[n % 2], 16)
            for n in range(11, 15):
                sp.wait_ge(evac, n + 1)
                sp.dma_start(m["kn"][n - 11], dest[n]).then_inc(stored[n % 2], 16)
            for g in range(2):
                sp.wait_ge(turned, g + 1)
                sp.dma_start(m["qr"][g], qraw[g]).then_inc(rows_stored, 16)
            sp.wait_ge(turned, 3)
            sp.dma_start(m["kr"], lat[0:ROPE, 5, :]).then_inc(rows_stored, 16)
            for q in stored:
                sp.wait_ge(q, 16 * 4)
            sp.wait_ge(rows_stored, 16 * 3)

        @block.tensor
        def _(pe):
            def unit(n, kk, lhs, rhs, rows=P):
                b = 4 + 2 * (n % 2)
                if n >= 2:
                    pe.wait_ge(evac, n - 1)
                for c in range(2):
                    for k in range(kk):
                        t = pe.matmul(ps[0:rows, b + c, :], lhs(k, c), rhs(k, c),
                                      start=(k == 0), stop=(k == kk - 1))
                t.then_inc(made, 1)

            col = lambda t, c: t[:, c * HALF:(c + 1) * HALF]
            pe.wait_ge(squared, 3)
            unit(0, 3, lambda k, c: core.col("ones"), lambda k, c: col(sq[k], c))
            pe.wait_ge(squared, 5)
            unit(1, 2, lambda k, c: core.col("ones"), lambda k, c: col(sq[3 + k], c))
            pe.wait_ge(uq_loaded, 16)
            pe.wait_ge(scaled, 3)
            for t in range(6):
                unit(2 + t, 3, lambda k, c: wuq[:, k, t * P:(t + 1) * P],
                     lambda k, c: col(lat[:, k, :], c))
            for g in range(2):
                pe.wait_ge(evac, 7 + g)
                unit(8 + g, 1, lambda k, c: core.col("swap"), lambda k, c: col(qraw[g], c))
            unit(10, 1, lambda k, c: core.col("swap")[0:ROPE, 0:ROPE],
                 lambda k, c: col(lat[0:ROPE, 5, :], c), ROPE)
            pe.wait_ge(ukv_loaded, 16)
            pe.wait_ge(scaled, 5)
            for t in range(4):
                unit(11 + t, 2, lambda k, c: wukv[:, k, t * P:(t + 1) * P],
                     lambda k, c: col(lat[:, 3 + k, :], c))
            for t in range(4):
                unit(15 + t, 2, lambda k, c: lat[:, 3 + k, (2 * t + c) * P:(2 * t + c + 1) * P],
                     lambda k, c: wukv[:, k, HALF:2 * HALF])
            pe.wait_ge(pw_loaded, 16)
            for g in range(4):
                pe.wait_ge(mixed, g + 1)
                unit(19 + g, 1, lambda k, c: wp[:, g, :], lambda k, c: col(u[:, g, PADU:], c))

        @block.scalar
        def _(a):
            for k in range(5):
                a.activation(sq[k], lat[:, k, :], ACT.Square).then_inc(squared, 1)
            for n in range(23):
                b = 4 + 2 * (n % 2)
                src = ps[:, b:b + 2, :]
                a.wait_ge(made, n + 1)
                if n in (4, 5):
                    a.wait_ge(stored[n % 2], 16)
                if n >= 11 and n < 15:
                    a.wait_ge(stored[n % 2], 16 * (2 + (n - 11) // 2))
                if n == 6:
                    a.wait_ge(squared, 5)
                    a.wait_ge(trig_args, 2)
                    a.activation(sin_t, sin_t, ACT.Sin).then_inc(trig, 1)
                    a.activation(cos_t, cos_t, ACT.Sin).then_inc(trig, 1)
                if n < 2:
                    a.activation(halves(dest[n]), src, ACT.Sqrt, bias=core.col("eps_rms"),
                                 scale=1.0 / (3 * P if n == 0 else 2 * P)).then_inc(evac, 1)
                elif n == 10:
                    a.activation(halves(ksw), src[0:ROPE], ACT.Copy).then_inc(evac, 1)
                elif n < 15:
                    a.activation(halves(dest[n]), src, ACT.Copy).then_inc(evac, 1)
                elif n < 19:
                    t = n - 15
                    a.activation(vt[:, 2 * t:2 * t + 2, :], src, ACT.Copy).then_inc(evac, 1)
                else:
                    g = n - 19
                    a.activation(halves(u[:, g, PADU:]), src, ACT.Copy,
                                 scale=core.col("pool_scale", g, g + 1)).then_inc(evac, 1)

        @block.vector
        def _(v):
            c = Chain(v, steps)
            v.sem_inc(taps, 4)
            v.wait_ge(evac, 2)
            for n in range(2):
                v.reciprocal(rs[n], rs[n]).then_inc(inverted, 1)
            for k in range(5):
                n = 0 if k < 3 else 1
                g = core.col("q_norm", k, k + 1) if k < 3 else core.col("kv_norm", k - 3, k - 2)
                v.wait_ge(inverted, n + 1)
                v.scalar_tensor_tensor(lat[:, k, :], lat[:, k, :], g, rs[n],
                                       ALU.mult, ALU.mult).then_inc(scaled, 1)
            v.wait_ge(pos_loaded, 16)
            rope_tables(c, core, positions, angles, sin_t, cos_t)
            c.step(v.tensor_scalar(sin_t, sin_t, core.col("sin_sign"), None, ALU.mult))
            v.tensor_scalar(cos_t, cos_t, 1.0, None, ALU.mult).then_inc(trig_args, 2)
            with v.Fori(FIRST_TAPS, TAPS) as k:
                conv_tap(v, core, z, acc, taps, k, k * 4 + (4 - 4 * FIRST_TAPS))
            v.wait_ge(taps, 4 + 4 * (TAPS - FIRST_TAPS))

        @block.gpsimd
        def _(g):
            c = Chain(g, pool_steps)
            c.did(g.memset(t1[:, 0:PADU], 0.0))
            c.step(g.memset(t2[:, 0:PADU], 0.0))
            for grp in range(4):
                cur = u[:, grp, :]
                for lvl in range(grp + 1):
                    nxt = (t1, t2)[lvl % 2]
                    c.step(g.tensor_tensor(nxt[:, PADU:], cur[:, PADU:],
                                           cur[:, PADU - 2 ** lvl:PADU + S - 2 ** lvl], ALU.add))
                    cur = nxt
                c.did(g.tensor_tensor(cur[:, PADU:2 * PADU], cur[:, PADU:2 * PADU],
                                      core.col("pool_inv", 16 * grp, 16 * grp + 16), ALU.mult))
                c.step(g.tensor_scalar(cur[:, 2 * PADU:], cur[:, 2 * PADU:],
                                       1.0 / WINDOWS[grp], None, ALU.mult))
                g.tensor_tensor(u[:, grp, PADU:], cur[:, PADU:], u[:, grp, PADU:],
                                ALU.subtract).then_inc(mixed, 1)
                g.wait_ge(mixed, grp + 1)
            g.wait_ge(trig, 2)
            for n, (raw, sw, rows) in enumerate(((qraw[0], qsw[0], P), (qraw[1], qsw[1], P),
                                                 (lat[0:ROPE, 5, :], ksw, ROPE))):
                g.wait_ge(evac, 9 + n)
                c.did(g.tensor_tensor(raw, raw, cos_t[0:rows], ALU.mult))
                c.step(g.tensor_tensor(sw, sw, sin_t[0:rows], ALU.mult))
                g.tensor_tensor(raw, raw, sw, ALU.add).then_inc(turned, 1)


def conv_finish(core, m):
    nc, ps, acc = core.nc, core.ps, m["acc"]
    sem = lambda n: core.semaphore("cf_" + n)
    summed, centred, squared, rooted, inverted, normed, shaped = map(sem, (
        "summed", "centred", "squared", "rooted", "inverted", "normed", "shaped"))
    sq = core.place(m["free"], 4, S)
    rstd = core.place(m["free"] + 4 * S, S)
    halves = lambda t: t.rearrange("p (a b) -> p a b", a=2)
    with nc.Block() as block:
        @block.tensor
        def _(pe):
            for b, src, ready in ((0, acc, None), (2, sq, squared)):
                for k in range(4):
                    if ready is not None:
                        pe.wait_ge(ready, k + 1)
                    for c in range(2):
                        t = pe.matmul(ps[:, b + c, :], core.col("ones"),
                                      src[:, k, c * HALF:(c + 1) * HALF], start=(k == 0), stop=(k == 3),
                                      skip_group_check=True)
                t.then_inc(summed, 1)

        @block.vector
        def _(v):
            v.wait_ge(summed, 1)
            for k in range(4):
                v.scalar_tensor_tensor(halves(acc[:, k, :]), ps[:, 0:2, :], -1.0 / (4 * P),
                                       halves(acc[:, k, :]), ALU.mult, ALU.add).then_inc(centred, 1)
            v.wait_ge(rooted, 1)
            v.reciprocal(rstd, rstd).then_inc(inverted, 1)
            v.wait_ge(inverted, 1)
            for k in range(4):
                v.tensor_tensor(acc[:, k, :], acc[:, k, :], rstd, ALU.mult).then_inc(normed, 1)

        @block.scalar
        def _(a):
            for k in range(4):
                a.wait_ge(centred, k + 1)
                a.activation(sq[:, k, :], acc[:, k, :], ACT.Square).then_inc(squared, 1)
            a.wait_ge(summed, 2)
            a.activation(halves(rstd), ps[:, 2:4, :], ACT.Sqrt, bias=core.col("eps_ln"),
                         scale=1.0 / (4 * P)).then_inc(rooted, 1)
            for k in range(4):
                a.wait_ge(normed, k + 1)
                a.activation(acc[:, k, :], acc[:, k, :], ACT.Silu, bias=core.col("conv_ln_b", k, k + 1),
                             scale=core.col("conv_ln_g", k, k + 1)).then_inc(shaped, 1)



def latent_attention(core, m):
    nc, ps, vt, oT = core.nc, core.ps, m["vt"], m["oT"]
    sem = lambda n: core.semaphore("at_" + n)
    q_loaded = [sem(f"q{i}") for i in range(2)]
    scored, biased, exped, turned, moved, summed, normed, steps, o_turned, o_moved = map(sem, (
        "scored", "biased", "exped", "turned", "moved", "summed", "normed", "steps", "o_turned",
        "o_moved"))
    at = m["free"]
    q = [core.place(at + i * 2 * S, S, parts=QD) for i in range(2)]
    k = [core.place(at + i * 2 * S + S, S, parts=QD) for i in range(2)]
    e = [core.place(at + 4 * S + i * S, S) for i in range(2)]
    pt = [core.place(at + 6 * S + i * S, NT, P) for i in range(2)]
    o = core.place(at + 8 * S, NT, NH1 * VH)
    tiny = core.place(at + 12 * S, 16)
    mx, nb, den, rec = (tiny[:, 4 * i:4 * i + 4] for i in range(4))
    scale = float(QD) ** -0.5
    N = 2 * NT
    with nc.Block() as block:
        @block.sync
        def _(sp):
            with sp.Fori(0, NH1 // 2) as it:
                for j in range(2):
                    sp.wait_ge(scored, it * N + (NT * j + NT))
                    h = it * 2 + j
                    for dst, src in ((q[j][0:NOPE], m["qn"].rearrange("t (h r) s -> (t h) r s", h=2)),
                                     (q[j][NOPE:QD], m["qr"].rearrange("t (h r) s -> (t h) r s", h=4)),
                                     (k[j][0:NOPE], m["kn"].rearrange("t (h r) s -> (t h) r s", h=2))):
                        sp.dma_start(dst, src[bass.ds(h, 1)].rearrange("a r s -> (a r) s"))\
                          .then_inc(q_loaded[j], 16)
                    sp.dma_start(k[j][NOPE:QD], m["kr"]).then_inc(q_loaded[j], 16)

        @block.tensor
        def _(pe):
            pe.sem_inc(scored, N)
            pe.sem_inc(turned, 2)
            pe.sem_inc(summed, 2)
            with pe.Fori(0, NH1 // 2) as it:
                def scores(n):
                    i, j = n % NT, n // NT
                    if i == 0:
                        pe.wait_ge(q_loaded[j], it * 64 + 64)
                    pe.wait_ge(exped, it * N + n + 1)
                    keys = (i + 1) * P
                    for c in range(0, keys, HALF):
                        wd = min(HALF, keys - c)
                        t = pe.matmul(ps[:, 2 * (n % 2) + c // HALF, 0:wd], q[j][:, i * P:(i + 1) * P],
                                      k[j][:, c:c + wd], start=True, stop=True)
                    t.then_inc(scored, 1)

                def turn(n):
                    i = n % NT
                    pe.wait_ge(exped, it * N + n + 3)
                    pe.wait_ge(moved, it * N + n)
                    for t in range(i + 1):
                        ins = pe.transpose(ps[:, 4 + t // 4, (t % 4) * P:(t % 4 + 1) * P],
                                           e[n % 2][:, t * P:(t + 1) * P], core.col("ident"))
                    ins.then_inc(turned, 1)

                def sums(n):
                    i, j = n % NT, n // NT
                    pe.wait_ge(moved, it * N + n + 1)
                    pe.wait_ge(normed, it * N + n + 3)
                    for t in range(i + 1):
                        ins = pe.matmul(ps[:, 6 + n % 2, 0:VH], pt[n % 2][:, t, :],
                                        vt[:, t, bass.ds(it * (2 * VH) + j * VH, VH)],
                                        start=(t == 0), stop=(t == i))
                    ins.then_inc(summed, 1)

                scores(0)
                scores(1)
                for n in range(N):
                    turn(n)
                    if n + 2 < N:
                        scores(n + 2)
                    if n:
                        sums(n - 1)
                sums(N - 1)
            for i in range(NT):
                pe.wait_ge(normed, NH1 * NT + 4)
                if i >= 2:
                    pe.wait_ge(o_moved, i - 1)
                for t in range(4):
                    ins = pe.transpose(ps[:, i % 2, t * P:(t + 1) * P], o[:, i, t * P:(t + 1) * P],
                                       core.col("ident"))
                ins.then_inc(o_turned, 1)

        @block.vector
        def _(v):
            v.sem_inc(normed, 4)
            per = 3 * N
            with v.Fori(0, NH1 // 2) as it:
                c = Chain(v, steps, it * per)

                def bias(n):
                    i = n % NT
                    v.wait_ge(scored, it * N + n + 1 + N)
                    row = ps[:, 2 * (n % 2):2 * (n % 2) + 2, :].rearrange("p a b -> p (a b)")
                    c.step(v.memset(row[0:64, i * P + 64:(i + 1) * P], -BIG))
                    c.step(v.reduce_max(mx[:, n % 2:n % 2 + 1], row[:, 0:(i + 1) * P], AX))
                    v.tensor_scalar(nb[:, n % 2:n % 2 + 1], mx[:, n % 2:n % 2 + 1], -scale, None,
                                    ALU.mult).then_inc(biased, 1)

                def normalise(n):
                    i, j, x = n % NT, n // NT, n % 4
                    v.wait_ge(summed, it * N + n + 3)
                    c.step(v.reciprocal(rec[:, x:x + 1], den[:, x:x + 1]))
                    v.tensor_scalar(o[:, i, bass.ds(it * (2 * VH) + j * VH, VH)],
                                    ps[:, 6 + n % 2, 0:VH], rec[:, x:x + 1], None,
                                    ALU.mult).then_inc(normed, 1)

                bias(0)
                bias(1)
                for n in range(N):
                    if n + 2 < N:
                        bias(n + 2)
                    if n:
                        normalise(n - 1)
                normalise(N - 1)
                assert c.n == per
            for i in range(NT):
                v.wait_ge(o_turned, i + 1)
                v.tensor_copy(oT[:, :, i * P:(i + 1) * P],
                              ps[:, i % 2, :].rearrange("p (a b) -> p a b", a=4)).then_inc(o_moved, 1)

        @block.scalar
        def _(a):
            a.sem_inc(exped, 2)
            with a.Fori(0, NH1 // 2) as it:
                def exp(n):
                    i = n % NT
                    a.wait_ge(biased, it * N + n + 1)
                    a.wait_ge(turned, it * N + n + 1)
                    a.wait_ge(normed, it * N + n + 1)
                    row = ps[:, 2 * (n % 2):2 * (n % 2) + 2, :].rearrange("p a b -> p (a b)")
                    a.activation(e[n % 2][:, 0:(i + 1) * P], row[:, 0:(i + 1) * P], ACT.Exp,
                                 bias=nb[:, n % 2:n % 2 + 1], scale=scale,
                                 accum_out=den[:, n % 4:n % 4 + 1]).then_inc(exped, 1)

                exp(0)
                for n in range(N):
                    i = n % NT
                    if n + 1 < N:
                        exp(n + 1)
                    a.wait_ge(turned, it * N + n + 3)
                    a.wait_ge(summed, it * N + n + 1)
                    src = ps[:, 4:6, :].rearrange("p a b -> p (a b)")
                    a.activation(pt[n % 2].rearrange("p a b -> p (a b)")[:, 0:(i + 1) * P],
                                 src[:, 0:(i + 1) * P], ACT.Copy).then_inc(moved, 1)



def merge(core, m):
    nc, ps, hT = core.nc, core.ps, m["hT"]
    branch = (m["poolT"], m["acc"], m["oT"])
    sem = lambda n: core.semaphore("mg_" + n)
    g_loaded, p_loaded, stored = ([sem(f"{n}{i}") for i in range(2)] for n in ("g", "p", "stored"))
    h_high, h_low, high_made, low_made, gates_made, gated, made, used, ready, steps = map(sem, (
        "h_high", "h_low", "high", "low", "gates_made", "gated", "made", "used", "ready", "steps"))
    GW, PW, NU = 24 * P, 12 * P + 4, 6
    at = m["split"]
    hh, hl = core.place(at, ND, S), core.place(at + ND * S, ND, S)
    wh, wl = core.place(at + 2 * ND * S, GW), core.place(at + 2 * ND * S + GW, GW)
    at = m["free"]
    wp = [core.place(at + i * PW, PW) for i in range(2)]
    part = [core.place(at + 2 * PW + i * HALF, HALF) for i in range(2)]
    out = [core.place(at + 2 * PW + 2 * HALF + i * S, S) for i in range(2)]
    wg = [core.place(m["hT_at"] + i * GW, GW) for i in range(2)]
    NSG = 4
    sg = [core.place(m["hT_at"] + 2 * GW + i * HALF, HALF) for i in range(NSG)]
    last = ND // 2 - 1

    with nc.Block() as block:
        @block.sync
        def _(sp):
            def load(it, j):
                t = it * 2 + j
                sp.wait_ge(low_made, t + 1)
                sp.dma_start(wg[j], core.ins["merge_w"][t][:, 0:GW]).then_inc(g_loaded[j], 16)
                sp.wait_ge(used, it * (2 * NU) + j * NU + 1)
                sp.dma_start(wp[j], core.ins["merge_w"][t][:, GW:GW + PW]).then_inc(p_loaded[j], 16)

            def store(it, j):
                sp.wait_ge(ready, it * 4 + 2 * j + 2)
                sp.dma_start(m["merged"][it * 2 + j], out[j]).then_inc(stored[j], 16)

            sp.wait_ge(h_low, ND)
            load(0, 0)
            load(0, 1)
            with sp.Fori(0, last) as it:
                for j in range(2):
                    store(it, j)
                    load(it + 1, j)
            store(last, 0)
            store(last, 1)
            for q in stored:
                sp.wait_ge(q, 16 * (ND // 2))

        @block.tensor
        def _(pe):
            with pe.Fori(0, ND // 2) as it:
                for j in range(2):
                    n0 = it * (2 * NU) + j * NU
                    for n in range(NU):
                        c, b = n // 3, n % 3
                        pe.wait_ge(low_made, it * 2 + j + 3)
                        pe.wait_ge(used, n0 + n + 7)
                        for k in range(ND):
                            x = (8 * b + k) * P
                            here = slice(c * HALF, (c + 1) * HALF)
                            t = three_passes(pe, ps[:, n, :], (wh[:, x:x + P], wl[:, x:x + P]),
                                             (hh[:, k, here], hl[:, k, here]), k == 0, k == ND - 1)
                        t.then_inc(gates_made, 1)
                    pe.wait_ge(p_loaded[j], it * 16 + 16)
                    for n in range(NU):
                        c, b = n // 3, n % 3
                        pe.wait_ge(used, n0 + n + 11)
                        for k in range(4):
                            x = (4 * b + k) * P
                            t = pe.matmul(ps[:, 6 + n % 2, :], wp[j][:, x:x + P],
                                          branch[b][:, k, c * HALF:(c + 1) * HALF],
                                          start=(k == 0), stop=(k == 3))
                        t.then_inc(made, 1)

        @block.scalar
        def _(a):
            for k in range(ND):
                a.activation(rounded(hh[:, k, :]), hT[:, k, :], ACT.Copy).then_inc(h_high, 1)

            def split(it, j):
                a.wait_ge(g_loaded[j], it * 16 + 16)
                a.activation(rounded(wh), wg[j], ACT.Copy).then_inc(high_made, 1)

            split(0, 0)

            def turn(it, j, nxt):
                n0 = it * (2 * NU) + j * NU
                a.wait_ge(p_loaded[j], it * 16 + 16)
                for n in range(NU):
                    b = n % 3
                    a.wait_ge(gates_made, n0 + n + 1)
                    a.wait_ge(used, n0 + n + 9)
                    a.activation(sg[(n + j * NU) % NSG], ps[:, n, :], ACT.Sigmoid,
                                 bias=wp[j][:, 12 * P + b:12 * P + b + 1]).then_inc(gated, 1)
                if nxt:
                    split(*nxt)

            with a.Fori(0, last) as it:
                turn(it, 0, (it, 1))
                turn(it, 1, (it + 1, 0))
            turn(last, 0, (last, 1))
            turn(last, 1, None)

        @block.vector
        def _(v):
            v.sem_inc(used, 2 * NU)
            v.sem_inc(low_made, 2)
            for k in range(ND):
                v.wait_ge(h_high, k + 1)
                v.tensor_tensor(rounded(hl[:, k, :]), hT[:, k, :], plain(hh[:, k, :]),
                                ALU.subtract).then_inc(h_low, 1)

            def split(it, j):
                v.wait_ge(high_made, it * 2 + j + 1)
                v.tensor_tensor(rounded(wl), wg[j], plain(wh), ALU.subtract).then_inc(low_made, 1)

            split(0, 0)

            def turn(ch, it, j, nxt):
                n0 = it * (2 * NU) + j * NU
                v.wait_ge(stored[j], it * 16)
                for n in range(NU):
                    c, b = n // 3, n % 3
                    if nxt and n == NU - NSG:
                        split(*nxt)
                    v.wait_ge(gated, n0 + n + 1)
                    v.wait_ge(made, n0 + n + 1)
                    ch.wait()
                    v.wait_ge(ready, it * 4 + 2 * j + c)
                    v.tensor_tensor(part[min(b, 1)], sg[(n + j * NU) % NSG], ps[:, 6 + n % 2, :],
                                    ALU.mult).then_inc(used, 1)
                    if b:
                        v.wait_ge(used, n0 + n + 13)
                    if b == 1:
                        ch.did(v.tensor_tensor(part[0], part[0], part[1], ALU.add))
                    elif b == 2:
                        v.tensor_tensor(out[j][:, c * HALF:(c + 1) * HALF], part[0], part[1],
                                        ALU.add).then_inc(ready, 1)

            with v.Fori(0, last) as it:
                ch = Chain(v, steps, it * 4)
                turn(ch, it, 0, (it, 1))
                turn(ch, it, 1, (it + 1, 0))
            ch = Chain(v, steps, last * 4)
            turn(ch, last, 0, (last, 1))
            turn(ch, last, 1, None)


def stats_of(core, c, v, st, mv, x):
    for j in range(2):
        c.did(v.bn_stats(st[:, 6 * j:6 * j + 6], x[:, HALF * j:HALF * (j + 1)]))
    c.wait()
    core.waited(v)
    return v.bn_aggr(mv, st)


def flat2(ps, b):
    return ps[:, b:b + 2, :].rearrange("p a b -> p (a b)")


def output_and_gate(core, m):
    nc, ps = core.nc, core.ps
    sem = lambda n: core.semaphore("og_" + n)
    m_loaded = [sem(f"m{i}") for i in range(2)]
    x_loaded = [sem(f"x{i}") for i in range(2)]
    p_loaded = [sem(f"p{i}") for i in range(2)]
    h_stored = [sem(f"h_stored{i}") for i in range(2)]
    r_stored = [sem(f"r_stored{i}") for i in range(2)]
    (wo_loaded, weights, made, taken, var_ready, rstd_ready, h_ready, turned, moved,
     routed, kept, gate_made, ple_made, sig_ready, e_taken, rest_ready, steps, pool_steps, moves) = map(
        sem, ("wo", "weights", "made", "taken", "var", "rstd", "h_ready", "turned",
              "moved", "routed", "kept", "gate_made", "ple_made", "sig_ready", "e_taken",
              "rest_ready", "steps", "pool_steps", "moves"))
    at = m["low"]
    wo, wg = core.place(at, ND, D), core.place(at + ND * D, ND, D)
    wp = core.place(at + 2 * ND * D, 2, D)
    wr = core.place(at + 2 * ND * D + 2 * D, ND, NE)
    at = UPPER
    ga, ba, g1, b1 = (core.place(at + i * D, D) for i in range(4))
    work = core.place(at + 4 * D, D)
    at = m["high"]
    names = ("xh0", "xh1", "mt0", "mt1", "h0", "h1", "rest0", "rest1", "hT", "sig")
    b = {n: core.place(at + i * D, D) for i, n in enumerate(names)}
    at += len(names) * D
    pin = [core.place(at + i * 2 * P, 2 * P) for i in range(2)]
    pT = core.place(at + 4 * P, 2, P)
    st, mv = core.place(at + 6 * P, 12), core.place(at + 6 * P + 12, 2)
    rstd = core.place(at + 6 * P + 16, 1)
    tile = lambda x: x.rearrange("p (a b) -> p a b", b=P)
    hT = tile(b["hT"])
    with nc.Block() as block:
        @block.sync
        def _(sp):
            merged = m["merged"].rearrange("k p s -> p k s")

            def load_merged(it, j):
                sp.wait_ge(made, it * 2 + j + 1)
                sp.dma_start(tile(b[f"mt{j}"]), merged[:, :, bass.ds(it * (2 * P) + j * P, P)])\
                  .then_inc(m_loaded[j], 16)

            load_merged(0, 0)
            sp.dma_start(wo, core.ins["w_out_k"]).then_inc(wo_loaded, 16)
            load_merged(0, 1)
            for dst, name in ((ga, "ln_in_g"), (ba, "ln_in_b"), (g1, "ln1_g"), (b1, "ln1_b")):
                sp.dma_start(dst, row_on_all(core.ins[name], D)).then_inc(weights, 16)
            sp.dma_start(wr, core.ins["w_router_k"]).then_inc(weights, 16)
            sp.dma_start(wp, core.ins["ple_proj_k"]).then_inc(weights, 16)
            sp.dma_start(wg, core.ins["ple_gate_k"]).then_inc(weights, 16)

            def load(it, j):
                n = it * 2 + j
                sp.wait_ge(taken, it * 2 + j + 1)
                sp.dma_start(b[f"xh{j}"], m["xhat"][n]).then_inc(x_loaded[j], 16)
                sp.wait_ge(turned, it * 2 + j + 1)
                sp.dma_start(pin[j], core.ins["p_tiles"][n]).then_inc(p_loaded[j], 16)

            load(0, 0)
            load(0, 1)
            with sp.Fori(1, NT // 2) as it:
                for j in range(2):
                    load_merged(it, j)
                    load(it, j)

        @block.gpsimd
        def _(g):
            def root(it, j):
                c = Chain(g, pool_steps, it * 2 + j)
                g.wait_ge(var_ready, it * 2 + j + 1)
                inverse_root(c, g, core, rstd, mv[:, 1:2], 1.0, LN_EPS).then_inc(rstd_ready, 1)

            with g.Fori(0, NT // 2) as it:
                root(it, 0)
                root(it, 1)

        @block.tensor
        def _(pe):
            pe.sem_inc(made, 2)
            pe.sem_inc(turned, 2)
            pe.wait_ge(wo_loaded, 16)

            def product(it, j):
                n = it * 2 + j
                pe.wait_ge(m_loaded[j], it * 16 + 16)
                pe.wait_ge(taken, n + 2)
                for c in range(2):
                    for k in range(ND):
                        t = pe.matmul(ps[:, c, :], tile(b[f"mt{j}"])[:, k, :],
                                      wo[:, k, c * HALF:(c + 1) * HALF], start=(k == 0), stop=(k == ND - 1))
                t.then_inc(made, 1)

            def after(it, j):
                n = it * 2 + j
                pe.wait_ge(h_ready, n + 1)
                pe.wait_ge(kept, n)
                for k in range(ND):
                    pe.transpose(ps[:, 2 + k // 4, (k % 4) * P:(k % 4 + 1) * P],
                                 b[f"h{j}"][:, k * P:(k + 1) * P], core.col("ident"))
                pe.wait_ge(p_loaded[j], it * 16 + 16)
                pe.wait_ge(e_taken, n)
                for k in range(2):
                    t = pe.transpose(ps[:, 6, k * P:(k + 1) * P], pin[j][:, k * P:(k + 1) * P],
                                     core.col("ident"))
                t.then_inc(turned, 1)
                pe.wait_ge(moved, n + 1)
                for k in range(ND):
                    t = pe.matmul(ps[:, 2, 0:NE], hT[:, k, :], wr[:, k, :], start=(k == 0), stop=(k == ND - 1))
                t.then_inc(routed, 1)
                pe.wait_ge(sig_ready, n)
                for c in range(2):
                    for k in range(ND):
                        t = pe.matmul(ps[:, 4 + c, :], hT[:, k, :], wg[:, k, c * HALF:(c + 1) * HALF],
                                      start=(k == 0), stop=(k == ND - 1))
                t.then_inc(gate_made, 1)
                for c in range(2):
                    for k in range(2):
                        t = pe.matmul(ps[:, 6 + c, :], pT[:, k, :], wp[:, k, c * HALF:(c + 1) * HALF],
                                      start=(k == 0), stop=(k == 1))
                t.then_inc(ple_made, 1)

            product(0, 0)
            pe.wait_ge(weights, 16 * 7)
            with pe.Fori(0, NT // 2 - 1) as it:
                product(it, 1)
                after(it, 0)
                product(it + 1, 0)
                after(it, 1)
            last = NT // 2 - 1
            product(last, 1)
            after(last, 0)
            after(last, 1)

        @block.scalar
        def _(a):
            with a.Fori(0, NT // 2) as it:
                for j in range(2):
                    n = it * 2 + j
                    a.wait_ge(turned, n + 3)
                    for c in range(2):
                        a.activation(b["hT"][:, c * HALF:(c + 1) * HALF], ps[:, 2 + c, :], ACT.Copy)
                    a.activation(pT.rearrange("p a b -> p (a b)"), ps[:, 6, 0:2 * P], ACT.Copy)\
                     .then_inc(moved, 1)
                    a.wait_ge(gate_made, n + 1)
                    a.wait_ge(e_taken, n)
                    a.activation(b["sig"], flat2(ps, 4), ACT.Sigmoid).then_inc(sig_ready, 1)
                    a.wait_ge(h_ready, n + 1)
                    a.dma_start(m["h1"][n], b[f"h{j}"]).then_inc(h_stored[j], 16)
                    a.wait_ge(rest_ready, n + 1)
                    a.dma_start(m["rest"][n], b[f"rest{j}"]).then_inc(r_stored[j], 16)
            for q in h_stored + r_stored:
                a.wait_ge(q, 16 * (NT // 2))

        @block.vector
        def _(v):
            v.sem_inc(taken, 2)
            c0 = Chain(v, steps)
            v.wait_ge(weights, 16 * 7)
            c0.did(v.tensor_scalar(ga, ga, ALPHA, None, ALU.mult))
            c0.step(v.tensor_scalar(ba, ba, ALPHA, None, ALU.mult))
            per = 6

            def norm(it, j):
                n = it * 2 + j
                c = Chain(v, steps, n * per + c0.n)
                v.wait_ge(x_loaded[j], it * 16 + 16)
                v.wait_ge(h_ready, n)
                c.step(v.tensor_tensor(work, b[f"xh{j}"], ga, ALU.mult))
                c.step(v.tensor_tensor(work, work, ba, ALU.add))
                v.wait_ge(made, n + 3)
                v.tensor_tensor(work, work, flat2(ps, 0), ALU.add).then_inc(taken, 1)
                v.wait_ge(taken, n + 3)
                stats_of(core, c, v, st, mv, work).then_inc(var_ready, 1)
                v.wait_ge(rstd_ready, n + 1)
                c.step(v.tensor_scalar(work, work, mv[:, 0:1], rstd, ALU.subtract, ALU.mult))
                c.step(v.tensor_tensor(work, work, g1, ALU.mult))
                v.wait_ge(h_stored[j], it * 16)
                v.tensor_tensor(b[f"h{j}"], work, b1, ALU.add).then_inc(h_ready, 1)
                assert c.n == per

            def residual(it, j):
                n = it * 2 + j
                v.wait_ge(routed, n + 1)
                v.tensor_copy(m["logits"][:, bass.ds(it * (2 * NE) + j * NE, NE)], ps[:, 2, 0:NE])\
                 .then_inc(kept, 1)
                v.wait_ge(sig_ready, n + 1)
                v.wait_ge(ple_made, n + 1)
                v.wait_ge(r_stored[j], it * 16)
                v.tensor_tensor(b[f"rest{j}"], b["sig"], flat2(ps, 6), ALU.mult).then_inc(e_taken, 1)
                v.wait_ge(e_taken, n + 1)
                v.scalar_tensor_tensor(b[f"rest{j}"], b[f"h{j}"], ALPHA, b[f"rest{j}"],
                                       ALU.mult, ALU.add).then_inc(rest_ready, 1)

            norm(0, 0)
            with v.Fori(0, NT // 2 - 1) as it:
                norm(it, 1)
                residual(it, 0)
                norm(it + 1, 0)
                residual(it, 1)
            last = NT // 2 - 1
            norm(last, 1)
            residual(last, 0)
            residual(last, 1)



def first_best(c, v, out, x, rank, peak, tmp, n):
    shape = list(x.shape)
    spread = lambda t: t.unsqueeze(2).to_broadcast(shape)
    c.step(v.tensor_reduce(peak, x, AX, ALU.max))
    c.step(v.tensor_tensor(tmp, x, spread(peak), ALU.is_equal))
    c.step(v.tensor_tensor(tmp, tmp, rank.unsqueeze(1).to_broadcast(shape), ALU.mult))
    c.step(v.tensor_reduce(peak, tmp, AX, ALU.max))
    c.step(v.tensor_tensor(out, tmp, spread(peak), ALU.is_equal))


def route(core, m):
    nc, ps = core.nc, core.ps
    sem = lambda n: core.semaphore("rt_" + n)
    (sig, steps, picked, counted, cleared, ready, listed, tok_loaded, tok_f, tok_turned,
     zeroed) = map(
        sem, ("sig", "steps", "picked", "counted", "cleared", "ready", "listed", "tok_loaded",
              "tok_f", "tok_turned", "zeroed"))
    at = m["free"]

    def take(*shape):
        nonlocal at
        n = int(np.prod(shape))
        at += n
        return core.place(at - n, *shape)

    aff, sel, tmp, selm, oh1, oh2, pick, rank = (take(NT, NE) for _ in range(8))
    pair, gs = take(NT * NG), take(NT * NG)
    keep, gtmp = take(NT, NG), take(NT, NG)
    peak, wk, off = take(NT), take(NT, 2), take(NT + 1, NE)
    nb, pend, pstart = take(NE), take(NE), take(NE)
    cmp = take(NBLK, NE)
    blk, need, slot = take(NBLK), take(NBLK), take(NBLK)
    dest = take(2, NT)
    rowsf = take(P)
    spread_t = lambda t: t.unsqueeze(1).to_broadcast([P, NT, NE])
    fl = lambda t: t.rearrange("p a b -> p (a b)")
    quads = lambda t: fl(t).rearrange("p (q e) -> p q e", e=EPG)
    toks = m["slot_token_rows"]
    with nc.Block() as block:
        @block.vector
        def _(v):
            c = Chain(v, steps)
            v.wait_ge(sig, 1)
            c.step(v.tensor_tensor(sel, aff, spread_t(core.col("bias_r")), ALU.add))
            q = quads(sel)
            first = True
            for x in range(EPG):
                for y in range(x + 1, EPG):
                    dst = gs if first else pair
                    c.step(v.tensor_tensor(dst, q[:, :, x], q[:, :, y], ALU.add))
                    if not first:
                        c.step(v.tensor_tensor(gs, gs, pair, ALU.max))
                    first = False
            first_best(c, v, keep, gs.rearrange("p (t g) -> p t g", g=NG), core.col("order4"), peak, gtmp, NG)
            kb = fl(keep)
            c.step(v.tensor_scalar(pair, kb, BIG, -BIG, ALU.mult, ALU.add))
            wide = lambda t: t.unsqueeze(2).to_broadcast([P, NT * NG, EPG])
            c.step(v.tensor_tensor(quads(selm), quads(sel), wide(kb), ALU.mult))
            c.step(v.tensor_tensor(quads(selm), quads(selm), wide(pair), ALU.add))
            first_best(c, v, oh1, selm, core.col("low16"), peak, tmp, NE)
            c.step(v.tensor_scalar(tmp, oh1, -BIG, None, ALU.mult))
            c.step(v.tensor_tensor(selm, selm, tmp, ALU.add))
            first_best(c, v, oh2, selm, core.col("low16"), peak, tmp, NE)
            v.tensor_tensor(pick, oh1, oh2, ALU.add).then_inc(picked, 1)
            for i, oh in enumerate((oh1, oh2)):
                c.step(v.tensor_tensor(tmp, aff, oh, ALU.mult))
                c.step(v.tensor_reduce(wk[:, :, i], tmp, AX, ALU.add))
            c.step(v.tensor_tensor(peak, wk[:, :, 0], wk[:, :, 1], ALU.add))
            c.step(v.reciprocal(peak, peak))
            c.step(v.tensor_tensor(m["weights"].rearrange("p (a b) -> p a b", b=2), wk,
                                   peak.unsqueeze(2).to_broadcast([P, NT, 2]), ALU.mult))
            v.wait_ge(counted, 1)
            tot = ps[:, 1, 0:P].rearrange("p (a b) -> p a b", b=NE)
            c.step(v.memset(off[:, 0, :], 0.0))
            for i in range(NT):
                c.step(v.tensor_tensor(off[:, i + 1, :], off[:, i, :], tot[:, i, :], ALU.add))
            c.did(v.tensor_tensor(fl(rank), fl(off[:, 0:NT, :]), ps[:, 0, 0:P], ALU.add))
            c.step(v.tensor_scalar(nb, off[:, NT, :], 0.0, None, ALU.is_gt))
            for i in range(1, NT):
                c.step(v.scalar_tensor_tensor(nb, off[:, NT, :], float(P * i), nb, ALU.is_gt, ALU.add))
            c.step(v.tensor_tensor_scan(pend, core.col("ones", 0, NE), nb, 0.0, ALU.mult, ALU.add))
            c.step(v.tensor_tensor(pstart, pend, nb, ALU.subtract))
            c.step(v.tensor_scalar(pstart, pstart, float(P), None, ALU.mult))
            c.step(v.tensor_tensor(rank, rank, spread_t(pstart), ALU.add))
            for i, oh in enumerate((oh1, oh2)):
                c.step(v.tensor_tensor(tmp, rank, oh, ALU.mult))
                c.step(v.tensor_reduce(dest[:, i, :], tmp, AX, ALU.add))
            c.step(v.tensor_copy(m["dest"], fl(dest)))
            v.tensor_copy(m["token"], core.col("token")).then_inc(ready, 1)
            c.step(v.tensor_tensor(cmp, pend.unsqueeze(1).to_broadcast([P, NBLK, NE]),
                                   core.col("block0", 0, NBLK).unsqueeze(2).to_broadcast([P, NBLK, NE]),
                                   ALU.is_le))
            c.step(v.tensor_reduce(blk, cmp, AX, ALU.add))
            c.step(v.tensor_scalar(blk, blk, float(NE - 1), None, ALU.min))
            c.step(v.memset(need[:, 0:1], 1.0))
            c.step(v.tensor_tensor(need[:, 1:], blk[:, 1:], blk[:, 0:NBLK - 1], ALU.not_equal))
            c.step(v.tensor_tensor_scan(slot, need, core.col("zeros", 0, NBLK), 0.0,
                                        ALU.not_equal, ALU.add))
            for i, x in enumerate((blk, need, slot)):
                c.did(v.tensor_copy(m["plan"][:, i * NBLK:(i + 1) * NBLK], x))
            v.wait_ge(tok_loaded, 16)
            v.tensor_copy(rowsf[0:NBLK], toks).then_inc(tok_f, 1)
            v.wait_ge(tok_turned, 1)
            c.did(v.tensor_copy(m["slot_token"], ps[:, 2, 0:NBLK]))

        @block.tensor
        def _(pe):
            pe.wait_ge(picked, 1)
            pe.matmul(ps[:, 0, 0:P], core.col("before"), fl(pick), start=True, stop=True)
            pe.matmul(ps[:, 1, 0:P], core.col("ones"), fl(pick), start=True, stop=True).then_inc(counted, 1)
            pe.wait_ge(tok_f, 1)
            pe.transpose(ps[:, 2, 0:NBLK], rowsf[0:NBLK], core.col("ident")[0:NBLK, 0:NBLK])\
              .then_inc(tok_turned, 1)

        @block.scalar
        def _(a):
            a.activation(fl(aff), m["logits"], ACT.Sigmoid).then_inc(sig, 1)

        @block.sync
        def _(sp):
            sp.wait_ge(zeroed, 1)
            sp.dma_start(m["slot_dram"].rearrange("(a b) c -> a (b c)", b=P), m["zero_i"][0:NBLK])\
              .then_inc(cleared, 16)
            sp.wait_ge(listed, 16 * 2 * NT)
            sp.dma_start(toks, m["slot_dram"].rearrange("(a b) c -> a (b c)", b=P)).then_inc(tok_loaded, 16)
            sp.wait_ge(tok_loaded, 16)

        @block.gpsimd
        def _(g):
            g.memset(m["zero_i"], 0).then_inc(zeroed, 1)
            g.wait_ge(cleared, 16)
            g.wait_ge(ready, 1)
            for i in range(NT):
                for j in range(2):
                    x = j * NT + i
                    g.indirect_dma_start(m["slot_dram"], bass.IndirectOffsetOnAxis(
                        ap=m["dest"][:, x:x + 1], axis=0), m["token"][:, i:i + 1], None).then_inc(listed, 16)
            g.wait_ge(listed, 16 * 2 * NT)


def grouped_experts(core, m):
    nc, ps = core.nc, core.ps
    sem = lambda n: core.semaphore("e1_" + n)
    NU, NS, W = 4, 6, 2 * D
    loaded = [sem(f"slab{s}") for s in range(NS)]
    high_made = {True: sem("high_up"), False: sem("high_down")}
    low_made = {True: sem("low_up"), False: sem("low_down")}
    used = {True: sem("up_used"), False: sem("down_used")}
    (gathered, picked, x_turned, x_high, x_low, silu_done, h_ready, h_turned, h_high, h_low,
     y_taken, y_stored) = map(sem, (
         "gathered", "picked", "x_turned", "x_high", "x_low", "silu_done", "h_ready", "h_turned",
         "h_high", "h_low", "y_taken", "y_stored"))
    at = m["low"]

    def take(*shape, dt=None):
        nonlocal at
        n = int(np.prod(shape))
        at += n
        return core.place(at - n, *shape, dt=dt)

    raw = [take(W) for _ in range(NS)]
    x, yo = take(D), take(D)
    sg, h = take(FE), take(FE)
    idx = take(1, dt=I32)
    at = UPPER
    high, low = ([take(W) for _ in range(NS)] for _ in range(2))
    xT = take(ND, P), take(ND, P)
    hT = take(4, P), take(4, P)
    plan = m["plan"]
    fl = lambda t: t.rearrange("p a b -> p (a b)")
    slabs = {True: range(0, NU), False: range(NU, NS)}

    def count(up, j, s):
        return j * NU + s + 1 if up else j * (NS - NU) + (s - NU) + 1

    with nc.Block() as block:
        @block.sync
        def _(sp):
            def load(j, up):
                e = sp.value_load(plan[0:1, bass.ds(j, 1)], min_val=0, max_val=NE - 1)
                need = sp.value_load(plan[0:1, bass.ds(j + NBLK, 1)], min_val=0, max_val=1)
                src = core.ins["exp_up_k"] if up else core.ins["exp_down_k"]
                for s in slabs[up]:
                    c = (s - slabs[up][0]) * W
                    sp.wait_ge(low_made[up], count(up, j, s))
                    core.waited(sp)
                    sp.dma_start(raw[s], src[bass.ds(e, 1), :, c:c + W].rearrange("a p n -> (a p) n"),
                                 cond=need, bounds_check="skip_entire_dma").then_inc(loaded[s], 16)

            load(0, True)
            with sp.Fori(0, NBLK - 1) as j:
                load(j + 1, True)
                load(j, False)
            load(NBLK - 1, False)
            for q in loaded:
                sp.wait_ge(q, 16 * NBLK)

        @block.gpsimd
        def _(g):
            def gather(j):
                g.wait_ge(x_turned, j)
                g.wait_ge(gathered, j * 16)
                core.waited(g)
                g.tensor_copy(idx, m["slot_token"][:, bass.ds(j, 1)]).then_inc(picked, 1)
                g.wait_ge(picked, j + 1)
                core.waited(g)
                g.indirect_dma_start(x, None, m["h1_rows"], bass.IndirectOffsetOnAxis(ap=idx, axis=0))\
                 .then_inc(gathered, 16)

            def store_y(j):
                g.wait_ge(y_taken, j + 1)
                core.waited(g)
                g.dma_start(m["y1"][j], yo).then_inc(y_stored, 16)

            gather(0)
            gather(1)
            gather(2)
            with g.Fori(1, NBLK - 2) as j:
                gather(j + 2)
                store_y(j - 1)
            for j in range(NBLK - 3, NBLK):
                store_y(j)
            g.wait_ge(y_stored, 16 * NBLK)

        @block.tensor
        def _(pe):
            def turn_x(j):
                pe.wait_ge(gathered, j * 16 + 16)
                pe.wait_ge(x_low, j)
                for k in range(ND):
                    t = pe.transpose(ps[:, 2 + k // 4, (k % 4) * P:(k % 4 + 1) * P],
                                     x[:, k * P:(k + 1) * P], core.col("ident"))
                t.then_inc(x_turned, 1)

            def products(j, up, act, bank):
                ks = 2 * len(slabs[up])
                for s in slabs[up]:
                    pe.wait_ge(low_made[up], count(up, j, s) + len(slabs[up]))
                    for k in range(2):
                        kk = 2 * (s - slabs[up][0]) + k
                        for c in range(2):
                            here = slice(k * D + c * HALF, k * D + (c + 1) * HALF)
                            t = three_passes(pe, ps[:, bank + c, :], (act[0][:, kk, :], act[1][:, kk, :]),
                                             (high[s][:, here], low[s][:, here]), kk == 0, kk == ks - 1)
                    t.then_inc(used[up], 1)

            def up(j):
                pe.wait_ge(x_low, j + 1)
                pe.wait_ge(h_ready, j)
                products(j, True, xT, 0)

            def turn_h(j):
                pe.wait_ge(h_ready, j + 1)
                pe.wait_ge(h_low, j)
                for k in range(4):
                    t = pe.transpose(ps[:, 4, k * P:(k + 1) * P], h[:, k * P:(k + 1) * P], core.col("ident"))
                t.then_inc(h_turned, 1)

            def down(j):
                pe.wait_ge(h_low, j + 1)
                pe.wait_ge(y_taken, j)
                products(j, False, hT, 5)

            turn_x(0)
            up(0)
            turn_x(1)
            turn_h(0)
            with pe.Fori(1, NBLK - 1) as j:
                up(j)
                turn_x(j + 1)
                down(j - 1)
                turn_h(j)
            last = NBLK - 1
            up(last)
            down(last - 1)
            turn_h(last)
            down(last)

        @block.scalar
        def _(a):
            def split(j, s):
                up = s < NU
                a.wait_ge(loaded[s], j * 16 + 16)
                a.wait_ge(used[up], count(up, j - 1, s) if not isinstance(j, int) or j else 0)
                a.activation(rounded(high[s]), raw[s], ACT.Copy).then_inc(high_made[up], 1)

            def move_x(j):
                a.wait_ge(x_turned, j + 1)
                a.wait_ge(used[True], j * NU)
                a.activation(rounded(fl(xT[0])), flat2(ps, 2), ACT.Copy).then_inc(x_high, 1)

            def silu(j):
                a.wait_ge(used[True], count(True, j, NU - 1))
                a.wait_ge(h_ready, j)
                a.activation(sg, ps[:, 0, :], ACT.Silu).then_inc(silu_done, 1)

            move_x(0)
            for s in range(NU):
                split(0, s)

            def take_y(j):
                a.wait_ge(used[False], count(False, j, NS - 1))
                a.wait_ge(y_stored, j * 16)
                a.activation(yo, flat2(ps, 5), ACT.Copy).then_inc(y_taken, 1)

            def step(j, more):
                if more:
                    for s in range(NU - 1):
                        split(j + 1, s)
                silu(j)
                if more:
                    split(j + 1, NU - 1)
                    move_x(j + 1)
                if not isinstance(j, int) or j:
                    take_y(j - 1)
                for s in range(NU, NS):
                    split(j, s)

            step(0, True)
            with a.Fori(1, NBLK - 1) as j:
                step(j, True)
            step(NBLK - 1, False)
            take_y(NBLK - 1)

        @block.vector
        def _(v):
            v.sem_inc(low_made[True], NU)
            v.sem_inc(low_made[False], NS - NU)

            def split(j, s):
                up = s < NU
                v.wait_ge(high_made[up], count(up, j, s))
                v.tensor_tensor(rounded(low[s]), raw[s], plain(high[s]), ALU.subtract).then_inc(low_made[up], 1)

            def move_x(j):
                v.wait_ge(x_high, j + 1)
                v.tensor_tensor(rounded(fl(xT[1])), flat2(ps, 2), plain(fl(xT[0])), ALU.subtract).then_inc(x_low, 1)

            def gate(j):
                v.wait_ge(silu_done, j + 1)
                v.wait_ge(h_turned, j)
                v.tensor_tensor(h, sg, ps[:, 1, :], ALU.mult).then_inc(h_ready, 1)

            def move_h(j):
                v.wait_ge(h_turned, j + 1)
                v.wait_ge(used[False], j * (NS - NU))
                v.tensor_copy(rounded(fl(hT[0])), ps[:, 4, :]).then_inc(h_high, 1)
                v.wait_ge(h_high, j + 1)
                v.tensor_tensor(rounded(fl(hT[1])), ps[:, 4, :], plain(fl(hT[0])), ALU.subtract).then_inc(h_low, 1)

            move_x(0)
            for s in range(NU):
                split(0, s)

            def step(j, more):
                if more:
                    for s in range(NU - 1):
                        split(j + 1, s)
                gate(j)
                if more:
                    split(j + 1, NU - 1)
                    move_x(j + 1)
                for s in range(NU, NS):
                    split(j, s)
                move_h(j)

            step(0, True)
            with v.Fori(1, NBLK - 1) as j:
                step(j, True)
            step(NBLK - 1, False)



def prepare_columns(core, m):
    nc = core.nc
    sem = lambda n: core.semaphore("pc_" + n)
    loaded, steps, exped, lam = map(sem, ("loaded", "steps", "exped", "lam"))
    mod = m["mod"]
    cols = m["mod_cols"]
    tiny = m["tiny"]
    tmp = core.place(m["free"], HD2)
    with nc.Block() as block:
        @block.sync
        def _(sp):
            with nc.allow_non_contiguous_dma(reason="four vectors of 1024 as columns, once"):
                for i, (row, part) in enumerate(((0, 0), (0, 1), (1, 0), (1, 1))):
                    sp.dma_start(cols[:, i * ND:(i + 1) * ND],
                                 mod[row, part * D:(part + 1) * D].rearrange("(k p) -> p k", p=P))\
                      .then_inc(loaded, 16)
            sp.wait_ge(loaded, 16 * 4)

        @block.vector
        def _(v):
            c = Chain(v, steps)
            lams = core.col("lams")
            for i in range(2):
                c.step(v.tensor_tensor(tmp, lams[:, 2 * i * HD2:(2 * i + 1) * HD2],
                                       lams[:, (2 * i + 1) * HD2:(2 * i + 2) * HD2], ALU.mult))
                c.step(v.tensor_reduce(tiny[:, i:i + 1], tmp, AX, ALU.add))
            v.tensor_copy(tiny[:, 2:4], tiny[:, 0:2]).then_inc(lam, 1)
            v.wait_ge(exped, 1)
            c.step(v.tensor_tensor(m["neg_lam"], tiny[:, 3:4], tiny[:, 2:3], ALU.subtract))
            c.step(v.tensor_scalar(m["neg_lam"], m["neg_lam"], -LAM_INIT, None, ALU.add))
            v.wait_ge(loaded, 16 * 4)
            for i in range(2):
                sc = cols[:, (2 * i + 1) * ND:(2 * i + 2) * ND]
                c.step(v.scalar_tensor_tensor(sc, sc, 1.0, core.col("pre_mix"), ALU.add, ALU.mult))

        @block.scalar
        def _(a):
            a.wait_ge(lam, 1)
            a.activation(tiny[:, 2:4], tiny[:, 2:4], ACT.Exp).then_inc(exped, 1)


def context_input(core, m):
    nc, ps, xnT = core.nc, core.ps, m["xnT"]
    sem = lambda n: core.semaphore("cx_" + n)
    loaded, squared, rooted, scaled, turned, moved, pool_steps = map(sem, (
        "loaded", "squared", "rooted", "scaled", "turned", "moved", "pool_steps"))
    at = m["free"]
    x = core.place(at, NTC, D)
    sq = core.place(at + NTC * D, D)
    ss, rs = core.place(at + (NTC + 1) * D, NTC), core.place(at + (NTC + 1) * D + 4, NTC)
    cols = m["mod_cols"]
    with nc.Block() as block:
        @block.sync
        def _(sp):
            sp.dma_start(x, core.ins["ctx"].rearrange("o (i p) d -> p (o i) d", p=P)).then_inc(loaded, 16)

        @block.scalar
        def _(a):
            a.wait_ge(loaded, 16)
            for i in range(NTC):
                a.activation(sq, x[:, i, :], ACT.Square, accum_out=ss[:, i:i + 1]).then_inc(squared, 1)
                a.wait_ge(squared, i + 1)
            for i in range(NTC):
                for k in range(ND):
                    if k % 4 == 0:
                        a.wait_ge(turned, 2 * i + k // 4 + 1)
                    a.activation(xnT[:, k, S + i * P:S + (i + 1) * P],
                                 ps[:, 2 * i + k // 4, (k % 4) * P:(k % 4 + 1) * P], ACT.Identity,
                                 scale=cols[:, 3 * ND + k:3 * ND + k + 1],
                                 bias=cols[:, 2 * ND + k:2 * ND + k + 1]).then_inc(moved, 1)

        @block.gpsimd
        def _(g):
            g.wait_ge(squared, NTC)
            inverse_root(Chain(g, pool_steps), g, core, rs, ss, 1.0 / D, RMS2_EPS).then_inc(rooted, 1)

        @block.vector
        def _(v):
            v.wait_ge(rooted, 1)
            for i in range(NTC):
                v.tensor_scalar(x[:, i, :], x[:, i, :], rs[:, i:i + 1], None, ALU.mult).then_inc(scaled, 1)

        @block.tensor
        def _(pe):
            for i in range(NTC):
                pe.wait_ge(scaled, i + 1)
                for k in range(ND):
                    t = pe.transpose(ps[:, 2 * i + k // 4, (k % 4) * P:(k % 4 + 1) * P],
                                     x[:, i, k * P:(k + 1) * P], core.col("ident"))
                    if k % 4 == 3:
                        t.then_inc(turned, 1)


def combine_experts(core, m):
    nc, ps, xnT = core.nc, core.ps, m["xnT"]
    sem = lambda n: core.semaphore("ce_" + n)
    r_loaded = [sem(f"r{i}") for i in range(2)]
    h_stored = [sem(f"h_stored{i}") for i in range(2)]
    gathered = [sem(f"y{i}") for i in range(2)]
    (weights, picked, summed, var_ready, rstd_ready, h_ready, squared, rs_ready, scaled, turned,
     moved, steps, pool_steps) = map(sem, (
         "weights", "picked", "summed", "var", "rstd", "h_ready", "squared", "rs_ready", "scaled",
         "turned", "moved", "steps", "pool_steps"))
    at = m["free"]

    def take(*shape, dt=None):
        nonlocal at
        n = int(np.prod(shape))
        if at < UPPER < at + n:
            at = UPPER
        at += n
        return core.place(at - n, *shape, dt=dt)

    g2, b2, sq, xr = (take(D) for _ in range(4))
    work, rest, h = ([take(D), take(D)] for _ in range(3))
    y = [[take(D), take(D)], [take(D), take(D)]]
    st, mv, rstd, ss, rs = ([take(n) for _ in range(2)] for n in (12, 2, 1, 1, 1))
    idx = [[take(1, dt=I32), take(1, dt=I32)] for _ in range(2)]
    cols = m["mod_cols"]
    last = NT // 2 - 1
    with nc.Block() as block:
        @block.sync
        def _(sp):
            sp.dma_start(g2, row_on_all(core.ins["ln2_g"], D)).then_inc(weights, 16)
            sp.dma_start(b2, row_on_all(core.ins["ln2_b"], D)).then_inc(weights, 16)
            with sp.Fori(0, NT // 2) as it:
                for j in range(2):
                    sp.wait_ge(summed, it * 2 + j + 1)
                    sp.dma_start(rest[j], m["rest"][it * 2 + j]).then_inc(r_loaded[j], 16)

        @block.gpsimd
        def _(g):
            def gather(it, j):
                n = it * 2 + j
                g.wait_ge(summed, n + 1)
                for i in range(2):
                    core.waited(g)
                    g.tensor_copy(idx[j][i], m["dest"][:, bass.ds(it * 2 + (j + i * NT), 1)])\
                     .then_inc(picked, 1)
                    g.wait_ge(picked, n * 2 + i + 1)
                    core.waited(g)
                    g.indirect_dma_start(y[j][i], None, m["y1_rows"], bass.IndirectOffsetOnAxis(
                        ap=idx[j][i], axis=0)).then_inc(gathered[j], 16)

            def norm_root(c, it, j):
                g.wait_ge(var_ready, it * 2 + j + 1)
                inverse_root(c, g, core, rstd[j], mv[j][:, 1:2], 1.0, LN_EPS).then_inc(rstd_ready, 1)

            def rms_root(c, it, j):
                g.wait_ge(squared, it * 2 + j + 1)
                inverse_root(c, g, core, rs[j], ss[j], 1.0 / D, RMS2_EPS).then_inc(rs_ready, 1)

            gather(0, 0)
            gather(0, 1)
            norm_root(Chain(g, pool_steps), 0, 0)
            with g.Fori(0, last) as it:
                c = Chain(g, pool_steps, it * 4 + 1)
                norm_root(c, it, 1)
                gather(it + 1, 0)
                rms_root(c, it, 0)
                norm_root(c, it + 1, 0)
                gather(it + 1, 1)
                rms_root(c, it, 1)
            c = Chain(g, pool_steps, last * 4 + 1)
            norm_root(c, last, 1)
            rms_root(c, last, 0)
            rms_root(c, last, 1)

        @block.vector
        def _(v):
            v.sem_inc(summed, 2)
            v.sem_inc(h_ready, 2)
            v.wait_ge(weights, 32)
            w = m["weights"]

            def combine(c, it, j):
                n = it * 2 + j
                v.wait_ge(r_loaded[j], it * 16 + 16)
                v.wait_ge(gathered[j], it * 32 + 32)
                v.wait_ge(h_ready, n + 1)
                c.step(v.scalar_tensor_tensor(work[j], y[j][0], w[:, bass.ds(it * 4 + 2 * j, 1)], rest[j],
                                              ALU.mult, ALU.add))
                v.scalar_tensor_tensor(work[j], y[j][1], w[:, bass.ds(it * 4 + (2 * j + 1), 1)], work[j],
                                       ALU.mult, ALU.add).then_inc(summed, 1)
                v.wait_ge(summed, n + 3)
                stats_of(core, c, v, st[j], mv[j], work[j]).then_inc(var_ready, 1)

            def norm(c, it, j):
                n = it * 2 + j
                v.wait_ge(rstd_ready, n + 1)
                c.step(v.tensor_scalar(work[j], work[j], mv[j][:, 0:1], rstd[j], ALU.subtract, ALU.mult))
                c.step(v.tensor_tensor(work[j], work[j], g2, ALU.mult))
                v.wait_ge(h_stored[j], it * 16)
                v.wait_ge(scaled, n + 1)
                v.tensor_tensor(h[j], work[j], b2, ALU.add).then_inc(h_ready, 1)

            combine(Chain(v, steps), 0, 0)
            with v.Fori(0, last) as it:
                c = Chain(v, steps, it * 10 + 3)
                combine(c, it, 1)
                norm(c, it, 0)
                combine(c, it + 1, 0)
                norm(c, it, 1)
                assert c.n == 10
            c = Chain(v, steps, last * 10 + 3)
            combine(c, last, 1)
            norm(c, last, 0)
            norm(c, last, 1)

        @block.tensor
        def _(pe):
            with pe.Fori(0, NT) as n:
                pe.wait_ge(scaled, n + 3)
                pe.wait_ge(moved, n)
                for k in range(ND):
                    t = pe.transpose(ps[:, k // 4, (k % 4) * P:(k % 4 + 1) * P],
                                     xr[:, k * P:(k + 1) * P], core.col("ident"))
                t.then_inc(turned, 1)

        @block.scalar
        def _(a):
            a.sem_inc(scaled, 2)

            def square(it, j):
                n = it * 2 + j
                a.wait_ge(h_ready, n + 3)
                a.wait_ge(squared, n)
                a.activation(sq, h[j], ACT.Square, accum_out=ss[j]).then_inc(squared, 1)
                a.dma_start(m["h2"][n], h[j]).then_inc(h_stored[j], 16)

            def scale(it, j):
                n = it * 2 + j
                a.wait_ge(rs_ready, n + 1)
                a.wait_ge(turned, n)
                a.activation(xr, h[j], ACT.Copy, scale=rs[j]).then_inc(scaled, 1)

            def move(it, j):
                a.wait_ge(turned, it * 2 + j + 1)
                core.waited(a)
                for k in range(ND):
                    t = a.activation(xnT[:, k, bass.ds(it * (2 * P) + j * P, P)],
                                     ps[:, k // 4, (k % 4) * P:(k % 4 + 1) * P], ACT.Identity,
                                     scale=cols[:, ND + k:ND + k + 1], bias=cols[:, k:k + 1])
                t.then_inc(moved, 1)

            square(0, 0)
            with a.Fori(0, last) as it:
                scale(it, 0)
                square(it, 1)
                move(it, 0)
                scale(it, 1)
                square(it + 1, 0)
                move(it, 1)
            scale(last, 0)
            square(last, 1)
            move(last, 0)
            scale(last, 1)
            move(last, 1)
            for q in h_stored:
                a.wait_ge(q, 16 * (NT // 2))



def second_projections(core, m):
    nc, ps, xnT = core.nc, core.ps, m["xnT"]
    sem = lambda n: core.semaphore("p2_" + n)
    loaded = [sem(f"w{i}") for i in range(2)]
    high_made = [sem(f"high{i}") for i in range(2)]
    low_made = [sem(f"low{i}") for i in range(2)]
    taken = [sem(f"taken{i}") for i in range(2)]
    done, x_high, x_low, copied = map(sem, ("done", "x_high", "x_low", "copied"))
    w = [core.place(m["free"] + i * D, ND, P) for i in range(2)]
    at = m["split"]
    xh, xl = core.place(at, ND, SA), core.place(at + ND * SA, ND, SA)
    at += 2 * ND * SA
    wh, wl = ([core.place(at + (2 * p + i) * D, ND, P) for i in range(2)] for p in range(2))
    fl = lambda t: t.rearrange("p a b -> p (a b)")
    NPAIR = 12
    latent, both = (HALF, HALF), (HALF, HALF, CTX)
    parts = ((0, 2, m["q"], latent), (2, 4, m["gb"], latent), (4, 8, None, latent),
             (8, 10, m["k"], both), (10, NPAIR, m["v"], both))

    def sections(eng, turn):
        for first, end, dst, widths in parts:
            stop = end - 1 if end == NPAIR else end
            with eng.Fori(first, stop) as i:
                turn(i, dst, first, widths, True)
        turn(NPAIR - 1, dst, first, widths, False)

    with nc.Block() as block:
        @block.sync
        def _(sp):
            for j in range(2):
                sp.dma_start(w[j], core.ins["w_in2_tiles"][j]).then_inc(loaded[j], 16)
            with sp.Fori(1, NPAIR) as i:
                for j in range(2):
                    sp.wait_ge(low_made[j], i)
                    sp.dma_start(w[j], core.ins["w_in2_tiles"][i * 2 + j]).then_inc(loaded[j], 16)

        @block.tensor
        def _(pe):
            pe.wait_ge(x_low, ND)

            def turn(i, dst, first, widths, more):
                nb = len(widths)
                for j in range(2):
                    pe.wait_ge(low_made[j], i + 1)
                    pe.wait_ge(taken[j], i + 1)
                    if dst is m["k"]:
                        pe.wait_ge(taken[1 - j], i + 1 if j == 0 else i + 2)
                    for c, width in enumerate(widths):
                        for k in range(ND):
                            here = slice(c * HALF, c * HALF + width)
                            t = three_passes(pe, ps[:, nb * j + c, 0:width], (wh[j][:, k, :], wl[j][:, k, :]),
                                             (xh[:, k, here], xl[:, k, here]), k == 0, k == ND - 1)
                    t.then_inc(done, 1)

            sections(pe, turn)

        @block.scalar
        def _(a):
            a.sem_inc(taken[0], 1)
            a.sem_inc(taken[1], 1)

            def split(i, j):
                a.wait_ge(loaded[j], i * 16 + 16)
                if not isinstance(i, int):
                    a.wait_ge(done, i * 2 + (j - 1))
                a.activation(rounded(fl(wh[j])), fl(w[j]), ACT.Copy).then_inc(high_made[j], 1)

            for k in range(ND):
                a.activation(rounded(xh[:, k, :]), xnT[:, k, :], ACT.Copy).then_inc(x_high, 1)
            split(0, 0)
            split(0, 1)
            a.wait_ge(x_low, ND)

            def turn(i, dst, first, widths, more):
                nb = len(widths)
                for j in range(2):
                    a.wait_ge(done, i * 2 + j + 1)
                    if dst is not None:
                        core.waited(a)
                        for c, width in enumerate(widths):
                            t = a.activation(dst[:, bass.ds(i * 2 + (j - 2 * first), 1), c * HALF:c * HALF + width],
                                             ps[:, nb * j + c:nb * j + c + 1, 0:width], ACT.Copy)
                        t.then_inc(taken[j], 1)
                    elif j == 0:
                        core.waited(a)
                        for c in range(2):
                            t = a.activation(m["u2"][:, bass.ds(i - first, 1), c * HALF:(c + 1) * HALF],
                                             ps[:, c:c + 1, :], ACT.Copy)
                        t.then_inc(taken[j], 1)
                    if more:
                        split(i + 1, j)

            sections(a, turn)

        @block.vector
        def _(v):
            for k in range(ND):
                v.wait_ge(x_high, k + 1)
                v.tensor_tensor(rounded(xl[:, k, :]), xnT[:, k, :], plain(xh[:, k, :]),
                                ALU.subtract).then_inc(x_low, 1)

            def split(i, j):
                v.wait_ge(high_made[j], i + 1)
                v.tensor_tensor(rounded(fl(wl[j])), fl(w[j]), plain(fl(wh[j])),
                                ALU.subtract).then_inc(low_made[j], 1)

            split(0, 0)
            split(0, 1)

            def turn(i, dst, first, widths, more):
                for j in range(2):
                    if dst is None and j == 1:
                        v.wait_ge(taken[0], i + 2)
                        v.wait_ge(done, i * 2 + 2)
                        for c in range(2):
                            u = m["u2"][:, bass.ds(i - first, 1), c * HALF:(c + 1) * HALF]
                            t = v.tensor_tensor(u, u, ps[:, 2 + c:3 + c, :], ALU.mult)
                        t.then_inc(taken[1], 1)
                    if more:
                        split(i + 1, j)

            sections(v, turn)


def rotate_and_convolve(core, m):
    nc, ps = core.nc, core.ps
    sem = lambda n: core.semaphore("rc_" + n)
    (tables, swapped, sined, cosined, added, v_turned, v_moved, copied, steps) = map(sem, (
        "tables", "swapped", "sined", "cosined", "added", "v_turned", "v_moved", "copied", "steps"))
    q, k, v1, q2, k2, vt, u, gb = (m[n] for n in ("q", "k", "v", "q2", "k2", "v2", "u2", "gb"))
    cos_t, sin_t = core.place(m["tables"], S), core.place(m["tables"] + S, S)
    tmp = [core.place(m["tmp"] + i * S, S) for i in range(2)]
    raw = [q[:, h, :] for h in range(4)] + [k[:, h, 0:S] for h in range(4)]
    dst = [q2[:, h] for h in range(4)] + [k2[:, h] for h in range(4)]
    acc = m["conv2"]
    NU = 8
    with nc.Block() as block:
        @block.sync
        def _(sp):
            sp.dma_start(cos_t, core.ins["cos2"]).then_inc(tables, 16)
            sp.dma_start(sin_t, core.ins["sin2"]).then_inc(tables, 16)

        @block.tensor
        def _(pe):
            for n in range(NU):
                if n >= 2:
                    pe.wait_ge(sined, n - 1)
                for c in range(2):
                    t = pe.matmul(ps[:, 2 * (n % 2) + c, :], core.col("turn"),
                                  raw[n][:, c * HALF:(c + 1) * HALF], start=True, stop=True)
                t.then_inc(swapped, 1)
            for i in range(NK2):
                if i >= 2:
                    pe.wait_ge(v_moved, i - 1)
                for h in range(4):
                    t = pe.transpose(ps[:, 4 + i % 2, h * P:(h + 1) * P],
                                     v1[:, h, i * P:(i + 1) * P], core.col("ident"))
                t.then_inc(v_turned, 1)

        @block.gpsimd
        def _(g):
            g.wait_ge(tables, 32)
            for n in range(NU):
                g.wait_ge(swapped, n + 1)
                g.tensor_tensor(raw[n], raw[n], cos_t, ALU.mult).then_inc(cosined, 1)

        @block.vector
        def _(v):
            c = Chain(v, steps)
            v.wait_ge(tables, 32)
            for n in range(NU):
                v.wait_ge(swapped, n + 1)
                v.tensor_tensor(tmp[n % 2], flat2(ps, 2 * (n % 2)), sin_t, ALU.mult).then_inc(sined, 1)
                v.wait_ge(sined, n + 1)
                v.wait_ge(cosined, n + 1)
                for i in range(2):
                    rows = slice(64 * i, 64 * i + 64)
                    v.tensor_tensor(dst[n][:, i, 0:S], tmp[n % 2][rows], raw[n][rows], ALU.add)\
                     .then_inc(added, 1)
            v.wait_ge(added, 2 * NU)
            wc = lambda h, t: core.col("conv2", 3 * h + t, 3 * h + t + 1)
            for h in range(4):
                src = u[:, h, :]
                c.did(v.tensor_scalar(acc[:, h, :], src, wc(h, 1), None, ALU.mult))
            c.wait()
            for h in range(4):
                src = u[:, h, :]
                c.did(v.scalar_tensor_tensor(acc[:, h, 1:S], src[:, 0:S - 1], wc(h, 0), acc[:, h, 1:S],
                                             ALU.mult, ALU.add))
            c.wait()
            for h in range(4):
                src = u[:, h, :]
                c.did(v.scalar_tensor_tensor(acc[:, h, 0:S - 1], src[:, 1:S], wc(h, 2), acc[:, h, 0:S - 1],
                                             ALU.mult, ALU.add))
            c.wait()
            for h in range(4):
                c.did(v.tensor_tensor(acc[:, h, :], acc[:, h, :], gb[:, h, :], ALU.mult))

        @block.scalar
        def _(a):
            for h in range(4):
                for i in range(2):
                    a.activation(k2[:, h, i, S:SA], k[64 * i:64 * i + 64, h, S:SA], ACT.Copy)\
                     .then_inc(copied, 1)
            a.wait_ge(added, 2 * NU)
            for i in range(NK2):
                a.wait_ge(v_turned, i + 1)
                a.activation(vt[:, i, :], ps[:, 4 + i % 2, :], ACT.Copy).then_inc(v_moved, 1)


def differential_attention(core, m):
    nc, ps, q2, k2, vt = core.nc, core.ps, m["q2"], m["k2"], m["v2"]
    sem = lambda n: core.semaphore("da_" + n)
    (staged, scored, biased, exped, combined, turned, moved, summed, kept, steps) = map(sem, (
        "staged", "scored", "biased", "exped", "combined", "turned", "moved", "summed", "kept", "steps"))
    at = m["free"]

    def take(*shape, parts=P):
        nonlocal at
        n = int(np.prod(shape))
        at += n
        return core.place(at - n, *shape, parts=parts)

    q = [take(2, P, parts=64) for _ in range(2)]
    e = [take(2, SA) for _ in range(2)]
    at = m["free_too"]
    at_ = [take(NK2, P) for _ in range(2)]
    mx, nb, den, co = take(4), take(4), take(4), take(4)
    o = m["o2"]
    kf = k2.rearrange("p a b c -> p (a b c)")
    scale = float(HD2) ** -0.5
    G = NH2 * NT
    GROUPS = ((0, 4), (4, 8), (8, NK2))
    last = G // 2 - 1
    full = ps[:].rearrange("p a b -> p (a b)")

    def where(it, j):
        return it // (NT // 2), (it % (NT // 2)) * 2 + j

    with nc.Block() as block:
        @block.gpsimd
        def _(g):
            def stage(it, j):
                h, i = where(it, j)
                g.wait_ge(scored, (it * 2 + j) * 2 + 2)
                core.waited(g)
                g.tensor_copy(q[j], q2.rearrange("p a b c -> p (a b) c")[
                    :, bass.ds(h * 2, 2), bass.ds(i * P, P)]).then_inc(staged, 1)

            stage(0, 0)
            stage(0, 1)
            with g.Fori(0, last) as it:
                for j in range(2):
                    stage(it + 1, j)

        @block.tensor
        def _(pe):
            pe.sem_inc(scored, 4)
            pe.sem_inc(turned, 6)
            pe.sem_inc(summed, 2)

            def scores(it, j, i):
                g = it * 2 + j
                h, _ = where(it, j)
                pe.wait_ge(staged, g + 1)
                pe.wait_ge(exped, g * 2 + i + 1)
                for c, wd in enumerate((HALF, HALF, CTX)):
                    t = pe.matmul(ps[:, 3 * i + c, 0:wd], q[j][:, i, :],
                                  kf[:, bass.ds(h * (2 * SA) + (i * SA + c * HALF), wd)],
                                  start=True, stop=True, skip_group_check=True)
                    if c == 0:
                        yield
                t.then_inc(scored, 1)

            def turn(it, j, r):
                g = it * 2 + j
                lo, hi = GROUPS[r]
                if r == 0:
                    pe.wait_ge(combined, g + 1)
                pe.wait_ge(moved, g * 3 + r + 1)
                if r == 1:
                    pe.wait_ge(kept, g + 2)
                for t in range(lo, hi):
                    ins = pe.transpose(ps[:, 6 + (j * 3 + r) % 2, (t - lo) * P:(t - lo + 1) * P],
                                       e[j][:, 1, t * P:(t + 1) * P], core.col("ident"))
                ins.then_inc(turned, 1)

            def sums(it, j):
                g = it * 2 + j
                h, _ = where(it, j)
                pe.wait_ge(moved, g * 3 + 5)
                for t in range(NK2):
                    ins = pe.matmul(ps[:, 6 + j, CTX:CTX + P], at_[j][:, t, :],
                                    vt[:, t, bass.ds(h * P, P)], start=(t == 0), stop=(t == NK2 - 1),
                                    skip_group_check=True)
                ins.then_inc(summed, 1)

            def step(it, j, nxt):
                if nxt:
                    for _ in scores(*nxt, 0):
                        pass
                turn(it, j, 0)
                turn(it, j, 1)
                if nxt:
                    for _ in scores(*nxt, 1):
                        turn(it, j, 2)
                else:
                    turn(it, j, 2)
                sums(it, j)

            for i in range(2):
                for _ in scores(0, 0, i):
                    pass
            with pe.Fori(0, last) as it:
                step(it, 0, (it, 1))
                step(it, 1, (it + 1, 0))
            step(last, 0, (last, 1))
            step(last, 1, None)

        @block.vector
        def _(v):
            v.sem_inc(kept, 2)
            per = 6

            def bias(c, it, j):
                g = it * 2 + j
                for i in range(2):
                    x = 2 * j + i
                    v.wait_ge(scored, g * 2 + i + 5)
                    c.step(v.reduce_max(mx[:, x:x + 1], full[:, 3 * i * HALF:3 * i * HALF + SA], AX))
                    v.tensor_scalar(nb[:, x:x + 1], mx[:, x:x + 1], -scale, None, ALU.mult).then_inc(biased, 1)

            def first(c, it, j):
                x = 2 * j
                v.wait_ge(exped, (it * 2 + j) * 2 + 3)
                c.step(v.reciprocal(co[:, x:x + 1], den[:, x:x + 1]))
                c.step(v.tensor_scalar(e[j][:, 0, :], e[j][:, 0, :], co[:, x:x + 1], None, ALU.mult))

            def combine(c, it, j):
                x = 2 * j + 1
                v.wait_ge(exped, (it * 2 + j) * 2 + 4)
                c.step(v.reciprocal(co[:, x:x + 1], den[:, x:x + 1]))
                c.step(v.tensor_tensor(co[:, x:x + 1], co[:, x:x + 1], m["neg_lam"], ALU.mult))
                v.scalar_tensor_tensor(e[j][:, 1, :], e[j][:, 1, :], co[:, x:x + 1], e[j][:, 0, :],
                                       ALU.mult, ALU.add).then_inc(combined, 1)

            def keep(it, j):
                g = it * 2 + j
                h, i = where(it, j)
                v.wait_ge(summed, g + 3)
                v.tensor_copy(o.rearrange("p a b -> p (a b)")[:, bass.ds(i * (NH2 * P) + h * P, P)],
                              ps[:, 6 + j, CTX:CTX + P]).then_inc(kept, 1)

            c = Chain(v, steps)
            bias(c, 0, 0)
            first(c, 0, 0)
            combine(c, 0, 0)
            bias(c, 0, 1)
            first(c, 0, 1)
            before = c.n
            with v.Fori(0, last) as it:
                c = Chain(v, steps, it * (2 * per) + before)
                combine(c, it, 1)
                keep(it, 0)
                bias(c, it + 1, 0)
                first(c, it + 1, 0)
                combine(c, it + 1, 0)
                keep(it, 1)
                bias(c, it + 1, 1)
                first(c, it + 1, 1)
                assert c.n == 2 * per
            c = Chain(v, steps, last * 2 * per + before)
            combine(c, last, 1)
            keep(last, 0)
            keep(last, 1)

        @block.scalar
        def _(a):
            a.sem_inc(exped, 2)
            a.sem_inc(moved, 2)

            def exp(it, j, i):
                g = it * 2 + j
                x = 2 * j + i
                a.wait_ge(biased, g * 2 + i + 1)
                a.wait_ge(turned, g * 3 + 3)
                a.activation(e[j][:, i, :], full[:, 3 * i * HALF:3 * i * HALF + SA], ACT.Exp,
                             bias=nb[:, x:x + 1], scale=scale, accum_out=den[:, x:x + 1]).then_inc(exped, 1)

            def move(it, j, r):
                g = it * 2 + j
                lo, hi = GROUPS[r]
                a.wait_ge(turned, g * 3 + r + 7)
                a.wait_ge(summed, g + 1)
                a.activation(at_[j].rearrange("p a b -> p (a b)")[:, lo * P:hi * P],
                             ps[:, 6 + (j * 3 + r) % 2, 0:(hi - lo) * P], ACT.Copy).then_inc(moved, 1)

            def step(it, j, nxt):
                move(it, j, 0)
                move(it, j, 1)
                if nxt:
                    exp(*nxt, 0)
                move(it, j, 2)
                if nxt:
                    exp(*nxt, 1)

            exp(0, 0, 0)
            exp(0, 0, 1)
            with a.Fori(0, last) as it:
                step(it, 0, (it, 1))
                step(it, 1, (it + 1, 0))
            step(last, 0, (last, 1))
            step(last, 1, None)


def attention_output(core, m):
    nc, ps, o, oT = core.nc, core.ps, m["o2"], m["o2T"]
    sem = lambda n: core.semaphore("ao_" + n)
    squared, reduced, rooted, normed, turned, moved, pool_steps = map(sem, (
        "squared", "reduced", "rooted", "normed", "turned", "moved", "pool_steps"))
    sq = core.place(m["free"], NT * NH2, P)
    ss = core.place(m["free"] + NT * NH2 * P, NT * NH2)
    rs = core.place(m["free"] + NT * NH2 * P + 64, NT * NH2)
    rows = o.rearrange("p a (h e) -> p (a h) e", e=P)
    with nc.Block() as block:
        @block.sync
        def _(sp):
            sp.dma_start(m["wr2"], core.ins["w_router2_k"]).then_inc(m["wo2_loaded"], 16)
            sp.dma_start(m["wo2"], core.ins["w_out2_k"]).then_inc(m["wo2_loaded"], 16)
            for i, part in enumerate((2, 3, 4, 5)):
                sp.dma_start(m["rows"][i], row_on_all(m["mod"][0, part * D:(part + 1) * D], D))\
                  .then_inc(m["rows_loaded"], 16)
            for i, name in enumerate(("norm_post_mix", "norm_pre_ffn", "norm_post_ffn")):
                sp.dma_start(m["rows"][4 + i], row_on_all(core.ins[name], D)).then_inc(m["rows_loaded"], 16)

        @block.scalar
        def _(a):
            a.activation(sq, rows, ACT.Square).then_inc(squared, 1)
            for i in range(NT):
                a.wait_ge(turned, i + 1)
                a.activation(oT[:, :, i * P:(i + 1) * P],
                             ps[:, i % 2, :].rearrange("p (a b) -> p a b", b=P), ACT.Copy).then_inc(moved, 1)

        @block.vector
        def _(v):
            v.wait_ge(squared, 1)
            v.tensor_reduce(ss, sq, AX, ALU.add).then_inc(reduced, 1)
            v.wait_ge(rooted, 1)
            for i in range(NT):
                r = rows[:, NH2 * i:NH2 * (i + 1), :]
                s_ = rs[:, NH2 * i:NH2 * (i + 1)].unsqueeze(2).to_broadcast([P, NH2, P])
                v.tensor_tensor(r, r, s_, ALU.mult).then_inc(normed, 1)
                v.wait_ge(normed, 2 * i + 1)
                v.scalar_tensor_tensor(r, r, 1.0 - LAM_INIT,
                                       core.col("subln").unsqueeze(1).to_broadcast([P, NH2, P]),
                                       ALU.mult, ALU.mult).then_inc(normed, 1)

        @block.gpsimd
        def _(g):
            g.wait_ge(reduced, 1)
            c = Chain(g, pool_steps)
            for i in range(4):
                t = inverse_root(c, g, core, rs[:, 8 * i:8 * i + 8], ss[:, 8 * i:8 * i + 8], 1.0 / P, RMS2_EPS)
                if i < 3:
                    c.did(t)
                else:
                    t.then_inc(rooted, 1)

        @block.tensor
        def _(pe):
            for i in range(NT):
                pe.wait_ge(normed, 2 * i + 2)
                if i >= 2:
                    pe.wait_ge(moved, i - 1)
                for h in range(NH2):
                    t = pe.transpose(ps[:, i % 2, h * P:(h + 1) * P], o[:, i, h * P:(h + 1) * P],
                                     core.col("ident"))
                t.then_inc(turned, 1)


def mix_output(core, m):
    nc, ps = core.nc, core.ps
    sem = lambda n: core.semaphore("mo_" + n)
    h_loaded = [sem(f"h{i}") for i in range(2)]
    h_stored = [sem(f"h_stored{i}") for i in range(2)]
    x_stored = [sem(f"x_stored{i}") for i in range(2)]
    (zeroed, staged, made, squared, rooted, taken, h_ready, h_squared, h_rooted, x_ready,
     turned, moved, routed, kept, steps, pool_steps, ff_cleared) = map(sem, (
         "zeroed", "staged", "made", "squared", "rooted", "taken", "h_ready",
         "h_squared", "h_rooted", "x_ready", "turned", "moved", "routed", "kept", "steps",
         "pool_steps", "ff_cleared"))
    row_steps = sem("row_steps")
    at = m["free"]

    def take(*shape):
        nonlocal at
        n = int(np.prod(shape))
        at += n
        return core.place(at - n, *shape)

    wo, wr, weights = m["wo2"], m["wr2"], m["wo2_loaded"]
    mt = [take(ND, P) for _ in range(2)]
    hin, h, xn = ([take(D) for _ in range(2)] for _ in range(3))
    xT, sq, t, zero = take(ND, P), take(D), take(D), take(D)
    ss, rs, hs, hr = (take(1) for _ in range(4))
    g1, sh2, sc2 = m["rows"][0:3]
    with nc.Block() as block:
        @block.sync
        def _(sp):
            with sp.Fori(0, NT // 2) as it:
                for j in range(2):
                    sp.wait_ge(h_ready, it * 2 + j + 1)
                    sp.dma_start(hin[j], m["h2"][it * 2 + j]).then_inc(h_loaded[j], 16)
            sp.wait_ge(zeroed, 1)
            for i in range(NT):
                sp.dma_start(m["ff"][i], zero).then_inc(ff_cleared, 16)
            sp.wait_ge(ff_cleared, 16 * NT)

        @block.gpsimd
        def _(g):
            g.memset(zero, 0.0).then_inc(zeroed, 1)

            def stage(it, j):
                g.wait_ge(made, it * 2 + j + 1)
                core.waited(g)
                for i, src in ((0, m["o2T"]), (4, m["conv2"])):
                    g.tensor_copy(mt[j][:, i:i + 4, :], src[:, :, bass.ds(it * (2 * P) + j * P, P)])\
                     .then_inc(staged, 1)

            def roots(it, j):
                n = it * 2 + j
                c = Chain(g, pool_steps, n * 2)
                g.wait_ge(squared, n + 1)
                inverse_root(c, g, core, rs, ss, 1.0 / D, RMS2_EPS).then_inc(rooted, 1)
                g.wait_ge(h_squared, n + 1)
                inverse_root(c, g, core, hr, hs, 1.0 / D, RMS2_EPS).then_inc(h_rooted, 1)

            stage(0, 0)
            with g.Fori(0, NT // 2 - 1) as it:
                stage(it, 1)
                roots(it, 0)
                stage(it + 1, 0)
                roots(it, 1)
            last = NT // 2 - 1
            stage(last, 1)
            roots(last, 0)
            roots(last, 1)

        @block.tensor
        def _(pe):
            pe.sem_inc(made, 2)
            pe.wait_ge(weights, 32)

            def product(it, j):
                n = it * 2 + j
                pe.wait_ge(staged, n * 2 + 2)
                pe.wait_ge(taken, n + 1)
                for c in range(2):
                    for k in range(ND):
                        x = pe.matmul(ps[:, 2 * j + c, :], mt[j][:, k, :],
                                      wo[:, k, c * HALF:(c + 1) * HALF], start=(k == 0), stop=(k == ND - 1))
                x.then_inc(made, 1)

            def after(it, j):
                n = it * 2 + j
                pe.wait_ge(x_ready, n + 1)
                for k in range(ND):
                    x = pe.transpose(ps[:, 4 + k // 4, (k % 4) * P:(k % 4 + 1) * P],
                                     xn[j][:, k * P:(k + 1) * P], core.col("ident"))
                x.then_inc(turned, 1)
                pe.wait_ge(moved, n + 1)
                pe.wait_ge(kept, n)
                for k in range(ND):
                    x = pe.matmul(ps[:, 6, 0:NE], xT[:, k, :], wr[:, k, :], start=(k == 0), stop=(k == ND - 1))
                x.then_inc(routed, 1)

            product(0, 0)
            with pe.Fori(0, NT // 2 - 1) as it:
                product(it, 1)
                after(it, 0)
                product(it + 1, 0)
                after(it, 1)
            last = NT // 2 - 1
            product(last, 1)
            after(last, 0)
            after(last, 1)

        @block.scalar
        def _(a):
            with a.Fori(0, NT // 2) as it:
                for j in range(2):
                    n = it * 2 + j
                    a.wait_ge(made, n + 3)
                    a.wait_ge(h_squared, n)
                    a.activation(sq, flat2(ps, 2 * j), ACT.Square, accum_out=ss).then_inc(squared, 1)
                    a.wait_ge(h_ready, n + 3)
                    a.wait_ge(squared, n + 1)
                    a.activation(sq, h[j], ACT.Square, accum_out=hs).then_inc(h_squared, 1)
                    a.dma_start(m["h3"][n], h[j]).then_inc(h_stored[j], 16)
                    a.wait_ge(x_ready, n + 1)
                    a.dma_start(m["xn"][n], xn[j]).then_inc(x_stored[j], 16)
                    a.wait_ge(turned, n + 1)
                    a.wait_ge(routed, n)
                    a.activation(xT.rearrange("p a b -> p (a b)"), flat2(ps, 4), ACT.Copy).then_inc(moved, 1)
            for q in h_stored + x_stored:
                a.wait_ge(q, 16 * (NT // 2))

        @block.vector
        def _(v):
            v.sem_inc(taken, 2)
            v.sem_inc(h_ready, 2)
            per = 1
            v.wait_ge(m["rows_loaded"], 16 * 7)
            c = Chain(v, row_steps)
            c.did(v.tensor_tensor(g1, g1, m["rows"][4], ALU.mult))
            c.did(v.scalar_tensor_tensor(sc2, sc2, 1.0, m["rows"][5], ALU.add, ALU.mult))
            c.step(v.tensor_tensor(m["rows"][3], m["rows"][3], m["rows"][6], ALU.mult))

            def step(it, j):
                n = it * 2 + j
                c = Chain(v, steps, n * per)
                v.wait_ge(x_ready, n)
                v.wait_ge(rooted, n + 1)
                v.scalar_tensor_tensor(t, flat2(ps, 2 * j), rs, g1, ALU.mult, ALU.mult).then_inc(taken, 1)
                v.wait_ge(taken, n + 3)
                v.wait_ge(h_loaded[j], it * 16 + 16)
                v.wait_ge(h_stored[j], it * 16)
                v.tensor_tensor(h[j], t, hin[j], ALU.add).then_inc(h_ready, 1)
                v.wait_ge(h_rooted, n + 1)
                v.wait_ge(h_ready, n + 3)
                c.step(v.scalar_tensor_tensor(t, h[j], hr, sc2, ALU.mult, ALU.mult))
                v.wait_ge(x_stored[j], it * 16)
                v.tensor_tensor(xn[j], t, sh2, ALU.add).then_inc(x_ready, 1)
                assert c.n == per
                v.wait_ge(routed, n + 1)
                v.tensor_copy(m["logits2"][:, bass.ds(it * (2 * NE) + j * NE, NE)], ps[:, 6, 0:NE])\
                 .then_inc(kept, 1)

            with v.Fori(0, NT // 2) as it:
                step(it, 0)
                step(it, 1)



RING = 4
SLABS = ND + NDN


def expert_choice(core, m):
    nc, ps = core.nc, core.ps
    sem = lambda n: core.semaphore("ec_" + n)
    centred, exped, ready, turned, steps, chosen, back = map(sem, (
        "centred", "exped", "ready", "turned", "steps", "chosen", "back"))
    at = m["free"]
    aff = core.place(at, NT, NE)
    peak = core.place(at + P, NT)
    affT = core.place(at + 2 * P, S, parts=NE)
    val = core.place(at + 2 * P + S, CAP, parts=NE)
    idx = core.place(at + 3 * P + S, CAP, parts=NE, dt=mybir.dt.uint32)
    idf = core.place(at + 4 * P + S, CAP, parts=NE)
    fl = aff.rearrange("p a b -> p (a b)")
    spread = peak.unsqueeze(2).to_broadcast([P, NT, NE])
    with nc.Block() as block:
        @block.sync
        def _(sp):
            for k in range(RING):
                sp.dma_start(m["ring"][k], core.ins["gate_up2"][k]).then_inc(m["ring_loaded"][k], 16)

        @block.vector
        def _(v):
            c = Chain(v, steps)
            lg = m["logits2"].rearrange("p (a b) -> p a b", b=NE)
            c.step(v.tensor_reduce(peak, lg, AX, ALU.max))
            v.tensor_tensor(aff, lg, spread, ALU.subtract).then_inc(centred, 1)
            v.wait_ge(exped, 1)
            c.step(v.tensor_reduce(peak, aff, AX, ALU.add))
            c.step(v.reciprocal(peak, peak))
            v.tensor_tensor(aff, aff, spread, ALU.mult).then_inc(ready, 1)
            v.wait_ge(turned, 1)
            c.step(v.tensor_copy(affT, flat2(ps, 0)[0:NE]))
            for r in range(CAP // 8):
                best, where = val[:, 8 * r:8 * r + 8], idx[:, 8 * r:8 * r + 8]
                c.step(v.max(best, affT))
                c.step(v.max_index(where, best, affT))
                c.step(v.match_replace(affT, best, affT, -1.0))
            v.tensor_copy(idf, idx).then_inc(chosen, 1)
            v.wait_ge(back, 1)
            c.did(v.tensor_copy(m["ec_weight"], ps[:, 2, 0:NE]))
            c.did(v.tensor_copy(m["ec_token"], ps[:, 3, 0:NE]))

        @block.scalar
        def _(a):
            a.wait_ge(centred, 1)
            a.activation(fl, fl, ACT.Exp).then_inc(exped, 1)

        @block.tensor
        def _(pe):
            pe.wait_ge(ready, 1)
            for i in range(NT):
                t = pe.transpose(ps[0:NE, i // 4, (i % 4) * P:(i % 4 + 1) * P], aff[:, i, :], core.col("ident"))
            t.then_inc(turned, 1)
            pe.wait_ge(chosen, 1)
            pe.transpose(ps[:, 2, 0:NE], val, core.col("ident")[0:NE, 0:NE])
            pe.transpose(ps[:, 3, 0:NE], idf, core.col("ident")[0:NE, 0:NE]).then_inc(back, 1)


def chosen_experts(core, m):
    nc, ps = core.nc, core.ps
    sem = lambda n: core.semaphore("e2_" + n)
    raw, loaded = m["ring"], m["ring_loaded"]
    (high_made, low_made, used, x_staged, gathered, x_turned, x_high, x_low, silu_done, h_ready,
     h_turned, h_high, h_low, y_ready, y_staged, added) = map(sem, (
         "high", "low", "used", "x_staged", "gathered", "x_turned", "x_high", "x_low", "silu_done",
         "h_ready", "h_turned", "h_high", "h_low", "y_ready", "y_staged", "added"))
    at = m["free"]

    def take(*shape, dt=None):
        nonlocal at
        n = int(np.prod(shape))
        at += n
        return core.place(at - n, *shape, dt=dt)

    x, sg, h, yo = take(D), take(FE2), take(FE2), take(D)
    xi, yi = take(1, dt=I32), take(1, dt=I32)
    at = m["split"]
    high, low = ([take(2 * D) for _ in range(RING)] for _ in range(2))
    xT, hT = ((take(ND, P), take(ND, P)) for _ in range(2))
    token = m["ec_token"]
    fl = lambda t: t.rearrange("p a b -> p (a b)")
    last = NE - 1

    def up_slab(e, k):
        if isinstance(e, int) and e == 0:
            return k, k // RING + 1
        return e * SLABS + (k - NDN), e * (SLABS // RING) + k // RING

    def down_slab(e, k):
        if isinstance(e, int) and e == last:
            return e * SLABS + (SLABS - NDN + k), e * (SLABS // RING) + SLABS // RING
        return e * SLABS + (SLABS + NDN + k), e * (SLABS // RING) + (SLABS // RING + 2)

    with nc.Block() as block:
        @block.sync
        def _(sp):
            def load(src, n, k):
                sp.wait_ge(low_made, n[0] - (RING - 1))
                sp.dma_start(raw[k % RING], src).then_inc(loaded[k % RING], 16)

            def up(e, first=0):
                for k in range(first, ND):
                    load(core.ins["gate_up2"][e * ND + k], up_slab(e, k), k)

            def down(e):
                for k in range(NDN):
                    load(core.ins["down2"][e * NDN + k], down_slab(e, k), k)

            up(0, RING)
            with sp.Fori(1, NE) as e:
                up(e)
                down(e - 1)
            down(last)

        @block.gpsimd
        def _(g):
            def gather(e):
                g.wait_ge(x_turned, e)
                g.wait_ge(gathered, e * 16)
                g.tensor_copy(xi, token[:, bass.ds(e, 1)]).then_inc(x_staged, 1)
                g.wait_ge(x_staged, e + 1)
                core.waited(g)
                g.indirect_dma_start(x, None, m["xn_rows"], bass.IndirectOffsetOnAxis(ap=xi, axis=0))\
                 .then_inc(gathered, 16)

            def add(e):
                g.wait_ge(added, e * 16)
                g.tensor_copy(yi, token[:, bass.ds(e, 1)]).then_inc(y_staged, 1)
                g.wait_ge(y_staged, e + 1)
                g.wait_ge(y_ready, e + 1)
                core.waited(g)
                g.indirect_dma_start(m["ff_rows"], bass.IndirectOffsetOnAxis(ap=yi, axis=0), yo, None,
                                     compute_op=ALU.add).then_inc(added, 16)

            gather(0)
            gather(1)
            with g.Fori(2, NE) as e:
                gather(e)
                add(e - 2)
            add(NE - 2)
            add(NE - 1)
            g.wait_ge(added, 16 * NE)

        @block.tensor
        def _(pe):
            def turn_x(e):
                pe.wait_ge(gathered, e * 16 + 16)
                if not isinstance(e, int):
                    pe.wait_ge(h_low, e - 1)
                for k in range(ND):
                    t = pe.transpose(ps[:, 4 + k // 4, (k % 4) * P:(k % 4 + 1) * P],
                                     x[:, k * P:(k + 1) * P], core.col("ident"))
                t.then_inc(x_turned, 1)

            def up(e):
                pe.wait_ge(x_low, e + 1)
                pe.wait_ge(h_ready, e)
                for k in range(ND):
                    pe.wait_ge(low_made, up_slab(e, k)[0] + 1)
                    for c in range(4):
                        here = slice(c * HALF, (c + 1) * HALF)
                        t = three_passes(pe, ps[:, c, :], (xT[0][:, k, :], xT[1][:, k, :]),
                                         (high[k % RING][:, here], low[k % RING][:, here]),
                                         k == 0, k == ND - 1)
                    t.then_inc(used, 1)

            def turn_h(e):
                pe.wait_ge(h_ready, e + 1)
                pe.wait_ge(x_low, NE if isinstance(e, int) and e == last else e + 2)
                for k in range(FE2 // P):
                    t = pe.transpose(ps[:, 4 + k // 4, (k % 4) * P:(k % 4 + 1) * P],
                                     h[:, k * P:(k + 1) * P], core.col("ident"))
                t.then_inc(h_turned, 1)

            def down(e):
                pe.wait_ge(h_low, e + 1)
                pe.wait_ge(y_ready, e)
                for k in range(NDN):
                    pe.wait_ge(low_made, down_slab(e, k)[0] + 1)
                    for kk in (2 * k, 2 * k + 1):
                        for c in range(2):
                            at = (kk % 2) * D + c * HALF
                            t = three_passes(pe, ps[:, 6 + c, :], (hT[0][:, kk, :], hT[1][:, kk, :]),
                                             (high[k][:, at:at + HALF], low[k][:, at:at + HALF]),
                                             kk == 0, kk == FE2 // P - 1)
                    t.then_inc(used, 1)

            turn_x(0)
            up(0)
            turn_x(1)
            turn_h(0)
            with pe.Fori(1, last) as e:
                up(e)
                turn_x(e + 1)
                down(e - 1)
                turn_h(e)
            up(last)
            down(last - 1)
            turn_h(last)
            down(last)

        @block.scalar
        def _(a):
            def split(n, k):
                before, fillings = n
                a.wait_ge(loaded[k % RING], fillings * 16)
                if not isinstance(before, int) or before >= RING:
                    a.wait_ge(used, before - (RING - 1))
                a.activation(rounded(high[k % RING]), raw[k % RING], ACT.Copy).then_inc(high_made, 1)

            def up(e):
                for k in range(ND):
                    split(up_slab(e, k), k)

            def down(e):
                for k in range(NDN):
                    split(down_slab(e, k), k)

            def move_x(e):
                a.wait_ge(x_turned, e + 1)
                a.activation(rounded(fl(xT[0])), flat2(ps, 4), ACT.Copy).then_inc(x_high, 1)

            def silu(e):
                a.wait_ge(used, up_slab(e, ND - 1)[0] + 1)
                a.wait_ge(h_ready, e)
                a.activation(sg, flat2(ps, 0), ACT.Silu).then_inc(silu_done, 1)

            move_x(0)
            up(0)
            silu(0)
            move_x(1)
            with a.Fori(1, last) as e:
                up(e)
                down(e - 1)
                silu(e)
                move_x(e + 1)
            up(last)
            down(last - 1)
            silu(last)
            down(last)

        @block.vector
        def _(v):
            def split(n, k):
                v.wait_ge(high_made, n[0] + 1)
                v.tensor_tensor(rounded(low[k % RING]), raw[k % RING], plain(high[k % RING]),
                                ALU.subtract).then_inc(low_made, 1)

            def up(e, ks):
                for k in ks:
                    split(up_slab(e, k), k)

            def down(e):
                for k in range(NDN):
                    split(down_slab(e, k), k)

            def move_x(e):
                v.wait_ge(x_high, e + 1)
                v.tensor_tensor(rounded(fl(xT[1])), flat2(ps, 4), plain(fl(xT[0])),
                                ALU.subtract).then_inc(x_low, 1)

            def gate(e):
                v.wait_ge(silu_done, e + 1)
                v.wait_ge(h_turned, e)
                v.tensor_tensor(h, sg, flat2(ps, 2), ALU.mult).then_inc(h_ready, 1)

            def move_h(e):
                v.wait_ge(h_turned, e + 1)
                v.tensor_copy(rounded(fl(hT[0])), flat2(ps, 4)).then_inc(h_high, 1)
                v.wait_ge(h_high, e + 1)
                v.tensor_tensor(rounded(fl(hT[1])), flat2(ps, 4), plain(fl(hT[0])),
                                ALU.subtract).then_inc(h_low, 1)

            def weigh(e):
                v.wait_ge(used, down_slab(e, NDN - 1)[0] + 1)
                v.wait_ge(added, e * 16)
                v.tensor_scalar(yo, flat2(ps, 6), m["ec_weight"][:, bass.ds(e, 1)], None,
                                ALU.mult).then_inc(y_ready, 1)

            def turn(e, weighed, nxt):
                up(e, range(RING))
                move_h(e - 1)
                if weighed:
                    weigh(e - 2)
                up(e, range(RING, ND))
                down(e - 1)
                gate(e)
                if nxt:
                    move_x(e + 1)

            move_x(0)
            up(0, range(ND))
            gate(0)
            move_x(1)
            turn(1, False, True)
            with v.Fori(2, last) as e:
                turn(e, True, True)
            turn(last, True, False)
            move_h(last)
            weigh(last - 1)
            down(last)
            weigh(last)


def last_residual(core, m):
    nc = core.nc
    sem = lambda n: core.semaphore("lr_" + n)
    NB = 4
    loaded = [sem(f"loaded{i}") for i in range(NB)]
    squared, rooted, ready, stored, pool_steps, scaled = map(sem, (
        "squared", "rooted", "ready", "stored", "pool_steps", "scaled"))
    at = m["free"]
    ff = [core.place(at + 2 * i * D, D) for i in range(NT)]
    h = [core.place(at + (2 * i + 1) * D, D) for i in range(NT)]
    sq = core.place(at + 2 * NT * D, D)
    ss, rs = core.place(at + (2 * NT + 1) * D, NT), core.place(at + (2 * NT + 1) * D + NT, NT)
    g2 = m["rows"][3]
    out = core.out.rearrange("o (i p) d -> (o i) p d", p=P)
    with nc.Block() as block:
        @block.sync
        def _(sp):
            for i in range(NT):
                sp.dma_start(ff[i], m["ff"][i]).then_inc(loaded[i % NB], 16)
                sp.dma_start(h[i], m["h3"][i]).then_inc(loaded[i % NB], 16)
                if i % NB == NB - 1 and i < NT - 1:
                    for q in loaded:
                        sp.wait_ge(q, 32 * (i // NB + 1))
            for i in range(NT):
                sp.wait_ge(ready, i + 1)
                sp.dma_start(out[i], h[i]).then_inc(stored, 16)
            sp.wait_ge(stored, 16 * NT)

        @block.scalar
        def _(a):
            for i in range(NT):
                a.wait_ge(loaded[i % NB], 32 * (i // NB + 1))
                if i:
                    a.wait_ge(squared, i)
                a.activation(sq, ff[i], ACT.Square, accum_out=ss[:, i:i + 1]).then_inc(squared, 1)

        @block.gpsimd
        def _(g):
            c = Chain(g, pool_steps)
            for i in range(NT):
                g.wait_ge(squared, i + 1)
                inverse_root(c, g, core, rs[:, i:i + 1], ss[:, i:i + 1], 1.0 / D, RMS2_EPS).then_inc(rooted, 1)

        @block.vector
        def _(v):
            for i in range(NT):
                v.wait_ge(rooted, i + 1)
                v.wait_ge(loaded[i % NB], 32 * (i // NB + 1))
                v.scalar_tensor_tensor(ff[i], ff[i], rs[:, i:i + 1], g2, ALU.mult, ALU.mult).then_inc(scaled, 1)
                v.wait_ge(scaled, i + 1)
                v.tensor_tensor(h[i], h[i], ff[i], ALU.add).then_inc(ready, 1)



def build(nc, ins, out):
    with ExitStack() as ctx:
        core = Core(nc, ctx, ins, out)
        small = NCOLS

        def keep(*shape, **kw):
            nonlocal small
            n = int(np.prod(shape))
            small += n
            assert small <= BASE, small
            return core.place(small - n, *shape, **kw)

        def at(x):
            return BASE + x

        def run(stage, *args):
            stage(core, *args)

        dram = core.scratch
        m = {
            "xhat": dram("xhat", [NT, P, D]), "h1": dram("h1", [NT, P, D]),
            "rest": dram("rest", [NT, P, D]), "qn": dram("q_nope", [4, P, S]),
            "qr": dram("q_rope", [2, P, S]), "kn": dram("k_nope", [4, P, S]),
            "kr": dram("k_rope", [ROPE, S]), "mod": dram("modulation", [2, 6 * D]),
            "slot_dram": dram("slot_token", [NBLK * P, 1], I32), "y1": dram("y1", [NBLK, P, D]),
            "h2": dram("h2", [NT, P, D]), "h3": dram("h3", [NT, P, D]), "xn": dram("xn", [NT, P, D]),
            "ff": dram("ff", [NT, P, D]), "merged": dram("merged", [ND, P, S]),
            "logits": keep(P), "weights": keep(2 * NT), "dest": keep(2 * NT, dt=I32),
            "token": keep(NT, dt=I32), "plan": keep(3 * NBLK, dt=I32),
            "slot_token": keep(NBLK, dt=I32), "slot_token_rows": keep(P, parts=NBLK, dt=I32),
            "zero_i": keep(P, dt=I32), "mod_cols": keep(4 * ND), "tiny": keep(4), "neg_lam": keep(1),
            "logits2": keep(P), "ec_weight": keep(NE), "ec_token": keep(NE, dt=I32),
        }
        for name in ("h1", "y1", "xn", "ff"):
            m[name + "_rows"] = m[name].rearrange("a p d -> (a p) d")

        m["hT"] = core.place(at(0), ND, S)
        m["u"] = core.place(at(8192), 4, PADU + S)
        m["z"] = core.place(at(12352), 4, PADZ + S)
        m["acc"] = core.place(at(16576), 4, S)
        m["poolT"] = m["u"][:, :, PADU:]
        m["oT"] = core.place(at(12352), 4, S)
        run(load_constants)
        with ExitStack() as own:
            core.open_upper(own, "upper_norm")
            run(norm_and_modulation, at(8192), m["xhat"], m["hT"], UPPER, m["mod"])
        lat_end = at(29056)
        kind = ExitStack()
        core.open_upper(kind, "upper_latent", F32, UPPER, lat_end)
        m["lat"] = core.place(UPPER, 6, S)
        m["w_at"], m["acc_at"], m["split"] = UPPER + 6 * S, at(16576), lat_end
        with ExitStack() as own:
            core.open_upper(own, "upper_split_in", F32R, lat_end)
            run(first_projections, m)
        core.open_upper(kind, "upper_heads", F32, lat_end)
        m["vt"] = core.place(lat_end, NT, HALF)
        m["free"] = lat_end + NT * HALF
        run(heads_and_branches, m)
        run(conv_finish, m)
        run(latent_attention, m)
        kind.close()
        core.regions = {}
        with ExitStack() as kind:
            m["hT_at"], m["free"], m["split"] = at(0), UPPER, at(27008)
            core.open_upper(kind, "upper_merge", F32, UPPER, at(27008))
            core.open_upper(kind, "upper_split_h", F32R, at(27008))
            run(merge, m)
        core.regions = {}
        kind = ExitStack()
        core.open_upper(kind, "upper_output")
        m["low"], m["high"] = at(0), at(37056)
        run(output_and_gate, m)
        m["free"] = at(0)
        core.free_semaphores()
        run(route, m)
        kind.close()
        with ExitStack() as kind:
            core.open_upper(kind, "upper_split", F32R)
            run(grouped_experts, m)

        middle = at(24960)
        core.open_upper(ctx, "upper_middle", F32, UPPER, middle)
        m["free"] = at(0)
        run(prepare_columns, m)
        m["xnT"] = core.place(at(0), ND, SA)
        m["free"] = at(10240)
        run(context_input, m)
        run(combine_experts, m)
        m["q"] = core.place(at(0), 4, S)
        m["u2"] = core.place(at(4096), 4, S)
        m["k"] = core.place(at(8192), 4, SA)
        m["v"] = core.place(at(13312), 4, SA)
        m["gb"] = core.place(UPPER, 4, S)
        m["free"], m["split"] = at(18432), middle
        with ExitStack() as kind:
            core.open_upper(kind, "upper_split_xn", F32R, middle)
            run(second_projections, m)
        kind = ExitStack()
        core.open_upper(kind, "upper_second", F32, middle)
        m["q2"] = core.place(middle, 4, 2, S, parts=64)
        m["k2"] = core.place(at(33152), 4, 2, SA, parts=64)
        m["tables"], m["tmp"] = at(43392), at(45440)
        m["v2"] = core.place(at(8192), NK2, HALF)
        m["conv2"] = core.place(at(0), 4, S)
        core.free_semaphores()
        run(rotate_and_convolve, m)
        m["free"], m["free_too"] = at(13312), at(43392)
        m["o2"] = core.place(at(4096), NT, HALF)
        run(differential_attention, m)
        m["o2T"] = core.place(UPPER, 4, S)
        m["rows"] = [core.place(at(8192 + i * D), D) for i in range(7)]
        m["wo2"] = core.place(at(41216), ND, D)
        m["wr2"] = core.place(at(41088), ND, NE)
        m["wo2_loaded"], m["rows_loaded"] = map(core.semaphore, ("wo2_loaded", "rows_loaded"))
        m["free"] = middle
        run(attention_output, m)
        run(mix_output, m)
        m["ring"] = [core.place(at(12288 + k * 2 * D), 2 * D) for k in range(RING)]
        m["ring_loaded"] = [core.semaphore(f"e2_ring{k}") for k in range(RING)]
        m["free"] = at(4352)
        run(expert_choice, m)
        kind.close()
        m["free"], m["split"] = at(0), middle
        with ExitStack() as kind:
            core.open_upper(kind, "upper_split_experts", F32R, middle)
            run(chosen_experts, m)
        core.open_upper(ctx, "upper_last", F32, middle)
        m["free"] = middle
        run(last_residual, m)


def columns(a, n):
    return np.asarray(a).reshape(n, P).T


def constants(f):
    part = np.arange(P)
    c = {name: np.zeros((P, n), np.float32) for name, (_, n) in COLS.items()}
    c["ident"][:] = np.eye(P)
    c["ones"][:] = 1
    c["before"][:] = part[:, None] < part[None, :]
    other = (part // 32) * 32 + (part % 32 + 16) % 32
    c["swap"][other, part] = 1
    c["turn"][other, part] = np.where(part % 32 < 16, -1, 1)
    c["sin_sign"][:, 0] = np.where(part % 32 < 16, -1, 1)
    freq = (10000.0 ** (-np.arange(0, ROPE, 2) / ROPE)).astype(np.float32)
    c["inv_freq"][:, 0] = freq[part % 16]
    for g, w in enumerate(WINDOWS):
        c["pool_inv"][:, 16 * g:16 * g + 16] = 1.0 / np.minimum(np.arange(16) + 1, w)
    c["low16"][:] = NE - np.arange(NE)
    c["order4"][:] = NG - np.arange(NG)
    c["block0"][:] = np.arange(NBLK + 1)
    c["token"][:] = np.arange(NT)[None, :] * P + part[:, None]
    c["neg_half"][:] = -0.5
    c["eps_rms"][:] = RMS_EPS
    c["eps_ln"][:] = LN_EPS
    for name, key in (("ln_in_g", "ln_in_g"), ("ln_in_b", "ln_in_b"), ("conv_b", "conv_b"),
                      ("conv_ln_g", "conv_ln_g"), ("conv_ln_b", "conv_ln_b"),
                      ("pool_scale", "pool_scale"), ("q_norm", "q_norm_g"), ("kv_norm", "kv_norm_g"),
                      ("pre_mix", "norm_pre_mix_2"), ("c", "c_2"), ("c_ctx", "c_ctx_2")):
        c[name][:] = columns(f[key], COLS[name][1])
    c["conv_dw"][:] = f["conv_dw"].reshape(TAPS, 4, P).transpose(2, 1, 0).reshape(P, 4 * TAPS)
    c["conv2"][:] = f["conv_w_2"].reshape(3, 4, P).transpose(2, 1, 0).reshape(P, 12)
    c["subln"][:] = f["subln_g_2"].reshape(1, P)
    c["bias_r"][:] = f["router_bias"].reshape(1, NE)
    c["lams"][:] = np.concatenate([f[k].reshape(-1) for k in (
        "lambda_q1_2", "lambda_k1_2", "lambda_q2_2", "lambda_k2_2")])[None, :]
    return np.ascontiguousarray(np.concatenate([c[name] for name in COLS], axis=1))


def by_k(w):
    return w.reshape(-1, P, w.shape[-1]).transpose(1, 0, 2)


def tiles_of(w):
    return w.reshape(ND, P, -1, P).transpose(2, 1, 0, 3)


def kernel(**inputs):
    import concourse.bacc as bacc
    from concourse.bass_utils import run_bass_kernel_spmd

    f = {k: np.asarray(v) for k, v in inputs.items()}
    w_in = f["w_in"][0]
    at = {"pool": 0, "a": 512, "gate": 1024, "cq": 1536, "ckv": 1920, "kr": 2176, "gates": 2208}
    first = []
    for t in range(4):
        first += [w_in[:, at["gate"] + t * P:at["gate"] + (t + 1) * P],
                  w_in[:, at["a"] + t * P:at["a"] + (t + 1) * P]]
    first += [w_in[:, 0:512], w_in[:, at["cq"]:at["kr"] + ROPE], np.zeros((D, P - ROPE), np.float32)]
    uq = f["w_uq"][0].reshape(3 * P, NH1, QD)
    ukv = f["w_ukv"][0].reshape(2 * P, NH1, NOPE + VH)
    w2 = f["w_in_2"][0]
    part = lambda i: w2[:, i * HALF:(i + 1) * HALF]
    mixed = [part(i)[:, t * P:(t + 1) * P] for t in range(4) for i in (4, 5)]
    gates = w_in[:, at["gates"]:].reshape(ND, P, 3, ND, P).transpose(3, 1, 2, 0, 4).reshape(ND, P, 24 * P)
    projs = np.stack([f[k][0] for k in ("pool_proj", "conv_proj", "mla_proj")])
    projs = projs.reshape(3, 4, P, ND, P).transpose(3, 2, 0, 1, 4).reshape(ND, P, 12 * P)
    biases = f["b_gate"][0].reshape(3, ND, P).transpose(1, 2, 0)
    pad = np.zeros((ND, P, 1), np.float32)
    axis = np.arange(S)
    inv = (np.float32(10000.0) ** (-np.arange(0, 32, 2, dtype=np.float32) / np.float32(32))).astype(np.float32)
    row = (axis // 64).astype(np.float32)[:, None] * inv
    colm = (axis % 64).astype(np.float32)[:, None] * inv
    ang = np.concatenate([row, row, colm, colm], axis=1).T
    ang = np.concatenate([ang, ang], axis=0)
    slab = lambda w: w.reshape(NE, ND, P, FE2)
    arrays = {
        "packed": constants(f), "x": f["x"], "ctx": f["ctx_2"], "b_ada": f["b_ada_2"],
        "w_ada": f["w_ada_2"][0].reshape(ND, P, 12, HALF).transpose(2, 1, 0, 3),
        "w_in_tiles": tiles_of(np.concatenate(first, axis=1)),
        "positions": f["positions"].reshape(S),
        "w_uq_k": by_k(np.concatenate([uq[:, :, :NOPE].reshape(3 * P, -1), uq[:, :, NOPE:].reshape(3 * P, -1)],
                                      axis=1)),
        "w_ukv_k": by_k(np.concatenate([ukv[:, :, :NOPE].reshape(2 * P, -1),
                                        ukv[:, :, NOPE:].reshape(2 * P, -1)], axis=1)),
        "pool_w_k": f["pool_w"][0].transpose(1, 0, 2),
        "merge_w": np.concatenate([gates, projs, biases, pad], axis=2),
        "w_out_k": by_k(f["w_out"][0]), "w_router_k": by_k(f["w_router"]),
        "ln_in_g": f["ln_in_g"], "ln_in_b": f["ln_in_b"], "ln1_g": f["ln1_g"][0], "ln1_b": f["ln1_b"][0],
        "ln2_g": f["ln2_g"][0], "ln2_b": f["ln2_b"][0], "norm_post_mix": f["norm_post_mix_2"][0],
        "norm_pre_ffn": f["norm_pre_ffn_2"][0], "norm_post_ffn": f["norm_post_ffn_2"][0],
        "ple_proj_k": by_k(f["ple_proj"][0]), "ple_gate_k": by_k(f["ple_gate"][0]),
        "p_tiles": f["p"].reshape(NT, P, 2 * P),
        "exp_up_k": f["exp_w_up"][0].reshape(NE, ND, P, 2 * FE).transpose(0, 2, 1, 3).reshape(NE, P, -1),
        "exp_down_k": f["exp_w_down"][0].reshape(NE, 4, P, D).transpose(0, 2, 1, 3).reshape(NE, P, -1),
        "w_in2_tiles": tiles_of(np.concatenate([part(0), part(3), *mixed, part(1), part(2)], axis=1)),
        "cos2": np.cos(ang), "sin2": np.sin(ang),
        "w_out2_k": by_k(f["w_out_2"][0]), "w_router2_k": by_k(f["w_router_2"][0]),
        "gate_up2": np.concatenate([slab(f["w_gate_2"][0]), slab(f["w_up_2"][0])], axis=3)
                      .reshape(NE * ND, P, 2 * FE2),
        "down2": f["w_down_2"][0].reshape(NE * 4, 2, P, D).transpose(0, 2, 1, 3).reshape(NE * 4, P, 2 * D),
    }
    arrays = {k: np.ascontiguousarray(v) for k, v in arrays.items()}
    for k, v in arrays.items():
        assert v.dtype == (np.int32 if k == "positions" else np.float32), (k, v.dtype)
    nc = bacc.Bacc("TRN2", target_bir_lowering=False, num_devices=1)
    ins = {k: nc.dram_tensor("in_" + k, v.shape, I32 if v.dtype == np.int32 else F32,
                             kind="ExternalInput").ap() for k, v in arrays.items()}
    out = nc.dram_tensor("out", (1, S, D), F32, kind="ExternalOutput").ap()
    build(nc, ins, out)
    r = run_bass_kernel_spmd(nc, [{"in_" + k: v for k, v in arrays.items()}], core_ids=[0])
    return r.results[0]["out"]
```
